# Optimizing a Trainium2 kernel written in Bass

```python
import math
import jax, jax.numpy as jnp
from jax import lax
import numpy as np

D_MODEL = 1024
BATCH = 1
SEQ = 1024
DEPTH = 2
DEC_BATCH = 8
DEC_SEQ = 1
PAST_LEN = 2048
PAGE_SIZE = 128

HEAD_DIM = 64
CONV_WIDTH = 256
CONV_K = 3
MLA_HEADS = 8
Q_RANK = 256
KV_RANK = 128
QK_NOPE = 64
QK_ROPE = 32
V_DIM = 64
ROPE_THETA = 10000.0
Q_BLOCK = 128
MLSTM_HEADS = 4
MLSTM_DH = 64
MLSTM_WIDTH = MLSTM_HEADS * MLSTM_DH
MLSTM_CHUNK = 64
MIX_WIDTH = CONV_WIDTH + MLA_HEADS * V_DIM + MLSTM_WIDTH
N_MIX_HEADS = MIX_WIDTH // HEAD_DIM
N_IN = 3 * CONV_WIDTH + Q_RANK + KV_RANK + QK_ROPE + 4 * MLSTM_WIDTH + 2 * MLSTM_HEADS
N_GROUPS = 4
EXPERTS_PER_GROUP = 8
N_EXPERTS = N_GROUPS * EXPERTS_PER_GROUP
TOP_K = 2
D_EXPERT = 256
MOE_BLOCK = 128
D_PLE = 256
DN_ALPHA = (2 * DEPTH) ** 0.25
DN_BETA = (8 * DEPTH) ** -0.25
LN_EPS = 1e-5
RMS_EPS = 1e-6

kernel_name = "hymba_conv_mla_mlstm_hmoe_step"

def layer_norm(x, g, b):
    xf = x.astype(jnp.float32)
    mu = jnp.mean(xf, -1, keepdims=True)
    var = jnp.mean(jnp.square(xf - mu), -1, keepdims=True)
    return ((xf - mu) * lax.rsqrt(var + LN_EPS) * g + b).astype(x.dtype)

def rms_norm(x, g):
    xf = x.astype(jnp.float32)
    return (xf * lax.rsqrt(jnp.mean(xf * xf, -1, keepdims=True) + RMS_EPS) * g).astype(x.dtype)

def rope(x, pos):
    half = QK_ROPE // 2
    inv = ROPE_THETA ** (-jnp.arange(half, dtype=jnp.float32) / half)
    ang = pos.astype(jnp.float32)[:, None] * inv
    ang = ang.reshape(ang.shape[:1] + (1,) * (x.ndim - 3) + ang.shape[1:])
    cos, sin = jnp.cos(ang), jnp.sin(ang)
    xf = x.astype(jnp.float32)
    x1, x2 = xf[..., :half], xf[..., half:]
    return jnp.concatenate([x1 * cos - x2 * sin, x1 * sin + x2 * cos], -1).astype(x.dtype)

def short_conv(u, buf, w):
    L = u.shape[1]
    full = jnp.concatenate([buf.astype(u.dtype), u], axis=1)
    y = full[:, 0:L] * w[0]
    for j in range(1, CONV_K):
        y = y + full[:, j:j + L] * w[j]
    return y, full[:, L:]

def mla_prompt_attention(q_nope, q_rope, k_nope, k_rope, v):
    B, S, H, _ = q_nope.shape
    scale = (QK_NOPE + QK_ROPE) ** -0.5
    kpos = jnp.arange(S)

    def block(i):
        qs = i * Q_BLOCK
        qn = lax.dynamic_slice_in_dim(q_nope, qs, Q_BLOCK, axis=1)
        qr = lax.dynamic_slice_in_dim(q_rope, qs, Q_BLOCK, axis=1)
        s = (jnp.einsum('bqhd,bkhd->bhqk', qn, k_nope, preferred_element_type=jnp.float32)
             + jnp.einsum('bqhd,bkd->bhqk', qr, k_rope, preferred_element_type=jnp.float32)) * scale
        qpos = qs + jnp.arange(Q_BLOCK)
        s = jnp.where(kpos[None, :] <= qpos[:, None], s, -jnp.inf)
        p = jax.nn.softmax(s, axis=-1)
        return jnp.einsum('bhqk,bkhd->bqhd', p.astype(v.dtype), v)

    out = lax.map(block, jnp.arange(S // Q_BLOCK))
    return jnp.moveaxis(out, 0, 1).reshape(B, S, H, V_DIM)

def mla_sample_attention(q_nope, q_rope, ckv_all, krope_all, w_uk, w_uv, past_len):
    S = q_nope.shape[1]
    scale = (QK_NOPE + QK_ROPE) ** -0.5
    q_lat = jnp.einsum('bshd,rhd->bshr', q_nope, w_uk)
    s = (jnp.einsum('bshr,bkr->bhsk', q_lat, ckv_all, preferred_element_type=jnp.float32)
         + jnp.einsum('bshd,bkd->bhsk', q_rope, krope_all, preferred_element_type=jnp.float32)) * scale
    kpos = jnp.arange(ckv_all.shape[1])
    qpos = past_len + jnp.arange(S)
    s = jnp.where(kpos[None, :] <= qpos[:, None], s, -jnp.inf)
    p = jax.nn.softmax(s, axis=-1)
    o_lat = jnp.einsum('bhsk,bkr->bshr', p.astype(ckv_all.dtype), ckv_all)
    return jnp.einsum('bshr,rhd->bshd', o_lat, w_uv)

def mlstm_chunkwise(q, k, v, ig, lf, C0, n0, m0):
    B, L, NH, DH = q.shape
    f32 = jnp.float32
    cl = MLSTM_CHUNK if L % MLSTM_CHUNK == 0 else L
    nc = L // cl

    def to_chunks(a):
        a = a.astype(f32).reshape((B, nc, cl) + a.shape[2:])
        return jnp.moveaxis(a, (1, 3), (0, 2))

    qc, kc, vc = to_chunks(q), to_chunks(k.astype(f32) * (DH ** -0.5)), to_chunks(v)
    ic, fc = to_chunks(ig), to_chunks(lf)
    causal = jnp.tril(jnp.ones((cl, cl), bool))

    def step(carry, xs):
        C, n, m = carry
        qb, kb, vb, ib, fb = xs
        b = jnp.cumsum(fb, axis=-1)
        log_d = jnp.where(causal, b[..., :, None] - b[..., None, :] + ib[..., None, :], -jnp.inf)
        m_inter = b + m[..., None]
        m_t = jnp.maximum(m_inter, jnp.max(log_d, axis=-1))
        d = jnp.exp(log_d - m_t[..., None])
        w_inter = jnp.exp(m_inter - m_t)
        s = jnp.einsum('bhtd,bhsd->bhts', qb, kb) * d
        num = jnp.einsum('bhts,bhsv->bhtv', s, vb) + w_inter[..., None] * jnp.einsum('bhvd,bhtd->bhtv', C, qb)
        den = jnp.sum(s, -1) + w_inter * jnp.einsum('bhd,bhtd->bht', n, qb)
        h = num / jnp.maximum(jnp.abs(den), jnp.exp(-m_t))[..., None]
        m_new = m_t[..., -1]
        w_old = jnp.exp(b[..., -1] + m - m_new)
        w_s = jnp.exp(b[..., -1:] - b + ib - m_new[..., None])
        C_new = w_old[..., None, None] * C + jnp.einsum('bhs,bhsv,bhsd->bhvd', w_s, vb, kb)
        n_new = w_old[..., None] * n + jnp.einsum('bhs,bhsd->bhd', w_s, kb)
        return (C_new, n_new, m_new), h

    (C, n, m), h = lax.scan(step, (C0.astype(f32), n0.astype(f32), m0.astype(f32)), (qc, kc, vc, ic, fc))
    h = jnp.moveaxis(h, (0, 2), (1, 3)).reshape(B, L, NH, DH)
    return h, C.astype(C0.dtype), n.astype(n0.dtype), m.astype(m0.dtype)

def grouped_experts(xf, expert_idx, expert_w, e_gate, e_up, e_down):
    T, D = xf.shape
    A = T * TOP_K
    flat_e = expert_idx.reshape(A)
    flat_t = jnp.repeat(jnp.arange(T, dtype=jnp.int32), TOP_K)
    flat_w = expert_w.reshape(A)
    order = jnp.argsort(flat_e)
    se = flat_e[order]
    counts = jnp.bincount(flat_e, length=N_EXPERTS)
    padded = (counts + MOE_BLOCK - 1) // MOE_BLOCK * MOE_BLOCK
    pad_end = jnp.cumsum(padded)
    pad_start = pad_end - padded
    start = jnp.cumsum(counts) - counts
    dest = pad_start[se] + jnp.arange(A) - start[se]
    n_blocks = -(-A // MOE_BLOCK) + N_EXPERTS
    n_rows = n_blocks * MOE_BLOCK
    row_tok = jnp.full((n_rows,), T, jnp.int32).at[dest].set(flat_t[order])
    row_w = jnp.zeros((n_rows,), xf.dtype).at[dest].set(flat_w[order].astype(xf.dtype))
    blk_expert = jnp.minimum(jnp.searchsorted(pad_end, jnp.arange(n_blocks) * MOE_BLOCK, side='right'), N_EXPERTS - 1)
    x_rows = jnp.concatenate([xf, jnp.zeros((1, D), xf.dtype)], 0)[row_tok].reshape(n_blocks, MOE_BLOCK, D)

    def run(args):
        xb, e = args
        hb = jax.nn.silu(xb @ e_gate[e]) * (xb @ e_up[e])
        return hb @ e_down[e]

    y_rows = lax.map(run, (x_rows, blk_expert)).reshape(n_rows, D)
    return jax.ops.segment_sum(y_rows * row_w[:, None], row_tok, num_segments=T + 1)[:T]

def hier_moe(xf, w_group, b_group, w_expert, b_expert, e_gate, e_up, e_down):
    T = xf.shape[0]
    g_logits = (xf @ w_group).astype(jnp.float32) + b_group
    g_prob = jax.nn.softmax(g_logits, axis=-1)
    g_sel = jnp.argmax(g_logits, axis=-1)
    g_w = jnp.max(g_prob, axis=-1, keepdims=True)
    e_logits = ((xf @ w_expert).astype(jnp.float32) + b_expert).reshape(T, N_GROUPS, EXPERTS_PER_GROUP)
    e_in = e_logits[jnp.arange(T), g_sel]
    top_w, top_i = lax.top_k(jax.nn.softmax(e_in, axis=-1), TOP_K)
    top_w = top_w / jnp.sum(top_w, -1, keepdims=True) * g_w
    expert_idx = g_sel[:, None] * EXPERTS_PER_GROUP + top_i
    return grouped_experts(xf, expert_idx, top_w, e_gate, e_up, e_down)

def hybrid_layer(x, p, pos, conv_buf, C0, n0, m0, past_ckv, past_krope, lw):
    (w_in, conv_w, q_norm_g, w_uq, kv_norm_g, w_ukv, mlstm_gate_b, mix_norm_g, w_out,
     ln1_g, ln1_b, w_group, b_group, w_expert, b_expert, e_gate, e_up, e_down,
     w_pe, w_pg, ln2_g, ln2_b) = lw
    B, L, D = x.shape
    f32 = jnp.float32
    z = jnp.einsum('bld,dn->bln', x, w_in)
    sizes = [CONV_WIDTH] * 3 + [Q_RANK, KV_RANK, QK_ROPE] + [MLSTM_WIDTH] * 4 + [MLSTM_HEADS] * 2
    cuts = [int(c) for c in np.cumsum(sizes)[:-1]]
    cb, cc, ch, c_q, c_kv, k_r, mq, mk, mv, mo, mi, mf = jnp.split(z, cuts, axis=-1)
    conv_out, conv_state = short_conv(cc * ch, conv_buf, conv_w)
    y_conv = cb * conv_out
    q = jnp.einsum('blr,rn->bln', rms_norm(c_q, q_norm_g), w_uq).reshape(B, L, MLA_HEADS, QK_NOPE + QK_ROPE)
    q_nope, q_rope = q[..., :QK_NOPE], rope(q[..., QK_NOPE:], pos)
    ckv = rms_norm(c_kv, kv_norm_g)
    krope = rope(k_r, pos)
    w_kv = w_ukv.reshape(KV_RANK, MLA_HEADS, QK_NOPE + V_DIM)
    w_uk, w_uv = w_kv[..., :QK_NOPE], w_kv[..., QK_NOPE:]
    if past_ckv is None:
        k_nope = jnp.einsum('blr,rhd->blhd', ckv, w_uk)
        v = jnp.einsum('blr,rhd->blhd', ckv, w_uv)
        att = mla_prompt_attention(q_nope, q_rope, k_nope, krope, v)
    else:
        att = mla_sample_attention(q_nope, q_rope, jnp.concatenate([past_ckv, ckv], 1),
                                   jnp.concatenate([past_krope, krope], 1), w_uk, w_uv, past_ckv.shape[1])
    y_mla = att.reshape(B, L, MLA_HEADS * V_DIM)
    ig = mi.astype(f32) + mlstm_gate_b[:MLSTM_HEADS].astype(f32)
    lf = jax.nn.log_sigmoid(mf.astype(f32) + mlstm_gate_b[MLSTM_HEADS:].astype(f32))
    heads = lambda a: a.reshape(B, L, MLSTM_HEADS, MLSTM_DH)
    h_m, C1, n1, m1 = mlstm_chunkwise(heads(mq), heads(mk), heads(mv), ig, lf, C0, n0, m0)
    y_mlstm = jax.nn.sigmoid(mo) * h_m.reshape(B, L, MLSTM_WIDTH).astype(x.dtype)
    y = jnp.concatenate([y_conv, y_mla, y_mlstm], -1).reshape(B, L, N_MIX_HEADS, HEAD_DIM)
    y = rms_norm(y, mix_norm_g.reshape(N_MIX_HEADS, HEAD_DIM)).reshape(B, L, MIX_WIDTH)
    h1 = layer_norm(DN_ALPHA * x + jnp.einsum('blm,md->bld', y, w_out), ln1_g, ln1_b)
    moe = hier_moe(h1.reshape(B * L, D), w_group, b_group, w_expert, b_expert, e_gate, e_up, e_down).reshape(B, L, D)
    ple = jnp.einsum('blp,pd->bld', p, w_pe) * jax.nn.sigmoid(jnp.einsum('bld,de->ble', h1, w_pg))
    out = layer_norm(DN_ALPHA * h1 + moe + ple, ln2_g, ln2_b)
    return out, ckv, krope, conv_state, C1, n1, m1

def setup_inputs(seed: int = 0) -> dict:
    key = jax.random.key(seed)
    ks = iter(jax.random.split(key, 48))
    nrm = lambda shape, scale=1.0: scale * jax.random.normal(next(ks), shape, jnp.float32)
    gain = lambda shape: 1.0 + nrm(shape, 0.02)
    n_pages = PAST_LEN // PAGE_SIZE
    n_phys = (DEC_BATCH * n_pages * 5 + 3) // 4
    inp = {}
    inp['x_prompt'] = nrm((BATCH, SEQ, D_MODEL))
    inp['x_sample'] = nrm((DEC_BATCH, DEC_SEQ, D_MODEL))
    inp['cache_ckv'] = nrm((DEPTH, n_phys, PAGE_SIZE, KV_RANK))
    inp['cache_krope'] = nrm((DEPTH, n_phys, PAGE_SIZE, QK_ROPE))
    inp['state_conv'] = nrm((DEPTH, DEC_BATCH, CONV_K - 1, CONV_WIDTH))
    inp['state_mlstm_C'] = nrm((DEPTH, DEC_BATCH, MLSTM_HEADS, MLSTM_DH, MLSTM_DH), 0.1)
    inp['state_mlstm_n'] = nrm((DEPTH, DEC_BATCH, MLSTM_HEADS, MLSTM_DH), 0.1)
    inp['state_mlstm_m'] = nrm((DEPTH, DEC_BATCH, MLSTM_HEADS))
    perm = jax.random.permutation(next(ks), n_phys)
    inp['page_table'] = perm[:DEC_BATCH * n_pages].reshape(DEC_BATCH, n_pages).astype(jnp.int32)
    inp['p_prompt'] = nrm((DEPTH, BATCH, SEQ, D_PLE))
    inp['p_sample'] = nrm((DEPTH, DEC_BATCH, DEC_SEQ, D_PLE))
    inp['ln0_g'] = gain((D_MODEL,))
    inp['ln0_b'] = nrm((D_MODEL,), 0.02)
    inp['w_in'] = nrm((DEPTH, D_MODEL, N_IN), D_MODEL ** -0.5)
    inp['conv_w'] = nrm((DEPTH, CONV_K, CONV_WIDTH), CONV_K ** -0.5)
    inp['q_norm_g'] = gain((DEPTH, Q_RANK))
    inp['w_uq'] = nrm((DEPTH, Q_RANK, MLA_HEADS * (QK_NOPE + QK_ROPE)), Q_RANK ** -0.5)
    inp['kv_norm_g'] = gain((DEPTH, KV_RANK))
    inp['w_ukv'] = nrm((DEPTH, KV_RANK, MLA_HEADS * (QK_NOPE + V_DIM)), KV_RANK ** -0.5)
    inp['mlstm_gate_b'] = jnp.concatenate([nrm((DEPTH, MLSTM_HEADS), 0.1),
                                           jnp.linspace(3.0, 6.0, MLSTM_HEADS)[None, :] + nrm((DEPTH, MLSTM_HEADS), 0.1)], -1)
    inp['mix_norm_g'] = gain((DEPTH, MIX_WIDTH))
    inp['w_out'] = nrm((DEPTH, MIX_WIDTH, D_MODEL), MIX_WIDTH ** -0.5 * DN_BETA)
    inp['ln1_g'] = gain((DEPTH, D_MODEL))
    inp['ln1_b'] = nrm((DEPTH, D_MODEL), 0.02)
    inp['w_group'] = nrm((DEPTH, D_MODEL, N_GROUPS), D_MODEL ** -0.5)
    inp['b_group'] = nrm((DEPTH, N_GROUPS), 0.01)
    inp['w_expert'] = nrm((DEPTH, D_MODEL, N_EXPERTS), D_MODEL ** -0.5)
    inp['b_expert'] = nrm((DEPTH, N_EXPERTS), 0.01)
    inp['e_gate'] = nrm((DEPTH, N_EXPERTS, D_MODEL, D_EXPERT), D_MODEL ** -0.5)
    inp['e_up'] = nrm((DEPTH, N_EXPERTS, D_MODEL, D_EXPERT), D_MODEL ** -0.5)
    inp['e_down'] = nrm((DEPTH, N_EXPERTS, D_EXPERT, D_MODEL), D_EXPERT ** -0.5 * DN_BETA)
    inp['w_pe'] = nrm((DEPTH, D_PLE, D_MODEL), D_PLE ** -0.5 * DN_BETA)
    inp['w_pg'] = nrm((DEPTH, D_MODEL, D_MODEL), D_MODEL ** -0.5)
    inp['ln2_g'] = gain((DEPTH, D_MODEL))
    inp['ln2_b'] = nrm((DEPTH, D_MODEL), 0.02)
    return inp

def reference(x_prompt, x_sample, cache_ckv, cache_krope, state_conv, state_mlstm_C, state_mlstm_n, state_mlstm_m,
              page_table, p_prompt, p_sample, ln0_g, ln0_b, w_in, conv_w, q_norm_g, w_uq, kv_norm_g, w_ukv,
              mlstm_gate_b, mix_norm_g, w_out, ln1_g, ln1_b, w_group, b_group, w_expert, b_expert,
              e_gate, e_up, e_down, w_pe, w_pg, ln2_g, ln2_b):
    B, S, _ = x_prompt.shape
    DB, DS, _ = x_sample.shape
    dt = x_prompt.dtype
    n_pages = PAST_LEN // PAGE_SIZE
    pos_p = jnp.arange(S)
    pos_s = PAST_LEN + jnp.arange(DS)
    hp = layer_norm(x_prompt, ln0_g, ln0_b)
    hs = layer_norm(x_sample, ln0_g, ln0_b)
    st_p, st_s = [], []
    for i in range(DEPTH):
        lw = (w_in[i], conv_w[i], q_norm_g[i], w_uq[i], kv_norm_g[i], w_ukv[i], mlstm_gate_b[i], mix_norm_g[i],
              w_out[i], ln1_g[i], ln1_b[i], w_group[i], b_group[i], w_expert[i], b_expert[i], e_gate[i], e_up[i],
              e_down[i], w_pe[i], w_pg[i], ln2_g[i], ln2_b[i])
        hp, *sp = hybrid_layer(hp, p_prompt[i], pos_p,
                               jnp.zeros((B, CONV_K - 1, CONV_WIDTH), dt),
                               jnp.zeros((B, MLSTM_HEADS, MLSTM_DH, MLSTM_DH), dt),
                               jnp.zeros((B, MLSTM_HEADS, MLSTM_DH), dt),
                               jnp.zeros((B, MLSTM_HEADS), dt), None, None, lw)
        past_ckv = cache_ckv[i][page_table].reshape(DB, n_pages * PAGE_SIZE, KV_RANK)
        past_kr = cache_krope[i][page_table].reshape(DB, n_pages * PAGE_SIZE, QK_ROPE)
        hs, *ss = hybrid_layer(hs, p_sample[i], pos_s, state_conv[i], state_mlstm_C[i], state_mlstm_n[i],
                               state_mlstm_m[i], past_ckv, past_kr, lw)
        st_p.append(sp)
        st_s.append(ss)
    ckv_p, krope_p, conv_p, C_p, n_p, m_p = [jnp.stack(a) for a in zip(*st_p)]
    ckv_s, krope_s, conv_s, C_s, n_s, m_s = [jnp.stack(a) for a in zip(*st_s)]
    return (hp, hs, ckv_p, krope_p, conv_p, C_p, n_p, m_p, ckv_s, krope_s, conv_s, C_s, n_s, m_s)


_drawn_inputs = setup_inputs


def setup_inputs(seed=0):
    import zlib

    import numpy as np

    out = dict(_drawn_inputs(seed))
    spreads = {}
    factors = {'q_norm_g': 5.196,
     'kv_norm_g': 2.847,
     'mix_norm_g': 3.824,
     'b_group': 8.0,
     'b_expert': 5.776}
    for name, (base, spread) in spreads.items():
        noise = np.random.default_rng([zlib.crc32(name.encode()), seed]).standard_normal(out[name].shape)
        drawn = base * np.exp(spread * noise) if base else spread * noise
        out[name] = __import__('jax').numpy.asarray(drawn.astype(out[name].dtype))
    for name, factor in factors.items():
        out[name] = (out[name] * factor).astype(out[name].dtype)
    return out
```

```python
from contextlib import ExitStack

import concourse.bass as bass
from concourse import mybir

F32 = mybir.dt.float32
I32 = mybir.dt.int32
ALU = mybir.AluOpType
ACT = mybir.ActivationFunctionType
AX = mybir.AxisListType
ds = bass.ds

P = 128
D = 1024
KC = D // P
SEQ, DECB, PAST = 1024, 8, 2048
DEPTH = 2
TP = SEQ // P
NT = TP + 1
ROWS = NT * P
N_IN = 2216
PAD = 2
CONVW, QR, KVR, ROPE, NOPE, VD = 256, 256, 128, 32, 64, 64
H, QK = 8, 96
HALF = ROPE // 2
NH, DH, MW = 4, 64, 256
C_CB, C_CC, C_CH, C_Q = 0, 256, 512, 768
C_KV, C_KR = C_Q + QR, C_Q + QR + KVR
C_MQ = C_KR + ROPE
C_MK, C_MV, C_MO, C_MI = C_MQ + MW, C_MQ + 2 * MW, C_MQ + 3 * MW, C_MQ + 4 * MW
MLA_COLS = QR + KVR + ROPE
NE, NG, EPG, DE = 32, 4, 8, 256
DPLE = 256
ALPHA = (2 * DEPTH) ** 0.25
LN_EPS, RMS_EPS = 1e-5, 1e-6
SCALE = float(QK) ** -0.5
PAGES, PAGE = PAST // P, P
NEG = -1e30
BLOCKS = -(-2 * (SEQ + DECB) // P) + NE
XROWS = 2 * (SEQ + DECB) + P


def tile_turns(eng, tiles=NT):
    with eng.Fori(0, tiles // 2) as r:
        for slot in range(2):
            yield 2 * r + slot, slot, r
    if tiles % 2:
        yield tiles - 1, 0, tiles // 2


class Steps:

    def __init__(self, eng, sem, turn, steps):
        self.eng, self.sem, self.base, self.steps, self.n = eng, sem, turn * steps, steps, 0

    def did(self, ins):
        self.n += 1
        ins.then_inc(self.sem, 1)

    def wait(self):
        self.eng.wait_ge(self.sem, self.base + self.n)

    def end(self):
        assert self.n == self.steps, (self.n, self.steps)


class Phase:

    def __init__(self, nc):
        self.nc, self.sems = nc, []

    def __enter__(self):
        self.ctx = ExitStack()
        self.ctx.__enter__()
        return self

    def sb(self, name, shape, dt=F32):
        return self.ctx.enter_context(self.nc.sbuf_tensor(name, shape, dt))

    def ps(self, name, shape, dt=F32):
        return self.ctx.enter_context(self.nc.psum_tensor(name, shape, dt))

    def sem(self, name):
        s = self.ctx.enter_context(self.nc.semaphore(name))
        self.sems.append(s.num)
        return s

    def sem2(self, name):
        return [self.sem(f"{name}{i}") for i in range(2)]

    def __exit__(self, *exc):
        if exc[0] is None:
            nums = sorted(self.sems)
            firsts = [n for n in nums if n - 1 not in nums]
            for lo in firsts:
                hi = lo
                while hi + 1 in nums:
                    hi += 1
                self.nc.all_engine_barrier(sems_to_clear=range(lo, hi + 1))
        return self.ctx.__exit__(*exc)


def rows(t, n=P):
    return ds(t * P, n)


def of_layer(ap, layer):
    inner = "abcd"[:len(ap.shape) - 1]
    return ap[ds(layer, 1)].rearrange(f"l {' '.join(inner)} -> (l {inner[0]}) {' '.join(inner[1:])}")


def row_of_layer(ap, layer):
    return ap[ds(layer, 1), :].broadcast_to([P, ap.shape[1]])



def layer_norm_steps(dve, st, x, stats, mv, rstd_in, hold):
    st.did(dve.bn_stats(stats[:, 0, :], x[:, 0:512]))
    st.did(dve.bn_stats(stats[:, 1, :], x[:, 512:1024]))
    st.wait()
    dve.memset(hold, 0.0)
    st.did(dve.bn_aggr(mv, stats[:, :, :]))
    st.wait()
    st.did(dve.tensor_scalar(rstd_in, mv[:, 1:2], LN_EPS, None, ALU.add))


def entry_norm(nc, d):
    with Phase(nc) as ph:
        x = ph.sb("en_x", [P, 2, D])
        o = ph.sb("en_o", [P, 2, D])
        g = ph.sb("en_g", [P, D])
        b = ph.sb("en_b", [P, D])
        zero = ph.sb("en_zero", [P, N_IN])
        stats = ph.sb("en_stats", [P, 2, 6])
        mv = ph.sb("en_mv", [P, 2])
        hold = ph.sb("en_hold", [1, 1])
        ve = ph.sb("en_ve", [P, 1])
        sd = ph.sb("en_sd", [P, 1])
        rs = ph.sb("en_rs", [P, 1])
        gains, loaded, stored = ph.sem("gains"), ph.sem2("x_loaded"), ph.sem2("o_stored")
        x_free, o_ready = ph.sem("x_free"), ph.sem("o_ready")
        var_ready, sqrt_done, steps = ph.sem("var_ready"), ph.sem("sqrt_done"), ph.sem("steps")
        zeroed, zero_stored = ph.sem("zeroed"), d["sw"]["zero_stored"]
        with nc.Block() as block:
            @block.sync
            def _(sp):
                sp.dma_start(g[:, :], d["ln0_g"].partition_broadcast(P)).then_inc(gains, 16)
                sp.dma_start(b[:, :], d["ln0_b"].partition_broadcast(P)).then_inc(gains, 16)
                for t, s, r in tile_turns(sp):
                    sp.wait_ge(x_free, t + 1)
                    sp.dma_start(x[:, s, :], d["x_all"][rows(t)]).then_inc(loaded[s], 16)

            @block.gpsimd
            def _(pool):
                pool.memset(zero[:, :], 0.0).then_inc(zeroed, 1)
                pool.wait_ge(zeroed, 1)
                pool.dma_start(d["Z"][0:PAD], zero[0:PAD, :]).then_inc(zero_stored, 16)
                pool.dma_start(d["XR"][XROWS - P:XROWS], zero[:, 0:D]).then_inc(zero_stored, 16)
                pool.dma_start(d["YR"][XROWS - P:XROWS], zero[:, 0:D]).then_inc(zero_stored, 16)
                pool.dma_start(d["Y"][SEQ:ROWS], zero[:, 0:D]).then_inc(zero_stored, 16)
                pool.wait_ge(zero_stored, 64)

            @block.scalar
            def _(act):
                for s in range(2):
                    act.sem_inc(stored[s], 16)
                for t, s, r in tile_turns(act):
                    act.wait_ge(var_ready, t + 1)
                    act.activation(sd[:, :], ve[:, :], ACT.Sqrt).then_inc(sqrt_done, 1)
                    act.wait_ge(o_ready, t + 1)
                    act.dma_start(d["H"][rows(t)], o[:, s, :]).then_inc(stored[s], 16)
                act.wait_ge(stored[0], 16 * (NT // 2 + 2))
                act.wait_ge(stored[1], 16 * (NT // 2 + 1))

            @block.vector
            def _(dve):
                dve.sem_inc(x_free, 2)
                dve.wait_ge(gains, 32)
                for t, s, r in tile_turns(dve):
                    st = Steps(dve, steps, t, 7)
                    dve.wait_ge(loaded[s], 16 * (r + 1))
                    layer_norm_steps(dve, st, x[:, s, :], stats, mv[:, :], ve[:, :], hold[:, :])
                    st.wait()
                    dve.sem_inc(var_ready, 1)
                    dve.wait_ge(sqrt_done, t + 1)
                    st.did(dve.reciprocal(rs[:, :], sd[:, :]))
                    st.wait()
                    dve.wait_ge(stored[s], 16 * (r + 1))
                    st.did(dve.tensor_scalar(o[:, s, :], x[:, s, :], mv[:, 0:1], rs[:, 0:1], ALU.subtract, ALU.mult))
                    st.wait()
                    dve.sem_inc(x_free, 1)
                    st.did(dve.tensor_tensor(o[:, s, :], o[:, s, :], g[:, :], ALU.mult))
                    st.wait()
                    dve.tensor_tensor(o[:, s, :], o[:, s, :], b[:, :], ALU.add).then_inc(o_ready, 1)
                    st.end()



Z_CHUNKS = [(c, min(512, N_IN - c)) for c in range(0, N_IN, 512)]


def input_projection(nc, d, layer, ident):
    with Phase(nc) as ph:
        w = ph.sb("ip_w", [P, KC, N_IN])
        x = ph.sb("ip_x", [P, 2, D])
        xT = ph.sb("ip_xT", [P, 2, KC, P])
        z = ph.sb("ip_z", [P, 2, N_IN])
        tp = [ph.ps(f"ip_tp{i}", [P, 4, P]) for i in range(2)]
        zp = [ph.ps(f"ip_zp{i}", [P, 512]) for i in range(5)]
        w_loaded, x_loaded, z_stored = ph.sem("w_loaded"), ph.sem2("x_loaded"), ph.sem2("z_stored")
        x_free, tp_done = ph.sem("x_free"), ph.sem("tp_done")
        xT_dve, xT_act = ph.sem("xT_dve"), ph.sem("xT_act")
        z_done, z_dve, z_act = ph.sem("z_done"), ph.sem("z_dve"), ph.sem("z_act")
        with nc.Block() as block:
            @block.sync
            def _(sp):
                for c in range(KC):
                    sp.dma_start(w[:, c, :], of_layer(d["w_in"], layer).rearrange("(p k) n -> p k n", k=KC)[:, c, :]).then_inc(w_loaded, 16)
                for t, s, r in tile_turns(sp):
                    sp.wait_ge(x_free, t + 1)
                    sp.dma_start(x[:, s, :], d["H"][rows(t)]).then_inc(x_loaded[s], 16)

            @block.tensor
            def _(pe):
                pe.sem_inc(x_free, 2)
                for t, s, r in tile_turns(pe):
                    pe.wait_ge(x_loaded[s], 16 * (r + 1))
                    pe.wait_ge(xT_dve, t + 1)
                    pe.wait_ge(xT_act, t + 1)
                    for c in range(KC):
                        last = pe.transpose(tp[c // 4][:, c % 4, :], x[:, s, c::KC], ident[:, :])
                        if c % 4 == 3:
                            last.then_inc(tp_done, 1)
                    pe.wait_ge(xT_dve, t + 2)
                    pe.wait_ge(xT_act, t + 2)
                    pe.wait_ge(w_loaded, 16 * KC)
                    for n, (c0, cn) in enumerate(Z_CHUNKS):
                        if n % 2 == 0:
                            pe.wait_ge(z_dve, 3 * t + n // 2 + 1)
                        else:
                            pe.wait_ge(z_act, 2 * t + n // 2 + 1)
                        for c in range(KC):
                            last = pe.matmul(zp[n][:, 0:cn], xT[:, s, c, :], w[:, c, c0:c0 + cn],
                                             start=(c == 0), stop=(c == KC - 1))
                            if n == c == 0:
                                last.then_inc(x_free, 1)
                        last.then_inc(z_done, 1)

            @block.vector
            def _(dve):
                dve.sem_inc(xT_dve, 1)
                dve.sem_inc(z_dve, 3)
                for t, s, r in tile_turns(dve):
                    dve.wait_ge(tp_done, 2 * t + 1)
                    dve.tensor_copy(xT[:, s, 0:4, :], tp[0][:, :, :]).then_inc(xT_dve, 1)
                    dve.wait_ge(z_stored[s], 16 * (r + 1))
                    for n in (0, 2, 4):
                        c0, cn = Z_CHUNKS[n]
                        dve.wait_ge(z_done, 5 * t + n + 1)
                        dve.tensor_copy(z[:, s, c0:c0 + cn], zp[n][:, 0:cn]).then_inc(z_dve, 1)

            @block.scalar
            def _(act):
                act.sem_inc(xT_act, 1)
                act.sem_inc(z_act, 2)
                for s in range(2):
                    act.sem_inc(z_stored[s], 16)
                for t, s, r in tile_turns(act):
                    act.wait_ge(tp_done, 2 * t + 2)
                    act.activation(xT[:, s, 4:8, :], tp[1][:, :, :], ACT.Copy).then_inc(xT_act, 1)
                    act.wait_ge(z_stored[s], 16 * (r + 1))
                    for n in (1, 3):
                        c0, cn = Z_CHUNKS[n]
                        act.wait_ge(z_done, 5 * t + n + 1)
                        act.activation(z[:, s, c0:c0 + cn], zp[n][:, 0:cn], ACT.Copy).then_inc(z_act, 1)
                    act.wait_ge(z_dve, 3 * t + 6)
                    act.wait_ge(z_act, 2 * t + 4)
                    act.dma_start(d["Z"][ds(PAD + t * P, P)], z[:, s, :]).then_inc(z_stored[s], 16)
                act.wait_ge(z_stored[0], 16 * (NT // 2 + 2))
                act.wait_ge(z_stored[1], 16 * (NT // 2 + 1))




def mla_prepare(nc, d, layer, ident):
    with Phase(nc) as ph:
        wuq = ph.sb("mp_wuq", [P, 2, H * QK])
        wukv = ph.sb("mp_wukv", [P, H, NOPE + VD])
        wuk = ph.sb("mp_wuk", [P, H, NOPE])
        wuv = ph.sb("mp_wuv", [P, H, VD])
        gq = ph.sb("mp_gq", [P, QR])
        gkv = ph.sb("mp_gkv", [P, KVR])
        zq = ph.sb("mp_zq", [P, 2, MLA_COLS])
        trig = ph.sb("mp_trig", [P, 2, 2 * HALF])
        sq = ph.sb("mp_sq", [P, QR])
        ss = ph.sb("mp_ss", [P, 2])
        ms = ph.sb("mp_ms", [P, 2])
        sd = ph.sb("mp_sd", [P, 2])
        rs = ph.sb("mp_rs", [P, 2])
        cqn = ph.sb("mp_cqn", [P, QR])
        ckvn = ph.sb("mp_ckvn", [P, 2, KVR])
        kpad = ph.sb("mp_kpad", [P, 2, QK])
        t4 = ph.sb("mp_t4", [P, 4, H, HALF])
        k4 = ph.sb("mp_k4", [P, 4, HALF])
        cT = ph.sb("mp_cT", [P, 2, 3, P])
        q = ph.sb("mp_q", [P, H, QK])
        qT = ph.sb("mp_qT", [QK, 2, H, P])
        kT = ph.sb("mp_kT", [QK, 2, H, P])
        v = ph.sb("mp_v", [P, 2, H * VD])
        tp = ph.ps("mp_tp", [P, 4, P])
        qp = [ph.ps(f"mp_qp{i}", [P, 4, QK]) for i in range(2)]
        qtp = [ph.ps(f"mp_qtp{i}", [QK, 4, P]) for i in range(2)]
        ktp = [ph.ps(f"mp_ktp{i}", [NOPE, 4, P]) for i in range(2)]
        vp = ph.ps("mp_vp", [P, H * VD])
        w_loaded, z_loaded = ph.sem("w_loaded"), ph.sem2("z_loaded")
        q_stored, kv_stored, c_stored = ph.sem2("q_stored"), ph.sem2("kv_stored"), ph.sem2("c_stored")
        z_free, squares, ms_ready, sd_ready = ph.sem("z_free"), ph.sem("squares"), ph.sem("ms_ready"), ph.sem("sd_ready")
        w_split, steps, lat_ready, tp_done = ph.sem("w_split"), ph.sem("steps"), ph.sem("lat_ready"), ph.sem("tp_done")
        cT_ready, kr_ready, q_done, kv_done = ph.sem("cT_ready"), ph.sem("kr_ready"), ph.sem("q_done"), ph.sem("kv_done")
        q_copied, q_rot, qt_done, qT_ready = ph.sem("q_copied"), ph.sem("q_rot"), ph.sem("qt_done"), ph.sem("qT_ready")
        kT_ready, v_ready = ph.sem("kT_ready"), ph.sem("v_ready")
        with nc.Block() as block:
            @block.sync
            def _(sp):
                sp.dma_start(wuq[:, :, :], of_layer(d["w_uq"], layer).rearrange("(k p) n -> p k n", k=2)).then_inc(w_loaded, 16)
                sp.dma_start(wukv[:, :, :].rearrange("p h n -> p (h n)"), of_layer(d["w_ukv"], layer)).then_inc(w_loaded, 16)
                sp.dma_start(gq[:, :], row_of_layer(d["q_norm_g"], layer)).then_inc(w_loaded, 16)
                sp.dma_start(gkv[:, :], row_of_layer(d["kv_norm_g"], layer)).then_inc(w_loaded, 16)
                for t, s, r in tile_turns(sp):
                    sp.wait_ge(z_free, t + 1)
                    sp.dma_start(zq[:, s, :], d["Z"][ds(PAD + t * P, P), C_Q:C_Q + MLA_COLS]).then_inc(z_loaded[s], 16)
                    sp.dma_start(trig[:, s, :], d["c_trig"][rows(t)]).then_inc(z_loaded[s], 16)

            @block.scalar
            def _(act):
                for s in range(2):
                    act.sem_inc(q_stored[s], 16)
                    act.sem_inc(kv_stored[s], 16)
                act.wait_ge(w_loaded, 64)
                act.activation(wuk[:, :, :], wukv[:, :, 0:NOPE], ACT.Copy).then_inc(w_split, 1)
                act.activation(wuv[:, :, :], wukv[:, :, NOPE:], ACT.Copy).then_inc(w_split, 1)
                for t, s, r in tile_turns(act):
                    act.wait_ge(z_loaded[s], 32 * (r + 1))
                    act.wait_ge(ms_ready, t + 1)
                    act.activation(sq[:, 0:QR], zq[:, s, 0:QR], ACT.Square, accum_out=ss[:, 0:1]).then_inc(squares, 1)
                    act.wait_ge(squares, 2 * t + 1)
                    act.activation(sq[:, 0:KVR], zq[:, s, QR:QR + KVR], ACT.Square, accum_out=ss[:, 1:2]).then_inc(squares, 1)
                    act.wait_ge(ms_ready, t + 2)
                    act.activation(sd[:, :], ms[:, :], ACT.Sqrt).then_inc(sd_ready, 1)
                    for n in range(2):
                        act.wait_ge(q_done, 2 * t + n + 1)
                        act.activation(q[:, 4 * n:4 * n + 4, :], qp[n][:, :, :], ACT.Copy).then_inc(q_copied, 1)
                    act.wait_ge(kv_done, 2 * t + 2)
                    act.wait_ge(kv_stored[s], 16 * (3 * r + 1))
                    act.activation(v[:, s, :], vp[:, :], ACT.Copy).then_inc(v_ready, 1)
                    act.wait_ge(q_stored[s], 16 * (r + 1))
                    for n in range(2):
                        act.wait_ge(qt_done, 2 * t + n + 1)
                        act.activation(qT[:, s, 4 * n:4 * n + 4, :], qtp[n][:, :, :], ACT.Copy).then_inc(qT_ready, 1)
                    act.wait_ge(qT_ready, 2 * t + 2)
                    act.dma_start(d["QT"][:, :, rows(t)].rearrange("h p n -> p h n"), qT[:, s]).then_inc(q_stored[s], 16)
                    act.wait_ge(kT_ready, 3 * t + 4)
                    act.dma_start(d["KT"][:, :, rows(t)].rearrange("h p n -> p h n"), kT[:, s]).then_inc(kv_stored[s], 16)
                    act.wait_ge(v_ready, t + 1)
                    act.dma_start(d["V"][rows(t)], v[:, s, :]).then_inc(kv_stored[s], 16)
                    act.dma_start(of_layer(d["ckv_all"], layer)[rows(t)], ckvn[:, s, :]).then_inc(kv_stored[s], 16)
                    act.dma_start(of_layer(d["krope_all"], layer)[rows(t)], kpad[:, s, NOPE:]).then_inc(c_stored[s], 16)
                for s in range(2):
                    act.wait_ge(q_stored[s], 16 * (NT // 2 + 2 - s))
                    act.wait_ge(kv_stored[s], 16 * (3 * (NT // 2 + 1 - s) + 1))
                    act.wait_ge(c_stored[s], 16 * (NT // 2 + 2 - s))

            @block.vector
            def _(dve):
                dve.sem_inc(z_free, 2)
                dve.sem_inc(ms_ready, 1)
                dve.sem_inc(kT_ready, 1)
                for s in range(2):
                    dve.sem_inc(c_stored[s], 16)
                dve.memset(kpad[:, :, :], 0.0).then_inc(w_split, 1)
                dve.wait_ge(w_split, 3)
                for t, s, r in tile_turns(dve):
                    st = Steps(dve, steps, t, 17)
                    dve.wait_ge(squares, 2 * t + 2)
                    st.did(dve.tensor_scalar(ms[:, 0:1], ss[:, 0:1], 1.0 / QR, RMS_EPS, ALU.mult, ALU.add))
                    dve.tensor_scalar(ms[:, 1:2], ss[:, 1:2], 1.0 / KVR, RMS_EPS, ALU.mult, ALU.add).then_inc(ms_ready, 1)
                    dve.wait_ge(sd_ready, t + 1)
                    st.did(dve.reciprocal(rs[:, :], sd[:, :]))
                    st.wait()
                    dve.wait_ge(kv_stored[s], 16 * (3 * r + 1))
                    dve.wait_ge(c_stored[s], 16 * (r + 1))
                    st.did(dve.scalar_tensor_tensor(cqn[:, :], zq[:, s, 0:QR], rs[:, 0:1], gq[:, :], ALU.mult, ALU.mult))
                    st.did(dve.scalar_tensor_tensor(ckvn[:, s, :], zq[:, s, QR:QR + KVR], rs[:, 1:2], gkv[:, :], ALU.mult, ALU.mult))
                    cos, sin = trig[:, s, 0:HALF], trig[:, s, HALF:]
                    k1, k2 = zq[:, s, QR + KVR:QR + KVR + HALF], zq[:, s, QR + KVR + HALF:]
                    st.did(dve.tensor_tensor(k4[:, 0, :], k1, cos, ALU.mult))
                    st.did(dve.tensor_tensor(k4[:, 1, :], k2, sin, ALU.mult))
                    st.did(dve.tensor_tensor(k4[:, 2, :], k1, sin, ALU.mult))
                    st.did(dve.tensor_tensor(k4[:, 3, :], k2, cos, ALU.mult))
                    st.wait()
                    st.did(dve.tensor_tensor(kpad[:, s, NOPE:NOPE + HALF], k4[:, 0, :], k4[:, 1, :], ALU.subtract))
                    st.did(dve.tensor_tensor(kpad[:, s, NOPE + HALF:], k4[:, 2, :], k4[:, 3, :], ALU.add))
                    st.wait()
                    dve.sem_inc(lat_ready, 1)
                    dve.wait_ge(tp_done, t + 1)
                    dve.tensor_copy(cT[:, s, :, :], tp[:, 0:3, :]).then_inc(cT_ready, 1)
                    st.did(dve.tensor_copy(kT[NOPE:QK, s, :, :], tp[NOPE:QK, 3:4, :].broadcast_to([ROPE, H, P])))
                    st.wait()
                    dve.sem_inc(kT_ready, 1)
                    for n in range(2):
                        dve.wait_ge(kv_done, 2 * t + 1)
                        dve.tensor_copy(kT[0:NOPE, s, 4 * n:4 * n + 4, :], ktp[n][:, :, :]).then_inc(kT_ready, 1)
                    dve.wait_ge(q_copied, 2 * t + 2)
                    q1, q2 = q[:, :, NOPE:NOPE + HALF], q[:, :, NOPE + HALF:]
                    cosb = trig[:, s:s + 1, 0:HALF].broadcast_to([P, H, HALF])
                    sinb = trig[:, s:s + 1, HALF:].broadcast_to([P, H, HALF])
                    st.did(dve.tensor_tensor(t4[:, 0], q1, cosb, ALU.mult))
                    st.did(dve.tensor_tensor(t4[:, 1], q2, sinb, ALU.mult))
                    st.did(dve.tensor_tensor(t4[:, 2], q1, sinb, ALU.mult))
                    st.did(dve.tensor_tensor(t4[:, 3], q2, cosb, ALU.mult))
                    st.wait()
                    dve.sem_inc(z_free, 1)
                    st.did(dve.tensor_tensor(q1, t4[:, 0], t4[:, 1], ALU.subtract))
                    st.did(dve.tensor_tensor(q2, t4[:, 2], t4[:, 3], ALU.add))
                    st.wait()
                    dve.sem_inc(q_rot, 1)
                    st.end()

            @block.tensor
            def _(pe):
                pe.wait_ge(w_loaded, 64)
                pe.wait_ge(w_split, 3)
                for t, s, r in tile_turns(pe):
                    pe.wait_ge(lat_ready, t + 1)
                    for c in range(2):
                        pe.transpose(tp[:, c, :], cqn[:, c * P:(c + 1) * P], ident[:, :])
                    pe.transpose(tp[:, 2, :], ckvn[:, s, :], ident[:, :])
                    pe.transpose(tp[0:QK, 3, :], kpad[:, s, :], ident[:, :]).then_inc(tp_done, 1)
                    pe.wait_ge(cT_ready, t + 1)
                    for n in range(2):
                        for c in range(2):
                            last = pe.matmul(qp[n][:, :, :].rearrange("p h n -> p (h n)"), cT[:, s, c, :], wuq[:, c, 4 * QK * n:4 * QK * (n + 1)],
                                             start=(c == 0), stop=(c == 1))
                        last.then_inc(q_done, 1)
                    pe.wait_ge(kT_ready, 3 * t + 1)
                    for h in range(H):
                        last = pe.matmul(ktp[h // 4][:, h % 4, :], wuk[:, h, :], cT[:, s, 2, :], start=True, stop=True)
                    last.then_inc(kv_done, 1)
                    pe.matmul(vp[:, :], cT[:, s, 2, :], wuv[:, :, :].rearrange("p h n -> p (h n)"), start=True, stop=True).then_inc(kv_done, 1)
                    pe.wait_ge(q_rot, t + 1)
                    for n in range(2):
                        for h in range(4):
                            last = pe.transpose(qtp[n][:, h, :], q[:, 4 * n + h, :], ident[:, :])
                        last.then_inc(qt_done, 1)



def attention(nc, d, layer, ident):
    units = [(s, qb) for s in range(2) for qb in range(TP)]
    n_units = len(units)
    groups = [[range(g, min(g + 4, qb + 1)) for g in range(0, qb + 1, 4)] for _, qb in units]
    first_group = [sum(len(g) for g in groups[:u]) for u in range(n_units)]
    n_groups = sum(len(g) for g in groups)
    n_even, n_odd = (n_groups + 1) // 2, n_groups // 2
    with Phase(nc) as ph:
        qT = ph.sb("at_qT", [QK, 2, SEQ])
        kT = ph.sb("at_kT", [QK, 2, SEQ])
        v = ph.sb("at_v", [P, 2, TP, VD])
        mask = ph.sb("at_mask", [P, P])
        probs = ph.sb("at_p", [P, 2, SEQ])
        pT = ph.sb("at_pT", [P, 2, TP, P])
        mx = ph.sb("at_mx", [P, 2])
        nmx = ph.sb("at_nmx", [P, 2])
        total = ph.sb("at_total", [P, 2])
        inv = ph.sb("at_inv", [P, 2])
        y = ph.sb("at_y", [P, 2, TP, VD])
        sc = [ph.ps(f"at_s{i}", [P, SEQ]) for i in range(2)]
        tp = [ph.ps(f"at_tp{i}", [P, 4, P]) for i in range(2)]
        op = [ph.ps(f"at_o{i}", [P, VD]) for i in range(2)]
        mask_loaded, loaded, y_stored = ph.sem("mask_loaded"), ph.sem2("loaded"), ph.sem2("y_stored")
        head_free, s_done, steps, mx_ready = ph.sem("head_free"), ph.sem("s_done"), ph.sem("steps"), ph.sem("mx_ready")
        p_ready, tp_done, pT_dve, pT_act = ph.sem("p_ready"), ph.sem("tp_done"), ph.sem("pT_dve"), ph.sem("pT_act")
        o_done, y_ready = ph.sem("o_done"), ph.sem("y_ready")

        cw = ph.sb("cv_w", [P, CONVW, 3])
        cwr = ph.sb("cv_wr", [P, 3, CONVW])
        cch = ph.sb("cv_cch", [P, 3, 2 * CONVW])
        cb = ph.sb("cv_b", [P, CONVW])
        u = ph.sb("cv_u", [P, 3, CONVW])
        yc = ph.sb("cv_y", [P, CONVW])
        past = ph.sb("cv_past", [DECB, 2, CONVW])
        cv_w, cv_in, cv_out, cv_state = (d["sw"][n] for n in ("cv_w", "cv_in", "cv_out", "cv_state"))
        cv, paced = ph.sem("cv"), ph.sem("paced")
        with nc.Block() as block:
            @block.sync
            def _(sp):
                sp.dma_start(mask[:, :], d["c_causal"]).then_inc(mask_loaded, 16)
                with sp.Fori(0, H // 2) as j:
                    for s in range(2):
                        head = 2 * j + s
                        sp.wait_ge(head_free, head + 1)
                        sp.dma_start(qT[:, s, :], d["QT"][ds(head, 1), :, 0:SEQ].rearrange("h p n -> (h p) n")).then_inc(loaded[s], 16)
                        sp.dma_start(kT[:, s, :], d["KT"][ds(head, 1), :, 0:SEQ].rearrange("h p n -> (h p) n")).then_inc(loaded[s], 16)
                        sp.dma_start(v[:, s, :, :], d["V"][0:SEQ, ds(head * VD, VD)].rearrange("(b p) n -> p b n", p=P)).then_inc(loaded[s], 16)

            @block.tensor
            def _(pe):
                with pe.Fori(0, H // 2) as j:
                    def scores(n):
                        s, qb = units[n]
                        if qb == 0:
                            pe.wait_ge(loaded[s], 48 * (j + 1))
                        pe.wait_ge(p_ready, j * n_units + n + 1)
                        keys = (qb + 1) * P
                        for c in range(0, keys, 512):
                            last = pe.matmul(sc[n % 2][:, c:min(c + 512, keys)], qT[:, s, qb * P:(qb + 1) * P],
                                             kT[:, s, c:min(c + 512, keys)], start=True, stop=True)
                        last.then_inc(s_done, 1)

                    def values(n):
                        s, qb = units[n]
                        pe.wait_ge(p_ready, j * n_units + n + 3)
                        for g, blocks in enumerate(groups[n]):
                            m = first_group[n] + g
                            if m % 2 == 0:
                                pe.wait_ge(pT_dve, j * n_even + m // 2 + 1)
                            else:
                                pe.wait_ge(pT_act, j * n_odd + m // 2 + 1)
                            for kb in blocks:
                                last = pe.transpose(tp[m % 2][:, kb % 4, :], probs[:, n % 2, kb * P:(kb + 1) * P], ident[:, :])
                            last.then_inc(tp_done, 1)
                        pe.wait_ge(y_ready, j * n_units + n + 1)
                        for g, blocks in enumerate(groups[n]):
                            m = first_group[n] + g
                            if m % 2 == 0:
                                pe.wait_ge(pT_dve, j * n_even + m // 2 + 2)
                            else:
                                pe.wait_ge(pT_act, j * n_odd + m // 2 + 2)
                            for kb in blocks:
                                last = pe.matmul(op[n % 2][:, :], pT[:, n % 2, kb, :], v[:, s, kb, :], start=(kb == 0), stop=(kb == qb))
                        last.then_inc(o_done, 1)

                    scores(0)
                    for n in range(1, n_units):
                        scores(n)
                        values(n - 1)
                    values(n_units - 1)

            @block.vector
            def _(dve):
                dve.sem_inc(head_free, 2)
                dve.sem_inc(pT_dve, 1)
                dve.sem_inc(y_ready, 2)
                dve.wait_ge(mask_loaded, 16)
                with dve.Fori(0, H // 2) as j:
                    st = Steps(dve, steps, j, 4 * n_units)

                    def maximum(n):
                        s, qb = units[n]
                        dve.wait_ge(s_done, j * n_units + n + 1)
                        diag = sc[n % 2][:, qb * P:(qb + 1) * P]
                        st.did(dve.tensor_tensor(diag, diag, mask[:, :], ALU.add))
                        st.wait()
                        st.did(dve.tensor_reduce(mx[:, n % 2:n % 2 + 1], sc[n % 2][:, 0:(qb + 1) * P], AX.X, ALU.max))
                        st.wait()
                        st.did(dve.tensor_scalar(nmx[:, n % 2:n % 2 + 1], mx[:, n % 2:n % 2 + 1], -SCALE, None, ALU.mult))
                        st.wait()
                        dve.sem_inc(mx_ready, 1)

                    def finish(n):
                        s, qb = units[n]
                        for g, blocks in enumerate(groups[n]):
                            m = first_group[n] + g
                            if m % 2 == 0:
                                dve.wait_ge(tp_done, j * n_groups + m + 1)
                                dve.tensor_copy(pT[:, n % 2, blocks[0]:blocks[-1] + 1, :], tp[0][:, 0:len(blocks), :]).then_inc(pT_dve, 1)
                        if qb == 0:
                            dve.wait_ge(y_stored[s], 16 * (j + 1))
                        dve.wait_ge(p_ready, j * n_units + n + 3)
                        st.did(dve.reciprocal(inv[:, n % 2:n % 2 + 1], total[:, n % 2:n % 2 + 1]))
                        st.wait()
                        dve.wait_ge(o_done, j * n_units + n + 1)
                        dve.tensor_scalar(y[:, s, qb, :], op[n % 2][:, :], inv[:, n % 2:n % 2 + 1], None, ALU.mult).then_inc(y_ready, 1)

                    maximum(0)
                    for n in range(1, n_units):
                        maximum(n)
                        finish(n - 1)
                        if units[n][1] == 0:
                            dve.wait_ge(y_ready, j * n_units + n + 2)
                            dve.sem_inc(head_free, 1)
                    finish(n_units - 1)
                    dve.wait_ge(y_ready, j * n_units + n_units + 2)
                    dve.sem_inc(head_free, 1)
                    st.end()

            @block.scalar
            def _(act):
                act.sem_inc(p_ready, 2)
                act.sem_inc(pT_act, 1)
                for s in range(2):
                    act.sem_inc(y_stored[s], 16)
                with act.Fori(0, H // 2) as j:
                    def exponentials(n):
                        s, qb = units[n]
                        act.wait_ge(mx_ready, j * n_units + n + 1)
                        act.activation(probs[:, n % 2, 0:(qb + 1) * P], sc[n % 2][:, 0:(qb + 1) * P], ACT.Exp,
                                       bias=nmx[:, n % 2:n % 2 + 1], scale=SCALE, accum_out=total[:, n % 2:n % 2 + 1]).then_inc(p_ready, 1)

                    def copies(n):
                        s, qb = units[n]
                        for g, blocks in enumerate(groups[n]):
                            m = first_group[n] + g
                            if m % 2 == 1:
                                act.wait_ge(tp_done, j * n_groups + m + 1)
                                act.activation(pT[:, n % 2, blocks[0]:blocks[-1] + 1, :], tp[1][:, 0:len(blocks), :], ACT.Copy).then_inc(pT_act, 1)
                        if qb == TP - 1:
                            act.wait_ge(y_ready, j * n_units + n + 3)
                            act.dma_start(d["Y"][0:SEQ, ds(CONVW + (2 * j + s) * VD, VD)].rearrange("(b p) n -> p b n", p=P),
                                          y[:, s, :, :]).then_inc(y_stored[s], 16)

                    exponentials(0)
                    for n in range(1, n_units):
                        exponentials(n)
                        copies(n - 1)
                    copies(n_units - 1)
                for s in range(2):
                    act.wait_ge(y_stored[s], 16 * (H // 2 + 1))

            @block.gpsimd
            def _(pool):
                IN_ALL = 64 * TP + 48
                pool.dma_start(cwr[:, :, :].rearrange("p k n -> p (k n)"),
                               d["conv_w"].rearrange("l k n -> l (k n)")[ds(layer, 1), :].broadcast_to([P, 3 * CONVW])).then_inc(cv_w, 16)
                pool.wait_ge(cv_w, 16 * (layer + 1))
                pool.sem_inc(paced, 1)

                def gated(st, n):
                    for k in range(3):
                        st.did(pool.tensor_tensor(yc[0:n, :] if k == 0 else cch[0:n, k, 0:CONVW], u[0:n, k, :], cwr[0:n, k, :], ALU.mult))
                    for k in range(1, 3):
                        st.wait()
                        st.did(pool.tensor_tensor(yc[0:n, :], yc[0:n, :], cch[0:n, k, 0:CONVW], ALU.add))
                    st.wait()
                    st.did(pool.tensor_tensor(yc[0:n, :], yc[0:n, :], cb[0:n, :], ALU.mult))
                    st.wait()

                with pool.Fori(0, TP) as t:
                    st = Steps(pool, cv, t, 9)
                    for k in range(3):
                        pool.dma_start(cch[:, k, :], d["Z"][ds(t * P + k, P), C_CC:C_CC + 2 * CONVW]).then_inc(cv_in, 16)
                    pool.dma_start(cb[:, :], d["Z"][ds(PAD + t * P, P), C_CB:C_CB + CONVW]).then_inc(cv_in, 16)
                    pool.wait_ge(cv_in, IN_ALL * layer + 64 * (t + 1))
                    for k in range(3):
                        st.did(pool.tensor_tensor(u[:, k, :], cch[:, k, 0:CONVW], cch[:, k, CONVW:], ALU.mult))
                    st.wait()
                    gated(st, P)
                    st.end()
                    pool.dma_start(d["Y"][rows(t), 0:CONVW], yc[:, :]).then_inc(cv_out, 16)
                    pool.wait_ge(cv_out, 16 * (TP + 1) * layer + 16 * (t + 1))
                    pool.sem_inc(paced, 1)
                pool.dma_start(of_layer(d["conv_p"], layer), u[P - 2:P, 2, :]).then_inc(cv_state, 16)
                pool.wait_ge(cv_state, 32 * layer + 16)
                pool.sem_inc(paced, 1)
                s0 = PAD + SEQ
                pool.dma_start(cch[0:DECB, 2, :], d["Z"][s0:s0 + DECB, C_CC:C_CC + 2 * CONVW]).then_inc(cv_in, 16)
                pool.dma_start(cb[0:DECB, :], d["Z"][s0:s0 + DECB, C_CB:C_CB + CONVW]).then_inc(cv_in, 16)
                pool.dma_start(u[0:DECB, 0:2, :], of_layer(d["state_conv"], layer)).then_inc(cv_in, 16)
                pool.wait_ge(cv_in, IN_ALL * (layer + 1))
                st = Steps(pool, cv, TP, 7)
                st.base = 9 * TP
                st.did(pool.tensor_tensor(u[0:DECB, 2, :], cch[0:DECB, 2, 0:CONVW], cch[0:DECB, 2, CONVW:], ALU.mult))
                st.wait()
                gated(st, DECB)
                pool.dma_start(d["Y"][SEQ:SEQ + DECB, 0:CONVW], yc[0:DECB, :]).then_inc(cv_out, 16)
                pool.dma_start(of_layer(d["conv_s"], layer), u[0:DECB, 1:3, :]).then_inc(cv_state, 16)
                pool.wait_ge(cv_out, 16 * (TP + 1) * (layer + 1))
                pool.sem_inc(paced, 1)
                pool.wait_ge(cv_state, 32 * (layer + 1))
                pool.sem_inc(paced, 1)



VX = DH + 1


def mlstm_prompt(nc, d, layer, ident):
    with Phase(nc) as ph:
        gz = ph.sb("ml_gz", [P, TP, 2 * NH])
        gbias = ph.sb("ml_gbias", [P, 2 * NH])
        headrow = ph.sb("ml_headrow", [NH, NH, P])
        maskT = ph.sb("ml_maskT", [P, P])
        gi = ph.sb("ml_gi", [NH, SEQ])
        gf = ph.sb("ml_gf", [NH, SEQ])
        lf = ph.sb("ml_lf", [NH, SEQ])
        w1 = ph.sb("ml_w1", [NH, SEQ])
        w2 = ph.sb("ml_w2", [NH, SEQ])
        w3 = ph.sb("ml_w3", [NH, SEQ])
        keep = ph.sb("ml_keep", [NH, SEQ])
        m = ph.sb("ml_m", [NH, SEQ])
        b = ph.sb("ml_b", [NH, SEQ])
        mprev = ph.sb("ml_mprev", [NH, TP])
        rows4 = ph.sb("ml_rows", [NH, 4, SEQ])
        a = ph.sb("ml_a", [NH, SEQ])
        cols = ph.sb("ml_cols", [P, 4, TP, NH])
        wold = ph.sb("ml_wold", [DH, NH, TP])
        x = ph.sb("ml_x", [P, 2, 4 * MW])
        ks = ph.sb("ml_ks", [P, 2, NH, DH])
        qs = ph.sb("ml_qs", [P, 2, NH, DH])
        vx = ph.sb("ml_vx", [P, 2, NH, VX])
        vw = ph.sb("ml_vw", [P, 2, NH, VX])
        qT = ph.sb("ml_qT", [DH, 2, NH, P])
        qsT = ph.sb("ml_qsT", [DH, 2, NH, P])
        kT = ph.sb("ml_kT", [DH, 2, NH, P])
        e = ph.sb("ml_e", [P, 2, NH, P])
        dd = ph.sb("ml_d", [P, 2, NH, P])
        sm = ph.sb("ml_s", [P, 2, NH, P])
        state = ph.sb("ml_state", [DH, 2, NH, VX])
        carry = ph.sb("ml_carry", [DH, NH, VX])
        den = ph.sb("ml_den", [P, NH])
        den2 = ph.sb("ml_den2", [P, NH])
        rden = ph.sb("ml_rden", [P, NH])
        so = ph.sb("ml_so", [P, 2, NH, DH])
        hh = ph.sb("ml_h", [P, NH, DH])
        y = ph.sb("ml_y", [P, 2, MW])
        cT = ph.sb("ml_cT", [VX, NH, DH])
        pg = [ph.ps(f"ml_pg{i}", [P, 512]) for i in range(3)]
        pa = ph.ps("ml_pa", [P, NH, P])
        pqk = ph.ps("ml_pqk", [P, NH, P])
        pn = ph.ps("ml_pn", [P, NH, VX])
        pu = ph.ps("ml_pu", [DH, NH, VX])
        px = ph.ps("ml_px", [P, 512])
        loaded0, x_loaded, y_stored = ph.sem("loaded0"), ph.sem2("x_loaded"), ph.sem2("y_stored")
        g_tp, g_steps, g_act, g_cols = ph.sem("g_tp"), ph.sem("g_steps"), ph.sem("g_act"), ph.sem("g_cols")
        v_steps, x_free, scaled, tp_done = ph.sem("v_steps"), ph.sem("x_free"), ph.sem("scaled"), ph.sem("tp_done")
        qT_ready, kT_ready, ab_done, e_ready = ph.sem("qT_ready"), ph.sem("kT_ready"), ph.sem("ab_done"), ph.sem("e_ready")
        d_ready, s_ready, n_done, u_done = ph.sem("d_ready"), ph.sem("s_ready"), ph.sem("n_done"), ph.sem("u_done")
        st_ready, den_ready, y_ready, so_ready = ph.sem("st_ready"), ph.sem("den_ready"), ph.sem("y_ready"), ph.sem("so_ready")
        carry_ready = ph.sem("carry_ready")
        final, out_done = ph.sem("final"), ph.sem("out_done")

        def chunks(eng):
            with eng.Fori(0, TP // 2) as r:
                for s in range(2):
                    yield 2 * r + s, s, r

        with nc.Block() as block:
            @block.sync
            def _(sp):
                sp.dma_start(gz[:, :, :], d["Z"][PAD:PAD + SEQ, C_MI:C_MI + 2 * NH].rearrange("(c p) n -> p c n", p=P)).then_inc(loaded0, 16)
                sp.dma_start(gbias[:, :], row_of_layer(d["mlstm_gate_b"], layer)).then_inc(loaded0, 16)
                sp.dma_start(headrow[:, :, :], d["c_headrow"]).then_inc(loaded0, 16)
                sp.dma_start(maskT[:, :], d["c_causalT"]).then_inc(loaded0, 16)
                for t, s, r in chunks(sp):
                    sp.wait_ge(x_free, t + 1)
                    sp.dma_start(x[:, s, :], d["Z"][ds(PAD + t * P, P), C_MQ:C_MQ + 4 * MW]).then_inc(x_loaded[s], 16)
                sp.wait_ge(final, 1)
                sp.dma_start(of_layer(d["C_p"], layer).rearrange("h v e -> v h e"), cT[0:DH, :, :]).then_inc(out_done, 16)
                sp.dma_start(of_layer(d["n_p"], layer).rearrange("(o h) e -> o h e", o=1), cT[DH:VX, :, :]).then_inc(out_done, 16)
                sp.dma_start(of_layer(d["m_p"], layer).rearrange("(h o) -> h o", o=1), m[:, SEQ - 1:SEQ]).then_inc(out_done, 16)
                sp.wait_ge(out_done, 48)

            @block.tensor
            def _(pe):
                pe.wait_ge(g_steps, 1)
                for c in range(TP):
                    pe.transpose(pg[c // 4][0:NH, (c % 4) * P:(c % 4 + 1) * P], gz[:, c, 0:NH], ident[:, :])
                for c in range(TP):
                    dst = (px, pg[2])[c // 4]
                    last = pe.transpose(dst[0:NH, (c % 4) * P:(c % 4 + 1) * P], gz[:, c, NH:], ident[:, :])
                last.then_inc(g_tp, 1)
                pe.wait_ge(g_cols, 1)
                for k in range(4):
                    for c in range(TP):
                        pe.transpose(pg[0][:, (k * TP + c) * NH:(k * TP + c + 1) * NH], rows4[:, k, c * P:(c + 1) * P], ident[0:NH, 0:NH])
                for h in range(NH):
                    last = pe.matmul(px[0:DH, h * TP:(h + 1) * TP], headrow[:, h, 0:DH],
                                     rows4[:, 1, :].rearrange("h (c t) -> h c t", c=TP)[:, :, P - 1], start=True, stop=True)
                last.then_inc(g_tp, 1)
                pe.wait_ge(g_cols, 2)
                for t, s, r in chunks(pe):
                    pe.wait_ge(x_loaded[s], 16 * (r + 1))
                    pe.wait_ge(scaled, t + 1)
                    for h in range(NH):
                        last = pe.matmul(pa[:, h, :], headrow[:, h, :], a[:, ds(t * P, P)], start=True, stop=True)
                    last.then_inc(ab_done, 1)
                    for h in range(NH):
                        pe.transpose(pg[0][0:DH, h * P:(h + 1) * P], x[:, s, h * DH:(h + 1) * DH], ident[:, :])
                    for h in range(NH):
                        pe.transpose(pg[1][0:DH, h * P:(h + 1) * P], qs[:, s, h, :], ident[:, :])
                    for h in range(NH):
                        last = pe.transpose(pg[2][0:DH, h * P:(h + 1) * P], ks[:, s, h, :], ident[:, :])
                    last.then_inc(tp_done, 1)
                    pe.wait_ge(qT_ready, 2 * (t + 1))
                    pe.wait_ge(kT_ready, t + 1)
                    for h in range(NH):
                        last = pe.matmul(pqk[:, h, :], kT[:, s, h, :], qT[:, s, h, :], start=True, stop=True)
                    last.then_inc(ab_done, 1)
                    for h in range(NH):
                        last = pe.matmul(pu[:, h, :], ks[:, s, h, :], vw[:, s, h, :], start=True, stop=True)
                    last.then_inc(u_done, 1)
                    pe.wait_ge(s_ready, t + 1)
                    pe.wait_ge(st_ready, t + 1)
                    for h in range(NH):
                        pe.matmul(pn[:, h, :], sm[:, s, h, :], vx[:, s, h, :], start=True, stop=False)
                        last = pe.matmul(pn[:, h, :], qsT[:, s, h, :], state[:, s, h, :], start=False, stop=True)
                    last.then_inc(n_done, 1)
                pe.wait_ge(carry_ready, 1)
                for h in range(NH):
                    last = pe.transpose(px[0:VX, h * DH:(h + 1) * DH], carry[:, h, :], ident[0:DH, 0:DH])
                last.then_inc(g_tp, 1)

            @block.vector
            def _(dve):
                g = Steps(dve, g_steps, 0, 29)
                dve.wait_ge(loaded0, 64)
                g.did(dve.tensor_tensor(gz[:, :, :], gz[:, :, :], gbias[:, :].unsqueeze(1).broadcast_to([P, TP, 2 * NH]), ALU.add))
                g.did(dve.memset(keep[:, :], 1.0))
                g.wait()
                g.did(dve.memset(keep[:, :].rearrange("h (c t) -> h c t", c=TP)[:, :, 0:1], 0.0))
                dve.wait_ge(g_tp, 1)
                for c in range(2):
                    half = slice(c * 512, (c + 1) * 512)
                    g.did(dve.tensor_copy(gi[:, half], pg[c][0:NH, :]))
                    g.did(dve.tensor_copy(gf[:, half], (px, pg[2])[c][0:NH, :]))
                g.wait()
                g.did(dve.tensor_scalar(w1[:, :], gf[:, :], -1.0, None, ALU.mult))
                g.wait()
                g.did(dve.tensor_tensor(w1[:, :], w1[:, :], gf[:, :], ALU.min))
                g.wait()
                dve.wait_ge(g_act, 1)
                g.did(dve.tensor_scalar(w1[:, :], w2[:, :], 1.0, None, ALU.add))
                g.wait()
                g.did(dve.tensor_scalar(w3[:, :], w1[:, :], -1.0, None, ALU.add))
                g.wait()
                g.did(dve.tensor_tensor(w3[:, :], w2[:, :], w3[:, :], ALU.subtract))
                g.did(dve.reciprocal(b[:, :], w1[:, :]))
                g.wait()
                g.did(dve.tensor_tensor(w3[:, :], w3[:, :], b[:, :], ALU.mult))
                dve.wait_ge(g_act, 2)
                g.wait()
                g.did(dve.tensor_tensor(w3[:, :], w3[:, :], lf[:, :], ALU.add))
                g.wait()
                g.did(dve.scalar_tensor_tensor(lf[:, :], gf[:, :], 0.0, w3[:, :], ALU.min, ALU.subtract))
                g.wait()
                g.did(dve.tensor_tensor_scan(m[:, :], lf[:, :], gi[:, :], 0.0, ALU.add, ALU.max))
                g.did(dve.tensor_tensor_scan(b[:, :], keep[:, :], lf[:, :], 0.0, ALU.mult, ALU.add))
                g.did(dve.memset(mprev[:, 0:1], 0.0))
                g.wait()
                g.did(dve.tensor_copy(mprev[:, 1:TP], m[:, :].rearrange("h (c t) -> h c t", c=TP)[:, 0:TP - 1, P - 1]))
                g.did(dve.tensor_tensor(a[:, :], b[:, :], m[:, :], ALU.subtract))
                g.did(dve.tensor_tensor(rows4[:, 0, :], gi[:, :], b[:, :], ALU.subtract))
                g.wait()
                chunked = lambda ap: ap.rearrange("h (c t) -> h c t", c=TP)
                g.did(dve.tensor_tensor(chunked(w1[:, :]), chunked(a[:, :]), mprev[:, :].unsqueeze(2).broadcast_to([NH, TP, P]), ALU.add))
                g.did(dve.tensor_tensor(chunked(w2[:, :]), chunked(rows4[:, 0, :]), chunked(a[:, :])[:, :, P - 1:P].broadcast_to([NH, TP, P]), ALU.add))
                g.did(dve.memset(carry[:, :, :], 0.0))
                g.did(dve.memset(state[:, :, :, :], 0.0))
                g.did(dve.memset(vx[:, :, :, :], 1.0))
                g.wait()
                dve.wait_ge(g_tp, 2)
                g.did(dve.tensor_copy(cols[:, :, :, :].rearrange("p k c h -> p (k c h)"), pg[0][:, 0:4 * TP * NH]))
                g.did(dve.tensor_copy(wold[:, :, :].rearrange("p h c -> p (h c)"), px[0:DH, 0:NH * TP]))
                g.wait()
                g.end()
                dve.sem_inc(g_cols, 1)
                dve.sem_inc(st_ready, 1)
                for t, s, r in chunks(dve):
                    v = Steps(dve, v_steps, t, 9)
                    c_col, wi, ws, em = (cols[:, k, ds(t, 1), :].rearrange("p c h -> p (c h)") for k in range(4))
                    xq, xk, xv = (x[:, s, i * MW:(i + 1) * MW].rearrange("p (h n) -> p h n", h=NH) for i in range(3))
                    dve.wait_ge(x_loaded[s], 16 * (r + 1))
                    dve.wait_ge(n_done, t + 1)
                    v.did(dve.tensor_scalar(ks[:, s], xk, DH ** -0.5, None, ALU.mult))
                    v.did(dve.tensor_tensor(qs[:, s], xq, wi.unsqueeze(2).broadcast_to([P, NH, DH]), ALU.mult))
                    v.did(dve.tensor_copy(vx[:, s, :, 0:DH], xv))
                    v.wait()
                    v.did(dve.tensor_tensor(vw[:, s], vx[:, s], ws.unsqueeze(2).broadcast_to([P, NH, VX]), ALU.mult))
                    v.wait()
                    dve.sem_inc(scaled, 1)
                    dve.wait_ge(ab_done, 2 * t + 1)
                    dve.tensor_tensor(e[:, s], pa[:, :, :], maskT[:, :].unsqueeze(1).broadcast_to([P, NH, P]), ALU.add).then_inc(e_ready, 1)
                    dve.wait_ge(tp_done, t + 1)
                    dve.tensor_copy(kT[:, s], pg[2][0:DH, :].rearrange("p (h n) -> p h n", h=NH)).then_inc(kT_ready, 1)
                    dve.wait_ge(d_ready, t + 1)
                    dve.wait_ge(ab_done, 2 * t + 2)
                    dve.tensor_tensor(sm[:, s], pqk[:, :, :], dd[:, s], ALU.mult).then_inc(s_ready, 1)
                    dve.wait_ge(u_done, t + 1)
                    for h in range(NH):
                        last = dve.scalar_tensor_tensor(state[:, 1 - s, h, :], state[:, s, h, :], wold[:, h, ds(t, 1)], pu[:, h, :], ALU.mult, ALU.add)
                    v.did(last)
                    v.wait()
                    dve.sem_inc(st_ready, 1)
                    dve.wait_ge(den_ready, t + 1)
                    v.did(dve.tensor_tensor(den2[:, :], den[:, :], em, ALU.max))
                    v.wait()
                    v.did(dve.reciprocal(rden[:, :], den2[:, :]))
                    v.wait()
                    v.did(dve.tensor_tensor(hh[:, :, :], pn[:, :, 0:DH], rden[:, :].unsqueeze(2).broadcast_to([P, NH, DH]), ALU.mult))
                    v.wait()
                    dve.wait_ge(so_ready, t + 1)
                    dve.wait_ge(y_stored[s], 16 * (r + 1))
                    v.did(dve.tensor_tensor(y[:, s, :].rearrange("p (h n) -> p h n", h=NH), hh[:, :, :], so[:, s], ALU.mult))
                    v.wait()
                    dve.sem_inc(y_ready, 1)
                    v.end()
                v = Steps(dve, v_steps, TP, 2)
                v.base = 9 * TP
                v.did(dve.tensor_copy(carry[:, :, :], state[:, 0]))
                v.wait()
                dve.sem_inc(carry_ready, 1)
                dve.wait_ge(g_tp, 3)
                v.did(dve.tensor_copy(cT[:, :, :], px[0:VX, 0:NH * DH].rearrange("p (h n) -> p h n", h=NH)))
                v.wait()
                dve.sem_inc(final, 1)

            @block.scalar
            def _(act):
                for s in range(2):
                    act.sem_inc(y_stored[s], 16)
                act.sem_inc(n_done, 2)
                act.sem_inc(x_free, 2)
                act.wait_ge(g_steps, 9)
                act.activation(w2[:, :], w1[:, :], ACT.Exp).then_inc(g_act, 1)
                act.wait_ge(g_steps, 10)
                act.activation(lf[:, :], w1[:, :], ACT.Ln).then_inc(g_act, 1)
                act.wait_ge(g_steps, 24)
                act.activation(rows4[:, 1, :], w1[:, :], ACT.Exp)
                act.activation(rows4[:, 2, :], w2[:, :], ACT.Exp)
                act.activation(rows4[:, 3, :], m[:, :], ACT.Exp, scale=-1.0).then_inc(g_act, 1)
                act.wait_ge(g_act, 3)
                act.sem_inc(g_cols, 1)
                act.wait_ge(g_cols, 2)
                for t, s, r in chunks(act):
                    act.wait_ge(tp_done, t + 1)
                    act.activation(qT[:, s], pg[0][0:DH, :].rearrange("p (h n) -> p h n", h=NH), ACT.Copy).then_inc(qT_ready, 1)
                    act.activation(qsT[:, s], pg[1][0:DH, :].rearrange("p (h n) -> p h n", h=NH), ACT.Copy).then_inc(qT_ready, 1)
                    act.wait_ge(e_ready, t + 1)
                    for h in range(NH):
                        last = act.activation(dd[:, s, h, :], e[:, s, h, :], ACT.Exp, bias=cols[:, 0, ds(t, 1), h])
                    last.then_inc(d_ready, 1)
                    act.activation(so[:, s], x[:, s, 3 * MW:].rearrange("p (h n) -> p h n", h=NH), ACT.Sigmoid).then_inc(so_ready, 1)
                    act.wait_ge(n_done, t + 3)
                    act.activation(den[:, :], pn[:, :, DH], ACT.Abs).then_inc(den_ready, 1)
                    act.wait_ge(so_ready, t + 1)
                    act.sem_inc(x_free, 1)
                    act.wait_ge(y_ready, t + 1)
                    act.dma_start(d["Y"][rows(t), CONVW + H * VD:], y[:, s, :]).then_inc(y_stored[s], 16)
                for s in range(2):
                    act.wait_ge(y_stored[s], 16 * (TP // 2 + 1))



def sample_attention(nc, d, layer, ident):
    BH = DECB * H
    LX = KVR + 1
    with Phase(nc) as ph:
        pt = ph.sb("sa_pt", [1, DECB * PAGES], I32)
        ckv = ph.sb("sa_ckv", [P, DECB * PAGES, LX])
        kr = ph.sb("sa_kr", [P, DECB * PAGES, ROPE])
        cn = ph.sb("sa_cn", [DECB, LX])
        krn = ph.sb("sa_krn", [DECB, ROPE])
        own = ph.sb("sa_own", [DECB, DECB, H])
        ones = ph.sb("sa_ones", [BH, P])
        wukv = ph.sb("sa_wukv", [P, H, NOPE + VD])
        wukT = ph.sb("sa_wukT", [NOPE, H, P])
        wuv = ph.sb("sa_wuv", [P, H, VD])
        qTs = ph.sb("sa_qT", [QK, H, DECB])
        qlat = ph.sb("sa_qlat", [P, DECB, H])
        qr = ph.sb("sa_qr", [ROPE, DECB, H])
        qrd = ph.sb("sa_qrd", [P, DECB, 4, H])
        cnT = ph.sb("sa_cnT", [P, DECB])
        krnT = ph.sb("sa_krnT", [ROPE, DECB])
        cT = ph.sb("sa_cT", [P, 2, PAGES, P])
        krT = ph.sb("sa_krT", [P, 2, PAGES // 4, P])
        S = ph.sb("sa_S", [P, DECB, PAGES, H])
        SX = ph.sb("sa_SX", [DECB, BH])
        mxp = ph.sb("sa_mxp", [P, DECB, H])
        mcol = ph.sb("sa_mcol", [BH, 1])
        mdiag = ph.sb("sa_mdiag", [BH, BH])
        mb = ph.sb("sa_mb", [P, DECB, H])
        pst = ph.sb("sa_pst", [P, 2, PAGES, H])
        pxst = ph.sb("sa_pxst", [DECB, 2, H])
        on = ph.sb("sa_on", [H, DECB, KVR])
        ro = ph.sb("sa_ro", [H, 2])
        ol = ph.sb("sa_ol", [P, H, DECB])
        att = ph.sb("sa_att", [DECB, H * VD])
        tpb = [ph.ps(f"sa_tp{i}", [P, 4, P]) for i in range(4)]
        ktp = ph.ps("sa_ktp", [P, 4, P])
        scp = [ph.ps(f"sa_sc{i}", [P, PAGES, H]) for i in range(2)]
        misc = ph.ps("sa_misc", [P, 512])
        loaded0, qloaded = ph.sem("loaded0"), ph.sem("pt_loaded")
        pages = [ph.sem(f"pages{b}") for b in range(DECB)]
        prep, pe_prep, st_q = ph.sem("prep"), ph.sem("pe_prep"), ph.sem("st_q")
        tp_done, cT_dve, cT_act, sc_done = ph.sem("tp_done"), ph.sem("cT_dve"), ph.sem("cT_act"), ph.sem("sc_done")
        S_ready, mx_done, glob, p_ready = ph.sem("S_ready"), ph.sem("mx_done"), ph.sem("glob"), ph.sem("p_ready")
        pst_ready, o_done, on_ready, oT_done = ph.sem("pst_ready"), ph.sem("o_done"), ph.sem("on_ready"), ph.sem("oT_done")
        ol_ready, b_steps, att_done, att_ready, out_done = (ph.sem(n) for n in ("ol_ready", "b_steps", "att_done", "att_ready", "out_done"))
        with nc.Block() as block:
            @block.sync
            def _(sp):
                sp.dma_start(pt[:, :], d["page_table"]).then_inc(qloaded, 16)
                sp.dma_start(wukv[:, :, :].rearrange("p h n -> p (h n)"), of_layer(d["w_ukv"], layer)).then_inc(loaded0, 16)
                sp.dma_start(qTs[:, :, :], d["QT"][:, :, SEQ:SEQ + DECB].rearrange("h p n -> p h n")).then_inc(loaded0, 16)
                sp.dma_start(cn[:, 0:KVR], of_layer(d["ckv_all"], layer)[SEQ:SEQ + DECB]).then_inc(loaded0, 16)
                sp.dma_start(krn[:, :], of_layer(d["krope_all"], layer)[SEQ:SEQ + DECB]).then_inc(loaded0, 16)
                sp.dma_start(own[:, :, :].rearrange("p b h -> p (b h)"), d["c_own"]).then_inc(loaded0, 16)
                sp.wait_ge(qloaded, 16)
                n_phys = d["cache_ckv"].shape[1]
                for b in range(DECB):
                    with sp.Fori(0, PAGES) as p:
                        page = sp.value_load(pt[0:1, ds(b * PAGES + p, 1)], min_val=0, max_val=n_phys - 1)
                        sp.dma_start(ckv[:, ds(b * PAGES + p, 1), 0:KVR].rearrange("k o n -> k (o n)"),
                                     d["cache_ckv"][ds(layer, 1), ds(page, 1)].rearrange("l g k n -> (l g k) n")).then_inc(pages[b], 16)
                        sp.dma_start(kr[:, ds(b * PAGES + p, 1), :].rearrange("k o n -> k (o n)"),
                                     d["cache_krope"][ds(layer, 1), ds(page, 1)].rearrange("l g k n -> (l g k) n")).then_inc(pages[b], 16)
                sp.wait_ge(att_ready, 1)
                sp.dma_start(d["Y"][SEQ:SEQ + DECB, CONVW:CONVW + H * VD], att[:, :]).then_inc(out_done, 16)
                sp.wait_ge(out_done, 16)

            @block.gpsimd
            def _(pool):
                pool.memset(ones[:, :], 1.0).then_inc(prep, 1)
                pool.memset(qrd[:, :, :, :], 0.0).then_inc(prep, 1)
                pool.memset(cn[:, KVR:], 1.0).then_inc(prep, 1)
                pool.memset(ckv[:, :, KVR:], 1.0).then_inc(prep, 1)

            @block.tensor
            def _(pe):
                pe.wait_ge(loaded0, 80)
                for h in range(H):
                    last = pe.transpose(tpb[h // 4][0:NOPE, h % 4, :], wukv[:, h, 0:NOPE], ident[:, :])
                pe.transpose(misc[:, 0:DECB], cn[:, 0:KVR], ident[0:DECB, 0:DECB])
                pe.transpose(misc[0:ROPE, DECB:2 * DECB], krn[:, :], ident[0:DECB, 0:DECB]).then_inc(pe_prep, 1)
                pe.wait_ge(st_q, 1)
                for h in range(H):
                    last = pe.matmul(misc[:, 64 + h * DECB:64 + (h + 1) * DECB], wukT[:, h, :], qTs[0:NOPE, h, :], start=True, stop=True)
                last.then_inc(pe_prep, 1)
                pe.wait_ge(st_q, 2)
                pe.matmul(misc[0:DECB, 256:256 + BH], cnT[:, :], qlat[:, :, :].rearrange("p b h -> p (b h)"), start=True, stop=False)
                pe.matmul(misc[0:DECB, 256:256 + BH], krnT[:, :], qr[0:ROPE, :, :].rearrange("p b h -> p (b h)"), start=False, stop=True).then_inc(pe_prep, 1)
                for b in range(DECB):
                    s = b % 2
                    pe.wait_ge(pages[b], 32 * PAGES)
                    for g in range(4):
                        pe.wait_ge((cT_dve, cT_act)[g % 2], (3 if g % 2 == 0 else 2) * b + (g // 2) + 1)
                        for c in range(4):
                            last = pe.transpose(tpb[g][:, c, :], ckv[:, b * PAGES + 4 * g + c, 0:KVR], ident[:, :])
                        last.then_inc(tp_done, 1)
                    pe.wait_ge(cT_dve, 3 * b + 3)
                    for c in range(4):
                        last = pe.transpose(ktp[:, c, :], kr[:, b * PAGES + 4 * c:b * PAGES + 4 * c + 4, :].rearrange("k o n -> k (o n)"), ident[:, :])
                    last.then_inc(tp_done, 1)
                    pe.wait_ge(cT_dve, 3 * b + 6)
                    pe.wait_ge(cT_act, 2 * b + 4)
                    pe.wait_ge(S_ready, b + 1)
                    for g in range(4):
                        pe.matmul(scp[s][:, 4 * g:4 * g + 4, :].rearrange("k c h -> k (c h)"), krT[:, s, g, :],
                                  qrd[:, b].rearrange("p c h -> p (c h)"), start=True, stop=True)
                        for c in range(4 * g, 4 * g + 4):
                            last = pe.matmul(scp[s][:, c, :], cT[:, s, c, :], qlat[:, b, :], start=False, stop=True, skip_group_check=True)
                    last.then_inc(sc_done, 1)
                pe.wait_ge(mx_done, DECB + 1)
                pe.transpose(tpb[0][0:BH, 0, :], mxp[:, :, :].rearrange("p b h -> p (b h)"), ident[:, :])
                pe.transpose(tpb[0][0:BH, 1, 0:DECB], SX[:, :], ident[0:DECB, 0:DECB]).then_inc(glob, 1)
                pe.wait_ge(mx_done, DECB + 2)
                pe.matmul(tpb[1][:, 0, 0:BH], ones[:, :], mdiag[:, :], start=True, stop=True).then_inc(glob, 1)
                with pe.Fori(0, DECB // 2) as r:
                    for s in range(2):
                        b = 2 * r + s
                        pe.wait_ge(on_ready, b + 1)
                        pe.wait_ge(pst_ready, b + 1)
                        o = tpb[2 + s][0:H, :, :].rearrange("p a b -> p (a b)")[:, 0:LX]
                        for c in range(PAGES):
                            pe.matmul(o, pst[:, s, c, :], ckv[:, ds(b * PAGES + c, 1), :].rearrange("k o n -> k (o n)"), start=(c == 0), stop=False)
                        pe.matmul(o, pxst[:, s, :], cn[:, :], start=False, stop=True).then_inc(o_done, 1)
                pe.wait_ge(on_ready, DECB + 2)
                for b in range(DECB):
                    last = pe.transpose(tpb[0][:, 0, b * H:(b + 1) * H], on[:, b, :], ident[0:H, 0:H])
                last.then_inc(oT_done, 1)
                pe.wait_ge(ol_ready, 1)
                for h in range(H):
                    last = pe.matmul(misc[0:DECB, h * VD:(h + 1) * VD], ol[:, h, :], wuv[:, h, :], start=True, stop=True)
                last.then_inc(att_done, 1)

            @block.vector
            def _(dve):
                dve.sem_inc(cT_dve, 3)
                dve.sem_inc(on_ready, 2)
                dve.sem_inc(S_ready, 1)
                dve.wait_ge(loaded0, 80)
                dve.wait_ge(prep, 4)
                st = Steps(dve, b_steps, 0, 0)
                st.did(dve.tensor_copy(wuv[:, :, :], wukv[:, :, NOPE:]))
                dve.wait_ge(pe_prep, 1)
                for g in range(2):
                    st.did(dve.tensor_copy(wukT[:, 4 * g:4 * g + 4, :], tpb[g][0:NOPE, :, :]))
                st.did(dve.tensor_copy(cnT[:, :], misc[:, 0:DECB]))
                st.did(dve.tensor_copy(krnT[:, :], misc[0:ROPE, DECB:2 * DECB]))
                st.did(dve.tensor_copy(qr[:, :, :], qTs[NOPE:QK, :, :].rearrange("p h b -> p b h")))
                for g in range(4):
                    st.did(dve.tensor_copy(qrd[32 * g:32 * g + 32, :, g, :], qTs[NOPE:QK, :, :].rearrange("p h b -> p b h")))
                st.wait()
                dve.sem_inc(st_q, 1)
                dve.wait_ge(pe_prep, 2)
                st.did(dve.tensor_copy(qlat[:, :, :], misc[:, 64:64 + BH].rearrange("p (h b) -> p b h", h=H)))
                st.wait()
                dve.sem_inc(st_q, 1)
                dve.wait_ge(pe_prep, 3)
                st.did(dve.tensor_tensor(SX[:, :], misc[0:DECB, 256:256 + BH], own[:, :, :].rearrange("p b h -> p (b h)"), ALU.add))
                st.wait()
                dve.sem_inc(mx_done, 1)
                n0 = st.n
                with dve.Fori(0, DECB // 2) as r:
                    for s in range(2):
                        b = 2 * r + s
                        for g in (0, 2):
                            dve.wait_ge(tp_done, 5 * b + g + 1)
                            dve.tensor_copy(cT[:, s, 4 * g:4 * g + 4, :], tpb[g][:, :, :]).then_inc(cT_dve, 1)
                        dve.wait_ge(tp_done, 5 * b + 5)
                        dve.tensor_copy(krT[:, s, :, :], ktp[:, :, :]).then_inc(cT_dve, 1)
                        dve.wait_ge(S_ready, b + 2)
                        dve.tensor_reduce(mxp[:, ds(b, 1), :].rearrange("p o h -> p (o h)"), S[:, ds(b, 1)].rearrange("p o c h -> p h (o c)"), AX.X, ALU.max).then_inc(mx_done, 1)
                st.n = n0
                dve.wait_ge(glob, 1)
                st.did(dve.tensor_reduce(mcol[:, :], tpb[0][0:BH, 0:2, :].rearrange("p a b -> p (a b)")[:, 0:P + DECB], AX.X, ALU.max))
                st.wait()
                st.did(dve.tensor_scalar(mdiag[:, :], ident[0:BH, 0:BH], mcol[:, 0:1], None, ALU.mult))
                st.wait()
                dve.sem_inc(mx_done, 1)
                dve.wait_ge(glob, 2)
                st.did(dve.tensor_copy(mb[:, :, :].rearrange("p b h -> p (b h)"), tpb[1][:, 0, 0:BH]))
                st.wait()
                dve.wait_ge(S_ready, DECB + 1)
                for b in range(DECB):
                    st.did(dve.tensor_tensor(S[:, b], S[:, b], mb[:, b:b + 1, :].broadcast_to([P, PAGES, H]), ALU.subtract))
                st.did(dve.tensor_tensor(SX[:, :], SX[:, :], mb[0:DECB, :, :].rearrange("p b h -> p (b h)"), ALU.subtract))
                st.wait()
                dve.sem_inc(glob, 1)
                dve.wait_ge(p_ready, 2)
                n1 = st.n
                with dve.Fori(0, DECB // 2) as r:
                    for s in range(2):
                        b = 2 * r + s
                        dve.tensor_copy(pst[:, s], S[:, ds(b, 1)].rearrange("p o c h -> p (o c) h"))
                        dve.tensor_copy(pxst[:, s, :], SX[:, ds(b * H, H)]).then_inc(pst_ready, 1)
                        dve.wait_ge(o_done, b + 1)
                        o = tpb[2 + s][0:H, :, :].rearrange("p a b -> p (a b)")[:, 0:LX]
                        dve.reciprocal(ro[:, s:s + 1], o[:, KVR:]).then_inc(b_steps, 1)
                        dve.wait_ge(b_steps, b + n1 + 1)
                        dve.tensor_scalar(on[:, ds(b, 1), :].rearrange("p o n -> p (o n)"), o[:, 0:KVR], ro[:, s:s + 1], None, ALU.mult).then_inc(on_ready, 1)
                dve.wait_ge(oT_done, 1)
                dve.tensor_copy(ol[:, :, :], tpb[0][:, 0, 0:BH].rearrange("p (b h) -> p h b", b=DECB)).then_inc(ol_ready, 1)
                dve.wait_ge(att_done, 1)
                dve.tensor_copy(att[:, :], misc[0:DECB, 0:H * VD]).then_inc(att_ready, 1)

            @block.scalar
            def _(act):
                act.sem_inc(cT_act, 2)
                with act.Fori(0, DECB // 2) as r:
                    for s in range(2):
                        b = 2 * r + s
                        for g in (1, 3):
                            act.wait_ge(tp_done, 5 * b + g + 1)
                            act.activation(cT[:, s, 4 * g:4 * g + 4, :], tpb[g][:, :, :], ACT.Copy).then_inc(cT_act, 1)
                        act.wait_ge(sc_done, b + 1)
                        act.activation(S[:, ds(b, 1)].rearrange("p o c h -> p (o c) h"), scp[s][:, :, :], ACT.Copy).then_inc(S_ready, 1)
                act.wait_ge(glob, 3)
                act.activation(S[:, :, :, :].rearrange("p b c h -> p (b c h)"), S[:, :, :, :].rearrange("p b c h -> p (b c h)"), ACT.Exp, scale=SCALE).then_inc(p_ready, 1)
                act.activation(SX[:, :], SX[:, :], ACT.Exp, scale=SCALE).then_inc(p_ready, 1)



def mlstm_sample(nc, d, layer, ident):
    BHN, VG, VR = DECB * NH, 4, DH // 4
    G_Q, G_K, G_N, G_I, G_F, G_M, G_BI, G_BF, G_ALL = 0, 64, 128, 192, 193, 194, 195, 196, 197
    with Phase(nc) as ph:
        g = ph.sb("ms_g", [BHN, G_ALL])
        rep = ph.sb("ms_rep", [BHN, P])
        G = ph.sb("ms_G", [P, G_ALL])
        v = ph.sb("ms_v", [P, VR])
        o = ph.sb("ms_o", [P, VR])
        C = ph.sb("ms_C", [P, VR, DH])
        CQ = ph.sb("ms_CQ", [P, VR, DH])
        VK = ph.sb("ms_VK", [P, VR, DH])
        c = ph.sb("ms_c", [P, 32])
        big = ph.sb("ms_big", [P, 2, DH])
        n1 = ph.sb("ms_n1", [P, DH])
        num = ph.sb("ms_num", [P, VR])
        dv = ph.sb("ms_dv", [P, VR])
        y = ph.sb("ms_y", [P, VR])
        gp = ph.ps("ms_gp", [P, G_ALL])
        loaded, repd, steps, acts, out_done = ph.sem("loaded"), ph.sem("repd"), ph.sem("steps"), ph.sem("acts"), ph.sem("out_done")
        ready = ph.sem("ready")
        col = lambda i: c[:, i:i + 1]
        with nc.Block() as block:
            @block.sync
            def _(sp):
                z = d["Z"][PAD + SEQ:PAD + SEQ + DECB]
                for c0, w, src in ((G_Q, DH, z[:, C_MQ:C_MQ + MW].rearrange("b (h n) -> b h n", h=NH)),
                                   (G_K, DH, z[:, C_MK:C_MK + MW].rearrange("b (h n) -> b h n", h=NH)),
                                   (G_I, 1, z[:, C_MI:C_MI + NH].rearrange("b (h o) -> b h o", o=1)),
                                   (G_F, 1, z[:, C_MI + NH:C_MI + 2 * NH].rearrange("b (h o) -> b h o", o=1)),
                                   (G_N, DH, of_layer(d["state_mlstm_n"], layer)),
                                   (G_M, 1, of_layer(d["state_mlstm_m"], layer).rearrange("b (h o) -> b h o", o=1)),
                                   (G_BI, 1, d["mlstm_gate_b"][ds(layer, 1), 0:NH].unsqueeze(2).broadcast_to([DECB, NH, 1])),
                                   (G_BF, 1, d["mlstm_gate_b"][ds(layer, 1), NH:].unsqueeze(2).broadcast_to([DECB, NH, 1]))):
                    sp.dma_start(g[:, c0:c0 + w], src).then_inc(loaded, 16)
                sp.dma_start(v[:, :], z[:, C_MV:C_MV + MW].rearrange("b (q n) -> b q n", n=VR)).then_inc(loaded, 16)
                sp.dma_start(o[:, :], z[:, C_MO:C_MO + MW].rearrange("b (q n) -> b q n", n=VR)).then_inc(loaded, 16)
                sp.dma_start(rep[:, :], d["c_rep"]).then_inc(loaded, 16)
                sp.dma_start(C[:, :, :].rearrange("p v n -> p (v n)"),
                             of_layer(d["state_mlstm_C"], layer).rearrange("b h (g v) n -> (b h g) (v n)", g=VG)).then_inc(loaded, 16)
                sp.wait_ge(ready, 1)
                sp.dma_start(d["Y"][SEQ:SEQ + DECB, CONVW + H * VD:].rearrange("b (q n) -> b q n", n=VR), y[:, :]).then_inc(out_done, 16)
                sp.dma_start(of_layer(d["C_s"], layer).rearrange("r (g m) -> (r g) m", g=VG), C[:, :, :].rearrange("p v n -> p (v n)")).then_inc(out_done, 16)
                sp.dma_start(of_layer(d["n_s"], layer), n1[0:P:VG, :]).then_inc(out_done, 16)
                sp.dma_start(of_layer(d["m_s"], layer).rearrange("(r o) -> r o", o=1), c[0:P:VG, 10:11]).then_inc(out_done, 16)
                sp.wait_ge(out_done, 64)

            @block.tensor
            def _(pe):
                pe.wait_ge(loaded, 192)
                pe.matmul(gp[:, :], rep[:, :], g[:, :], start=True, stop=True).then_inc(repd, 1)

            @block.scalar
            def _(act):
                act.wait_ge(loaded, 192)
                act.activation(o[:, :], o[:, :], ACT.Sigmoid).then_inc(acts, 1)
                act.wait_ge(steps, 5)
                act.activation(col(3), col(2), ACT.Exp).then_inc(acts, 1)
                act.wait_ge(steps, 6)
                act.activation(col(8), col(4), ACT.Ln).then_inc(acts, 1)
                act.wait_ge(steps, 16)
                act.activation(c[:, 13:15], c[:, 11:13], ACT.Exp).then_inc(acts, 1)
                act.activation(col(15), col(10), ACT.Exp, scale=-1.0).then_inc(acts, 1)
                act.wait_ge(steps, 26)
                act.activation(col(20), col(19), ACT.Abs).then_inc(acts, 1)

            @block.vector
            def _(dve):
                st = Steps(dve, steps, 0, 34)

                def do(ins):
                    st.did(ins)
                    st.wait()
                TT, TS = dve.tensor_tensor, dve.tensor_scalar
                dve.wait_ge(repd, 1)
                do(dve.tensor_copy(G[:, :], gp[:, :]))
                q, k, n, i, f, m0 = G[:, G_Q:G_K], G[:, G_K:G_N], G[:, G_N:G_I], G[:, G_I:G_F], G[:, G_F:G_M], G[:, G_M:G_BI]
                do(TT(col(0), i, G[:, G_BI:G_BF], ALU.add))
                do(TT(col(1), f, G[:, G_BF:G_ALL], ALU.add))
                do(TS(col(16), col(1), -1.0, None, ALU.mult))
                do(TT(col(2), col(1), col(16), ALU.min))
                dve.wait_ge(acts, 2)
                do(TS(col(4), col(3), 1.0, None, ALU.add))
                do(TS(col(5), col(4), -1.0, None, ALU.add))
                do(TT(col(5), col(3), col(5), ALU.subtract))
                do(dve.reciprocal(col(6), col(4)))
                do(TT(col(5), col(5), col(6), ALU.mult))
                dve.wait_ge(acts, 3)
                do(TT(col(5), col(5), col(8), ALU.add))
                do(dve.scalar_tensor_tensor(col(7), col(1), 0.0, col(5), ALU.min, ALU.subtract))
                do(TT(col(9), col(7), m0, ALU.add))
                do(TT(col(10), col(9), col(0), ALU.max))
                do(TT(col(11), col(0), col(10), ALU.subtract))
                do(TT(col(12), col(9), col(10), ALU.subtract))
                do(TS(k, k, DH ** -0.5, None, ALU.mult))
                st.did(TT(big[:, 0, :], q, k, ALU.mult))
                do(TT(big[:, 1, :], q, n, ALU.mult))
                do(dve.tensor_reduce(c[:, 17:19], big[:, :, :], AX.X, ALU.add))
                st.did(TT(CQ[:, :, :], C[:, :, :], q.unsqueeze(1).broadcast_to([P, VR, DH]), ALU.mult))
                dve.wait_ge(acts, 5)
                dd, w, em = col(13), col(14), col(15)
                do(TT(col(21), col(17), dd, ALU.mult))
                do(dve.tensor_reduce(num[:, :], CQ[:, :, :], AX.X, ALU.add))
                do(dve.scalar_tensor_tensor(col(19), col(18), w, col(21), ALU.mult, ALU.add))
                do(TS(num[:, :], num[:, :], w, None, ALU.mult))
                do(dve.scalar_tensor_tensor(num[:, :], v[:, :], col(21), num[:, :], ALU.mult, ALU.add))
                dve.wait_ge(acts, 6)
                do(TT(col(22), col(20), em, ALU.max))
                do(dve.reciprocal(col(23), col(22)))
                do(dve.scalar_tensor_tensor(y[:, :], num[:, :], col(23), o[:, :], ALU.mult, ALU.mult))
                do(TS(dv[:, :], v[:, :], dd, None, ALU.mult))
                do(TT(VK[:, :, :], dv[:, :].unsqueeze(2).broadcast_to([P, VR, DH]), k.unsqueeze(1).broadcast_to([P, VR, DH]), ALU.mult))
                do(dve.scalar_tensor_tensor(C[:, :, :], C[:, :, :], w, VK[:, :, :], ALU.mult, ALU.add))
                do(TS(n1[:, :], k, dd, None, ALU.mult))
                do(dve.scalar_tensor_tensor(n1[:, :], n, w, n1[:, :], ALU.mult, ALU.add))
                dve.sem_inc(ready, 1)
                st.end()



NR = NG + NE
ASSIGN = NT * 2


def output_and_route(nc, d, layer, ident):
    w_tok, dx = d["sb_weight"], d["sb_row"]
    with Phase(nc) as ph:
        wout = ph.sb("op_wout", [P, KC, D])
        wpg = ph.sb("op_wpg", [P, KC, D])
        wpe = ph.sb("op_wpe", [P, 2, D])
        wr = ph.sb("op_wr", [P, KC, NR])
        mixg = ph.sb("op_mixg", [P, D])
        g1 = ph.sb("op_g1", [P, D])
        b1 = ph.sb("op_b1", [P, D])
        y = ph.sb("op_y", [P, 2, D])
        x = ph.sb("op_x", [P, 2, D])
        pp = ph.sb("op_p", [P, 2, DPLE])
        T = ph.sb("op_T", [P, KC, P])
        pT = ph.sb("op_pT", [P, 2, P])
        h1 = ph.sb("op_h1", [P, NT, D])
        tmp = ph.sb("op_tmp", [P, D])
        base = ph.sb("op_base", [P, D])
        ss = ph.sb("op_ss", [P, 16])
        sd = ph.sb("op_sd", [P, 16])
        stats = ph.sb("op_stats", [P, 2, 6])
        mv = ph.sb("op_mv", [P, 2])
        hold = ph.sb("op_hold", [1, 1])
        L = ph.sb("op_L", [P, NT, NR])
        tp = [ph.ps(f"op_tp{i}", [P, 4, P]) for i in range(2)]
        op = [ph.ps(f"op_o{i}", [P, 512]) for i in range(2)]
        gp = [ph.ps(f"op_gp{i}", [P, 512]) for i in range(2)]
        lp = ph.ps("op_lp", [P, 512])
        ptp = ph.ps("op_pt", [P, 2, P])
        w_loaded, loaded, base_stored = ph.sem("w_loaded"), ph.sem2("loaded"), ph.sem("base_stored")
        slot_free, steps, sq_done, ms_ready, sd_done = (ph.sem(n) for n in ("slot_free", "steps", "sq_done", "ms_ready", "sd_done"))
        y_ready, tp_done, T_dve, T_act, o_done = (ph.sem(n) for n in ("y_ready", "tp_done", "T_dve", "T_act", "o_done"))
        h1_ready, g_done, sig_done, base_ready = (ph.sem(n) for n in ("h1_ready", "g_done", "sig_done", "base_ready"))
        rb = ph.sb("ro_b", [P, NR])
        idx = ph.sb("ro_idx", [P, NE])
        idxm = ph.sb("ro_idxm", [P, EPG])
        valid = ph.sb("ro_valid", [P, NT])
        before = ph.sb("ro_before", [P, P])
        ones = ph.sb("ro_ones", [P, P])
        part = ph.sb("ro_part", [P, 1])
        m1 = ph.sb("ro_m1", [P, NT])
        m2 = ph.sb("ro_m2", [P, NT])
        f1 = ph.sb("ro_f1", [P, NT])
        gd = ph.sb("ro_gd", [P, NT, NG])
        ge = ph.sb("ro_ge", [P, NT, NG])
        gw = ph.sb("ro_gw", [P, NT])
        ohg = ph.sb("ro_ohg", [P, NT, NG])
        ein = ph.sb("ro_ein", [P, NT, EPG])
        eq = ph.sb("ro_eq", [P, NT, EPG])
        oh = ph.sb("ro_oh", [P, 2, NT, EPG])
        big = ph.sb("ro_big", [P, NT, NE])
        OH = ph.sb("ro_OH", [P, 2, NT, NE])
        OS = ph.sb("ro_OS", [P, NT, NE])
        pre = ph.sb("ro_pre", [P, NT, NE])
        rank = ph.sb("ro_rank", [P, NT, NE])
        cnt = ph.sb("ro_cnt", [P, NE])
        cnti = ph.sb("ro_cnti", [P, NE], I32)
        nb = ph.sb("ro_nb", [P, NE])
        one = ph.sb("ro_one", [P, NE])
        incl = ph.sb("ro_incl", [P, NE])
        start = ph.sb("ro_start", [P, NE])
        bincl = ph.sb("ro_bincl", [P, NE])
        bstart = ph.sb("ro_bstart", [P, NE])
        tx = ph.sb("ro_tx", [P, NE])
        ty = ph.sb("ro_ty", [P, NE])
        sx = ph.sb("ro_sx", [P, NT, NE])
        dxf = ph.sb("ro_dxf", [P, 2, NT])
        tabf = ph.sb("ro_tabf", [P, 4])
        tab = ph.sb("ro_tab", [P, 4], I32)
        r_steps, r_act, r_pe, tab_stored = (ph.sem(n) for n in ("r_steps", "r_act", "r_pe", "tab_stored"))
        scattered = d["sw"]["scattered"]
        r_ready = ph.sem("r_ready")
        with nc.Block() as block:
            @block.sync
            def _(sp):
                for buf, src in ((mixg[:, :], row_of_layer(d["mix_norm_g"], layer)), (g1[:, :], row_of_layer(d["ln1_g"], layer)),
                                 (b1[:, :], row_of_layer(d["ln1_b"], layer)), (rb[:, :], row_of_layer(d["b_route"], layer)),
                                 (wr[:, :, :].rearrange("p k n -> p (k n)"), of_layer(d["w_route"], layer).rearrange("(p k) n -> p (k n)", k=KC)),
                                 (wpe[:, :, :].rearrange("p k n -> p (k n)"), of_layer(d["w_pe"], layer).rearrange("(p k) n -> p (k n)", k=2)),
                                 (idx[:, :], d["c_idx"]), (valid[:, :], d["c_valid"]), (before[:, :], d["c_before"]), (part[:, :], d["c_part"])):
                    sp.dma_start(buf, src).then_inc(w_loaded, 16)
                for buf, src in ((wout, "w_out"), (wpg, "w_pg")):
                    sp.dma_start(buf[:, :, :].rearrange("p k n -> p (k n)"), of_layer(d[src], layer).rearrange("(p k) n -> p (k n)", k=KC)).then_inc(w_loaded, 16)
                for t, s, r in tile_turns(sp):
                    sp.wait_ge(slot_free, t + 1)
                    sp.dma_start(y[:, s, :], d["Y"][rows(t)]).then_inc(loaded[s], 16)
                    sp.dma_start(x[:, s, :], d["H"][rows(t)]).then_inc(loaded[s], 16)
                    sp.dma_start(pp[:, s, :], of_layer(d["p_all"], layer)[rows(t)]).then_inc(loaded[s], 16)
                sp.wait_ge(r_ready, 2)
                sp.dma_start(d["BTAB"].rearrange("o (b n) -> (o b) n", n=4), tab[:, :]).then_inc(tab_stored, 16)
                sp.wait_ge(tab_stored, 16)

            @block.tensor
            def _(pe):
                def transposes(src, t, n):
                    pe.wait_ge(T_dve, 2 * t + n + 1)
                    pe.wait_ge(T_act, 2 * t + n + 1)
                    for c in range(KC):
                        last = pe.transpose(tp[c // 4][:, c % 4, :], src(c), ident[:, :])
                        if c % 4 == 3:
                            last.then_inc(tp_done, 1)
                    pe.wait_ge(T_dve, 2 * t + n + 2)
                    pe.wait_ge(T_act, 2 * t + n + 2)

                pe.wait_ge(w_loaded, 192)
                for t in range(NT):
                    s = t % 2
                    pe.wait_ge(y_ready, t + 1)
                    transposes(lambda c: y[:, s, c::KC], t, 0)
                    for n in range(2):
                        for c in range(KC):
                            last = pe.matmul(op[n][:, :], T[:, c, :], wout[:, c, n * 512:(n + 1) * 512], start=(c == 0), stop=(c == KC - 1))
                        last.then_inc(o_done, 1)
                    for c in range(2):
                        last = pe.transpose(ptp[:, c, :], pp[:, s, c::2], ident[:, :])
                    last.then_inc(g_done, 1)
                    pe.wait_ge(h1_ready, t + 1)
                    transposes(lambda c: h1[:, t, c::KC], t, 1)
                    for n in range(2):
                        for c in range(KC):
                            last = pe.matmul(gp[n][:, :], T[:, c, :], wpg[:, c, n * 512:(n + 1) * 512], start=(c == 0), stop=(c == KC - 1))
                        last.then_inc(g_done, 1)
                    for c in range(KC):
                        last = pe.matmul(lp[:, 0:NR], T[:, c, :], wr[:, c, :], start=(c == 0), stop=(c == KC - 1))
                    for n in range(2):
                        for c in range(2):
                            last = pe.matmul(op[n][:, :], pT[:, c, :], wpe[:, c, n * 512:(n + 1) * 512], start=(c == 0), stop=(c == 1))
                    last.then_inc(g_done, 1)
                pe.wait_ge(r_ready, 1)
                pe.matmul(gp[0][:, 0:NT * NE], ones[:, :], OS[:, :, :].rearrange("p t e -> p (t e)"), start=True, stop=True)
                pe.matmul(gp[1][:, 0:NT * NE], before[:, :], OS[:, :, :].rearrange("p t e -> p (t e)"), start=True, stop=True).then_inc(r_pe, 1)

            @block.scalar
            def _(act):
                act.sem_inc(T_act, 1)
                for t in range(NT):
                    s = t % 2
                    act.wait_ge(loaded[s], 48 * (t // 2 + 1))
                    if t >= 1:
                        act.wait_ge(base_ready, t)
                    act.activation(tmp[:, :], y[:, s, :], ACT.Square).then_inc(sq_done, 1)
                    act.wait_ge(ms_ready, 2 * t + 1)
                    act.activation(sd[:, :], ss[:, :], ACT.Sqrt).then_inc(sd_done, 1)
                    act.wait_ge(tp_done, 4 * t + 2)
                    act.activation(T[:, 4:8, :], tp[1][:, :, :], ACT.Copy).then_inc(T_act, 1)
                    act.wait_ge(ms_ready, 2 * t + 2)
                    act.activation(sd[:, 0:1], ss[:, 0:1], ACT.Sqrt).then_inc(sd_done, 1)
                    act.wait_ge(g_done, 4 * t + 1)
                    act.activation(pT[:, :, :], ptp[:, :, :], ACT.Copy)
                    act.wait_ge(tp_done, 4 * t + 4)
                    act.activation(T[:, 4:8, :], tp[1][:, :, :], ACT.Copy).then_inc(T_act, 1)
                    for n in range(2):
                        act.wait_ge(g_done, 4 * t + 2 + n)
                        act.activation(tmp[:, n * 512:(n + 1) * 512], gp[n][:, :], ACT.Sigmoid).then_inc(sig_done, 1)
                    act.wait_ge(base_ready, t + 1)
                    act.dma_start(d["BASE"][rows(t)], base[:, :]).then_inc(base_stored, 16)
                act.wait_ge(base_stored, 16 * NT)
                act.wait_ge(r_steps, 2)
                act.activation(ge[:, :, :], gd[:, :, :], ACT.Exp).then_inc(r_act, 1)
                act.wait_ge(r_steps, 26)
                act.activation(f1[:, :], m1[:, :], ACT.Exp).then_inc(r_act, 1)

            @block.vector
            def _(dve):
                dve.sem_inc(slot_free, 2)
                dve.sem_inc(T_dve, 1)
                dve.wait_ge(w_loaded, 192)
                st = Steps(dve, steps, 0, 0)
                for t in range(NT):
                    s = t % 2
                    y16 = y[:, s, :].rearrange("p (h n) -> p h n", h=16)
                    dve.wait_ge(sq_done, t + 1)
                    st.did(dve.tensor_reduce(ss[:, :], tmp[:, :].rearrange("p (h n) -> p h n", h=16), AX.X, ALU.add))
                    st.wait()
                    st.did(dve.tensor_scalar(ss[:, :], ss[:, :], 1.0 / 64, RMS_EPS, ALU.mult, ALU.add))
                    st.wait()
                    dve.sem_inc(ms_ready, 1)
                    dve.wait_ge(sd_done, 2 * t + 1)
                    st.did(dve.reciprocal(ss[:, :], sd[:, :]))
                    st.wait()
                    st.did(dve.tensor_tensor(y16, y16, ss[:, :].unsqueeze(2).broadcast_to([P, 16, 64]), ALU.mult))
                    st.wait()
                    dve.tensor_tensor(y[:, s, :], y[:, s, :], mixg[:, :], ALU.mult).then_inc(y_ready, 1)
                    dve.wait_ge(tp_done, 4 * t + 1)
                    dve.tensor_copy(T[:, 0:4, :], tp[0][:, :, :]).then_inc(T_dve, 1)
                    for n in range(2):
                        dve.wait_ge(o_done, 2 * t + n + 1)
                        st.did(dve.scalar_tensor_tensor(x[:, s, n * 512:(n + 1) * 512], x[:, s, n * 512:(n + 1) * 512], ALPHA, op[n][:, :], ALU.mult, ALU.add))
                    st.wait()
                    layer_norm_steps(dve, st, x[:, s, :], stats, mv[:, :], ss[:, 0:1], hold[:, :])
                    st.wait()
                    dve.sem_inc(ms_ready, 1)
                    dve.wait_ge(sd_done, 2 * t + 2)
                    st.did(dve.reciprocal(ss[:, 0:1], sd[:, 0:1]))
                    st.wait()
                    st.did(dve.tensor_scalar(h1[:, t, :], x[:, s, :], mv[:, 0:1], ss[:, 0:1], ALU.subtract, ALU.mult))
                    st.wait()
                    st.did(dve.tensor_tensor(h1[:, t, :], h1[:, t, :], g1[:, :], ALU.mult))
                    st.wait()
                    dve.tensor_tensor(h1[:, t, :], h1[:, t, :], b1[:, :], ALU.add).then_inc(h1_ready, 1)
                    dve.wait_ge(tp_done, 4 * t + 3)
                    dve.tensor_copy(T[:, 0:4, :], tp[0][:, :, :]).then_inc(T_dve, 1)
                    dve.wait_ge(g_done, 4 * t + 4)
                    st.did(dve.tensor_tensor(L[:, t, :], lp[:, 0:NR], rb[:, :], ALU.add))
                    if t >= 1:
                        dve.wait_ge(base_stored, 16 * t)
                    for n in range(2):
                        half = slice(n * 512, (n + 1) * 512)
                        dve.wait_ge(sig_done, 2 * t + n + 1)
                        st.did(dve.tensor_tensor(base[:, half], op[n][:, :], tmp[:, half], ALU.mult))
                    st.wait()
                    dve.scalar_tensor_tensor(base[:, :], h1[:, t, :], ALPHA, base[:, :], ALU.mult, ALU.add).then_inc(base_ready, 1)
                    dve.sem_inc(slot_free, 1)
                q = Steps(dve, r_steps, 0, 0)

                def do(ins):
                    q.did(ins)
                    q.wait()
                TT = dve.tensor_tensor
                bt = lambda ap, n: ap.unsqueeze(2).broadcast_to([P, NT, n])
                lg, le = L[:, :, 0:NG], L[:, :, NG:].rearrange("p t (g e) -> p t g e", g=NG)
                st.wait()
                do(dve.tensor_reduce(m1[:, :], lg, AX.X, ALU.max))
                do(TT(gd[:, :, :], lg, bt(m1[:, :], NG), ALU.subtract))
                do(TT(ohg[:, :, :], lg, bt(m1[:, :], NG), ALU.is_equal))
                do(dve.tensor_scalar(idxm[:, :], idx[:, 0:EPG], -64.0, None, ALU.add))
                mid = lambda n: idxm[:, 0:n].unsqueeze(1).broadcast_to([P, NT, n])

                def first_of(onehot, n):
                    do(TT(onehot, onehot, mid(n), ALU.mult))
                    do(dve.tensor_reduce(m2[:, :], onehot, AX.X, ALU.min))
                    do(TT(onehot, mid(n), bt(m2[:, :], n), ALU.is_equal))
                first_of(ohg[:, :, :], NG)
                dve.wait_ge(r_act, 1)
                do(dve.tensor_reduce(gw[:, :], ge[:, :, :], AX.X, ALU.add))
                do(dve.reciprocal(gw[:, :], gw[:, :]))
                for g in range(NG):
                    do(TT(big[:, :, g * EPG:(g + 1) * EPG], le[:, :, g, :], ohg[:, :, g:g + 1].broadcast_to([P, NT, EPG]), ALU.mult))
                do(dve.tensor_reduce(ein[:, :, :], big[:, :, :].rearrange("p t (g e) -> p t e g", g=NG), AX.X, ALU.add))
                do(dve.tensor_reduce(m1[:, :], ein[:, :, :], AX.X, ALU.max))
                do(TT(oh[:, 0], ein[:, :, :], bt(m1[:, :], EPG), ALU.is_equal))
                first_of(oh[:, 0], EPG)
                do(dve.scalar_tensor_tensor(ein[:, :, :], oh[:, 0], NEG, ein[:, :, :], ALU.mult, ALU.add))
                do(dve.tensor_reduce(f1[:, :], ein[:, :, :], AX.X, ALU.max))
                do(TT(oh[:, 1], ein[:, :, :], bt(f1[:, :], EPG), ALU.is_equal))
                first_of(oh[:, 1], EPG)
                do(TT(m1[:, :], f1[:, :], m1[:, :], ALU.subtract))
                assert q.n == 26
                for k in range(2):
                    for g in range(NG):
                        q.did(TT(OH[:, k, :, g * EPG:(g + 1) * EPG], oh[:, k], ohg[:, :, g:g + 1].broadcast_to([P, NT, EPG]), ALU.mult))
                q.wait()
                for k in range(2):
                    q.did(TT(OH[:, k], OH[:, k], bt(valid[:, :], NE), ALU.mult))
                q.did(dve.memset(ones[:, :], 1.0))
                q.did(dve.memset(one[:, :], 1.0))
                q.wait()
                do(TT(OS[:, :, :], OH[:, 0], OH[:, 1], ALU.add))
                dve.sem_inc(r_ready, 1)
                dve.wait_ge(r_act, 2)
                do(dve.tensor_scalar(m1[:, :], f1[:, :], 1.0, None, ALU.add))
                do(dve.reciprocal(m1[:, :], m1[:, :]))
                do(TT(w_tok[:, 0, :], m1[:, :], gw[:, :], ALU.mult))
                do(TT(w_tok[:, 1, :], w_tok[:, 0, :], f1[:, :], ALU.mult))
                dve.wait_ge(r_pe, 1)
                q.did(dve.memset(pre[:, 0, :], 0.0))
                for t in range(1, NT):
                    q.wait()
                    q.did(TT(pre[:, t, :], gp[0][:, (t - 1) * NE:t * NE], pre[:, t - 1, :], ALU.add))
                q.wait()
                do(TT(cnt[:, :], gp[0][:, (NT - 1) * NE:NT * NE], pre[:, NT - 1, :], ALU.add))
                do(TT(rank[:, :, :].rearrange("p t e -> p (t e)"), gp[1][:, 0:NT * NE], pre[:, :, :].rearrange("p t e -> p (t e)"), ALU.add))
                do(dve.tensor_scalar(cnti[:, :], cnt[:, :], float(P - 1), None, ALU.add))
                do(dve.tensor_scalar(cnti[:, :], cnti[:, :], 7, None, ALU.arith_shift_right))
                do(dve.tensor_copy(nb[:, :], cnti[:, :]))
                do(dve.tensor_tensor_scan(incl[:, :], one[:, :], cnt[:, :], 0.0, ALU.mult, ALU.add))
                do(dve.tensor_tensor_scan(bincl[:, :], one[:, :], nb[:, :], 0.0, ALU.mult, ALU.add))
                do(TT(start[:, :], incl[:, :], cnt[:, :], ALU.subtract))
                do(TT(bstart[:, :], bincl[:, :], nb[:, :], ALU.subtract))
                do(dve.tensor_scalar(bstart[:, :], bstart[:, :], float(P), None, ALU.mult))
                do(TT(sx[:, :, :], rank[:, :, :], start[:, :].unsqueeze(1).broadcast_to([P, NT, NE]), ALU.add))
                for k in range(2):
                    do(TT(big[:, :, :], sx[:, :, :], OH[:, k], ALU.mult))
                    do(dve.tensor_reduce(dxf[:, k, :], big[:, :, :], AX.X, ALU.add))
                do(dve.tensor_copy(dx[:, :, :], dxf[:, :, :]))
                do(dve.tensor_scalar(tx[:, :], bincl[:, :], part[:, 0:1], None, ALU.is_le))
                do(dve.tensor_reduce(tabf[:, 0:1], tx[:, :], AX.X, ALU.add))
                do(dve.tensor_scalar(tx[:, :], idx[:, :], tabf[:, 0:1], None, ALU.is_equal))
                do(TT(ty[:, :], start[:, :], bstart[:, :], ALU.subtract))
                do(TT(ty[:, :], ty[:, :], tx[:, :], ALU.mult))
                do(dve.tensor_reduce(tabf[:, 1:2], ty[:, :], AX.X, ALU.add))
                do(dve.scalar_tensor_tensor(tabf[:, 1:2], part[:, :], float(P), tabf[:, 1:2], ALU.mult, ALU.add))
                do(dve.tensor_copy(tabf[:, 2:3], bincl[:, NE - 1:NE]))
                do(dve.memset(tabf[:, 3:4], 0.0))
                do(dve.tensor_copy(tab[:, :], tabf[:, :]))
                dve.sem_inc(r_ready, 1)

            @block.gpsimd
            def _(pool):
                pool.wait_ge(r_ready, 2)
                n = 0
                for t in range(NT):
                    m = P if t < TP else DECB
                    for k in range(2):
                        pool.indirect_dma_start(d["XR"], bass.IndirectOffsetOnAxis(ap=dx[0:m, k, t:t + 1], axis=0),
                                                h1[0:m, t, :], None, bounds_check=XROWS - P - 1, oob_is_err=True).then_inc(scattered, 16)
                        n += 16
                pool.wait_ge(scattered, n * (layer + 1))



SLOTS = 2


def block_turns(eng):
    with eng.Fori(0, -(-BLOCKS // SLOTS)) as r:
        for slot in range(SLOTS):
            yield SLOTS * r + slot, slot, r


def experts(nc, d, layer, ident):
    with Phase(nc) as ph:
        tab = ph.sb("ex_tab", [1, 4 * P], I32)
        wgu = ph.sb("ex_wgu", [P, SLOTS, 2, KC, DE])
        wd = ph.sb("ex_wd", [P, SLOTS, 2, D])
        x = ph.sb("ex_x", [P, SLOTS, D])
        xT = ph.sb("ex_xT", [P, 2, KC, P])
        sil = ph.sb("ex_sil", [P, 2, DE])
        h = ph.sb("ex_h", [P, 2, DE])
        hT = ph.sb("ex_hT", [P, 2, 2, P])
        y = ph.sb("ex_y", [P, 2, D])
        tp = [ph.ps(f"ex_tp{i}", [P, 4, P]) for i in range(2)]
        gu = [ph.ps(f"ex_gu{i}", [P, 2, DE]) for i in range(2)]
        htp = [ph.ps(f"ex_ht{i}", [P, 2, P]) for i in range(2)]
        yp = [ph.ps(f"ex_yp{i}", [P, 512]) for i in range(2)]
        tab_loaded = ph.sem("tab_loaded")
        loaded = [ph.sem(f"loaded{i}") for i in range(SLOTS)]
        stored = ph.sem2("stored")
        slot_free, tp_done, xT_dve, xT_act, gu_done = (ph.sem(n) for n in ("slot_free", "tp_done", "xT_dve", "xT_act", "gu_done"))
        sil_done, h_ready, ht_done, hT_ready, y_done = (ph.sem(n) for n in ("sil_done", "h_ready", "ht_done", "hT_ready", "y_done"))
        y_dve, y_act = ph.sem("y_dve"), ph.sem("y_act")
        TOTAL = 2
        assert SLOTS == 2
        with nc.Block() as block:
            @block.sync
            def _(sp):
                sp.dma_start(tab[:, :], d["BTAB"]).then_inc(tab_loaded, 16)
                sp.wait_ge(tab_loaded, 16)
                used = sp.value_load(tab[0:1, TOTAL:TOTAL + 1], min_val=0, max_val=BLOCKS)
                for b, s, r in block_turns(sp):
                    with sp.If(b < used):
                        e = sp.value_load(tab[0:1, ds(4 * b, 1)], min_val=0, max_val=NE - 1)
                        row = sp.value_load(tab[0:1, ds(4 * b + 1, 1)], min_val=0, max_val=XROWS - P)
                        sp.wait_ge(slot_free, b + 1)
                        sp.dma_start(x[:, s, :], d["XR"][ds(row, P)]).then_inc(loaded[s], 16)
                        for n, w in enumerate(("e_gate", "e_up")):
                            sp.dma_start(wgu[:, s, n].rearrange("p k n -> p (k n)"),
                                         d[w][ds(layer, 1), ds(e, 1)].rearrange("l e (p k) n -> (l e p) (k n)", k=KC)).then_inc(loaded[s], 16)
                        sp.dma_start(wd[:, s].rearrange("p k n -> p (k n)"),
                                     d["e_down"][ds(layer, 1), ds(e, 1)].rearrange("l e (p k) n -> (l e p) (k n)", k=2)).then_inc(loaded[s], 16)

            @block.tensor
            def _(pe):
                pe.sem_inc(slot_free, SLOTS)
                pe.wait_ge(tab_loaded, 16)
                used = pe.value_load(tab[0:1, TOTAL:TOTAL + 1], min_val=0, max_val=BLOCKS)
                for b, s, r in block_turns(pe):
                    with pe.If(b < used):
                        pe.wait_ge(loaded[s], 64 * (r + 1))
                        pe.wait_ge(xT_dve, b + 1)
                        pe.wait_ge(xT_act, b + 1)
                        for c in range(KC):
                            last = pe.transpose(tp[c // 4][:, c % 4, :], x[:, s, c::KC], ident[:, :])
                            if c % 4 == 3:
                                last.then_inc(tp_done, 1)
                        pe.wait_ge(xT_dve, b + 2)
                        pe.wait_ge(xT_act, b + 2)
                        for c in range(KC):
                            last = pe.matmul(gu[s][:, :, :], xT[:, s, c, :], wgu[:, s, :, c, :], start=(c == 0), stop=(c == KC - 1))
                        last.then_inc(gu_done, 1)
                        pe.wait_ge(h_ready, b + 1)
                        for c in range(2):
                            last = pe.transpose(htp[s][:, c, :], h[:, s, c::2], ident[:, :])
                        last.then_inc(ht_done, 1)
                        pe.wait_ge(y_dve, b + 1)
                        pe.wait_ge(y_act, b + 1)
                        pe.wait_ge(hT_ready, b + 1)
                        for n in range(2):
                            for c in range(2):
                                last = pe.matmul(yp[n][:, :], hT[:, s, c, :], wd[:, s, c, n * 512:(n + 1) * 512], start=(c == 0), stop=(c == 1))
                            if n == 0:
                                last.then_inc(y_done, 1)
                        last.then_inc(slot_free, 1)

            @block.vector
            def _(dve):
                dve.sem_inc(xT_dve, 1)
                dve.sem_inc(y_dve, 1)
                dve.wait_ge(tab_loaded, 16)
                used = dve.value_load(tab[0:1, TOTAL:TOTAL + 1], min_val=0, max_val=BLOCKS)
                for b, s, r in block_turns(dve):
                    with dve.If(b < used):
                        dve.wait_ge(tp_done, 2 * b + 1)
                        dve.tensor_copy(xT[:, s, 0:4, :], tp[0][:, :, :]).then_inc(xT_dve, 1)
                        dve.wait_ge(sil_done, b + 1)
                        dve.tensor_tensor(h[:, s, :], sil[:, s, :], gu[s][:, 1, :], ALU.mult).then_inc(h_ready, 1)
                        dve.wait_ge(ht_done, b + 1)
                        dve.tensor_copy(hT[:, s, :, :], htp[s][:, :, :]).then_inc(hT_ready, 1)
                        dve.wait_ge(stored[s], 16 * (r + 1))
                        dve.wait_ge(y_done, b + 1)
                        dve.tensor_copy(y[:, s, 0:512], yp[0][:, :]).then_inc(y_dve, 1)

            @block.scalar
            def _(act):
                act.sem_inc(xT_act, 1)
                act.sem_inc(y_act, 1)
                for s in range(2):
                    act.sem_inc(stored[s], 16)
                act.wait_ge(tab_loaded, 16)
                used = act.value_load(tab[0:1, TOTAL:TOTAL + 1], min_val=0, max_val=BLOCKS)
                for b, s, r in block_turns(act):
                    with act.If(b < used):
                        row = act.value_load(tab[0:1, ds(4 * b + 1, 1)], min_val=0, max_val=XROWS - P)
                        act.wait_ge(tp_done, 2 * b + 2)
                        act.activation(xT[:, s, 4:8, :], tp[1][:, :, :], ACT.Copy).then_inc(xT_act, 1)
                        act.wait_ge(gu_done, b + 1)
                        act.activation(sil[:, s, :], gu[s][:, 0, :], ACT.Silu).then_inc(sil_done, 1)
                        act.wait_ge(stored[s], 16 * (r + 1))
                        act.wait_ge(slot_free, b + SLOTS + 1)
                        act.activation(y[:, s, 512:], yp[1][:, :], ACT.Copy).then_inc(y_act, 1)
                        act.wait_ge(y_dve, b + 2)
                        act.wait_ge(y_act, b + 2)
                        act.wait_ge(stored[1 - s], 16 * (r + s + 1))
                        act.dma_start(d["YR"][ds(row, P)], y[:, s, :]).then_inc(stored[s], 16)
                act.wait_ge(stored[0], 16 * ((used + 1) // 2) + 16)
                act.wait_ge(stored[1], 16 * (used // 2) + 16)
                act.sem_inc(y_act, 1)



def combine(nc, d, layer, ident):
    w_tok, row = d["sb_weight"], d["sb_row"]
    with Phase(nc) as ph:
        g = ph.sb("co_g", [P, D])
        b = ph.sb("co_b", [P, D])
        base = ph.sb("co_base", [P, 2, D])
        r1 = ph.sb("co_r1", [P, 2, D])
        r2 = ph.sb("co_r2", [P, 2, D])
        o = ph.sb("co_o", [P, 2, D])
        stats = ph.sb("co_stats", [P, 2, 6])
        mv = ph.sb("co_mv", [P, 2])
        ve = ph.sb("co_ve", [P, 1])
        sd = ph.sb("co_sd", [P, 1])
        rs = ph.sb("co_rs", [P, 1])
        hold = ph.sb("co_hold", [1, 1])
        gains, loaded, gathered, stored = ph.sem("gains"), ph.sem2("loaded"), [d["sw"][f"gathered{i}"] for i in range(2)], ph.sem2("stored")
        free, var_ready, sqrt_done, steps, o_ready, zeroed = (ph.sem(n) for n in ("free", "var_ready", "sqrt_done", "steps", "o_ready", "zeroed"))
        with nc.Block() as block:
            @block.sync
            def _(sp):
                sp.dma_start(g[:, :], row_of_layer(d["ln2_g"], layer)).then_inc(gains, 16)
                sp.dma_start(b[:, :], row_of_layer(d["ln2_b"], layer)).then_inc(gains, 16)
                for t in range(NT):
                    if t >= 2:
                        sp.wait_ge(free, t - 1)
                    sp.dma_start(base[:, t % 2, :], d["BASE"][rows(t)]).then_inc(loaded[t % 2], 16)

            @block.gpsimd
            def _(pool):
                for t in range(NT):
                    m = P if t < TP else DECB
                    if t >= 2:
                        pool.wait_ge(free, t - 1)
                    if t == TP:
                        pool.memset(r1[:, t % 2, :], 0.0).then_inc(zeroed, 1)
                        pool.memset(r2[:, t % 2, :], 0.0).then_inc(zeroed, 1)
                        pool.wait_ge(zeroed, 2)
                    for k, r in ((0, r1), (1, r2)):
                        pool.indirect_dma_start(r[0:m, t % 2, :], None, d["YR"], bass.IndirectOffsetOnAxis(ap=row[0:m, k, t:t + 1], axis=0),
                                                bounds_check=XROWS - P - 1, oob_is_err=True).then_inc(gathered[t % 2], 16)

            @block.scalar
            def _(act):
                for t in range(NT):
                    s = t % 2
                    act.wait_ge(var_ready, t + 1)
                    act.activation(sd[:, :], ve[:, :], ACT.Sqrt).then_inc(sqrt_done, 1)
                    act.wait_ge(o_ready, t + 1)
                    act.dma_start(d["H"][rows(t)], o[:, s, :]).then_inc(stored[s], 16)
                    act.dma_start(d["y_all"][rows(t)], o[:, s, :]).then_inc(stored[s], 16)
                act.wait_ge(stored[0], 32 * (NT // 2 + 1))
                act.wait_ge(stored[1], 32 * (NT // 2))

            @block.vector
            def _(dve):
                dve.wait_ge(gains, 32)
                for t in range(NT):
                    s, r = t % 2, t // 2
                    st = Steps(dve, steps, t, 9)
                    dve.wait_ge(loaded[s], 16 * (r + 1))
                    dve.wait_ge(gathered[s], 32 * ((NT + 1 - s) // 2) * layer + 32 * (r + 1))
                    acc = base[:, s, :]
                    st.did(dve.scalar_tensor_tensor(acc, r1[:, s, :], w_tok[:, 0, t:t + 1], acc, ALU.mult, ALU.add))
                    st.wait()
                    st.did(dve.scalar_tensor_tensor(acc, r2[:, s, :], w_tok[:, 1, t:t + 1], acc, ALU.mult, ALU.add))
                    st.wait()
                    layer_norm_steps(dve, st, acc, stats, mv[:, :], ve[:, :], hold[:, :])
                    st.wait()
                    dve.sem_inc(var_ready, 1)
                    dve.wait_ge(sqrt_done, t + 1)
                    st.did(dve.reciprocal(rs[:, :], sd[:, :]))
                    st.wait()
                    if r:
                        dve.wait_ge(stored[s], 32 * r)
                    st.did(dve.tensor_scalar(o[:, s, :], acc, mv[:, 0:1], rs[:, 0:1], ALU.subtract, ALU.mult))
                    st.wait()
                    dve.sem_inc(free, 1)
                    st.did(dve.tensor_tensor(o[:, s, :], o[:, s, :], g[:, :], ALU.mult))
                    st.wait()
                    dve.tensor_tensor(o[:, s, :], o[:, s, :], b[:, :], ALU.add).then_inc(o_ready, 1)
                    st.end()



PHASES = [input_projection, mla_prepare, attention, mlstm_prompt, sample_attention, mlstm_sample, output_and_route,
          experts, combine]


def decoder_trunk(nc, d):
    for name, shape in (("H", (ROWS, D)), ("Z", (PAD + ROWS, N_IN)), ("XR", (XROWS, D)), ("YR", (XROWS, D)),
                        ("Y", (ROWS, D)), ("QT", (H, QK, ROWS)), ("KT", (H, QK, ROWS)), ("V", (ROWS, H * VD)),
                        ("BASE", (ROWS, D)), ("BTAB", (1, 4 * P))):
        d[name] = nc.dram_tensor(f"scratch_{name}", shape, I32 if name == "BTAB" else F32, kind="Internal").ap()
    with ExitStack() as ctx:
        ident = ctx.enter_context(nc.sbuf_tensor("ident", [P, P], F32))
        d["sb_weight"] = ctx.enter_context(nc.sbuf_tensor("route_weight", [P, 2, NT], F32))
        d["sb_row"] = ctx.enter_context(nc.sbuf_tensor("route_row", [P, 2, NT], mybir.dt.uint32))
        d["sw"] = {n: ctx.enter_context(nc.semaphore(f"sw_{n}")) for n in
                   ("zero_stored", "cv_w", "cv_in", "cv_out", "cv_state", "scattered", "gathered0", "gathered1")}
        with Phase(nc) as ph:
            got = ph.sem("ident_loaded")
            with nc.Block() as block:
                @block.sync
                def _(sp):
                    sp.dma_start(ident[:, :], d["c_ident"]).then_inc(got, 16)
                    sp.wait_ge(got, 16)
        entry_norm(nc, d)
        with nc.Fori(0, LAYERS) as layer:
            for phase in PHASES:
                phase(nc, d, layer, ident)



LAYERS = DEPTH


def constants():
    import numpy as np
    inv = (np.float32(10000.0) ** (-np.arange(HALF, dtype=np.float32) / np.float32(HALF))).astype(np.float32)
    pos = np.concatenate([np.arange(SEQ), np.full(P, PAST)]).astype(np.float32)
    ang = (pos[:, None] * inv).astype(np.float32)
    q, k = np.arange(P)[:, None], np.arange(P)[None, :]
    return {
        "c_ident": np.eye(P, dtype=np.float32),
        "c_trig": np.concatenate([np.cos(ang), np.sin(ang)], 1).astype(np.float32),
        "c_causal": np.where(k <= q, 0.0, NEG).astype(np.float32),
        "c_causalT": np.where(q <= k, 0.0, NEG).astype(np.float32),
        "c_own": np.repeat(np.where(np.eye(DECB) > 0, 0.0, NEG).astype(np.float32), H, 1),
        "c_rep": np.repeat(np.eye(DECB * NH, dtype=np.float32), 4, 1),
        "c_idx": np.tile(np.arange(NE, dtype=np.float32), (P, 1)),
        "c_valid": (np.arange(NT)[None, :] * P + q < SEQ + DECB).astype(np.float32),
        "c_part": np.arange(P, dtype=np.float32)[:, None],
        "c_before": (q < k).astype(np.float32),
        "c_headrow": np.repeat(np.eye(NH, dtype=np.float32)[:, :, None], P, 2),
    }


OUTS = [("y_all", (ROWS, D)), ("ckv_all", (DEPTH, ROWS, KVR)), ("krope_all", (DEPTH, ROWS, ROPE)),
        ("conv_p", (DEPTH, 2, CONVW)), ("C_p", (DEPTH, NH, DH, DH)), ("n_p", (DEPTH, NH, DH)), ("m_p", (DEPTH, NH)),
        ("conv_s", (DEPTH, DECB, 2, CONVW)), ("C_s", (DEPTH, DECB * NH, DH * DH)), ("n_s", (DEPTH, DECB * NH, DH)),
        ("m_s", (DEPTH, DECB * NH))]
PLAIN = ["cache_ckv", "cache_krope", "state_conv", "state_mlstm_C", "state_mlstm_n", "state_mlstm_m", "page_table",
         "ln0_g", "ln0_b", "w_in", "conv_w", "q_norm_g", "w_uq", "kv_norm_g", "w_ukv", "mlstm_gate_b", "mix_norm_g",
         "w_out", "ln1_g", "ln1_b", "e_gate", "e_up", "e_down", "w_pe", "w_pg", "ln2_g", "ln2_b"]


def laid_out(inputs):
    import numpy as np
    a = {n: np.ascontiguousarray(inputs[n]) for n in PLAIN}
    rest = ROWS - SEQ - DECB
    xp, xs = np.asarray(inputs["x_prompt"])[0], np.asarray(inputs["x_sample"])[:, 0]
    a["x_all"] = np.concatenate([xp, xs, np.zeros((rest, D), np.float32)], 0)
    pp, ps = np.asarray(inputs["p_prompt"])[:, 0], np.asarray(inputs["p_sample"])[:, :, 0]
    a["p_all"] = np.concatenate([pp, ps, np.zeros((DEPTH, rest, DPLE), np.float32)], 1)
    a["w_route"] = np.concatenate([np.asarray(inputs["w_group"]), np.asarray(inputs["w_expert"])], 2)
    a["b_route"] = np.concatenate([np.asarray(inputs["b_group"]), np.asarray(inputs["b_expert"])], 1)
    a["page_table"] = np.asarray(inputs["page_table"]).reshape(1, DECB * PAGES)
    a.update(constants())
    return a


def kernel(**inputs):
    import concourse.bacc as _bacc
    from concourse.bass_utils import run_bass_kernel_spmd as _run

    arrays = laid_out(inputs)
    nc = _bacc.Bacc("TRN2", target_bir_lowering=False, num_devices=1)
    d = {n: nc.dram_tensor(f"in_{n}", a.shape, mybir.dt.from_np(a.dtype), kind="ExternalInput").ap()
         for n, a in arrays.items()}
    for n, shape in OUTS:
        d[n] = nc.dram_tensor(f"out_{n}", shape, F32, kind="ExternalOutput").ap()
    decoder_trunk(nc, d)
    r = _run(nc, [{f"in_{n}": a for n, a in arrays.items()}], core_ids=[0])
    o = {n: r.results[0][f"out_{n}"] for n, _ in OUTS}
    y, ckv, kr, dec = o["y_all"], o["ckv_all"], o["krope_all"], SEQ + DECB
    return (y[None, :SEQ], y[SEQ:dec, None], ckv[:, None, :SEQ], kr[:, None, :SEQ], o["conv_p"][:, None],
            o["C_p"][:, None], o["n_p"][:, None], o["m_p"][:, None],
            ckv[:, SEQ:dec, None], kr[:, SEQ:dec, None], o["conv_s"],
            o["C_s"].reshape(DEPTH, DECB, NH, DH, DH), o["n_s"].reshape(DEPTH, DECB, NH, DH),
            o["m_s"].reshape(DEPTH, DECB, NH))
```

```python
from contextlib import ExitStack

import concourse.bass as bass
from concourse import mybir

F32 = mybir.dt.float32
I32 = mybir.dt.int32
ALU = mybir.AluOpType
ACT = mybir.ActivationFunctionType
AX = mybir.AxisListType
ds = bass.ds

P = 128
D = 1024
KC = D // P
SEQ, DECB, PAST = 1024, 8, 2048
DEPTH = 2
TP = SEQ // P
NT = TP + 1
ROWS = NT * P
N_IN = 2216
PAD = 2
CONVW, QR, KVR, ROPE, NOPE, VD = 256, 256, 128, 32, 64, 64
H, QK = 8, 96
HALF = ROPE // 2
NH, DH, MW = 4, 64, 256
C_CB, C_CC, C_CH, C_Q = 0, 256, 512, 768
C_KV, C_KR = C_Q + QR, C_Q + QR + KVR
C_MQ = C_KR + ROPE
C_MK, C_MV, C_MO, C_MI = C_MQ + MW, C_MQ + 2 * MW, C_MQ + 3 * MW, C_MQ + 4 * MW
MLA_COLS = QR + KVR + ROPE
NE, NG, EPG, DE = 32, 4, 8, 256
DPLE = 256
ALPHA = (2 * DEPTH) ** 0.25
LN_EPS, RMS_EPS = 1e-5, 1e-6
SCALE = float(QK) ** -0.5
PAGES, PAGE = PAST // P, P
NEG = -1e30
BLOCKS = -(-2 * (SEQ + DECB) // P) + NE
XROWS = 2 * (SEQ + DECB) + P


def tile_turns(eng, tiles=NT):
    with eng.Fori(0, tiles // 2) as r:
        for slot in range(2):
            yield 2 * r + slot, slot, r
    if tiles % 2:
        yield tiles - 1, 0, tiles // 2


class Steps:

    def __init__(self, eng, sem, turn, steps):
        self.eng, self.sem, self.base, self.steps, self.n = eng, sem, turn * steps, steps, 0

    def did(self, ins):
        self.n += 1
        ins.then_inc(self.sem, 1)

    def wait(self):
        self.eng.wait_ge(self.sem, self.base + self.n)

    def end(self):
        assert self.n == self.steps, (self.n, self.steps)


class Phase:

    def __init__(self, nc):
        self.nc, self.sems = nc, []

    def __enter__(self):
        self.ctx = ExitStack()
        self.ctx.__enter__()
        return self

    def sb(self, name, shape, dt=F32):
        return self.ctx.enter_context(self.nc.sbuf_tensor(name, shape, dt))

    def ps(self, name, shape, dt=F32):
        return self.ctx.enter_context(self.nc.psum_tensor(name, shape, dt))

    def sem(self, name):
        s = self.ctx.enter_context(self.nc.semaphore(name))
        self.sems.append(s.num)
        return s

    def sem2(self, name):
        return [self.sem(f"{name}{i}") for i in range(2)]

    def __exit__(self, *exc):
        if exc[0] is None:
            nums = sorted(self.sems)
            firsts = [n for n in nums if n - 1 not in nums]
            for lo in firsts:
                hi = lo
                while hi + 1 in nums:
                    hi += 1
                self.nc.all_engine_barrier(sems_to_clear=range(lo, hi + 1))
        return self.ctx.__exit__(*exc)


def rows(t, n=P):
    return ds(t * P, n)


def of_layer(ap, layer):
    inner = "abcd"[:len(ap.shape) - 1]
    return ap[ds(layer, 1)].rearrange(f"l {' '.join(inner)} -> (l {inner[0]}) {' '.join(inner[1:])}")


def row_of_layer(ap, layer):
    return ap[ds(layer, 1), :].broadcast_to([P, ap.shape[1]])



def layer_norm_steps(dve, st, x, stats, mv, rstd_in, hold):
    st.did(dve.bn_stats(stats[:, 0, :], x[:, 0:512]))
    st.did(dve.bn_stats(stats[:, 1, :], x[:, 512:1024]))
    st.wait()
    dve.memset(hold, 0.0)
    st.did(dve.bn_aggr(mv, stats[:, :, :]))
    st.wait()
    st.did(dve.tensor_scalar(rstd_in, mv[:, 1:2], LN_EPS, None, ALU.add))


def entry_norm(nc, d):
    with Phase(nc) as ph:
        x = ph.sb("en_x", [P, 2, D])
        o = ph.sb("en_o", [P, 2, D])
        g = ph.sb("en_g", [P, D])
        b = ph.sb("en_b", [P, D])
        zero = ph.sb("en_zero", [P, N_IN])
        stats = ph.sb("en_stats", [P, 2, 6])
        mv = ph.sb("en_mv", [P, 2])
        hold = ph.sb("en_hold", [1, 1])
        ve = ph.sb("en_ve", [P, 1])
        sd = ph.sb("en_sd", [P, 1])
        rs = ph.sb("en_rs", [P, 1])
        gains, loaded, stored = ph.sem("gains"), ph.sem2("x_loaded"), ph.sem2("o_stored")
        x_free, o_ready = ph.sem("x_free"), ph.sem("o_ready")
        var_ready, sqrt_done, steps = ph.sem("var_ready"), ph.sem("sqrt_done"), ph.sem("steps")
        zeroed, zero_stored = ph.sem("zeroed"), d["sw"]["zero_stored"]
        with nc.Block() as block:
            @block.sync
            def _(sp):
                sp.dma_start(g[:, :], d["ln0_g"].partition_broadcast(P)).then_inc(gains, 16)
                sp.dma_start(b[:, :], d["ln0_b"].partition_broadcast(P)).then_inc(gains, 16)
                for t, s, r in tile_turns(sp):
                    sp.wait_ge(x_free, t + 1)
                    sp.dma_start(x[:, s, :], d["x_all"][rows(t)]).then_inc(loaded[s], 16)

            @block.gpsimd
            def _(pool):
                pool.memset(zero[:, :], 0.0).then_inc(zeroed, 1)
                pool.wait_ge(zeroed, 1)
                pool.dma_start(d["Z"][0:PAD], zero[0:PAD, :]).then_inc(zero_stored, 16)
                pool.dma_start(d["XR"][XROWS - P:XROWS], zero[:, 0:D]).then_inc(zero_stored, 16)
                pool.dma_start(d["YR"][XROWS - P:XROWS], zero[:, 0:D]).then_inc(zero_stored, 16)
                pool.dma_start(d["Y"][SEQ:ROWS], zero[:, 0:D]).then_inc(zero_stored, 16)
                pool.wait_ge(zero_stored, 64)

            @block.scalar
            def _(act):
                for s in range(2):
                    act.sem_inc(stored[s], 16)
                for t, s, r in tile_turns(act):
                    act.wait_ge(var_ready, t + 1)
                    act.activation(sd[:, :], ve[:, :], ACT.Sqrt).then_inc(sqrt_done, 1)
                    act.wait_ge(o_ready, t + 1)
                    act.dma_start(d["H"][rows(t)], o[:, s, :]).then_inc(stored[s], 16)
                act.wait_ge(stored[0], 16 * (NT // 2 + 2))
                act.wait_ge(stored[1], 16 * (NT // 2 + 1))

            @block.vector
            def _(dve):
                dve.sem_inc(x_free, 2)
                dve.wait_ge(gains, 32)
                for t, s, r in tile_turns(dve):
                    st = Steps(dve, steps, t, 7)
                    dve.wait_ge(loaded[s], 16 * (r + 1))
                    layer_norm_steps(dve, st, x[:, s, :], stats, mv[:, :], ve[:, :], hold[:, :])
                    st.wait()
                    dve.sem_inc(var_ready, 1)
                    dve.wait_ge(sqrt_done, t + 1)
                    st.did(dve.reciprocal(rs[:, :], sd[:, :]))
                    st.wait()
                    dve.wait_ge(stored[s], 16 * (r + 1))
                    st.did(dve.tensor_scalar(o[:, s, :], x[:, s, :], mv[:, 0:1], rs[:, 0:1], ALU.subtract, ALU.mult))
                    st.wait()
                    dve.sem_inc(x_free, 1)
                    st.did(dve.tensor_tensor(o[:, s, :], o[:, s, :], g[:, :], ALU.mult))
                    st.wait()
                    dve.tensor_tensor(o[:, s, :], o[:, s, :], b[:, :], ALU.add).then_inc(o_ready, 1)
                    st.end()



LX = KVR + 1


class PagedCache:

    COUNTS = (8 * NT, 24, 4 * H)
    assert sum(COUNTS) == DECB * PAGES

    def __init__(self, ph):
        self.table = ph.sb("pc_table", [1, DECB * PAGES], I32)
        self.ckv = ph.sb("pc_ckv", [P, DECB * PAGES, LX])
        self.kr = ph.sb("pc_kr", [P, DECB * PAGES, ROPE])
        self.table_loaded = ph.sem("table_loaded")
        self.pages_loaded = [ph.sem(f"pages_loaded{i}") for i in range(3)]

    def load(self, eng, d, layer, first, count, phase):
        n_phys = d["cache_ckv"].shape[1]
        with eng.Fori(0, count) as p:
            page = eng.value_load(self.table[0:1, ds(first + p, 1)], min_val=0, max_val=n_phys - 1)
            eng.dma_start(self.ckv[:, ds(first + p, 1), 0:KVR].rearrange("k o n -> k (o n)"),
                          d["cache_ckv"][ds(layer, 1), ds(page, 1)].rearrange("l g k n -> (l g k) n")).then_inc(self.pages_loaded[phase], 16)
            eng.dma_start(self.kr[:, ds(first + p, 1), :].rearrange("k o n -> k (o n)"),
                          d["cache_krope"][ds(layer, 1), ds(page, 1)].rearrange("l g k n -> (l g k) n")).then_inc(self.pages_loaded[phase], 16)



Z_CHUNKS = [(c, min(512, N_IN - c)) for c in range(0, N_IN, 512)]


def input_projection(nc, d, layer, ident, cache):
    with Phase(nc) as ph:
        w = ph.sb("ip_w", [P, KC, N_IN])
        x = ph.sb("ip_x", [P, 2, D])
        xT = ph.sb("ip_xT", [P, 2, KC, P])
        z = ph.sb("ip_z", [P, 2, N_IN])
        tp = [ph.ps(f"ip_tp{i}", [P, 4, P]) for i in range(2)]
        zp = [ph.ps(f"ip_zp{i}", [P, 512]) for i in range(5)]
        w_loaded = [ph.sem(f"w_loaded{n}") for n in range(len(Z_CHUNKS))]
        x_loaded, z_stored = ph.sem2("x_loaded"), ph.sem2("z_stored")
        x_free, tp_done = ph.sem("x_free"), ph.sem("tp_done")
        xT_dve, xT_act = ph.sem("xT_dve"), ph.sem("xT_act")
        z_done, z_dve, z_act = ph.sem("z_done"), ph.sem("z_dve"), ph.sem("z_act")
        with nc.Block() as block:
            @block.sync
            def _(sp):
                sp.dma_start(cache.table[:, :], d["page_table"]).then_inc(cache.table_loaded, 16)
                for t, s, r in tile_turns(sp):
                    sp.wait_ge(x_free, t + 1)
                    sp.dma_start(x[:, s, :], d["H"][rows(t)]).then_inc(x_loaded[s], 16)
                    sp.wait_ge(cache.table_loaded, 16)
                    cache.load(sp, d, layer, t * 8, 8, 0)

            @block.tensor
            def _(pe):
                pe.sem_inc(x_free, 2)
                for t, s, r in tile_turns(pe):
                    pe.wait_ge(x_loaded[s], 16 * (r + 1))
                    pe.wait_ge(xT_dve, t + 1)
                    pe.wait_ge(xT_act, t + 1)
                    for c in range(KC):
                        last = pe.transpose(tp[c // 4][:, c % 4, :], x[:, s, c::KC], ident[:, :])
                        if c % 4 == 3:
                            last.then_inc(tp_done, 1)
                    pe.wait_ge(xT_dve, t + 2)
                    pe.wait_ge(xT_act, t + 2)
                    for n, (c0, cn) in enumerate(Z_CHUNKS):
                        pe.wait_ge(w_loaded[n], 16)
                        if n % 2 == 0:
                            pe.wait_ge(z_dve, 3 * t + n // 2 + 1)
                        else:
                            pe.wait_ge(z_act, 2 * t + n // 2 + 1)
                        for c in range(KC):
                            last = pe.matmul(zp[n][:, 0:cn], xT[:, s, c, :], w[:, c, c0:c0 + cn],
                                             start=(c == 0), stop=(c == KC - 1))
                            if n == c == 0:
                                last.then_inc(x_free, 1)
                        last.then_inc(z_done, 1)

            @block.vector
            def _(dve):
                dve.sem_inc(xT_dve, 1)
                dve.sem_inc(z_dve, 3)
                for t, s, r in tile_turns(dve):
                    dve.wait_ge(tp_done, 2 * t + 1)
                    dve.tensor_copy(xT[:, s, 0:4, :], tp[0][:, :, :]).then_inc(xT_dve, 1)
                    dve.wait_ge(z_stored[s], 16 * (r + 1))
                    for n in (0, 2, 4):
                        c0, cn = Z_CHUNKS[n]
                        dve.wait_ge(z_done, 5 * t + n + 1)
                        dve.tensor_copy(z[:, s, c0:c0 + cn], zp[n][:, 0:cn]).then_inc(z_dve, 1)

            @block.scalar
            def _(act):
                act.sem_inc(xT_act, 1)
                act.sem_inc(z_act, 2)
                for s in range(2):
                    act.sem_inc(z_stored[s], 16)
                for n, (c0, cn) in enumerate(Z_CHUNKS):
                    act.dma_start(w[:, :, c0:c0 + cn], of_layer(d["w_in"], layer).rearrange("(p k) n -> p k n", k=KC)[:, :, c0:c0 + cn]).then_inc(w_loaded[n], 16)
                for t, s, r in tile_turns(act):
                    act.wait_ge(tp_done, 2 * t + 2)
                    act.activation(xT[:, s, 4:8, :], tp[1][:, :, :], ACT.Copy).then_inc(xT_act, 1)
                    act.wait_ge(z_stored[s], 16 * (r + 1))
                    for n in (1, 3):
                        c0, cn = Z_CHUNKS[n]
                        act.wait_ge(z_done, 5 * t + n + 1)
                        act.activation(z[:, s, c0:c0 + cn], zp[n][:, 0:cn], ACT.Copy).then_inc(z_act, 1)
                    act.wait_ge(z_dve, 3 * t + 6)
                    act.wait_ge(z_act, 2 * t + 4)
                    act.dma_start(d["Z"][ds(PAD + t * P, P)], z[:, s, :]).then_inc(z_stored[s], 16)
                act.wait_ge(z_stored[0], 16 * (NT // 2 + 2))
                act.wait_ge(z_stored[1], 16 * (NT // 2 + 1))




def skewed_turns(eng, turn):
    turn(0, 0, 0, True, False)
    with eng.Fori(0, (NT - 3) // 2) as r:
        turn(2 * r + 1, 1, r, False, False)
        turn(2 * r + 2, 0, r + 1, False, False)
    turn(NT - 2, 1, (NT - 2) // 2, False, False)
    turn(NT - 1, 0, (NT - 1) // 2, False, True)


def mla_prepare(nc, d, layer, ident, cache):
    with Phase(nc) as ph:
        wuq = ph.sb("mp_wuq", [P, 2, H * QK])
        wukv = ph.sb("mp_wukv", [P, H, NOPE + VD])
        wuk = ph.sb("mp_wuk", [P, H, NOPE])
        wuv = ph.sb("mp_wuv", [P, H, VD])
        gq = ph.sb("mp_gq", [P, QR])
        gkv = ph.sb("mp_gkv", [P, KVR])
        zq = ph.sb("mp_zq", [P, NT, MLA_COLS])
        trig = ph.sb("mp_trig", [P, NT, 2 * HALF])
        sq = ph.sb("mp_sq", [P, QR])
        ss = ph.sb("mp_ss", [P, 2])
        ms = ph.sb("mp_ms", [P, 2])
        sd = ph.sb("mp_sd", [P, 2])
        rs = ph.sb("mp_rs", [P, 2])
        cqn = ph.sb("mp_cqn", [P, QR])
        ckvn = ph.sb("mp_ckvn", [P, 2, KVR])
        kpad = ph.sb("mp_kpad", [P, 2, QK])
        t4 = ph.sb("mp_t4", [P, 4, H, HALF])
        k4 = ph.sb("mp_k4", [P, 4, HALF])
        cT = ph.sb("mp_cT", [P, 2, 3, P])
        q = ph.sb("mp_q", [P, H, QK])
        qT = ph.sb("mp_qT", [QK, 2, H, P])
        kT = ph.sb("mp_kT", [QK, 2, H, P])
        v = ph.sb("mp_v", [P, 2, H * VD])
        tp = ph.ps("mp_tp", [P, 4, P])
        qp = [ph.ps(f"mp_qp{i}", [P, 4, QK]) for i in range(2)]
        qtp = [ph.ps(f"mp_qtp{i}", [QK, 4, P]) for i in range(2)]
        ktp = [ph.ps(f"mp_ktp{i}", [NOPE, 4, P]) for i in range(2)]
        vp = ph.ps("mp_vp", [P, H * VD])
        w_loaded, z_loaded = ph.sem("w_loaded"), ph.sem("z_loaded")
        q_stored, kv_stored, c_stored = ph.sem2("q_stored"), ph.sem2("kv_stored"), ph.sem2("c_stored")
        squares, ms_ready, sd_ready = ph.sem("squares"), ph.sem("ms_ready"), ph.sem("sd_ready")
        w_split, lat_ready, tp_done = ph.sem("w_split"), ph.sem("lat_ready"), ph.sem("tp_done")
        n_steps, r_steps = ph.sem("n_steps"), ph.sem("r_steps")
        cT_ready, kr_ready, q_done, kv_done = ph.sem("cT_ready"), ph.sem("kr_ready"), ph.sem("q_done"), ph.sem("kv_done")
        q_copied, q_rot, qt_done, qT_ready = ph.sem("q_copied"), ph.sem("q_rot"), ph.sem("qt_done"), ph.sem("qT_ready")
        kT_ready, v_ready = ph.sem("kT_ready"), ph.sem("v_ready")
        with nc.Block() as block:
            @block.sync
            def _(sp):
                sp.dma_start(zq[:, :, :], d["Z"][PAD:PAD + ROWS, C_Q:C_Q + MLA_COLS].rearrange("(t p) n -> p t n", p=P)).then_inc(z_loaded, 16)
                sp.dma_start(gq[:, :], row_of_layer(d["q_norm_g"], layer)).then_inc(w_loaded, 16)
                sp.dma_start(gkv[:, :], row_of_layer(d["kv_norm_g"], layer)).then_inc(w_loaded, 16)
                sp.dma_start(trig[:, :, :], d["c_trig"].rearrange("(t p) n -> p t n", p=P)).then_inc(w_loaded, 16)
                sp.dma_start(wuq[:, :, :], of_layer(d["w_uq"], layer).rearrange("(k p) n -> p k n", k=2)).then_inc(w_loaded, 16)
                sp.dma_start(wukv[:, :, :].rearrange("p h n -> p (h n)"), of_layer(d["w_ukv"], layer)).then_inc(w_loaded, 16)
                cache.load(sp, d, layer, cache.COUNTS[0], cache.COUNTS[1], 1)

            def of_tile(buf, t, c0, c1):
                return buf[:, ds(t, 1), c0:c1].rearrange("p t n -> p (t n)")

            @block.scalar
            def _(act):
                def squares_of(t):
                    act.wait_ge(ms_ready, t + 1)
                    act.activation(sq[:, 0:QR], of_tile(zq, t, 0, QR), ACT.Square, accum_out=ss[:, 0:1]).then_inc(squares, 1)
                    act.wait_ge(squares, 2 * t + 1)
                    act.activation(sq[:, 0:KVR], of_tile(zq, t, QR, QR + KVR), ACT.Square, accum_out=ss[:, 1:2]).then_inc(squares, 1)
                    act.wait_ge(ms_ready, t + 2)
                    act.activation(sd[:, :], ms[:, :], ACT.Sqrt).then_inc(sd_ready, 1)

                def queries_out(t, s, r):
                    act.wait_ge(q_stored[s], 16 * (r + 1))
                    for n in range(2):
                        act.wait_ge(qt_done, 2 * t + n + 1)
                        act.activation(qT[:, s, 4 * n:4 * n + 4, :], qtp[n][:, :, :], ACT.Copy).then_inc(qT_ready, 1)
                    act.wait_ge(qT_ready, 2 * t + 2)
                    act.dma_start(d["QT"][:, :, rows(t)].rearrange("h p n -> p h n"), qT[:, s]).then_inc(q_stored[s], 16)

                def turn(t, s, r, first, last_tile):
                    if not last_tile:
                        squares_of(t + 1)
                    if not first:
                        queries_out(t - 1, 1 - s, r - 1 + s)
                    for n in range(2):
                        act.wait_ge(q_done, 2 * t + n + 1)
                        act.activation(q[:, 4 * n:4 * n + 4, :], qp[n][:, :, :], ACT.Copy).then_inc(q_copied, 1)
                    act.wait_ge(kv_done, 2 * t + 2)
                    act.wait_ge(kv_stored[s], 16 * (3 * r + 1))
                    act.activation(v[:, s, :], vp[:, :], ACT.Copy).then_inc(v_ready, 1)
                    act.wait_ge(kT_ready, 3 * t + 4)
                    act.dma_start(d["KT"][:, :, rows(t)].rearrange("h p n -> p h n"), kT[:, s]).then_inc(kv_stored[s], 16)
                    act.wait_ge(v_ready, t + 2)
                    act.dma_start(d["V"][rows(t)], v[:, s, :]).then_inc(kv_stored[s], 16)
                    act.dma_start(of_layer(d["ckv_all"], layer)[rows(t)], ckvn[:, s, :]).then_inc(kv_stored[s], 16)
                    act.dma_start(of_layer(d["krope_all"], layer)[rows(t)], kpad[:, s, NOPE:]).then_inc(c_stored[s], 16)

                for s in range(2):
                    act.sem_inc(q_stored[s], 16)
                    act.sem_inc(kv_stored[s], 16)
                act.sem_inc(v_ready, 1)
                act.wait_ge(z_loaded, 16)
                squares_of(0)
                act.wait_ge(w_loaded, 80)
                act.activation(wuk[:, :, :], wukv[:, :, 0:NOPE], ACT.Copy).then_inc(w_split, 1)
                act.activation(wuv[:, :, :], wukv[:, :, NOPE:], ACT.Copy).then_inc(w_split, 1)
                skewed_turns(act, turn)
                queries_out(NT - 1, 0, NT // 2)
                for s in range(2):
                    act.wait_ge(q_stored[s], 16 * (NT // 2 + 2 - s))
                    act.wait_ge(kv_stored[s], 16 * (3 * (NT // 2 + 1 - s) + 1))
                    act.wait_ge(c_stored[s], 16 * (NT // 2 + 2 - s))

            @block.vector
            def _(dve):
                NORM_STEPS, ROTATE_STEPS = 10, 7

                def normalise(t, s, r):
                    st = Steps(dve, n_steps, t, NORM_STEPS)
                    dve.wait_ge(squares, 2 * t + 2)
                    st.did(dve.tensor_scalar(ms[:, 0:1], ss[:, 0:1], 1.0 / QR, RMS_EPS, ALU.mult, ALU.add))
                    dve.tensor_scalar(ms[:, 1:2], ss[:, 1:2], 1.0 / KVR, RMS_EPS, ALU.mult, ALU.add).then_inc(ms_ready, 1)
                    dve.wait_ge(sd_ready, t + 1)
                    st.did(dve.reciprocal(rs[:, :], sd[:, :]))
                    st.wait()
                    dve.wait_ge(kv_stored[s], 16 * (3 * r + 1))
                    dve.wait_ge(c_stored[s], 16 * (r + 1))
                    st.did(dve.scalar_tensor_tensor(cqn[:, :], of_tile(zq, t, 0, QR), rs[:, 0:1], gq[:, :], ALU.mult, ALU.mult))
                    st.did(dve.scalar_tensor_tensor(ckvn[:, s, :], of_tile(zq, t, QR, QR + KVR), rs[:, 1:2], gkv[:, :], ALU.mult, ALU.mult))
                    cos, sin = of_tile(trig, t, 0, HALF), of_tile(trig, t, HALF, 2 * HALF)
                    k1, k2 = of_tile(zq, t, QR + KVR, QR + KVR + HALF), of_tile(zq, t, QR + KVR + HALF, MLA_COLS)
                    st.did(dve.tensor_tensor(k4[:, 0, :], k1, cos, ALU.mult))
                    st.did(dve.tensor_tensor(k4[:, 1, :], k2, sin, ALU.mult))
                    st.did(dve.tensor_tensor(k4[:, 2, :], k1, sin, ALU.mult))
                    st.did(dve.tensor_tensor(k4[:, 3, :], k2, cos, ALU.mult))
                    st.wait()
                    st.did(dve.tensor_tensor(kpad[:, s, NOPE:NOPE + HALF], k4[:, 0, :], k4[:, 1, :], ALU.subtract))
                    st.did(dve.tensor_tensor(kpad[:, s, NOPE + HALF:], k4[:, 2, :], k4[:, 3, :], ALU.add))
                    st.wait()
                    dve.sem_inc(lat_ready, 1)
                    st.end()

                def turn(t, s, r, first, last_tile):
                    st = Steps(dve, r_steps, t, ROTATE_STEPS)
                    dve.wait_ge(tp_done, t + 1)
                    dve.tensor_copy(cT[:, s, :, :], tp[:, 0:3, :]).then_inc(cT_ready, 1)
                    st.did(dve.tensor_copy(kT[NOPE:QK, s, :, :], tp[NOPE:QK, 3:4, :].broadcast_to([ROPE, H, P])))
                    st.wait()
                    dve.sem_inc(kT_ready, 1)
                    if not last_tile:
                        normalise(t + 1, 1 - s, r + s)
                    for n in range(2):
                        dve.wait_ge(kv_done, 2 * t + 1)
                        dve.tensor_copy(kT[0:NOPE, s, 4 * n:4 * n + 4, :], ktp[n][:, :, :]).then_inc(kT_ready, 1)
                    dve.wait_ge(q_copied, 2 * t + 2)
                    q1, q2 = q[:, :, NOPE:NOPE + HALF], q[:, :, NOPE + HALF:]
                    cosb = trig[:, ds(t, 1), 0:HALF].broadcast_to([P, H, HALF])
                    sinb = trig[:, ds(t, 1), HALF:].broadcast_to([P, H, HALF])
                    st.did(dve.tensor_tensor(t4[:, 0], q1, cosb, ALU.mult))
                    st.did(dve.tensor_tensor(t4[:, 1], q2, sinb, ALU.mult))
                    st.did(dve.tensor_tensor(t4[:, 2], q1, sinb, ALU.mult))
                    st.did(dve.tensor_tensor(t4[:, 3], q2, cosb, ALU.mult))
                    st.wait()
                    st.did(dve.tensor_tensor(q1, t4[:, 0], t4[:, 1], ALU.subtract))
                    st.did(dve.tensor_tensor(q2, t4[:, 2], t4[:, 3], ALU.add))
                    st.wait()
                    dve.sem_inc(q_rot, 1)
                    st.end()

                dve.sem_inc(ms_ready, 1)
                dve.sem_inc(kT_ready, 1)
                for s in range(2):
                    dve.sem_inc(c_stored[s], 16)
                dve.memset(kpad[:, :, :], 0.0).then_inc(w_split, 1)
                dve.wait_ge(w_loaded, 80)
                normalise(0, 0, 0)
                skewed_turns(dve, turn)

            @block.tensor
            def _(pe):
                def queries(t):
                    pe.wait_ge(q_rot, t + 1)
                    for n in range(2):
                        for h in range(4):
                            last = pe.transpose(qtp[n][:, h, :], q[:, 4 * n + h, :], ident[:, :])
                        last.then_inc(qt_done, 1)

                def turn(t, s, r, first, last_tile):
                    pe.wait_ge(lat_ready, t + 1)
                    for c in range(2):
                        pe.transpose(tp[:, c, :], cqn[:, c * P:(c + 1) * P], ident[:, :])
                    pe.transpose(tp[:, 2, :], ckvn[:, s, :], ident[:, :])
                    pe.transpose(tp[0:QK, 3, :], kpad[:, s, :], ident[:, :]).then_inc(tp_done, 1)
                    if not first:
                        queries(t - 1)
                    pe.wait_ge(cT_ready, t + 1)
                    for n in range(2):
                        for c in range(2):
                            last = pe.matmul(qp[n][:, :, :].rearrange("p h n -> p (h n)"), cT[:, s, c, :], wuq[:, c, 4 * QK * n:4 * QK * (n + 1)],
                                             start=(c == 0), stop=(c == 1))
                        last.then_inc(q_done, 1)
                    pe.wait_ge(kT_ready, 3 * t + 1)
                    for h in range(H):
                        last = pe.matmul(ktp[h // 4][:, h % 4, :], wuk[:, h, :], cT[:, s, 2, :], start=True, stop=True)
                    last.then_inc(kv_done, 1)
                    pe.wait_ge(v_ready, t + 1)
                    pe.matmul(vp[:, :], cT[:, s, 2, :], wuv[:, :, :].rearrange("p h n -> p (h n)"), start=True, stop=True).then_inc(kv_done, 1)

                pe.wait_ge(w_loaded, 80)
                pe.wait_ge(w_split, 3)
                skewed_turns(pe, turn)
                queries(NT - 1)



def attention(nc, d, layer, ident, cache):
    units = [(s, qb) for s in range(2) for qb in range(TP)]
    n_units = len(units)
    groups = [[range(g, min(g + 4, qb + 1)) for g in range(0, qb + 1, 4)] for _, qb in units]
    first_group = [sum(len(g) for g in groups[:u]) for u in range(n_units)]
    n_groups = sum(len(g) for g in groups)
    n_even, n_odd = (n_groups + 1) // 2, n_groups // 2
    with Phase(nc) as ph:
        qT = ph.sb("at_qT", [QK, 2, SEQ])
        kT = ph.sb("at_kT", [QK, 2, SEQ])
        v = ph.sb("at_v", [P, 2, TP, VD])
        mask = ph.sb("at_mask", [P, P])
        probs = ph.sb("at_p", [P, 2, SEQ])
        pT = ph.sb("at_pT", [P, 2, TP, P])
        mx = ph.sb("at_mx", [P, 2])
        nmx = ph.sb("at_nmx", [P, 2])
        total = ph.sb("at_total", [P, 2])
        inv = ph.sb("at_inv", [P, 2])
        y = ph.sb("at_y", [P, 2, TP, VD])
        sc = [ph.ps(f"at_s{i}", [P, SEQ]) for i in range(2)]
        tp = [ph.ps(f"at_tp{i}", [P, 4, P]) for i in range(2)]
        op = [ph.ps(f"at_o{i}", [P, VD]) for i in range(2)]
        mask_loaded, loaded, y_stored = ph.sem("mask_loaded"), ph.sem2("loaded"), ph.sem2("y_stored")
        head_free, s_done, steps, mx_ready = ph.sem("head_free"), ph.sem("s_done"), ph.sem("steps"), ph.sem("mx_ready")
        p_ready, tp_done, pT_dve, pT_act = ph.sem("p_ready"), ph.sem("tp_done"), ph.sem("pT_dve"), ph.sem("pT_act")
        o_done, y_ready = ph.sem("o_done"), ph.sem("y_ready")

        cw = ph.sb("cv_w", [P, CONVW, 3])
        cwr = ph.sb("cv_wr", [P, 3, CONVW])
        cch = ph.sb("cv_cch", [P, 3, 2 * CONVW])
        cb = ph.sb("cv_b", [P, CONVW])
        u = ph.sb("cv_u", [P, 3, CONVW])
        yc = ph.sb("cv_y", [P, CONVW])
        past = ph.sb("cv_past", [DECB, 2, CONVW])
        cv_w, cv_in, cv_out, cv_state = (d["sw"][n] for n in ("cv_w", "cv_in", "cv_out", "cv_state"))
        cv, paced = ph.sem("cv"), ph.sem("paced")
        with nc.Block() as block:
            @block.sync
            def _(sp):
                sp.dma_start(mask[:, :], d["c_causal"]).then_inc(mask_loaded, 16)
                with sp.Fori(0, H // 2) as j:
                    for s in range(2):
                        head = 2 * j + s
                        sp.wait_ge(head_free, head + 1)
                        sp.dma_start(qT[:, s, :], d["QT"][ds(head, 1), :, 0:SEQ].rearrange("h p n -> (h p) n")).then_inc(loaded[s], 16)
                        sp.dma_start(kT[:, s, :], d["KT"][ds(head, 1), :, 0:SEQ].rearrange("h p n -> (h p) n")).then_inc(loaded[s], 16)
                        sp.dma_start(v[:, s, :, :], d["V"][0:SEQ, ds(head * VD, VD)].rearrange("(b p) n -> p b n", p=P)).then_inc(loaded[s], 16)
                        cache.load(sp, d, layer, cache.COUNTS[0] + cache.COUNTS[1] + 4 * head, 4, 2)

            def pair_turns(eng, turn):
                with eng.Fori(0, H // 2 - 1) as j:
                    turn(j, False)
                turn(H // 2 - 1, True)

            @block.tensor
            def _(pe):
                def scores(j, n):
                    s, qb = units[n % n_units]
                    if qb == 0:
                        pe.wait_ge(loaded[s], 48 * (j + n // n_units + 1))
                    keys = (qb + 1) * P
                    for c in range(0, keys, 512):
                        last = pe.matmul(sc[n % 2][:, c:min(c + 512, keys)], qT[:, s, qb * P:(qb + 1) * P],
                                         kT[:, s, c:min(c + 512, keys)], start=True, stop=True)
                    last.then_inc(s_done, 1)

                def turn(j, last_turn):
                    for n, (s, qb) in enumerate(units):
                        pe.wait_ge(p_ready, j * n_units + n + 1)
                        for g, blocks in enumerate(groups[n]):
                            m = first_group[n] + g
                            if m % 2 == 0:
                                pe.wait_ge(pT_dve, j * n_even + m // 2 + 1)
                            else:
                                pe.wait_ge(pT_act, j * n_odd + m // 2 + 1)
                            for kb in blocks:
                                last = pe.transpose(tp[m % 2][:, kb % 4, :], probs[:, n % 2, kb * P:(kb + 1) * P], ident[:, :])
                            last.then_inc(tp_done, 1)
                        if not (last_turn and n + 2 >= n_units):
                            scores(j, n + 2)
                        pe.wait_ge(y_ready, j * n_units + n + 1)
                        for g, blocks in enumerate(groups[n]):
                            m = first_group[n] + g
                            if m % 2 == 0:
                                pe.wait_ge(pT_dve, j * n_even + m // 2 + 2)
                            else:
                                pe.wait_ge(pT_act, j * n_odd + m // 2 + 2)
                            for kb in blocks:
                                last = pe.matmul(op[n % 2][:, :], pT[:, n % 2, kb, :], v[:, s, kb, :], start=(kb == 0), stop=(kb == qb))
                        last.then_inc(o_done, 1)

                scores(0, 0)
                scores(0, 1)
                pair_turns(pe, turn)

            @block.vector
            def _(dve):
                dve.sem_inc(head_free, 2)
                dve.sem_inc(pT_dve, 1)
                dve.sem_inc(y_ready, 2)
                dve.wait_ge(mask_loaded, 16)

                def maximum(st, j, n):
                    s, qb = units[n % n_units]
                    dve.wait_ge(s_done, j * n_units + n + 1)
                    diag = sc[n % 2][:, qb * P:(qb + 1) * P]
                    st.did(dve.tensor_tensor(diag, diag, mask[:, :], ALU.add))
                    st.wait()
                    st.did(dve.tensor_reduce(mx[:, n % 2:n % 2 + 1], sc[n % 2][:, 0:(qb + 1) * P], AX.X, ALU.max))
                    st.wait()
                    dve.tensor_scalar(nmx[:, n % 2:n % 2 + 1], mx[:, n % 2:n % 2 + 1], -SCALE, None, ALU.mult).then_inc(mx_ready, 1)

                def turn(j, last_turn):
                    st = Steps(dve, steps, j, 3 * n_units)
                    st.base = st.base + 4
                    for n, (s, qb) in enumerate(units):
                        for g, blocks in enumerate(groups[n]):
                            m = first_group[n] + g
                            if m % 2 == 0:
                                dve.wait_ge(tp_done, j * n_groups + m + 1)
                                dve.tensor_copy(pT[:, n % 2, blocks[0]:blocks[-1] + 1, :], tp[0][:, 0:len(blocks), :]).then_inc(pT_dve, 1)
                        dve.wait_ge(p_ready, j * n_units + n + 1)
                        st.did(dve.reciprocal(inv[:, n % 2:n % 2 + 1], total[:, n % 2:n % 2 + 1]))
                        st.wait()
                        if not (last_turn and n + 2 >= n_units):
                            maximum(st, j, n + 2)
                        if qb == 0:
                            dve.wait_ge(y_stored[s], 16 * (j + 1))
                        dve.wait_ge(o_done, j * n_units + n + 1)
                        dve.tensor_scalar(y[:, s, qb, :], op[n % 2][:, :], inv[:, n % 2:n % 2 + 1], None, ALU.mult).then_inc(y_ready, 1)
                        if qb == TP - 1:
                            dve.sem_inc(head_free, 1)
                first = Steps(dve, steps, 0, 4)
                for n in range(2):
                    maximum(first, 0, n)
                first.end()
                pair_turns(dve, turn)

            @block.scalar
            def _(act):
                act.sem_inc(pT_act, 1)
                for s in range(2):
                    act.sem_inc(y_stored[s], 16)

                def exponentials(j, n):
                    s, qb = units[n % n_units]
                    act.wait_ge(mx_ready, j * n_units + n + 1)
                    act.activation(probs[:, n % 2, 0:(qb + 1) * P], sc[n % 2][:, 0:(qb + 1) * P], ACT.Exp,
                                   bias=nmx[:, n % 2:n % 2 + 1], scale=SCALE, accum_out=total[:, n % 2:n % 2 + 1]).then_inc(p_ready, 1)

                def turn(j, last_turn):
                    for n, (s, qb) in enumerate(units):
                        for g, blocks in enumerate(groups[n]):
                            m = first_group[n] + g
                            if m % 2 == 1:
                                act.wait_ge(tp_done, j * n_groups + m + 1)
                                act.activation(pT[:, n % 2, blocks[0]:blocks[-1] + 1, :], tp[1][:, 0:len(blocks), :], ACT.Copy).then_inc(pT_act, 1)
                        if not (last_turn and n + 2 >= n_units):
                            exponentials(j, n + 2)
                        if qb == TP - 1:
                            act.wait_ge(y_ready, j * n_units + n + 3)
                            act.dma_start(d["Y"][0:SEQ, ds(CONVW + (2 * j + s) * VD, VD)].rearrange("(b p) n -> p b n", p=P),
                                          y[:, s, :, :]).then_inc(y_stored[s], 16)
                exponentials(0, 0)
                exponentials(0, 1)
                pair_turns(act, turn)
                for s in range(2):
                    act.wait_ge(y_stored[s], 16 * (H // 2 + 1))

            @block.gpsimd
            def _(pool):
                IN_ALL = 64 * TP + 48
                pool.dma_start(cwr[:, :, :].rearrange("p k n -> p (k n)"),
                               d["conv_w"].rearrange("l k n -> l (k n)")[ds(layer, 1), :].broadcast_to([P, 3 * CONVW])).then_inc(cv_w, 16)
                pool.wait_ge(cv_w, 16 * (layer + 1))
                pool.sem_inc(paced, 1)

                def gated(st, n):
                    for k in range(3):
                        st.did(pool.tensor_tensor(yc[0:n, :] if k == 0 else cch[0:n, k, 0:CONVW], u[0:n, k, :], cwr[0:n, k, :], ALU.mult))
                    for k in range(1, 3):
                        st.wait()
                        st.did(pool.tensor_tensor(yc[0:n, :], yc[0:n, :], cch[0:n, k, 0:CONVW], ALU.add))
                    st.wait()
                    st.did(pool.tensor_tensor(yc[0:n, :], yc[0:n, :], cb[0:n, :], ALU.mult))
                    st.wait()

                with pool.Fori(0, TP) as t:
                    st = Steps(pool, cv, t, 9)
                    for k in range(3):
                        pool.dma_start(cch[:, k, :], d["Z"][ds(t * P + k, P), C_CC:C_CC + 2 * CONVW]).then_inc(cv_in, 16)
                    pool.dma_start(cb[:, :], d["Z"][ds(PAD + t * P, P), C_CB:C_CB + CONVW]).then_inc(cv_in, 16)
                    pool.wait_ge(cv_in, IN_ALL * layer + 64 * (t + 1))
                    for k in range(3):
                        st.did(pool.tensor_tensor(u[:, k, :], cch[:, k, 0:CONVW], cch[:, k, CONVW:], ALU.mult))
                    st.wait()
                    gated(st, P)
                    st.end()
                    pool.dma_start(d["Y"][rows(t), 0:CONVW], yc[:, :]).then_inc(cv_out, 16)
                    pool.wait_ge(cv_out, 16 * (TP + 1) * layer + 16 * (t + 1))
                    pool.sem_inc(paced, 1)
                pool.dma_start(of_layer(d["conv_p"], layer), u[P - 2:P, 2, :]).then_inc(cv_state, 16)
                pool.wait_ge(cv_state, 32 * layer + 16)
                pool.sem_inc(paced, 1)
                s0 = PAD + SEQ
                pool.dma_start(cch[0:DECB, 2, :], d["Z"][s0:s0 + DECB, C_CC:C_CC + 2 * CONVW]).then_inc(cv_in, 16)
                pool.dma_start(cb[0:DECB, :], d["Z"][s0:s0 + DECB, C_CB:C_CB + CONVW]).then_inc(cv_in, 16)
                pool.dma_start(u[0:DECB, 0:2, :], of_layer(d["state_conv"], layer)).then_inc(cv_in, 16)
                pool.wait_ge(cv_in, IN_ALL * (layer + 1))
                st = Steps(pool, cv, TP, 7)
                st.base = 9 * TP
                st.did(pool.tensor_tensor(u[0:DECB, 2, :], cch[0:DECB, 2, 0:CONVW], cch[0:DECB, 2, CONVW:], ALU.mult))
                st.wait()
                gated(st, DECB)
                pool.dma_start(d["Y"][SEQ:SEQ + DECB, 0:CONVW], yc[0:DECB, :]).then_inc(cv_out, 16)
                pool.dma_start(of_layer(d["conv_s"], layer), u[0:DECB, 1:3, :]).then_inc(cv_state, 16)
                pool.wait_ge(cv_out, 16 * (TP + 1) * (layer + 1))
                pool.sem_inc(paced, 1)
                pool.wait_ge(cv_state, 32 * (layer + 1))
                pool.sem_inc(paced, 1)



VX = DH + 1


def mlstm_prompt(nc, d, layer, ident):
    with Phase(nc) as ph:
        gz = ph.sb("ml_gz", [P, TP, 2 * NH])
        gbias = ph.sb("ml_gbias", [P, 2 * NH])
        headrow = ph.sb("ml_headrow", [NH, NH, P])
        maskT = ph.sb("ml_maskT", [P, P])
        fw = ph.sb("ml_fw", [P, 5, TP, NH])
        gi = ph.sb("ml_gi", [NH, SEQ])
        lf = ph.sb("ml_lf", [NH, SEQ])
        w1 = ph.sb("ml_w1", [NH, SEQ])
        w2 = ph.sb("ml_w2", [NH, SEQ])
        keep = ph.sb("ml_keep", [NH, SEQ])
        m = ph.sb("ml_m", [NH, SEQ])
        b = ph.sb("ml_b", [NH, SEQ])
        mprev = ph.sb("ml_mprev", [NH, TP])
        rows4 = ph.sb("ml_rows", [NH, 4, SEQ])
        a = ph.sb("ml_a", [NH, SEQ])
        cols = ph.sb("ml_cols", [P, 4, TP, NH])
        wold = ph.sb("ml_wold", [DH, NH, TP])
        x = ph.sb("ml_x", [P, 2, 3 * MW])
        ks = ph.sb("ml_ks", [P, 2, NH, DH])
        qs = ph.sb("ml_qs", [P, 2, NH, DH])
        vx = ph.sb("ml_vx", [P, 2, NH, VX])
        vw = ph.sb("ml_vw", [P, 2, NH, VX])
        qT = ph.sb("ml_qT", [DH, 2, NH, P])
        qsT = ph.sb("ml_qsT", [DH, 2, NH, P])
        kT = ph.sb("ml_kT", [DH, 2, NH, P])
        e = ph.sb("ml_e", [P, 2, NH, P])
        dd = ph.sb("ml_d", [P, 2, NH, P])
        sm = ph.sb("ml_s", [P, 2, NH, P])
        state = ph.sb("ml_state", [DH, 2, NH, VX])
        carry = ph.sb("ml_carry", [DH, NH, VX])
        den = ph.sb("ml_den", [P, NH])
        den2 = ph.sb("ml_den2", [P, NH])
        rden = ph.sb("ml_rden", [P, NH])
        so = ph.sb("ml_so", [P, TP, NH, DH])
        hh = ph.sb("ml_h", [P, NH, DH])
        y = ph.sb("ml_y", [P, 2, MW])
        cT = ph.sb("ml_cT", [VX, NH, DH])
        pg = [ph.ps(f"ml_pg{i}", [P, 512]) for i in range(3)]
        pa = ph.ps("ml_pa", [P, NH, P])
        pqk = ph.ps("ml_pqk", [P, NH, P])
        pn = ph.ps("ml_pn", [P, NH, VX])
        pu = ph.ps("ml_pu", [DH, NH, VX])
        px = ph.ps("ml_px", [P, 512])
        loaded0, x_loaded, y_stored = ph.sem("loaded0"), ph.sem2("x_loaded"), ph.sem2("y_stored")
        g_tp, g_steps, g_act, g_cols = ph.sem("g_tp"), ph.sem("g_steps"), ph.sem("g_act"), ph.sem("g_cols")
        v_steps, x_free, scaled, tp_done = ph.sem("v_steps"), ph.sem("x_free"), ph.sem("scaled"), ph.sem("tp_done")
        qT_ready, kT_ready, a_done, e_ready = ph.sem("qT_ready"), ph.sem("kT_ready"), ph.sem("a_done"), ph.sem("e_ready")
        d_ready, s_ready, n_done, u_done = ph.sem("d_ready"), ph.sem("s_ready"), ph.sem("n_done"), ph.sem("u_done")
        st_ready, den_ready, y_ready, so_ready = ph.sem("st_ready"), ph.sem("den_ready"), ph.sem("y_ready"), ph.sem("so_ready")
        carry_ready, so_loaded, b_done = ph.sem("carry_ready"), ph.sem("so_loaded"), ph.sem("b_done")
        final, out_done = ph.sem("final"), ph.sem("out_done")

        def chunks(eng, turn):
            with eng.Fori(0, TP // 2 - 1) as r:
                for s in range(2):
                    turn(2 * r + s, s, r, False)
            for s in range(2):
                turn(TP - 2 + s, s, TP // 2 - 1, s == 1)

        with nc.Block() as block:
            @block.sync
            def _(sp):
                sp.dma_start(gz[:, :, :], d["Z"][PAD:PAD + SEQ, C_MI:C_MI + 2 * NH].rearrange("(c p) n -> p c n", p=P)).then_inc(loaded0, 16)
                sp.dma_start(gbias[:, :], row_of_layer(d["mlstm_gate_b"], layer)).then_inc(loaded0, 16)
                sp.dma_start(headrow[:, :, :], d["c_headrow"]).then_inc(loaded0, 16)
                sp.dma_start(maskT[:, :], d["c_causalT"]).then_inc(loaded0, 16)
                sp.dma_start(so[:, :, :, :].rearrange("p c h n -> p c (h n)"),
                             d["Z"][PAD:PAD + SEQ, C_MO:C_MO + MW].rearrange("(c p) n -> p c n", p=P)).then_inc(so_loaded, 16)
                with sp.Fori(0, TP // 2) as r:
                    for s in range(2):
                        t = 2 * r + s
                        sp.wait_ge(x_free, t + 1)
                        sp.dma_start(x[:, s, :], d["Z"][ds(PAD + t * P, P), C_MQ:C_MQ + 3 * MW]).then_inc(x_loaded[s], 16)
                sp.wait_ge(final, 1)
                sp.dma_start(of_layer(d["C_p"], layer).rearrange("h v e -> v h e"), cT[0:DH, :, :]).then_inc(out_done, 16)
                sp.dma_start(of_layer(d["n_p"], layer).rearrange("(o h) e -> o h e", o=1), cT[DH:VX, :, :]).then_inc(out_done, 16)
                sp.dma_start(of_layer(d["m_p"], layer).rearrange("(h o) -> h o", o=1), m[:, SEQ - 1:SEQ]).then_inc(out_done, 16)
                sp.wait_ge(out_done, 48)

            @block.tensor
            def _(pe):
                pe.wait_ge(g_steps, 12)
                for c in range(TP):
                    pe.transpose(pg[c // 4][0:NH, (c % 4) * P:(c % 4 + 1) * P], gz[:, c, 0:NH], ident[:, :])
                for c in range(TP):
                    dst = (px, pg[2])[c // 4]
                    last = pe.transpose(dst[0:NH, (c % 4) * P:(c % 4 + 1) * P], gz[:, c, NH:], ident[:, :])
                last.then_inc(g_tp, 1)
                pe.wait_ge(g_cols, 1)
                for k in range(4):
                    for c in range(TP):
                        pe.transpose(pg[0][:, (k * TP + c) * NH:(k * TP + c + 1) * NH], rows4[:, k, c * P:(c + 1) * P], ident[0:NH, 0:NH])
                for h in range(NH):
                    last = pe.matmul(px[0:DH, h * TP:(h + 1) * TP], headrow[:, h, 0:DH],
                                     rows4[:, 1, :].rearrange("h (c t) -> h c t", c=TP)[:, :, P - 1], start=True, stop=True)
                last.then_inc(g_tp, 1)
                pe.wait_ge(g_cols, 2)
                def transposes(t, s, r):
                    pe.wait_ge(x_loaded[s], 16 * (r + 1))
                    pe.wait_ge(scaled, t + 1)
                    for h in range(NH):
                        last = pe.matmul(pa[:, h, :], headrow[:, h, :], a[:, ds(t * P, P)], start=True, stop=True)
                    last.then_inc(a_done, 1)
                    for h in range(NH):
                        pe.transpose(pg[0][0:DH, h * P:(h + 1) * P], x[:, s, h * DH:(h + 1) * DH], ident[:, :])
                    for h in range(NH):
                        pe.transpose(pg[1][0:DH, h * P:(h + 1) * P], qs[:, s, h, :], ident[:, :])
                    for h in range(NH):
                        last = pe.transpose(pg[2][0:DH, h * P:(h + 1) * P], ks[:, s, h, :], ident[:, :])
                    last.then_inc(tp_done, 1)

                def turn(t, s, r, last_chunk):
                    pe.wait_ge(qT_ready, 2 * (t + 1))
                    pe.wait_ge(kT_ready, t + 1)
                    for h in range(NH):
                        last = pe.matmul(pqk[:, h, :], kT[:, s, h, :], qT[:, s, h, :], start=True, stop=True)
                    last.then_inc(b_done, 1)
                    pe.wait_ge(st_ready, t + 1)
                    for h in range(NH):
                        last = pe.matmul(pu[:, h, :], ks[:, s, h, :], vw[:, s, h, :], start=True, stop=True)
                    last.then_inc(u_done, 1)
                    if not last_chunk:
                        transposes(t + 1, 1 - s, r + s)
                    pe.wait_ge(s_ready, t + 1)
                    for h in range(NH):
                        pe.matmul(pn[:, h, :], sm[:, s, h, :], vx[:, s, h, :], start=True, stop=False)
                        last = pe.matmul(pn[:, h, :], qsT[:, s, h, :], state[:, s, h, :], start=False, stop=True)
                    last.then_inc(n_done, 1)
                transposes(0, 0, 0)
                chunks(pe, turn)
                pe.wait_ge(carry_ready, 1)
                for h in range(NH):
                    last = pe.transpose(px[0:VX, h * DH:(h + 1) * DH], carry[:, h, :], ident[0:DH, 0:DH])
                last.then_inc(g_tp, 1)

            @block.vector
            def _(dve):
                g = Steps(dve, g_steps, 0, 29)
                dve.wait_ge(loaded0, 64)
                g.did(dve.tensor_tensor(gz[:, :, :], gz[:, :, :], gbias[:, :].unsqueeze(1).broadcast_to([P, TP, 2 * NH]), ALU.add))
                g.did(dve.memset(keep[:, :], 1.0))
                g.wait()
                g.did(dve.memset(keep[:, :].rearrange("h (c t) -> h c t", c=TP)[:, :, 0:1], 0.0))
                f, (neg, u, w, rw, c1) = gz[:, :, NH:], (fw[:, i] for i in range(5))
                g.did(dve.tensor_scalar(neg, f, -1.0, None, ALU.mult))
                g.wait()
                g.did(dve.tensor_tensor(neg, neg, f, ALU.min))
                dve.wait_ge(g_act, 1)
                g.did(dve.tensor_scalar(w, u, 1.0, None, ALU.add))
                g.wait()
                g.did(dve.tensor_scalar(c1, w, -1.0, None, ALU.add))
                g.wait()
                g.did(dve.tensor_tensor(c1, u, c1, ALU.subtract))
                g.did(dve.reciprocal(rw, w))
                g.wait()
                g.did(dve.tensor_tensor(c1, c1, rw, ALU.mult))
                dve.wait_ge(g_act, 2)
                g.wait()
                g.did(dve.tensor_tensor(c1, c1, neg, ALU.add))
                g.wait()
                g.did(dve.scalar_tensor_tensor(f, f, 0.0, c1, ALU.min, ALU.subtract))
                assert g.n == 12
                dve.wait_ge(g_tp, 1)
                for c in range(2):
                    half = slice(c * 512, (c + 1) * 512)
                    g.did(dve.tensor_copy(gi[:, half], pg[c][0:NH, :]))
                    g.did(dve.tensor_copy(lf[:, half], (px, pg[2])[c][0:NH, :]))
                g.wait()
                g.did(dve.tensor_tensor_scan(m[:, :], lf[:, :], gi[:, :], 0.0, ALU.add, ALU.max))
                g.did(dve.tensor_tensor_scan(b[:, :], keep[:, :], lf[:, :], 0.0, ALU.mult, ALU.add))
                g.did(dve.memset(mprev[:, 0:1], 0.0))
                g.wait()
                g.did(dve.tensor_copy(mprev[:, 1:TP], m[:, :].rearrange("h (c t) -> h c t", c=TP)[:, 0:TP - 1, P - 1]))
                g.did(dve.tensor_tensor(a[:, :], b[:, :], m[:, :], ALU.subtract))
                g.did(dve.tensor_tensor(rows4[:, 0, :], gi[:, :], b[:, :], ALU.subtract))
                g.wait()
                chunked = lambda ap: ap.rearrange("h (c t) -> h c t", c=TP)
                g.did(dve.tensor_tensor(chunked(w1[:, :]), chunked(a[:, :]), mprev[:, :].unsqueeze(2).broadcast_to([NH, TP, P]), ALU.add))
                g.did(dve.tensor_tensor(chunked(w2[:, :]), chunked(rows4[:, 0, :]), chunked(a[:, :])[:, :, P - 1:P].broadcast_to([NH, TP, P]), ALU.add))
                g.did(dve.memset(carry[:, :, :], 0.0))
                g.did(dve.memset(state[:, :, :, :], 0.0))
                g.did(dve.memset(vx[:, :, :, :], 1.0))
                g.wait()
                dve.wait_ge(g_tp, 2)
                g.did(dve.tensor_copy(cols[:, :, :, :].rearrange("p k c h -> p (k c h)"), pg[0][:, 0:4 * TP * NH]))
                g.did(dve.tensor_copy(wold[:, :, :].rearrange("p h c -> p (h c)"), px[0:DH, 0:NH * TP]))
                g.wait()
                g.end()
                dve.sem_inc(g_cols, 1)
                dve.sem_inc(st_ready, 1)
                AHEAD, TURN = 4, 9

                def scale(v, t, s, r):
                    wi, ws = (cols[:, k, ds(t, 1), :].rearrange("p c h -> p (c h)") for k in (1, 2))
                    xq, xk, xv = (x[:, s, i * MW:(i + 1) * MW].rearrange("p (h n) -> p h n", h=NH) for i in range(3))
                    dve.wait_ge(x_loaded[s], 16 * (r + 1))
                    dve.wait_ge(n_done, t + 1)
                    v.did(dve.tensor_scalar(ks[:, s], xk, DH ** -0.5, None, ALU.mult))
                    v.did(dve.tensor_tensor(qs[:, s], xq, wi.unsqueeze(2).broadcast_to([P, NH, DH]), ALU.mult))
                    v.did(dve.tensor_copy(vx[:, s, :, 0:DH], xv))
                    v.wait()
                    v.did(dve.tensor_tensor(vw[:, s], vx[:, s], ws.unsqueeze(2).broadcast_to([P, NH, VX]), ALU.mult))
                    v.wait()
                    dve.sem_inc(scaled, 1)

                def decay_and_keys(t, s):
                    dve.wait_ge(a_done, t + 1)
                    dve.tensor_tensor(e[:, s], pa[:, :, :], maskT[:, :].unsqueeze(1).broadcast_to([P, NH, P]), ALU.add).then_inc(e_ready, 1)
                    dve.wait_ge(tp_done, t + 1)
                    dve.tensor_copy(kT[:, s], pg[2][0:DH, :].rearrange("p (h n) -> p h n", h=NH)).then_inc(kT_ready, 1)

                def turn(t, s, r, last_chunk):
                    v = Steps(dve, v_steps, t, TURN)
                    v.base = v.base + AHEAD
                    if not last_chunk:
                        scale(v, t + 1, 1 - s, r + s)
                    dve.wait_ge(d_ready, t + 1)
                    dve.wait_ge(b_done, t + 1)
                    dve.tensor_tensor(sm[:, s], pqk[:, :, :], dd[:, s], ALU.mult).then_inc(s_ready, 1)
                    dve.wait_ge(u_done, t + 1)
                    dve.wait_ge(n_done, t + 2)
                    for h in range(NH):
                        last = dve.scalar_tensor_tensor(state[:, 1 - s, h, :], state[:, s, h, :], wold[:, h, ds(t, 1)], pu[:, h, :], ALU.mult, ALU.add)
                    v.did(last)
                    v.wait()
                    dve.sem_inc(st_ready, 1)
                    if not last_chunk:
                        decay_and_keys(t + 1, 1 - s)
                    em = cols[:, 3, ds(t, 1), :].rearrange("p c h -> p (c h)")
                    dve.wait_ge(den_ready, t + 1)
                    v.did(dve.tensor_tensor(den2[:, :], den[:, :], em, ALU.max))
                    v.wait()
                    v.did(dve.reciprocal(rden[:, :], den2[:, :]))
                    v.wait()
                    v.did(dve.tensor_tensor(hh[:, :, :], pn[:, :, 0:DH], rden[:, :].unsqueeze(2).broadcast_to([P, NH, DH]), ALU.mult))
                    v.wait()
                    dve.wait_ge(so_ready, 1)
                    dve.wait_ge(y_stored[s], 16 * (r + 1))
                    v.did(dve.tensor_tensor(y[:, s, :].rearrange("p (h n) -> p h n", h=NH), hh[:, :, :], so[:, ds(t, 1)].rearrange("p c h n -> p (c h) n"), ALU.mult))
                    v.wait()
                    dve.sem_inc(y_ready, 1)
                    assert v.n == TURN - (AHEAD if last_chunk else 0)
                scale(Steps(dve, v_steps, 0, AHEAD), 0, 0, 0)
                decay_and_keys(0, 0)
                chunks(dve, turn)
                v = Steps(dve, v_steps, TP, 2)
                v.base = 9 * TP
                v.did(dve.tensor_copy(carry[:, :, :], state[:, 0]))
                v.wait()
                dve.sem_inc(carry_ready, 1)
                dve.wait_ge(g_tp, 3)
                v.did(dve.tensor_copy(cT[:, :, :], px[0:VX, 0:NH * DH].rearrange("p (h n) -> p h n", h=NH)))
                v.wait()
                dve.sem_inc(final, 1)

            @block.scalar
            def _(act):
                for s in range(2):
                    act.sem_inc(y_stored[s], 16)
                act.sem_inc(n_done, 2)
                act.sem_inc(x_free, 2)
                act.wait_ge(so_loaded, 16)
                act.activation(so[:, :, :, :].rearrange("p c h n -> p (c h n)"), so[:, :, :, :].rearrange("p c h n -> p (c h n)"), ACT.Sigmoid).then_inc(so_ready, 1)
                act.wait_ge(g_steps, 5)
                act.activation(fw[:, 1], fw[:, 0], ACT.Exp).then_inc(g_act, 1)
                act.wait_ge(g_steps, 6)
                act.activation(fw[:, 0], fw[:, 2], ACT.Ln).then_inc(g_act, 1)
                act.wait_ge(g_steps, 24)
                act.activation(rows4[:, 1, :], w1[:, :], ACT.Exp)
                act.activation(rows4[:, 2, :], w2[:, :], ACT.Exp)
                act.activation(rows4[:, 3, :], m[:, :], ACT.Exp, scale=-1.0).then_inc(g_act, 1)
                act.wait_ge(g_act, 3)
                act.sem_inc(g_cols, 1)
                act.wait_ge(g_cols, 2)
                def ahead(t, s):
                    act.wait_ge(tp_done, t + 1)
                    act.activation(qT[:, s], pg[0][0:DH, :].rearrange("p (h n) -> p h n", h=NH), ACT.Copy).then_inc(qT_ready, 1)
                    act.activation(qsT[:, s], pg[1][0:DH, :].rearrange("p (h n) -> p h n", h=NH), ACT.Copy).then_inc(qT_ready, 1)
                    act.sem_inc(x_free, 1)
                    act.wait_ge(e_ready, t + 1)
                    for h in range(NH):
                        last = act.activation(dd[:, s, h, :], e[:, s, h, :], ACT.Exp, bias=cols[:, 0, ds(t, 1), h])
                    last.then_inc(d_ready, 1)

                def turn(t, s, r, last_chunk):
                    if not last_chunk:
                        ahead(t + 1, 1 - s)
                    act.wait_ge(n_done, t + 3)
                    act.activation(den[:, :], pn[:, :, DH], ACT.Abs).then_inc(den_ready, 1)
                    act.wait_ge(y_ready, t + 1)
                    act.dma_start(d["Y"][rows(t), CONVW + H * VD:], y[:, s, :]).then_inc(y_stored[s], 16)
                ahead(0, 0)
                chunks(act, turn)
                for s in range(2):
                    act.wait_ge(y_stored[s], 16 * (TP // 2 + 1))



def sample_attention(nc, d, layer, ident, cache):
    BH = DECB * H
    ckv, kr = cache.ckv, cache.kr
    with Phase(nc) as ph:
        cn = ph.sb("sa_cn", [DECB, LX])
        krn = ph.sb("sa_krn", [DECB, ROPE])
        own = ph.sb("sa_own", [DECB, DECB, H])
        ones = ph.sb("sa_ones", [BH, P])
        wukv = ph.sb("sa_wukv", [P, H, NOPE + VD])
        wukT = ph.sb("sa_wukT", [NOPE, H, P])
        wuv = ph.sb("sa_wuv", [P, H, VD])
        qTs = ph.sb("sa_qT", [QK, H, DECB])
        qlat = ph.sb("sa_qlat", [P, DECB, H])
        qr = ph.sb("sa_qr", [ROPE, DECB, H])
        qrd = ph.sb("sa_qrd", [P, DECB, 4, H])
        cnT = ph.sb("sa_cnT", [P, DECB])
        krnT = ph.sb("sa_krnT", [ROPE, DECB])
        cT = ph.sb("sa_cT", [P, 2, PAGES, P])
        krT = ph.sb("sa_krT", [P, 2, PAGES // 4, P])
        S = ph.sb("sa_S", [P, DECB, PAGES, H])
        SX = ph.sb("sa_SX", [DECB, BH])
        mxp = ph.sb("sa_mxp", [P, DECB, H])
        mcol = ph.sb("sa_mcol", [BH, 1])
        mdiag = ph.sb("sa_mdiag", [BH, BH])
        mb = ph.sb("sa_mb", [P, DECB, H])
        pst = ph.sb("sa_pst", [P, 2, PAGES, H])
        pxst = ph.sb("sa_pxst", [DECB, 2, H])
        on = ph.sb("sa_on", [H, DECB, KVR])
        ro = ph.sb("sa_ro", [H, 2])
        ol = ph.sb("sa_ol", [P, H, DECB])
        att = ph.sb("sa_att", [DECB, H * VD])
        tpb = [ph.ps(f"sa_tp{i}", [P, 4, P]) for i in range(4)]
        ktp = ph.ps("sa_ktp", [P, 4, P])
        scp = [ph.ps(f"sa_sc{i}", [P, PAGES, H]) for i in range(2)]
        misc = ph.ps("sa_misc", [P, 512])
        loaded0 = ph.sem("loaded0")
        prep, pe_prep, st_q = ph.sem("prep"), ph.sem("pe_prep"), ph.sem("st_q")
        tp_done, cT_dve, cT_act, sc_done = ph.sem("tp_done"), ph.sem("cT_dve"), ph.sem("cT_act"), ph.sem("sc_done")
        S_ready, mx_done, glob, p_ready = ph.sem("S_ready"), ph.sem("mx_done"), ph.sem("glob"), ph.sem("p_ready")
        pst_ready, o_done, on_ready, oT_done = ph.sem("pst_ready"), ph.sem("o_done"), ph.sem("on_ready"), ph.sem("oT_done")
        ol_ready, b_steps, att_done, att_ready, out_done = (ph.sem(n) for n in ("ol_ready", "b_steps", "att_done", "att_ready", "out_done"))
        with nc.Block() as block:
            @block.sync
            def _(sp):
                sp.dma_start(wukv[:, :, :].rearrange("p h n -> p (h n)"), of_layer(d["w_ukv"], layer)).then_inc(loaded0, 16)
                sp.dma_start(qTs[:, :, :], d["QT"][:, :, SEQ:SEQ + DECB].rearrange("h p n -> p h n")).then_inc(loaded0, 16)
                sp.dma_start(cn[:, 0:KVR], of_layer(d["ckv_all"], layer)[SEQ:SEQ + DECB]).then_inc(loaded0, 16)
                sp.dma_start(krn[:, :], of_layer(d["krope_all"], layer)[SEQ:SEQ + DECB]).then_inc(loaded0, 16)
                sp.dma_start(own[:, :, :].rearrange("p b h -> p (b h)"), d["c_own"]).then_inc(loaded0, 16)
                sp.wait_ge(att_ready, 1)
                sp.dma_start(d["Y"][SEQ:SEQ + DECB, CONVW:CONVW + H * VD], att[:, :]).then_inc(out_done, 16)
                sp.wait_ge(out_done, 16)

            @block.gpsimd
            def _(pool):
                pool.memset(ones[:, :], 1.0).then_inc(prep, 1)
                pool.memset(qrd[:, :, :, :], 0.0).then_inc(prep, 1)
                pool.memset(cn[:, KVR:], 1.0).then_inc(prep, 1)
                pool.memset(ckv[:, :, KVR:], 1.0).then_inc(prep, 1)

            @block.tensor
            def _(pe):
                pe.wait_ge(loaded0, 80)
                for h in range(H):
                    last = pe.transpose(tpb[h // 4][0:NOPE, h % 4, :], wukv[:, h, 0:NOPE], ident[:, :])
                pe.transpose(misc[:, 0:DECB], cn[:, 0:KVR], ident[0:DECB, 0:DECB])
                pe.transpose(misc[0:ROPE, DECB:2 * DECB], krn[:, :], ident[0:DECB, 0:DECB]).then_inc(pe_prep, 1)
                pe.wait_ge(st_q, 1)
                for h in range(H):
                    last = pe.matmul(misc[:, 64 + h * DECB:64 + (h + 1) * DECB], wukT[:, h, :], qTs[0:NOPE, h, :], start=True, stop=True)
                last.then_inc(pe_prep, 1)
                pe.wait_ge(st_q, 2)
                pe.matmul(misc[0:DECB, 256:256 + BH], cnT[:, :], qlat[:, :, :].rearrange("p b h -> p (b h)"), start=True, stop=False)
                pe.matmul(misc[0:DECB, 256:256 + BH], krnT[:, :], qr[0:ROPE, :, :].rearrange("p b h -> p (b h)"), start=False, stop=True).then_inc(pe_prep, 1)
                for n, loaded in zip(cache.COUNTS, cache.pages_loaded):
                    pe.wait_ge(loaded, 32 * n)
                for b in range(DECB + 1):
                    if b < DECB:
                        for g in range(4):
                            pe.wait_ge((cT_dve, cT_act)[g % 2], (3 if g % 2 == 0 else 2) * b + (g // 2) + 1)
                            for c in range(4):
                                last = pe.transpose(tpb[g][:, c, :], ckv[:, b * PAGES + 4 * g + c, 0:KVR], ident[:, :])
                            last.then_inc(tp_done, 1)
                        pe.wait_ge(cT_dve, 3 * b + 3)
                        for c in range(4):
                            last = pe.transpose(ktp[:, c, :], kr[:, b * PAGES + 4 * c:b * PAGES + 4 * c + 4, :].rearrange("k o n -> k (o n)"), ident[:, :])
                        last.then_inc(tp_done, 1)
                    if b == 0:
                        continue
                    a, s = b - 1, (b - 1) % 2
                    pe.wait_ge(cT_dve, 3 * a + 6)
                    pe.wait_ge(cT_act, 2 * a + 4)
                    pe.wait_ge(S_ready, a + 1)
                    for g in range(4):
                        pe.matmul(scp[s][:, 4 * g:4 * g + 4, :].rearrange("k c h -> k (c h)"), krT[:, s, g, :],
                                  qrd[:, a].rearrange("p c h -> p (c h)"), start=True, stop=True)
                        for c in range(4 * g, 4 * g + 4):
                            last = pe.matmul(scp[s][:, c, :], cT[:, s, c, :], qlat[:, a, :], start=False, stop=True, skip_group_check=True)
                    last.then_inc(sc_done, 1)
                pe.wait_ge(mx_done, DECB + 1)
                pe.transpose(tpb[0][0:BH, 0, :], mxp[:, :, :].rearrange("p b h -> p (b h)"), ident[:, :])
                pe.transpose(tpb[0][0:BH, 1, 0:DECB], SX[:, :], ident[0:DECB, 0:DECB]).then_inc(glob, 1)
                pe.wait_ge(mx_done, DECB + 2)
                pe.matmul(tpb[1][:, 0, 0:BH], ones[:, :], mdiag[:, :], start=True, stop=True).then_inc(glob, 1)
                with pe.Fori(0, DECB // 2) as r:
                    for s in range(2):
                        b = 2 * r + s
                        pe.wait_ge(on_ready, b + 1)
                        pe.wait_ge(pst_ready, b + 1)
                        o = tpb[2 + s][0:H, :, :].rearrange("p a b -> p (a b)")[:, 0:LX]
                        for c in range(PAGES):
                            pe.matmul(o, pst[:, s, c, :], ckv[:, ds(b * PAGES + c, 1), :].rearrange("k o n -> k (o n)"), start=(c == 0), stop=False)
                        pe.matmul(o, pxst[:, s, :], cn[:, :], start=False, stop=True).then_inc(o_done, 1)
                pe.wait_ge(on_ready, DECB + 2)
                for b in range(DECB):
                    last = pe.transpose(tpb[0][:, 0, b * H:(b + 1) * H], on[:, b, :], ident[0:H, 0:H])
                last.then_inc(oT_done, 1)
                pe.wait_ge(ol_ready, 1)
                for h in range(H):
                    last = pe.matmul(misc[0:DECB, h * VD:(h + 1) * VD], ol[:, h, :], wuv[:, h, :], start=True, stop=True)
                last.then_inc(att_done, 1)

            @block.vector
            def _(dve):
                dve.sem_inc(cT_dve, 3)
                dve.sem_inc(on_ready, 2)
                dve.sem_inc(S_ready, 1)
                dve.wait_ge(loaded0, 80)
                dve.wait_ge(prep, 4)
                st = Steps(dve, b_steps, 0, 0)
                st.did(dve.tensor_copy(wuv[:, :, :], wukv[:, :, NOPE:]))
                dve.wait_ge(pe_prep, 1)
                for g in range(2):
                    st.did(dve.tensor_copy(wukT[:, 4 * g:4 * g + 4, :], tpb[g][0:NOPE, :, :]))
                st.did(dve.tensor_copy(cnT[:, :], misc[:, 0:DECB]))
                st.did(dve.tensor_copy(krnT[:, :], misc[0:ROPE, DECB:2 * DECB]))
                st.did(dve.tensor_copy(qr[:, :, :], qTs[NOPE:QK, :, :].rearrange("p h b -> p b h")))
                for g in range(4):
                    st.did(dve.tensor_copy(qrd[32 * g:32 * g + 32, :, g, :], qTs[NOPE:QK, :, :].rearrange("p h b -> p b h")))
                st.wait()
                dve.sem_inc(st_q, 1)
                dve.wait_ge(pe_prep, 2)
                st.did(dve.tensor_copy(qlat[:, :, :], misc[:, 64:64 + BH].rearrange("p (h b) -> p b h", h=H)))
                st.wait()
                dve.sem_inc(st_q, 1)
                dve.wait_ge(pe_prep, 3)
                st.did(dve.tensor_tensor(SX[:, :], misc[0:DECB, 256:256 + BH], own[:, :, :].rearrange("p b h -> p (b h)"), ALU.add))
                st.wait()
                dve.sem_inc(mx_done, 1)
                n0 = st.n
                with dve.Fori(0, DECB // 2) as r:
                    for s in range(2):
                        b = 2 * r + s
                        for g in (0, 2):
                            dve.wait_ge(tp_done, 5 * b + g + 1)
                            dve.tensor_copy(cT[:, s, 4 * g:4 * g + 4, :], tpb[g][:, :, :]).then_inc(cT_dve, 1)
                        dve.wait_ge(tp_done, 5 * b + 5)
                        dve.tensor_copy(krT[:, s, :, :], ktp[:, :, :]).then_inc(cT_dve, 1)
                        dve.wait_ge(S_ready, b + 2)
                        dve.tensor_reduce(mxp[:, ds(b, 1), :].rearrange("p o h -> p (o h)"), S[:, ds(b, 1)].rearrange("p o c h -> p h (o c)"), AX.X, ALU.max).then_inc(mx_done, 1)
                st.n = n0
                dve.wait_ge(glob, 1)
                st.did(dve.tensor_reduce(mcol[:, :], tpb[0][0:BH, 0:2, :].rearrange("p a b -> p (a b)")[:, 0:P + DECB], AX.X, ALU.max))
                st.wait()
                st.did(dve.tensor_scalar(mdiag[:, :], ident[0:BH, 0:BH], mcol[:, 0:1], None, ALU.mult))
                st.wait()
                dve.sem_inc(mx_done, 1)
                dve.wait_ge(glob, 2)
                st.did(dve.tensor_copy(mb[:, :, :].rearrange("p b h -> p (b h)"), tpb[1][:, 0, 0:BH]))
                st.wait()
                dve.wait_ge(S_ready, DECB + 1)
                for b in range(DECB):
                    st.did(dve.tensor_tensor(S[:, b], S[:, b], mb[:, b:b + 1, :].broadcast_to([P, PAGES, H]), ALU.subtract))
                st.did(dve.tensor_tensor(SX[:, :], SX[:, :], mb[0:DECB, :, :].rearrange("p b h -> p (b h)"), ALU.subtract))
                st.wait()
                dve.sem_inc(glob, 1)
                dve.wait_ge(p_ready, 2)
                n1 = st.n

                def weights_of(b, s):
                    dve.tensor_copy(pst[:, s], S[:, ds(b, 1)].rearrange("p o c h -> p (o c) h"))
                    dve.tensor_copy(pxst[:, s, :], SX[:, ds(b * H, H)]).then_inc(pst_ready, 1)

                def outputs_of(b, s):
                    dve.wait_ge(o_done, b + 1)
                    o = tpb[2 + s][0:H, :, :].rearrange("p a b -> p (a b)")[:, 0:LX]
                    dve.reciprocal(ro[:, s:s + 1], o[:, KVR:]).then_inc(b_steps, 1)
                    dve.wait_ge(b_steps, b + n1 + 1)
                    dve.tensor_scalar(on[:, ds(b, 1), :].rearrange("p o n -> p (o n)"), o[:, 0:KVR], ro[:, s:s + 1], None, ALU.mult).then_inc(on_ready, 1)

                weights_of(0, 0)
                with dve.Fori(0, DECB // 2 - 1) as r:
                    for s in range(2):
                        weights_of(2 * r + s + 1, 1 - s)
                        outputs_of(2 * r + s, s)
                weights_of(DECB - 1, 1)
                for s in range(2):
                    outputs_of(DECB - 2 + s, s)
                dve.wait_ge(oT_done, 1)
                dve.tensor_copy(ol[:, :, :], tpb[0][:, 0, 0:BH].rearrange("p (b h) -> p h b", b=DECB)).then_inc(ol_ready, 1)
                dve.wait_ge(att_done, 1)
                dve.tensor_copy(att[:, :], misc[0:DECB, 0:H * VD]).then_inc(att_ready, 1)

            @block.scalar
            def _(act):
                act.sem_inc(cT_act, 2)
                with act.Fori(0, DECB // 2) as r:
                    for s in range(2):
                        b = 2 * r + s
                        for g in (1, 3):
                            act.wait_ge(tp_done, 5 * b + g + 1)
                            act.activation(cT[:, s, 4 * g:4 * g + 4, :], tpb[g][:, :, :], ACT.Copy).then_inc(cT_act, 1)
                        act.wait_ge(sc_done, b + 1)
                        act.activation(S[:, ds(b, 1)].rearrange("p o c h -> p (o c) h"), scp[s][:, :, :], ACT.Copy).then_inc(S_ready, 1)
                act.wait_ge(glob, 3)
                act.activation(S[:, :, :, :].rearrange("p b c h -> p (b c h)"), S[:, :, :, :].rearrange("p b c h -> p (b c h)"), ACT.Exp, scale=SCALE).then_inc(p_ready, 1)
                act.activation(SX[:, :], SX[:, :], ACT.Exp, scale=SCALE).then_inc(p_ready, 1)



def mlstm_sample(nc, d, layer, ident):
    BHN, VG, VR = DECB * NH, 4, DH // 4
    G_Q, G_K, G_N, G_I, G_F, G_M, G_BI, G_BF, G_ALL = 0, 64, 128, 192, 193, 194, 195, 196, 197
    with Phase(nc) as ph:
        g = ph.sb("ms_g", [BHN, G_ALL])
        rep = ph.sb("ms_rep", [BHN, P])
        G = ph.sb("ms_G", [P, G_ALL])
        v = ph.sb("ms_v", [P, VR])
        o = ph.sb("ms_o", [P, VR])
        C = ph.sb("ms_C", [P, VR, DH])
        CQ = ph.sb("ms_CQ", [P, VR, DH])
        VK = ph.sb("ms_VK", [P, VR, DH])
        c = ph.sb("ms_c", [P, 32])
        big = ph.sb("ms_big", [P, 2, DH])
        n1 = ph.sb("ms_n1", [P, DH])
        num = ph.sb("ms_num", [P, VR])
        dv = ph.sb("ms_dv", [P, VR])
        y = ph.sb("ms_y", [P, VR])
        gp = ph.ps("ms_gp", [P, G_ALL])
        loaded, repd, steps, acts, out_done = ph.sem("loaded"), ph.sem("repd"), ph.sem("steps"), ph.sem("acts"), ph.sem("out_done")
        ready = ph.sem("ready")
        col = lambda i: c[:, i:i + 1]
        with nc.Block() as block:
            @block.sync
            def _(sp):
                z = d["Z"][PAD + SEQ:PAD + SEQ + DECB]
                for c0, w, src in ((G_Q, DH, z[:, C_MQ:C_MQ + MW].rearrange("b (h n) -> b h n", h=NH)),
                                   (G_K, DH, z[:, C_MK:C_MK + MW].rearrange("b (h n) -> b h n", h=NH)),
                                   (G_I, 1, z[:, C_MI:C_MI + NH].rearrange("b (h o) -> b h o", o=1)),
                                   (G_F, 1, z[:, C_MI + NH:C_MI + 2 * NH].rearrange("b (h o) -> b h o", o=1)),
                                   (G_N, DH, of_layer(d["state_mlstm_n"], layer)),
                                   (G_M, 1, of_layer(d["state_mlstm_m"], layer).rearrange("b (h o) -> b h o", o=1)),
                                   (G_BI, 1, d["mlstm_gate_b"][ds(layer, 1), 0:NH].unsqueeze(2).broadcast_to([DECB, NH, 1])),
                                   (G_BF, 1, d["mlstm_gate_b"][ds(layer, 1), NH:].unsqueeze(2).broadcast_to([DECB, NH, 1]))):
                    sp.dma_start(g[:, c0:c0 + w], src).then_inc(loaded, 16)
                sp.dma_start(v[:, :], z[:, C_MV:C_MV + MW].rearrange("b (q n) -> b q n", n=VR)).then_inc(loaded, 16)
                sp.dma_start(o[:, :], z[:, C_MO:C_MO + MW].rearrange("b (q n) -> b q n", n=VR)).then_inc(loaded, 16)
                sp.dma_start(rep[:, :], d["c_rep"]).then_inc(loaded, 16)
                sp.dma_start(C[:, :, :].rearrange("p v n -> p (v n)"),
                             of_layer(d["state_mlstm_C"], layer).rearrange("b h (g v) n -> (b h g) (v n)", g=VG)).then_inc(loaded, 16)
                sp.wait_ge(ready, 1)
                sp.dma_start(d["Y"][SEQ:SEQ + DECB, CONVW + H * VD:].rearrange("b (q n) -> b q n", n=VR), y[:, :]).then_inc(out_done, 16)
                sp.dma_start(of_layer(d["C_s"], layer).rearrange("r (g m) -> (r g) m", g=VG), C[:, :, :].rearrange("p v n -> p (v n)")).then_inc(out_done, 16)
                sp.dma_start(of_layer(d["n_s"], layer), n1[0:P:VG, :]).then_inc(out_done, 16)
                sp.dma_start(of_layer(d["m_s"], layer).rearrange("(r o) -> r o", o=1), c[0:P:VG, 10:11]).then_inc(out_done, 16)
                sp.wait_ge(out_done, 64)

            @block.tensor
            def _(pe):
                pe.wait_ge(loaded, 192)
                pe.matmul(gp[:, :], rep[:, :], g[:, :], start=True, stop=True).then_inc(repd, 1)

            @block.scalar
            def _(act):
                act.wait_ge(loaded, 192)
                act.activation(o[:, :], o[:, :], ACT.Sigmoid).then_inc(acts, 1)
                act.wait_ge(steps, 5)
                act.activation(col(3), col(2), ACT.Exp).then_inc(acts, 1)
                act.wait_ge(steps, 6)
                act.activation(col(8), col(4), ACT.Ln).then_inc(acts, 1)
                act.wait_ge(steps, 16)
                act.activation(c[:, 13:15], c[:, 11:13], ACT.Exp).then_inc(acts, 1)
                act.activation(col(15), col(10), ACT.Exp, scale=-1.0).then_inc(acts, 1)
                act.wait_ge(steps, 26)
                act.activation(col(20), col(19), ACT.Abs).then_inc(acts, 1)

            @block.vector
            def _(dve):
                st = Steps(dve, steps, 0, 34)

                def do(ins):
                    st.did(ins)
                    st.wait()
                TT, TS = dve.tensor_tensor, dve.tensor_scalar
                dve.wait_ge(repd, 1)
                do(dve.tensor_copy(G[:, :], gp[:, :]))
                q, k, n, i, f, m0 = G[:, G_Q:G_K], G[:, G_K:G_N], G[:, G_N:G_I], G[:, G_I:G_F], G[:, G_F:G_M], G[:, G_M:G_BI]
                do(TT(col(0), i, G[:, G_BI:G_BF], ALU.add))
                do(TT(col(1), f, G[:, G_BF:G_ALL], ALU.add))
                do(TS(col(16), col(1), -1.0, None, ALU.mult))
                do(TT(col(2), col(1), col(16), ALU.min))
                dve.wait_ge(acts, 2)
                do(TS(col(4), col(3), 1.0, None, ALU.add))
                do(TS(col(5), col(4), -1.0, None, ALU.add))
                do(TT(col(5), col(3), col(5), ALU.subtract))
                do(dve.reciprocal(col(6), col(4)))
                do(TT(col(5), col(5), col(6), ALU.mult))
                dve.wait_ge(acts, 3)
                do(TT(col(5), col(5), col(8), ALU.add))
                do(dve.scalar_tensor_tensor(col(7), col(1), 0.0, col(5), ALU.min, ALU.subtract))
                do(TT(col(9), col(7), m0, ALU.add))
                do(TT(col(10), col(9), col(0), ALU.max))
                do(TT(col(11), col(0), col(10), ALU.subtract))
                do(TT(col(12), col(9), col(10), ALU.subtract))
                do(TS(k, k, DH ** -0.5, None, ALU.mult))
                st.did(TT(big[:, 0, :], q, k, ALU.mult))
                do(TT(big[:, 1, :], q, n, ALU.mult))
                do(dve.tensor_reduce(c[:, 17:19], big[:, :, :], AX.X, ALU.add))
                st.did(TT(CQ[:, :, :], C[:, :, :], q.unsqueeze(1).broadcast_to([P, VR, DH]), ALU.mult))
                dve.wait_ge(acts, 5)
                dd, w, em = col(13), col(14), col(15)
                do(TT(col(21), col(17), dd, ALU.mult))
                do(dve.tensor_reduce(num[:, :], CQ[:, :, :], AX.X, ALU.add))
                do(dve.scalar_tensor_tensor(col(19), col(18), w, col(21), ALU.mult, ALU.add))
                do(TS(num[:, :], num[:, :], w, None, ALU.mult))
                do(dve.scalar_tensor_tensor(num[:, :], v[:, :], col(21), num[:, :], ALU.mult, ALU.add))
                dve.wait_ge(acts, 6)
                do(TT(col(22), col(20), em, ALU.max))
                do(dve.reciprocal(col(23), col(22)))
                do(dve.scalar_tensor_tensor(y[:, :], num[:, :], col(23), o[:, :], ALU.mult, ALU.mult))
                do(TS(dv[:, :], v[:, :], dd, None, ALU.mult))
                do(TT(VK[:, :, :], dv[:, :].unsqueeze(2).broadcast_to([P, VR, DH]), k.unsqueeze(1).broadcast_to([P, VR, DH]), ALU.mult))
                do(dve.scalar_tensor_tensor(C[:, :, :], C[:, :, :], w, VK[:, :, :], ALU.mult, ALU.add))
                do(TS(n1[:, :], k, dd, None, ALU.mult))
                do(dve.scalar_tensor_tensor(n1[:, :], n, w, n1[:, :], ALU.mult, ALU.add))
                dve.sem_inc(ready, 1)
                st.end()



NR = NG + NE
ASSIGN = NT * 2

STAGES = [("A", 0)] + [st for t in range(1, NT) for st in (("A", t), ("B", t - 1))] + [("B", NT - 1)]


def output_and_route(nc, d, layer, ident):
    w_tok, dx = d["sb_weight"], d["sb_row"]
    with Phase(nc) as ph:
        wout = ph.sb("op_wout", [P, KC, D])
        wpg = ph.sb("op_wpg", [P, KC, D])
        wpe = ph.sb("op_wpe", [P, 2, D])
        wr = ph.sb("op_wr", [P, KC, NR])
        mixg = ph.sb("op_mixg", [P, D])
        g1 = ph.sb("op_g1", [P, D])
        b1 = ph.sb("op_b1", [P, D])
        y = ph.sb("op_y", [P, 2, D])
        x = ph.sb("op_x", [P, 2, D])
        pp = ph.sb("op_p", [P, 2, DPLE])
        T = ph.sb("op_T", [P, 2, KC, P])
        pT = ph.sb("op_pT", [P, 2, 2, P])
        h1 = ph.sb("op_h1", [P, NT, D])
        sq = ph.sb("op_sq", [P, D])
        sig = ph.sb("op_sig", [P, D])
        base = ph.sb("op_base", [P, D])
        ss = ph.sb("op_ss", [P, 16])
        sd = ph.sb("op_sd", [P, 16])
        vx = ph.sb("op_vx", [P, 1])
        dx1 = ph.sb("op_dx1", [P, 1])
        rx = ph.sb("op_rx", [P, 1])
        stats = ph.sb("op_stats", [P, 2, 6])
        mv = ph.sb("op_mv", [P, 2])
        hold = ph.sb("op_hold", [1, 1])
        L = ph.sb("op_L", [P, NT, NR])
        tp = [ph.ps(f"op_tp{i}", [P, 4, P]) for i in range(2)]
        op = [ph.ps(f"op_o{i}", [P, 512]) for i in range(2)]
        gp = [ph.ps(f"op_gp{i}", [P, 512]) for i in range(2)]
        lp = ph.ps("op_lp", [P, 512])
        ptp = ph.ps("op_pt", [P, 2, P])
        c_loaded, wout_loaded, wpg_loaded = ph.sem("c_loaded"), ph.sem("wout_loaded"), ph.sem("wpg_loaded")
        y_loaded, x_loaded, base_stored = ph.sem2("y_loaded"), ph.sem2("x_loaded"), ph.sem("base_stored")
        steps, sq_done, ms_ready, sd_done = (ph.sem(n) for n in ("steps", "sq_done", "ms_ready", "sd_done"))
        y_ready, tp_done, T_dve, T_act, o_done = (ph.sem(n) for n in ("y_ready", "tp_done", "T_dve", "T_act", "o_done"))
        x_ready, var_ready, xd_done = (ph.sem(n) for n in ("x_ready", "var_ready", "xd_done"))
        h1_ready, pt_done, pT_ready, g_done, e_done = (ph.sem(n) for n in ("h1_ready", "pt_done", "pT_ready", "g_done", "e_done"))
        sig_done, mul_done, base_ready = (ph.sem(n) for n in ("sig_done", "mul_done", "base_ready"))
        rb = ph.sb("ro_b", [P, NR])
        idx = ph.sb("ro_idx", [P, NE])
        idxm = ph.sb("ro_idxm", [P, EPG])
        valid = ph.sb("ro_valid", [P, NT])
        before = ph.sb("ro_before", [P, P])
        ones = ph.sb("ro_ones", [P, P])
        part = ph.sb("ro_part", [P, 1])
        m1 = ph.sb("ro_m1", [P, NT])
        m2 = ph.sb("ro_m2", [P, NT])
        f1 = ph.sb("ro_f1", [P, NT])
        gd = ph.sb("ro_gd", [P, NT, NG])
        ge = ph.sb("ro_ge", [P, NT, NG])
        gw = ph.sb("ro_gw", [P, NT])
        ohg = ph.sb("ro_ohg", [P, NT, NG])
        ein = ph.sb("ro_ein", [P, NT, EPG])
        eq = ph.sb("ro_eq", [P, NT, EPG])
        oh = ph.sb("ro_oh", [P, 2, NT, EPG])
        big = ph.sb("ro_big", [P, NT, NE])
        OH = ph.sb("ro_OH", [P, 2, NT, NE])
        OS = ph.sb("ro_OS", [P, NT, NE])
        pre = ph.sb("ro_pre", [P, NT, NE])
        rank = ph.sb("ro_rank", [P, NT, NE])
        cnt = ph.sb("ro_cnt", [P, NE])
        cnti = ph.sb("ro_cnti", [P, NE], I32)
        nb = ph.sb("ro_nb", [P, NE])
        one = ph.sb("ro_one", [P, NE])
        incl = ph.sb("ro_incl", [P, NE])
        start = ph.sb("ro_start", [P, NE])
        bincl = ph.sb("ro_bincl", [P, NE])
        bstart = ph.sb("ro_bstart", [P, NE])
        tx = ph.sb("ro_tx", [P, NE])
        ty = ph.sb("ro_ty", [P, NE])
        sx = ph.sb("ro_sx", [P, NT, NE])
        dxf = ph.sb("ro_dxf", [P, 2, NT])
        tabf = ph.sb("ro_tabf", [P, 4])
        tab = ph.sb("ro_tab", [P, 4], I32)
        r_steps, r_act, r_pe, tab_stored = (ph.sem(n) for n in ("r_steps", "r_act", "r_pe", "tab_stored"))
        scattered = d["sw"]["scattered"]
        r_ready = ph.sem("r_ready")
        with nc.Block() as block:
            @block.sync
            def _(sp):
                def load_y(t):
                    sp.dma_start(y[:, t % 2, :], d["Y"][rows(t)]).then_inc(y_loaded[t % 2], 16)

                def load_x(t):
                    sp.dma_start(x[:, t % 2, :], d["H"][rows(t)]).then_inc(x_loaded[t % 2], 16)
                    sp.dma_start(pp[:, t % 2, :], of_layer(d["p_all"], layer)[rows(t)]).then_inc(x_loaded[t % 2], 16)

                def load_w(w, src, sem):
                    sp.dma_start(w[:, :, :].rearrange("p k n -> p (k n)"), of_layer(d[src], layer).rearrange("(p k) n -> p (k n)", k=KC)).then_inc(sem, 16)
                load_y(0)
                load_w(wout, "w_out", wout_loaded)
                for buf, src in ((mixg[:, :], row_of_layer(d["mix_norm_g"], layer)), (g1[:, :], row_of_layer(d["ln1_g"], layer)),
                                 (b1[:, :], row_of_layer(d["ln1_b"], layer))):
                    sp.dma_start(buf, src).then_inc(c_loaded, 16)
                load_y(1)
                load_x(0)
                load_x(1)
                load_w(wpg, "w_pg", wpg_loaded)
                for buf, src in ((rb[:, :], row_of_layer(d["b_route"], layer)),
                                 (wr[:, :, :].rearrange("p k n -> p (k n)"), of_layer(d["w_route"], layer).rearrange("(p k) n -> p (k n)", k=KC)),
                                 (wpe[:, :, :].rearrange("p k n -> p (k n)"), of_layer(d["w_pe"], layer).rearrange("(p k) n -> p (k n)", k=2)),
                                 (idx[:, :], d["c_idx"]), (valid[:, :], d["c_valid"]), (before[:, :], d["c_before"]), (part[:, :], d["c_part"])):
                    sp.dma_start(buf, src).then_inc(wpg_loaded, 16)
                for k, (stage, t) in enumerate(STAGES):
                    if t + 2 < NT:
                        sp.wait_ge(tp_done, 2 * (k + 1))
                        if stage == "A":
                            load_y(t + 2)
                        else:
                            sp.wait_ge(pt_done, t + 1)
                            load_x(t + 2)
                sp.wait_ge(r_ready, 2)
                sp.dma_start(d["BTAB"].rearrange("o (b n) -> (o b) n", n=4), tab[:, :]).then_inc(tab_stored, 16)
                sp.wait_ge(tab_stored, 16)

            @block.tensor
            def _(pe):
                def transposes(k):
                    stage, t = STAGES[k]
                    if stage == "A":
                        pe.wait_ge(y_ready, t + 1)
                    else:
                        pe.wait_ge(h1_ready, t + 1)
                    if k:
                        pe.wait_ge(T_dve, k)
                        pe.wait_ge(T_act, k)
                    for c in range(KC):
                        last = pe.transpose(tp[c // 4][:, c % 4, :], y[:, t % 2, c::KC] if stage == "A" else h1[:, t, c::KC], ident[:, :])
                        if c % 4 == 3:
                            last.then_inc(tp_done, 1)
                    if stage == "B":
                        if t >= 1:
                            pe.wait_ge(pT_ready, t)
                        pe.wait_ge(x_loaded[t % 2], 32 * (t // 2 + 1))
                        for c in range(2):
                            last = pe.transpose(ptp[:, c, :], pp[:, t % 2, c::2], ident[:, :])
                        last.then_inc(pt_done, 1)

                transposes(0)
                for k, (stage, t) in enumerate(STAGES):
                    if k + 1 < len(STAGES):
                        transposes(k + 1)
                    pe.wait_ge(T_dve, k + 1)
                    pe.wait_ge(T_act, k + 1)
                    if stage == "A":
                        pe.wait_ge(wout_loaded, 16)
                        if t >= 2:
                            pe.wait_ge(mul_done, t - 1)
                        for n in range(2):
                            for c in range(KC):
                                last = pe.matmul(op[n][:, :], T[:, k % 2, c, :], wout[:, c, n * 512:(n + 1) * 512], start=(c == 0), stop=(c == KC - 1))
                            last.then_inc(o_done, 1)
                    else:
                        pe.wait_ge(wpg_loaded, 16 * 8)
                        if t >= 1:
                            pe.wait_ge(sig_done, 2 * t)
                            pe.wait_ge(mul_done, t)
                        for n in range(2):
                            for c in range(KC):
                                last = pe.matmul(gp[n][:, :], T[:, k % 2, c, :], wpg[:, c, n * 512:(n + 1) * 512], start=(c == 0), stop=(c == KC - 1))
                            last.then_inc(g_done, 1)
                        for c in range(KC):
                            last = pe.matmul(lp[:, 0:NR], T[:, k % 2, c, :], wr[:, c, :], start=(c == 0), stop=(c == KC - 1))
                        pe.wait_ge(pT_ready, t + 1)
                        pe.wait_ge(x_ready, 2 * min(t + 2, NT))
                        for n in range(2):
                            for c in range(2):
                                last = pe.matmul(op[n][:, :], pT[:, t % 2, c, :], wpe[:, c, n * 512:(n + 1) * 512], start=(c == 0), stop=(c == 1))
                        last.then_inc(e_done, 1)
                pe.wait_ge(r_ready, 1)
                pe.matmul(gp[0][:, 0:NT * NE], ones[:, :], OS[:, :, :].rearrange("p t e -> p (t e)"), start=True, stop=True)
                pe.matmul(gp[1][:, 0:NT * NE], before[:, :], OS[:, :, :].rearrange("p t e -> p (t e)"), start=True, stop=True).then_inc(r_pe, 1)

            @block.scalar
            def _(act):
                def head_squares(t):
                    act.wait_ge(y_loaded[t % 2], 16 * (t // 2 + 1))
                    if t >= 1:
                        act.wait_ge(y_ready, t)
                    act.activation(sq[:, :], y[:, t % 2, :], ACT.Square).then_inc(sq_done, 1)
                    act.wait_ge(ms_ready, t + 1)
                    act.activation(sd[:, :], ss[:, :], ACT.Sqrt).then_inc(sd_done, 1)

                def copy(k):
                    act.wait_ge(tp_done, 2 * k + 2)
                    act.activation(T[:, k % 2, 4:8, :], tp[1][:, :, :], ACT.Copy).then_inc(T_act, 1)
                for t in range(2):
                    head_squares(t)
                    copy(t)
                for t in range(NT + 1):
                    if t < NT:
                        act.wait_ge(var_ready, t + 1)
                        act.activation(dx1[:, :], vx[:, :], ACT.Sqrt).then_inc(xd_done, 1)
                    if t >= 1:
                        if t >= 2:
                            act.wait_ge(mul_done, t - 1)
                        for n in range(2):
                            act.wait_ge(g_done, 2 * (t - 1) + n + 1)
                            act.activation(sig[:, n * 512:(n + 1) * 512], gp[n][:, :], ACT.Sigmoid).then_inc(sig_done, 1)
                    if t < NT:
                        copy(STAGES.index(("B", t)))
                        act.wait_ge(pt_done, t + 1)
                        act.activation(pT[:, t % 2], ptp[:, :, :], ACT.Copy).then_inc(pT_ready, 1)
                    if t >= 1:
                        act.wait_ge(base_ready, t)
                        act.dma_start(d["BASE"][rows(t - 1)], base[:, :]).then_inc(base_stored, 16)
                    if t + 2 < NT:
                        head_squares(t + 2)
                        copy(STAGES.index(("A", t + 2)))
                act.wait_ge(base_stored, 16 * NT)
                act.wait_ge(r_steps, 2)
                act.activation(ge[:, :, :], gd[:, :, :], ACT.Exp).then_inc(r_act, 1)
                act.wait_ge(r_steps, 26)
                act.activation(f1[:, :], m1[:, :], ACT.Exp).then_inc(r_act, 1)

            @block.vector
            def _(dve):
                dve.wait_ge(c_loaded, 48)
                st = Steps(dve, steps, 0, 0)

                def head_norm(t):
                    s = t % 2
                    y16 = y[:, s, :].rearrange("p (h n) -> p h n", h=16)
                    dve.wait_ge(sq_done, t + 1)
                    st.did(dve.tensor_reduce(ss[:, :], sq[:, :].rearrange("p (h n) -> p h n", h=16), AX.X, ALU.add))
                    st.wait()
                    dve.tensor_scalar(ss[:, :], ss[:, :], 1.0 / 64, RMS_EPS, ALU.mult, ALU.add).then_inc(ms_ready, 1)
                    dve.wait_ge(sd_done, t + 1)
                    st.did(dve.reciprocal(ss[:, :], sd[:, :]))
                    st.wait()
                    st.did(dve.tensor_tensor(y16, y16, ss[:, :].unsqueeze(2).broadcast_to([P, 16, 64]), ALU.mult))
                    st.wait()
                    dve.tensor_tensor(y[:, s, :], y[:, s, :], mixg[:, :], ALU.mult).then_inc(y_ready, 1)

                def copy(k):
                    dve.wait_ge(tp_done, 2 * k + 1)
                    dve.tensor_copy(T[:, k % 2, 0:4, :], tp[0][:, :, :]).then_inc(T_dve, 1)

                def residual_norm(t):
                    s = t % 2
                    dve.wait_ge(x_loaded[s], 32 * (t // 2 + 1))
                    for n in range(2):
                        dve.wait_ge(o_done, 2 * t + n + 1)
                        dve.scalar_tensor_tensor(x[:, s, n * 512:(n + 1) * 512], x[:, s, n * 512:(n + 1) * 512], ALPHA, op[n][:, :], ALU.mult, ALU.add).then_inc(x_ready, 1)
                    dve.wait_ge(x_ready, 2 * t + 2)
                    layer_norm_steps(dve, st, x[:, s, :], stats, mv[:, :], vx[:, :], hold[:, :])
                    st.wait()
                    dve.sem_inc(var_ready, 1)
                    dve.wait_ge(xd_done, t + 1)
                    st.did(dve.reciprocal(rx[:, :], dx1[:, :]))
                    st.wait()
                    st.did(dve.tensor_scalar(h1[:, t, :], x[:, s, :], mv[:, 0:1], rx[:, 0:1], ALU.subtract, ALU.mult))
                    st.wait()
                    st.did(dve.tensor_tensor(h1[:, t, :], h1[:, t, :], g1[:, :], ALU.mult))
                    st.wait()
                    dve.tensor_tensor(h1[:, t, :], h1[:, t, :], b1[:, :], ALU.add).then_inc(h1_ready, 1)

                def gate(t):
                    dve.wait_ge(e_done, t + 1)
                    st.did(dve.tensor_tensor(L[:, t, :], lp[:, 0:NR], rb[:, :], ALU.add))
                    if t >= 1:
                        dve.wait_ge(base_stored, 16 * t)
                    for n in range(2):
                        half = slice(n * 512, (n + 1) * 512)
                        dve.wait_ge(sig_done, 2 * t + n + 1)
                        st.did(dve.tensor_tensor(base[:, half], op[n][:, :], sig[:, half], ALU.mult))
                    st.wait()
                    dve.sem_inc(mul_done, 1)

                for t in range(2):
                    head_norm(t)
                    copy(t)
                for t in range(NT + 1):
                    if t < NT:
                        residual_norm(t)
                    if t >= 1:
                        gate(t - 1)
                    if t < NT:
                        copy(STAGES.index(("B", t)))
                    if t >= 1:
                        dve.scalar_tensor_tensor(base[:, :], h1[:, t - 1, :], ALPHA, base[:, :], ALU.mult, ALU.add).then_inc(base_ready, 1)
                    if t + 2 < NT:
                        head_norm(t + 2)
                        copy(STAGES.index(("A", t + 2)))
                dve.wait_ge(wpg_loaded, 16 * 8)
                q = Steps(dve, r_steps, 0, 0)

                def do(ins):
                    q.did(ins)
                    q.wait()
                TT = dve.tensor_tensor
                bt = lambda ap, n: ap.unsqueeze(2).broadcast_to([P, NT, n])
                lg, le = L[:, :, 0:NG], L[:, :, NG:].rearrange("p t (g e) -> p t g e", g=NG)
                st.wait()
                do(dve.tensor_reduce(m1[:, :], lg, AX.X, ALU.max))
                do(TT(gd[:, :, :], lg, bt(m1[:, :], NG), ALU.subtract))
                do(TT(ohg[:, :, :], lg, bt(m1[:, :], NG), ALU.is_equal))
                do(dve.tensor_scalar(idxm[:, :], idx[:, 0:EPG], -64.0, None, ALU.add))
                mid = lambda n: idxm[:, 0:n].unsqueeze(1).broadcast_to([P, NT, n])

                def first_of(onehot, n):
                    do(TT(onehot, onehot, mid(n), ALU.mult))
                    do(dve.tensor_reduce(m2[:, :], onehot, AX.X, ALU.min))
                    do(TT(onehot, mid(n), bt(m2[:, :], n), ALU.is_equal))
                first_of(ohg[:, :, :], NG)
                dve.wait_ge(r_act, 1)
                do(dve.tensor_reduce(gw[:, :], ge[:, :, :], AX.X, ALU.add))
                do(dve.reciprocal(gw[:, :], gw[:, :]))
                for g in range(NG):
                    do(TT(big[:, :, g * EPG:(g + 1) * EPG], le[:, :, g, :], ohg[:, :, g:g + 1].broadcast_to([P, NT, EPG]), ALU.mult))
                do(dve.tensor_reduce(ein[:, :, :], big[:, :, :].rearrange("p t (g e) -> p t e g", g=NG), AX.X, ALU.add))
                do(dve.tensor_reduce(m1[:, :], ein[:, :, :], AX.X, ALU.max))
                do(TT(oh[:, 0], ein[:, :, :], bt(m1[:, :], EPG), ALU.is_equal))
                first_of(oh[:, 0], EPG)
                do(dve.scalar_tensor_tensor(ein[:, :, :], oh[:, 0], NEG, ein[:, :, :], ALU.mult, ALU.add))
                do(dve.tensor_reduce(f1[:, :], ein[:, :, :], AX.X, ALU.max))
                do(TT(oh[:, 1], ein[:, :, :], bt(f1[:, :], EPG), ALU.is_equal))
                first_of(oh[:, 1], EPG)
                do(TT(m1[:, :], f1[:, :], m1[:, :], ALU.subtract))
                assert q.n == 26
                for k in range(2):
                    for g in range(NG):
                        q.did(TT(OH[:, k, :, g * EPG:(g + 1) * EPG], oh[:, k], ohg[:, :, g:g + 1].broadcast_to([P, NT, EPG]), ALU.mult))
                q.wait()
                for k in range(2):
                    q.did(TT(OH[:, k], OH[:, k], bt(valid[:, :], NE), ALU.mult))
                q.did(dve.memset(ones[:, :], 1.0))
                q.did(dve.memset(one[:, :], 1.0))
                q.wait()
                do(TT(OS[:, :, :], OH[:, 0], OH[:, 1], ALU.add))
                dve.sem_inc(r_ready, 1)
                dve.wait_ge(r_act, 2)
                do(dve.tensor_scalar(m1[:, :], f1[:, :], 1.0, None, ALU.add))
                do(dve.reciprocal(m1[:, :], m1[:, :]))
                do(TT(w_tok[:, 0, :], m1[:, :], gw[:, :], ALU.mult))
                do(TT(w_tok[:, 1, :], w_tok[:, 0, :], f1[:, :], ALU.mult))
                dve.wait_ge(r_pe, 1)
                q.did(dve.memset(pre[:, 0, :], 0.0))
                for t in range(1, NT):
                    q.wait()
                    q.did(TT(pre[:, t, :], gp[0][:, (t - 1) * NE:t * NE], pre[:, t - 1, :], ALU.add))
                q.wait()
                do(TT(cnt[:, :], gp[0][:, (NT - 1) * NE:NT * NE], pre[:, NT - 1, :], ALU.add))
                do(TT(rank[:, :, :].rearrange("p t e -> p (t e)"), gp[1][:, 0:NT * NE], pre[:, :, :].rearrange("p t e -> p (t e)"), ALU.add))
                do(dve.tensor_scalar(cnti[:, :], cnt[:, :], float(P - 1), None, ALU.add))
                do(dve.tensor_scalar(cnti[:, :], cnti[:, :], 7, None, ALU.arith_shift_right))
                do(dve.tensor_copy(nb[:, :], cnti[:, :]))
                do(dve.tensor_tensor_scan(incl[:, :], one[:, :], cnt[:, :], 0.0, ALU.mult, ALU.add))
                do(dve.tensor_tensor_scan(bincl[:, :], one[:, :], nb[:, :], 0.0, ALU.mult, ALU.add))
                do(TT(start[:, :], incl[:, :], cnt[:, :], ALU.subtract))
                do(TT(bstart[:, :], bincl[:, :], nb[:, :], ALU.subtract))
                do(dve.tensor_scalar(bstart[:, :], bstart[:, :], float(P), None, ALU.mult))
                do(TT(sx[:, :, :], rank[:, :, :], start[:, :].unsqueeze(1).broadcast_to([P, NT, NE]), ALU.add))
                for k in range(2):
                    do(TT(big[:, :, :], sx[:, :, :], OH[:, k], ALU.mult))
                    do(dve.tensor_reduce(dxf[:, k, :], big[:, :, :], AX.X, ALU.add))
                do(dve.tensor_copy(dx[:, :, :], dxf[:, :, :]))
                do(dve.tensor_scalar(tx[:, :], bincl[:, :], part[:, 0:1], None, ALU.is_le))
                do(dve.tensor_reduce(tabf[:, 0:1], tx[:, :], AX.X, ALU.add))
                do(dve.tensor_scalar(tx[:, :], idx[:, :], tabf[:, 0:1], None, ALU.is_equal))
                do(TT(ty[:, :], start[:, :], bstart[:, :], ALU.subtract))
                do(TT(ty[:, :], ty[:, :], tx[:, :], ALU.mult))
                do(dve.tensor_reduce(tabf[:, 1:2], ty[:, :], AX.X, ALU.add))
                do(dve.scalar_tensor_tensor(tabf[:, 1:2], part[:, :], float(P), tabf[:, 1:2], ALU.mult, ALU.add))
                do(dve.tensor_copy(tabf[:, 2:3], bincl[:, NE - 1:NE]))
                do(dve.memset(tabf[:, 3:4], 0.0))
                do(dve.tensor_copy(tab[:, :], tabf[:, :]))
                dve.sem_inc(r_ready, 1)

            @block.gpsimd
            def _(pool):
                pool.wait_ge(r_ready, 2)
                n = 0
                for t in range(NT):
                    m = P if t < TP else DECB
                    for k in range(2):
                        pool.indirect_dma_start(d["XR"], bass.IndirectOffsetOnAxis(ap=dx[0:m, k, t:t + 1], axis=0),
                                                h1[0:m, t, :], None, bounds_check=XROWS - P - 1, oob_is_err=True).then_inc(scattered, 16)
                        n += 16
                pool.wait_ge(scattered, n * (layer + 1))



SLOTS = 4


def block_turns(eng, blocks):
    with eng.Fori(0, -(-blocks // SLOTS)) as r:
        for slot in range(SLOTS):
            yield SLOTS * r + slot, slot, r


def overlapped_turns(eng, used, step):
    assert 2 * (SEQ + DECB) > 2 * P
    step((0, 0, 0), None, (1, 1, 0))
    with eng.Fori(0, -(-BLOCKS // SLOTS)) as r:
        for i in range(SLOTS):
            b = SLOTS * r + i + 1
            before, now, after = ((b + k, (i + 1 + k) % SLOTS, r + (i + 1 + k) // SLOTS) for k in (-1, 0, 1))
            with eng.If(b + 1 < used):
                step(now, before, after)
            with eng.If(b + 1 == used):
                step(now, before, None)
            with eng.If(b == used):
                step(None, before, None)


def experts(nc, d, layer, ident):
    with Phase(nc) as ph:
        tab = ph.sb("ex_tab", [1, 4 * P], I32)
        wgu = ph.sb("ex_wgu", [P, SLOTS, 2, KC, DE])
        wd = ph.sb("ex_wd", [P, SLOTS, 2, D])
        x = ph.sb("ex_x", [P, SLOTS, D])
        xT = ph.sb("ex_xT", [P, 2, KC, P])
        sil = ph.sb("ex_sil", [P, 2, DE])
        h = ph.sb("ex_h", [P, 2, DE])
        hT = ph.sb("ex_hT", [P, 2, 2, P])
        y = ph.sb("ex_y", [P, 2, D])
        tp = [ph.ps(f"ex_tp{i}", [P, 4, P]) for i in range(2)]
        gu = [ph.ps(f"ex_gu{i}", [P, 2, DE]) for i in range(2)]
        htp = [ph.ps(f"ex_ht{i}", [P, 2, P]) for i in range(2)]
        yp = [ph.ps(f"ex_yp{i}", [P, 512]) for i in range(2)]
        tab_loaded = ph.sem("tab_loaded")
        loaded = [ph.sem(f"loaded{i}") for i in range(SLOTS)]
        stored = ph.sem2("stored")
        slot_free, tp_done, xT_dve, gu_done = (ph.sem(n) for n in ("slot_free", "tp_done", "xT_dve", "gu_done"))
        sil_done, h_ready, ht_done, hT_ready, y_done = (ph.sem(n) for n in ("sil_done", "h_ready", "ht_done", "hT_ready", "y_done"))
        y_dve, last_stored = ph.sem("y_dve"), ph.sem("last_stored")
        TOTAL = 2
        assert SLOTS % 2 == 0
        with nc.Block() as block:
            @block.sync
            def _(sp):
                sp.dma_start(tab[:, :], d["BTAB"]).then_inc(tab_loaded, 16)
                sp.wait_ge(tab_loaded, 16)
                used = sp.value_load(tab[0:1, TOTAL:TOTAL + 1], min_val=0, max_val=BLOCKS)
                for b, s, r in block_turns(sp, BLOCKS):
                    with sp.If(b < used):
                        e = sp.value_load(tab[0:1, ds(4 * b, 1)], min_val=0, max_val=NE - 1)
                        row = sp.value_load(tab[0:1, ds(4 * b + 1, 1)], min_val=0, max_val=XROWS - P)
                        sp.wait_ge(slot_free, b + 1)
                        sp.dma_start(x[:, s, :], d["XR"][ds(row, P)]).then_inc(loaded[s], 16)
                        for n, w in enumerate(("e_gate", "e_up")):
                            sp.dma_start(wgu[:, s, n].rearrange("p k n -> p (k n)"),
                                         d[w][ds(layer, 1), ds(e, 1)].rearrange("l e (p k) n -> (l e p) (k n)", k=KC)).then_inc(loaded[s], 16)
                        sp.dma_start(wd[:, s].rearrange("p k n -> p (k n)"),
                                     d["e_down"][ds(layer, 1), ds(e, 1)].rearrange("l e (p k) n -> (l e p) (k n)", k=2)).then_inc(loaded[s], 16)

            @block.tensor
            def _(pe):
                pe.sem_inc(slot_free, SLOTS)
                pe.wait_ge(tab_loaded, 16)
                used = pe.value_load(tab[0:1, TOTAL:TOTAL + 1], min_val=0, max_val=BLOCKS)

                def transposes(b, s, r):
                    pe.wait_ge(loaded[s], 64 * (r + 1))
                    pe.wait_ge(xT_dve, 2 * b + 2)
                    for c in range(KC):
                        last = pe.transpose(tp[c // 4][:, c % 4, :], x[:, s, c::KC], ident[:, :])
                        if c % 4 == 3:
                            last.then_inc(tp_done, 1)

                def step(now, before, after):
                    if now:
                        b, s, r = now
                        pe.wait_ge(xT_dve, 2 * b + 4)
                        for c in range(KC):
                            last = pe.matmul(gu[s % 2][:, :, :], xT[:, s % 2, c, :], wgu[:, s, :, c, :], start=(c == 0), stop=(c == KC - 1))
                        last.then_inc(gu_done, 1)
                    if after:
                        transposes(*after)
                    if before:
                        b0, s0, r0 = before
                        pe.wait_ge(y_dve, 2 * b0 + 2)
                        pe.wait_ge(hT_ready, b0 + 1)
                        for n in range(2):
                            for c in range(2):
                                last = pe.matmul(yp[n][:, :], hT[:, s0 % 2, c, :], wd[:, s0, c, n * 512:(n + 1) * 512], start=(c == 0), stop=(c == 1))
                            if n == 0:
                                last.then_inc(y_done, 1)
                        last.then_inc(slot_free, 1)
                    if now:
                        pe.wait_ge(h_ready, b + 1)
                        for c in range(2):
                            last = pe.transpose(htp[s % 2][:, c, :], h[:, s % 2, c::2], ident[:, :])
                        last.then_inc(ht_done, 1)
                transposes(0, 0, 0)
                overlapped_turns(pe, used, step)

            @block.vector
            def _(dve):
                dve.sem_inc(xT_dve, 2)
                dve.sem_inc(y_dve, 2)
                dve.wait_ge(tab_loaded, 16)
                used = dve.value_load(tab[0:1, TOTAL:TOTAL + 1], min_val=0, max_val=BLOCKS)

                def rows_turned(b, s, r):
                    for n in range(2):
                        dve.wait_ge(tp_done, 2 * b + n + 1)
                        dve.tensor_copy(xT[:, s % 2, 4 * n:4 * n + 4, :], tp[n][:, :, :]).then_inc(xT_dve, 1)

                def step(now, before, after):
                    if now:
                        b, s, r = now
                        dve.wait_ge(sil_done, b + 1)
                        dve.tensor_tensor(h[:, s % 2, :], sil[:, s % 2, :], gu[s % 2][:, 1, :], ALU.mult).then_inc(h_ready, 1)
                    if after:
                        rows_turned(*after)
                    if before:
                        b0, s0, r0 = before
                        dve.wait_ge(stored[s0 % 2], 16 * (SLOTS // 2 * r0 + s0 // 2 + 1))
                        dve.wait_ge(y_done, b0 + 1)
                        dve.tensor_copy(y[:, s0 % 2, 0:512], yp[0][:, :]).then_inc(y_dve, 1)
                        dve.wait_ge(slot_free, b0 + SLOTS + 1)
                        dve.tensor_copy(y[:, s0 % 2, 512:], yp[1][:, :]).then_inc(y_dve, 1)
                    if now:
                        dve.wait_ge(ht_done, b + 1)
                        dve.tensor_copy(hT[:, s % 2, :, :], htp[s % 2][:, :, :]).then_inc(hT_ready, 1)
                rows_turned(0, 0, 0)
                overlapped_turns(dve, used, step)

            @block.scalar
            def _(act):
                for s in range(2):
                    act.sem_inc(stored[s], 16)
                act.wait_ge(tab_loaded, 16)
                used = act.value_load(tab[0:1, TOTAL:TOTAL + 1], min_val=0, max_val=BLOCKS)

                def step(now, before, after):
                    if now:
                        b, s, r = now
                        act.wait_ge(gu_done, b + 1)
                        act.activation(sil[:, s % 2, :], gu[s % 2][:, 0, :], ACT.Silu).then_inc(sil_done, 1)
                    if before:
                        b0, s0, r0 = before
                        turn = SLOTS // 2 * r0 + s0 // 2
                        row = act.value_load(tab[0:1, ds(4 * b0 + 1, 1)], min_val=0, max_val=XROWS - P)
                        act.wait_ge(y_dve, 2 * b0 + 4)
                        act.wait_ge(stored[1 - s0 % 2], 16 * (turn + s0 % 2 + 1))
                        act.dma_start(d["YR"][ds(row, P)], y[:, s0 % 2, :]).then_inc(stored[s0 % 2], 16)
                overlapped_turns(act, used, step)
                act.wait_ge(stored[0], 16 * ((used + 1) // 2) + 16)
                act.wait_ge(stored[1], 16 * (used // 2) + 16)
                act.sem_inc(last_stored, 1)



def combine(nc, d, layer, ident):
    w_tok, row = d["sb_weight"], d["sb_row"]
    with Phase(nc) as ph:
        g = ph.sb("co_g", [P, D])
        b = ph.sb("co_b", [P, D])
        base = ph.sb("co_base", [P, 2, D])
        r1 = ph.sb("co_r1", [P, 2, D])
        r2 = ph.sb("co_r2", [P, 2, D])
        o = ph.sb("co_o", [P, 2, D])
        stats = ph.sb("co_stats", [P, 2, 6])
        mv = ph.sb("co_mv", [P, 2])
        ve = ph.sb("co_ve", [P, 1])
        sd = ph.sb("co_sd", [P, 1])
        rs = ph.sb("co_rs", [P, 1])
        hold = ph.sb("co_hold", [1, 1])
        gains, loaded, gathered, stored = ph.sem("gains"), ph.sem2("loaded"), [d["sw"][f"gathered{i}"] for i in range(2)], ph.sem2("stored")
        free, var_ready, sqrt_done, steps, o_ready, zeroed = (ph.sem(n) for n in ("free", "var_ready", "sqrt_done", "steps", "o_ready", "zeroed"))
        with nc.Block() as block:
            @block.sync
            def _(sp):
                sp.dma_start(g[:, :], row_of_layer(d["ln2_g"], layer)).then_inc(gains, 16)
                sp.dma_start(b[:, :], row_of_layer(d["ln2_b"], layer)).then_inc(gains, 16)
                for t in range(NT):
                    if t >= 2:
                        sp.wait_ge(free, t - 1)
                    sp.dma_start(base[:, t % 2, :], d["BASE"][rows(t)]).then_inc(loaded[t % 2], 16)

            @block.gpsimd
            def _(pool):
                for t in range(NT):
                    m = P if t < TP else DECB
                    if t >= 2:
                        pool.wait_ge(free, t - 1)
                    if t == TP:
                        pool.memset(r1[:, t % 2, :], 0.0).then_inc(zeroed, 1)
                        pool.memset(r2[:, t % 2, :], 0.0).then_inc(zeroed, 1)
                        pool.wait_ge(zeroed, 2)
                    for k, r in ((0, r1), (1, r2)):
                        pool.indirect_dma_start(r[0:m, t % 2, :], None, d["YR"], bass.IndirectOffsetOnAxis(ap=row[0:m, k, t:t + 1], axis=0),
                                                bounds_check=XROWS - P - 1, oob_is_err=True).then_inc(gathered[t % 2], 16)

            @block.scalar
            def _(act):
                for t in range(NT):
                    s = t % 2
                    act.wait_ge(var_ready, t + 1)
                    act.activation(sd[:, :], ve[:, :], ACT.Sqrt).then_inc(sqrt_done, 1)
                    act.wait_ge(o_ready, t + 1)
                    act.dma_start(d["H"][rows(t)], o[:, s, :]).then_inc(stored[s], 16)
                    act.dma_start(d["y_all"][rows(t)], o[:, s, :]).then_inc(stored[s], 16)
                act.wait_ge(stored[0], 32 * (NT // 2 + 1))
                act.wait_ge(stored[1], 32 * (NT // 2))

            @block.vector
            def _(dve):
                dve.wait_ge(gains, 32)
                for t in range(NT):
                    s, r = t % 2, t // 2
                    st = Steps(dve, steps, t, 9)
                    dve.wait_ge(loaded[s], 16 * (r + 1))
                    dve.wait_ge(gathered[s], 32 * ((NT + 1 - s) // 2) * layer + 32 * (r + 1))
                    acc = base[:, s, :]
                    st.did(dve.scalar_tensor_tensor(acc, r1[:, s, :], w_tok[:, 0, t:t + 1], acc, ALU.mult, ALU.add))
                    st.wait()
                    st.did(dve.scalar_tensor_tensor(acc, r2[:, s, :], w_tok[:, 1, t:t + 1], acc, ALU.mult, ALU.add))
                    st.wait()
                    layer_norm_steps(dve, st, acc, stats, mv[:, :], ve[:, :], hold[:, :])
                    st.wait()
                    dve.sem_inc(var_ready, 1)
                    dve.wait_ge(sqrt_done, t + 1)
                    st.did(dve.reciprocal(rs[:, :], sd[:, :]))
                    st.wait()
                    if r:
                        dve.wait_ge(stored[s], 32 * r)
                    st.did(dve.tensor_scalar(o[:, s, :], acc, mv[:, 0:1], rs[:, 0:1], ALU.subtract, ALU.mult))
                    st.wait()
                    dve.sem_inc(free, 1)
                    st.did(dve.tensor_tensor(o[:, s, :], o[:, s, :], g[:, :], ALU.mult))
                    st.wait()
                    dve.tensor_tensor(o[:, s, :], o[:, s, :], b[:, :], ALU.add).then_inc(o_ready, 1)
                    st.end()



def decoder_trunk(nc, d):
    for name, shape in (("H", (ROWS, D)), ("Z", (PAD + ROWS, N_IN)), ("XR", (XROWS, D)), ("YR", (XROWS, D)),
                        ("Y", (ROWS, D)), ("QT", (H, QK, ROWS)), ("KT", (H, QK, ROWS)), ("V", (ROWS, H * VD)),
                        ("BASE", (ROWS, D)), ("BTAB", (1, 4 * P))):
        d[name] = nc.dram_tensor(f"scratch_{name}", shape, I32 if name == "BTAB" else F32, kind="Internal").ap()
    with ExitStack() as ctx:
        ident = ctx.enter_context(nc.sbuf_tensor("ident", [P, P], F32))
        d["sb_weight"] = ctx.enter_context(nc.sbuf_tensor("route_weight", [P, 2, NT], F32))
        d["sb_row"] = ctx.enter_context(nc.sbuf_tensor("route_row", [P, 2, NT], mybir.dt.uint32))
        d["sw"] = {n: ctx.enter_context(nc.semaphore(f"sw_{n}")) for n in
                   ("zero_stored", "cv_w", "cv_in", "cv_out", "cv_state", "scattered", "gathered0", "gathered1")}
        with Phase(nc) as ph:
            got = ph.sem("ident_loaded")
            with nc.Block() as block:
                @block.sync
                def _(sp):
                    sp.dma_start(ident[:, :], d["c_ident"]).then_inc(got, 16)
                    sp.wait_ge(got, 16)
        entry_norm(nc, d)
        with nc.Fori(0, LAYERS) as layer:
            with Phase(nc) as shared:
                cache = PagedCache(shared)
                input_projection(nc, d, layer, ident, cache)
                mla_prepare(nc, d, layer, ident, cache)
                attention(nc, d, layer, ident, cache)
                mlstm_prompt(nc, d, layer, ident)
                sample_attention(nc, d, layer, ident, cache)
            mlstm_sample(nc, d, layer, ident)
            output_and_route(nc, d, layer, ident)
            experts(nc, d, layer, ident)
            combine(nc, d, layer, ident)



LAYERS = DEPTH


def constants():
    import numpy as np
    inv = (np.float32(10000.0) ** (-np.arange(HALF, dtype=np.float32) / np.float32(HALF))).astype(np.float32)
    pos = np.concatenate([np.arange(SEQ), np.full(P, PAST)]).astype(np.float32)
    ang = (pos[:, None] * inv).astype(np.float32)
    q, k = np.arange(P)[:, None], np.arange(P)[None, :]
    return {
        "c_ident": np.eye(P, dtype=np.float32),
        "c_trig": np.concatenate([np.cos(ang), np.sin(ang)], 1).astype(np.float32),
        "c_causal": np.where(k <= q, 0.0, NEG).astype(np.float32),
        "c_causalT": np.where(q <= k, 0.0, NEG).astype(np.float32),
        "c_own": np.repeat(np.where(np.eye(DECB) > 0, 0.0, NEG).astype(np.float32), H, 1),
        "c_rep": np.repeat(np.eye(DECB * NH, dtype=np.float32), 4, 1),
        "c_idx": np.tile(np.arange(NE, dtype=np.float32), (P, 1)),
        "c_valid": (np.arange(NT)[None, :] * P + q < SEQ + DECB).astype(np.float32),
        "c_part": np.arange(P, dtype=np.float32)[:, None],
        "c_before": (q < k).astype(np.float32),
        "c_headrow": np.repeat(np.eye(NH, dtype=np.float32)[:, :, None], P, 2),
    }


OUTS = [("y_all", (ROWS, D)), ("ckv_all", (DEPTH, ROWS, KVR)), ("krope_all", (DEPTH, ROWS, ROPE)),
        ("conv_p", (DEPTH, 2, CONVW)), ("C_p", (DEPTH, NH, DH, DH)), ("n_p", (DEPTH, NH, DH)), ("m_p", (DEPTH, NH)),
        ("conv_s", (DEPTH, DECB, 2, CONVW)), ("C_s", (DEPTH, DECB * NH, DH * DH)), ("n_s", (DEPTH, DECB * NH, DH)),
        ("m_s", (DEPTH, DECB * NH))]
PLAIN = ["cache_ckv", "cache_krope", "state_conv", "state_mlstm_C", "state_mlstm_n", "state_mlstm_m", "page_table",
         "ln0_g", "ln0_b", "w_in", "conv_w", "q_norm_g", "w_uq", "kv_norm_g", "w_ukv", "mlstm_gate_b", "mix_norm_g",
         "w_out", "ln1_g", "ln1_b", "e_gate", "e_up", "e_down", "w_pe", "w_pg", "ln2_g", "ln2_b"]


def laid_out(inputs):
    import numpy as np
    a = {n: np.ascontiguousarray(inputs[n]) for n in PLAIN}
    rest = ROWS - SEQ - DECB
    xp, xs = np.asarray(inputs["x_prompt"])[0], np.asarray(inputs["x_sample"])[:, 0]
    a["x_all"] = np.concatenate([xp, xs, np.zeros((rest, D), np.float32)], 0)
    pp, ps = np.asarray(inputs["p_prompt"])[:, 0], np.asarray(inputs["p_sample"])[:, :, 0]
    a["p_all"] = np.concatenate([pp, ps, np.zeros((DEPTH, rest, DPLE), np.float32)], 1)
    a["w_route"] = np.concatenate([np.asarray(inputs["w_group"]), np.asarray(inputs["w_expert"])], 2)
    a["b_route"] = np.concatenate([np.asarray(inputs["b_group"]), np.asarray(inputs["b_expert"])], 1)
    a["page_table"] = np.asarray(inputs["page_table"]).reshape(1, DECB * PAGES)
    a.update(constants())
    return a


def kernel(**inputs):
    import concourse.bacc as _bacc
    from concourse.bass_utils import run_bass_kernel_spmd as _run

    arrays = laid_out(inputs)
    nc = _bacc.Bacc("TRN2", target_bir_lowering=False, num_devices=1)
    d = {n: nc.dram_tensor(f"in_{n}", a.shape, mybir.dt.from_np(a.dtype), kind="ExternalInput").ap()
         for n, a in arrays.items()}
    for n, shape in OUTS:
        d[n] = nc.dram_tensor(f"out_{n}", shape, F32, kind="ExternalOutput").ap()
    decoder_trunk(nc, d)
    r = _run(nc, [{f"in_{n}": a for n, a in arrays.items()}], core_ids=[0])
    o = {n: r.results[0][f"out_{n}"] for n, _ in OUTS}
    y, ckv, kr, dec = o["y_all"], o["ckv_all"], o["krope_all"], SEQ + DECB
    return (y[None, :SEQ], y[SEQ:dec, None], ckv[:, None, :SEQ], kr[:, None, :SEQ], o["conv_p"][:, None],
            o["C_p"][:, None], o["n_p"][:, None], o["m_p"][:, None],
            ckv[:, SEQ:dec, None], kr[:, SEQ:dec, None], o["conv_s"],
            o["C_s"].reshape(DEPTH, DECB, NH, DH, DH), o["n_s"].reshape(DEPTH, DECB, NH, DH),
            o["m_s"].reshape(DEPTH, DECB, NH))
```

```python
from contextlib import ExitStack, nullcontext

import concourse.bass as bass
from concourse import mybir

F32 = mybir.dt.float32
I32 = mybir.dt.int32
ALU = mybir.AluOpType
ACT = mybir.ActivationFunctionType
AX = mybir.AxisListType
ds = bass.ds

P = 128
D = 1024
KC = D // P
SEQ, DECB, PAST = 1024, 8, 2048
DEPTH = 2
TP = SEQ // P
NT = TP + 1
ROWS = NT * P
N_IN = 2216
PAD = 2
CONVW, QR, KVR, ROPE, NOPE, VD = 256, 256, 128, 32, 64, 64
H, QK = 8, 96
HALF = ROPE // 2
NH, DH, MW = 4, 64, 256
C_CB, C_CC, C_CH, C_Q = 0, 256, 512, 768
C_KV, C_KR = C_Q + QR, C_Q + QR + KVR
C_MQ = C_KR + ROPE
C_MK, C_MV, C_MO, C_MI = C_MQ + MW, C_MQ + 2 * MW, C_MQ + 3 * MW, C_MQ + 4 * MW
MLA_COLS = QR + KVR + ROPE
NE, NG, EPG, DE = 32, 4, 8, 256
DPLE = 256
ALPHA = (2 * DEPTH) ** 0.25
LN_EPS, RMS_EPS = 1e-5, 1e-6
SCALE = float(QK) ** -0.5
PAGES, PAGE = PAST // P, P
NEG = -1e30
BLOCKS = -(-2 * (SEQ + DECB) // P) + NE
XROWS = 2 * (SEQ + DECB) + P


class Steps:

    def __init__(self, eng, sem, turn, steps):
        self.eng, self.sem, self.base, self.steps, self.n = eng, sem, turn * steps, steps, 0

    def did(self, ins):
        self.n += 1
        ins.then_inc(self.sem, 1)

    def wait(self):
        self.eng.wait_ge(self.sem, self.base + self.n)

    def end(self):
        assert self.n == self.steps, (self.n, self.steps)


class Phase:

    def __init__(self, nc):
        self.nc, self.sems = nc, []

    def __enter__(self):
        self.ctx = ExitStack()
        self.ctx.__enter__()
        return self

    def sb(self, name, shape, dt=F32):
        return self.ctx.enter_context(self.nc.sbuf_tensor(name, shape, dt))

    def ps(self, name, shape, dt=F32):
        return self.ctx.enter_context(self.nc.psum_tensor(name, shape, dt))

    def sem(self, name):
        s = self.ctx.enter_context(self.nc.semaphore(name))
        self.sems.append(s.num)
        return s

    def sem2(self, name):
        return [self.sem(f"{name}{i}") for i in range(2)]

    def __exit__(self, *exc):
        if exc[0] is None and self.sems:
            nums = sorted(self.sems)
            firsts = [n for n in nums if n - 1 not in nums]
            for lo in firsts:
                hi = lo
                while hi + 1 in nums:
                    hi += 1
                self.nc.all_engine_barrier(sems_to_clear=range(lo, hi + 1))
        return self.ctx.__exit__(*exc)


def rows(t, n=P):
    return ds(t * P, n)


def of_layer(ap, layer):
    inner = "abcd"[:len(ap.shape) - 1]
    return ap[ds(layer, 1)].rearrange(f"l {' '.join(inner)} -> (l {inner[0]}) {' '.join(inner[1:])}")


def row_of_layer(ap, layer):
    return ap[ds(layer, 1), :].broadcast_to([P, ap.shape[1]])



def layer_norm_steps(dve, st, x, stats, mv, rstd_in, hold):
    st.did(dve.bn_stats(stats[:, 0, :], x[:, 0:512]))
    st.did(dve.bn_stats(stats[:, 1, :], x[:, 512:1024]))
    st.wait()
    dve.memset(hold, 0.0)
    st.did(dve.bn_aggr(mv, stats[:, :, :]))
    st.wait()
    st.did(dve.tensor_scalar(rstd_in, mv[:, 1:2], LN_EPS, None, ALU.add))



LX = KVR + 1


class PagedCache:

    COUNTS = (32, 9 * H, 3 * TP)
    assert sum(COUNTS) == DECB * PAGES

    def __init__(self, ph):
        self.table = ph.sb("pc_table", [1, DECB * PAGES], I32)
        self.ckv = ph.sb("pc_ckv", [P, DECB * PAGES, LX])
        self.kr = ph.sb("pc_kr", [P, DECB * PAGES, ROPE])
        self.table_loaded = ph.sem("table_loaded")
        self.pages_loaded = [ph.sem(f"pages_loaded{i}") for i in range(3)]

    def load(self, eng, d, layer, first, count, phase):
        n_phys = d["cache_ckv"].shape[1]
        with eng.Fori(0, count) as p:
            page = eng.value_load(self.table[0:1, ds(first + p, 1)], min_val=0, max_val=n_phys - 1)
            eng.dma_start(self.ckv[:, ds(first + p, 1), 0:KVR].rearrange("k o n -> k (o n)"),
                          d["cache_ckv"][ds(layer, 1), ds(page, 1)].rearrange("l g k n -> (l g k) n")).then_inc(self.pages_loaded[phase], 16)
            eng.dma_start(self.kr[:, ds(first + p, 1), :].rearrange("k o n -> k (o n)"),
                          d["cache_krope"][ds(layer, 1), ds(page, 1)].rearrange("l g k n -> (l g k) n")).then_inc(self.pages_loaded[phase], 16)



Z_CHUNKS = [(c, min(512, N_IN - c)) for c in range(0, N_IN, 512)]
NZ = len(Z_CHUNKS)
R_SLOTS = 3


def stream_and_project(nc, d, layer, ident):
    w_tok, row = d["sb_weight"], d["sb_row"]
    entry = layer is None
    following = 0 if entry else (layer + 1) % DEPTH
    assert NT % R_SLOTS == 0
    with Phase(nc) as ph:
        name = "en" if entry else "co"
        w = ph.sb(f"{name}_w", [P, KC, N_IN])
        xT = ph.sb(f"{name}_xT", [P, 2, KC, P])
        z = ph.sb(f"{name}_z", [P, 2, N_IN])
        g = ph.sb(f"{name}_g", [P, D])
        b = ph.sb(f"{name}_b", [P, D])
        base = ph.sb(f"{name}_base", [P, R_SLOTS, D])
        o = ph.sb(f"{name}_o", [P, R_SLOTS, D])
        stats = ph.sb(f"{name}_stats", [P, 2, 6])
        mv = ph.sb(f"{name}_mv", [P, 2, 2])
        ve = ph.sb(f"{name}_ve", [P, 2])
        sd = ph.sb(f"{name}_sd", [P, 2])
        rs = ph.sb(f"{name}_rs", [P, 2])
        hold = ph.sb(f"{name}_hold", [1, 1])
        if entry:
            zero = ph.sb("en_zero", [P, N_IN])
            zero_stored = d["sw"]["zero_stored"]
        else:
            r1 = ph.sb("co_r1", [P, R_SLOTS, D])
            r2 = ph.sb("co_r2", [P, R_SLOTS, D])
            gathered = [d["sw"][f"gathered{i}"] for i in range(R_SLOTS)]
        tp = [ph.ps(f"{name}_tp{i}", [P, 4, P]) for i in range(2)]
        zp = [ph.ps(f"{name}_zp{i}", [P, 512]) for i in range(NZ)]
        gains, z_stored = ph.sem("gains"), ph.sem2("z_stored")
        loaded, stored = ([ph.sem(f"{n}{i}") for i in range(R_SLOTS)] for n in ("loaded", "stored"))
        w_loaded = [ph.sem(f"w_loaded{n}") for n in range(NZ)]
        free, var_ready, sqrt_done, a_steps, b_steps, o_ready, o_free, zeroed = (
            ph.sem(n) for n in ("free", "var_ready", "sqrt_done", "a_steps", "b_steps", "o_ready", "o_free", "zeroed"))
        tp_done, xT_ready, z_done, z_ready, z_ended = (ph.sem(n) for n in ("tp_done", "xT_ready", "z_done", "z_ready", "z_ended"))

        def projecting(eng):
            return nullcontext() if entry else eng.If(layer + 1 < LAYERS)

        with nc.Block() as block:
            @block.sync
            def _(sp):
                def load(t):
                    if t >= R_SLOTS:
                        sp.wait_ge(free, t - R_SLOTS + 1)
                    sp.dma_start(base[:, t % R_SLOTS, :], d["x_all" if entry else "BASE"][rows(t)]).then_inc(loaded[t % R_SLOTS], 16)
                for t in range(R_SLOTS):
                    load(t)
                    if t == 0:
                        for buf, which in ((g, "g"), (b, "b")):
                            src = d[f"ln0_{which}"].partition_broadcast(P) if entry else row_of_layer(d[f"ln2_{which}"], layer)
                            sp.dma_start(buf[:, :], src).then_inc(gains, 16)
                for t in range(NT):
                    if t + R_SLOTS < NT:
                        load(t + R_SLOTS)
                    with projecting(sp):
                        sp.wait_ge(z_ready, NZ * (t + 1))
                        sp.dma_start(d["Z"][ds(PAD + t * P, P)], z[:, t % 2, :]).then_inc(z_stored[t % 2], 16)
                with projecting(sp):
                    sp.wait_ge(z_stored[0], 16 * (NT // 2 + 1))
                    sp.wait_ge(z_stored[1], 16 * (NT // 2))
                    sp.sem_inc(z_ended, 1)

            @block.gpsimd
            def _(pool):
                if entry:
                    pool.memset(zero[:, :], 0.0).then_inc(zeroed, 1)
                    pool.wait_ge(zeroed, 1)
                    pool.dma_start(d["Z"][0:PAD], zero[0:PAD, :]).then_inc(zero_stored, 16)
                    pool.dma_start(d["XR"][XROWS - P:XROWS], zero[:, 0:D]).then_inc(zero_stored, 16)
                    pool.dma_start(d["YR"][XROWS - P:XROWS], zero[:, 0:D]).then_inc(zero_stored, 16)
                    pool.dma_start(d["Y"][SEQ:ROWS], zero[:, 0:D]).then_inc(zero_stored, 16)
                    pool.wait_ge(zero_stored, 64)
                    return
                for t in range(NT):
                    m, s = P if t < TP else DECB, t % R_SLOTS
                    if t >= R_SLOTS:
                        pool.wait_ge(free, t - R_SLOTS + 1)
                    if t == TP:
                        pool.memset(r1[:, s, :], 0.0).then_inc(zeroed, 1)
                        pool.memset(r2[:, s, :], 0.0).then_inc(zeroed, 1)
                        pool.wait_ge(zeroed, 2)
                    for k, r in ((0, r1), (1, r2)):
                        pool.indirect_dma_start(r[0:m, s, :], None, d["YR"], bass.IndirectOffsetOnAxis(ap=row[0:m, k, t:t + 1], axis=0),
                                                bounds_check=XROWS - P - 1, oob_is_err=True).then_inc(gathered[s], 16)

            @block.tensor
            def _(pe):
                def transposes(t):
                    pe.wait_ge(o_ready, t + 1)
                    if t >= 1:
                        pe.wait_ge(xT_ready, 2 * t)
                    for c in range(KC):
                        last = pe.transpose(tp[c // 4][:, c % 4, :], o[:, t % R_SLOTS, c::KC], ident[:, :])
                        if c % 4 == 3:
                            last.then_inc(tp_done, 1)
                with projecting(pe):
                    transposes(0)
                    for t in range(NT):
                        if t + 1 < NT:
                            transposes(t + 1)
                        else:
                            pe.wait_ge(xT_ready, 2 * t + 2)
                        for n, (c0, cn) in enumerate(Z_CHUNKS):
                            if t == 0:
                                pe.wait_ge(w_loaded[n], 16)
                            else:
                                pe.wait_ge(z_ready, NZ * (t - 1) + n + 1)
                            for c in range(KC):
                                last = pe.matmul(zp[n][:, 0:cn], xT[:, t % 2, c, :], w[:, c, c0:c0 + cn],
                                                 start=(c == 0), stop=(c == KC - 1))
                            last.then_inc(z_done, 1)

            @block.scalar
            def _(act):
                def root(t):
                    if t < NT:
                        act.wait_ge(var_ready, t + 1)
                        act.activation(sd[:, t % 2:t % 2 + 1], ve[:, t % 2:t % 2 + 1], ACT.Sqrt).then_inc(sqrt_done, 1)

                def store(t):
                    if t < NT:
                        act.wait_ge(o_ready, t + 1)
                        act.dma_start(d["y_all"][rows(t)], o[:, t % R_SLOTS, :]).then_inc(stored[t % R_SLOTS], 16)

                def copy_transposes(t):
                    for n in range(2):
                        act.wait_ge(tp_done, 2 * t + n + 1)
                        act.activation(xT[:, t % 2, 4 * n:4 * n + 4, :], tp[n][:, :, :], ACT.Copy).then_inc(xT_ready, 1)

                root(0)
                with projecting(act):
                    for n, (c0, cn) in enumerate(Z_CHUNKS):
                        act.dma_start(w[:, :, c0:c0 + cn], of_layer(d["w_in"], following).rearrange("(p k) n -> p k n", k=KC)[:, :, c0:c0 + cn]).then_inc(w_loaded[n], 16)
                root(1)
                store(0)
                with projecting(act):
                    copy_transposes(0)
                act.sem_inc(o_free, 1)
                for t in range(NT):
                    if t + 1 < NT:
                        with projecting(act):
                            copy_transposes(t + 1)
                        act.sem_inc(o_free, 1)
                    root(t + 2)
                    store(t + 1)
                    with projecting(act):
                        if t >= 2:
                            act.wait_ge(z_stored[t % 2], 16 * (t // 2))
                        for n, (c0, cn) in enumerate(Z_CHUNKS):
                            act.wait_ge(z_done, NZ * t + n + 1)
                            act.activation(z[:, t % 2, c0:c0 + cn], zp[n][:, 0:cn], ACT.Copy).then_inc(z_ready, 1)
                for s in range(R_SLOTS):
                    act.wait_ge(stored[s], 16 * (NT // R_SLOTS))

            @block.vector
            def _(dve):
                def sum_and_variance(t):
                    s, r = t % R_SLOTS, t // R_SLOTS
                    st = Steps(dve, a_steps, t, 4 if entry else 6)
                    dve.wait_ge(loaded[s], 16 * (r + 1))
                    acc = base[:, s, :]
                    if not entry:
                        dve.wait_ge(gathered[s], 32 * (NT // R_SLOTS) * layer + 32 * (r + 1))
                        for k, rk in ((0, r1), (1, r2)):
                            st.did(dve.scalar_tensor_tensor(acc, rk[:, s, :], w_tok[:, k, t:t + 1], acc, ALU.mult, ALU.add))
                            st.wait()
                    layer_norm_steps(dve, st, acc, stats, mv[:, t % 2, :], ve[:, t % 2:t % 2 + 1], hold[:, :])
                    st.wait()
                    dve.sem_inc(var_ready, 1)
                    st.end()

                def normalise(t):
                    s, k = t % R_SLOTS, t % 2
                    st = Steps(dve, b_steps, t, 3)
                    dve.wait_ge(sqrt_done, t + 1)
                    st.did(dve.reciprocal(rs[:, k:k + 1], sd[:, k:k + 1]))
                    st.wait()
                    if t >= R_SLOTS:
                        dve.wait_ge(o_free, t - R_SLOTS + 1)
                        dve.wait_ge(stored[s], 16 * (t // R_SLOTS))
                    st.did(dve.tensor_scalar(o[:, s, :], base[:, s, :], mv[:, k, 0:1], rs[:, k:k + 1], ALU.subtract, ALU.mult))
                    st.wait()
                    dve.sem_inc(free, 1)
                    st.did(dve.tensor_tensor(o[:, s, :], o[:, s, :], g[:, :], ALU.mult))
                    st.wait()
                    dve.tensor_tensor(o[:, s, :], o[:, s, :], b[:, :], ALU.add).then_inc(o_ready, 1)
                    st.end()

                sum_and_variance(0)
                dve.wait_ge(gains, 32)
                for t in range(1, NT):
                    sum_and_variance(t)
                    normalise(t - 1)
                normalise(NT - 1)





def skewed_turns(eng, turn):
    turn(0, 0, 0, True, False)
    with eng.Fori(0, (NT - 3) // 2) as r:
        turn(2 * r + 1, 1, r, False, False)
        turn(2 * r + 2, 0, r + 1, False, False)
    turn(NT - 2, 1, (NT - 2) // 2, False, False)
    turn(NT - 1, 0, (NT - 1) // 2, False, True)


def mla_prepare(nc, d, layer, ident, cache):
    with Phase(nc) as ph:
        wuq = ph.sb("mp_wuq", [P, 2, H * QK])
        wukv = ph.sb("mp_wukv", [P, H, NOPE + VD])
        wuk = ph.sb("mp_wuk", [P, H, NOPE])
        wuv = ph.sb("mp_wuv", [P, H, VD])
        gq = ph.sb("mp_gq", [P, QR])
        gkv = ph.sb("mp_gkv", [P, KVR])
        zq = ph.sb("mp_zq", [P, NT, MLA_COLS])
        trig = ph.sb("mp_trig", [P, NT, 2 * HALF])
        sq = ph.sb("mp_sq", [P, QR])
        ss = ph.sb("mp_ss", [P, 2])
        ms = ph.sb("mp_ms", [P, 2])
        sd = ph.sb("mp_sd", [P, 2])
        rs = ph.sb("mp_rs", [P, 2])
        cqn = ph.sb("mp_cqn", [P, QR])
        ckvn = ph.sb("mp_ckvn", [P, 2, KVR])
        kpad = ph.sb("mp_kpad", [P, 2, QK])
        t4 = ph.sb("mp_t4", [P, 4, H, HALF])
        k4 = ph.sb("mp_k4", [P, 4, HALF])
        cT = ph.sb("mp_cT", [P, 2, 3, P])
        q = ph.sb("mp_q", [P, H, QK])
        qT = ph.sb("mp_qT", [QK, 2, H, P])
        kT = ph.sb("mp_kT", [QK, 2, H, P])
        v = ph.sb("mp_v", [P, 2, H * VD])
        tp = ph.ps("mp_tp", [P, 4, P])
        qp = [ph.ps(f"mp_qp{i}", [P, 4, QK]) for i in range(2)]
        qtp = [ph.ps(f"mp_qtp{i}", [QK, 4, P]) for i in range(2)]
        ktp = [ph.ps(f"mp_ktp{i}", [NOPE, 4, P]) for i in range(2)]
        vp = ph.ps("mp_vp", [P, H * VD])
        w_loaded, g_loaded, z_loaded, z_first = ph.sem("w_loaded"), ph.sem("g_loaded"), ph.sem("z_loaded"), ph.sem("z_first")
        q_stored, kv_stored, c_stored = ph.sem2("q_stored"), ph.sem2("kv_stored"), ph.sem2("c_stored")
        squares, ms_ready, sd_ready = ph.sem("squares"), ph.sem("ms_ready"), ph.sem("sd_ready")
        w_split, lat_ready, tp_done = ph.sem("w_split"), ph.sem("lat_ready"), ph.sem("tp_done")
        n_steps, r_steps = ph.sem("n_steps"), ph.sem("r_steps")
        cT_ready, q_done, kv_done = ph.sem("cT_ready"), ph.sem("q_done"), ph.sem("kv_done")
        q_copied, q_rot, qt_done, qT_ready = ph.sem("q_copied"), ph.sem("q_rot"), ph.sem("qt_done"), ph.sem("qT_ready")
        kT_ready, v_ready = ph.sem("kT_ready"), ph.sem("v_ready")
        with nc.Block() as block:
            @block.sync
            def _(sp):
                sp.dma_start(zq[:, 0, :], d["Z"][PAD:PAD + P, C_Q:C_Q + MLA_COLS]).then_inc(z_first, 16)
                sp.dma_start(gq[:, :], row_of_layer(d["q_norm_g"], layer)).then_inc(g_loaded, 16)
                sp.dma_start(gkv[:, :], row_of_layer(d["kv_norm_g"], layer)).then_inc(g_loaded, 16)
                sp.dma_start(trig[:, :, :], d["c_trig"].rearrange("(t p) n -> p t n", p=P)).then_inc(g_loaded, 16)
                sp.dma_start(wuq[:, :, :], of_layer(d["w_uq"], layer).rearrange("(k p) n -> p k n", k=2)).then_inc(w_loaded, 16)
                sp.dma_start(wukv[:, :, :].rearrange("p h n -> p (h n)"), of_layer(d["w_ukv"], layer)).then_inc(w_loaded, 16)
                sp.dma_start(cache.table[:, :], d["page_table"]).then_inc(cache.table_loaded, 16)
                sp.dma_start(zq[:, 1:, :], d["Z"][PAD + P:PAD + ROWS, C_Q:C_Q + MLA_COLS].rearrange("(t p) n -> p t n", p=P)).then_inc(z_loaded, 16)
                sp.wait_ge(cache.table_loaded, 16)
                cache.load(sp, d, layer, 0, cache.COUNTS[0], 0)

            def of_tile(buf, t, c0, c1):
                return buf[:, ds(t, 1), c0:c1].rearrange("p t n -> p (t n)")

            @block.scalar
            def _(act):
                def squares_of(t):
                    act.wait_ge(ms_ready, t + 1)
                    act.activation(sq[:, 0:QR], of_tile(zq, t, 0, QR), ACT.Square, accum_out=ss[:, 0:1]).then_inc(squares, 1)
                    act.wait_ge(squares, 2 * t + 1)
                    act.activation(sq[:, 0:KVR], of_tile(zq, t, QR, QR + KVR), ACT.Square, accum_out=ss[:, 1:2]).then_inc(squares, 1)
                    act.wait_ge(ms_ready, t + 2)
                    act.activation(sd[:, :], ms[:, :], ACT.Sqrt).then_inc(sd_ready, 1)

                def queries_out(t, s, r):
                    act.wait_ge(q_stored[s], 16 * (r + 1))
                    for n in range(2):
                        act.wait_ge(qt_done, 2 * t + n + 1)
                        act.activation(qT[:, s, 4 * n:4 * n + 4, :], qtp[n][:, :, :], ACT.Copy).then_inc(qT_ready, 1)
                    act.wait_ge(qT_ready, 2 * t + 2)
                    act.dma_start(d["QT"][:, :, rows(t)].rearrange("h p n -> p h n"), qT[:, s]).then_inc(q_stored[s], 16)

                def turn(t, s, r, first, last_tile):
                    if not last_tile:
                        squares_of(t + 1)
                    if not first:
                        queries_out(t - 1, 1 - s, r - 1 + s)
                    for n in range(2):
                        act.wait_ge(q_done, 2 * t + n + 1)
                        act.activation(q[:, 4 * n:4 * n + 4, :], qp[n][:, :, :], ACT.Copy).then_inc(q_copied, 1)
                    act.wait_ge(kv_done, 2 * t + 2)
                    act.wait_ge(kv_stored[s], 16 * (3 * r + 1))
                    act.activation(v[:, s, :], vp[:, :], ACT.Copy).then_inc(v_ready, 1)
                    act.wait_ge(kT_ready, 3 * t + 4)
                    act.dma_start(d["KT"][:, :, rows(t)].rearrange("h p n -> p h n"), kT[:, s]).then_inc(kv_stored[s], 16)
                    act.wait_ge(v_ready, t + 2)
                    act.dma_start(d["V"][rows(t)], v[:, s, :]).then_inc(kv_stored[s], 16)
                    act.dma_start(of_layer(d["ckv_all"], layer)[rows(t)], ckvn[:, s, :]).then_inc(kv_stored[s], 16)
                    act.dma_start(of_layer(d["krope_all"], layer)[rows(t)], kpad[:, s, NOPE:]).then_inc(c_stored[s], 16)

                for s in range(2):
                    act.sem_inc(q_stored[s], 16)
                    act.sem_inc(kv_stored[s], 16)
                act.sem_inc(v_ready, 1)
                act.wait_ge(z_first, 16)
                squares_of(0)
                act.wait_ge(w_loaded, 32)
                act.activation(wuk[:, :, :], wukv[:, :, 0:NOPE], ACT.Copy).then_inc(w_split, 1)
                act.activation(wuv[:, :, :], wukv[:, :, NOPE:], ACT.Copy).then_inc(w_split, 1)
                act.wait_ge(z_loaded, 16)
                skewed_turns(act, turn)
                queries_out(NT - 1, 0, NT // 2)
                for s in range(2):
                    act.wait_ge(q_stored[s], 16 * (NT // 2 + 2 - s))
                    act.wait_ge(kv_stored[s], 16 * (3 * (NT // 2 + 1 - s) + 1))
                    act.wait_ge(c_stored[s], 16 * (NT // 2 + 2 - s))

            @block.vector
            def _(dve):
                NORM_STEPS, ROTATE_STEPS = 10, 7

                def normalise(t, s, r):
                    st = Steps(dve, n_steps, t, NORM_STEPS)
                    dve.wait_ge(squares, 2 * t + 2)
                    st.did(dve.tensor_scalar(ms[:, 0:1], ss[:, 0:1], 1.0 / QR, RMS_EPS, ALU.mult, ALU.add))
                    dve.tensor_scalar(ms[:, 1:2], ss[:, 1:2], 1.0 / KVR, RMS_EPS, ALU.mult, ALU.add).then_inc(ms_ready, 1)
                    dve.wait_ge(sd_ready, t + 1)
                    st.did(dve.reciprocal(rs[:, :], sd[:, :]))
                    st.wait()
                    dve.wait_ge(kv_stored[s], 16 * (3 * r + 1))
                    dve.wait_ge(c_stored[s], 16 * (r + 1))
                    st.did(dve.scalar_tensor_tensor(cqn[:, :], of_tile(zq, t, 0, QR), rs[:, 0:1], gq[:, :], ALU.mult, ALU.mult))
                    st.did(dve.scalar_tensor_tensor(ckvn[:, s, :], of_tile(zq, t, QR, QR + KVR), rs[:, 1:2], gkv[:, :], ALU.mult, ALU.mult))
                    cos, sin = of_tile(trig, t, 0, HALF), of_tile(trig, t, HALF, 2 * HALF)
                    k1, k2 = of_tile(zq, t, QR + KVR, QR + KVR + HALF), of_tile(zq, t, QR + KVR + HALF, MLA_COLS)
                    st.did(dve.tensor_tensor(k4[:, 0, :], k1, cos, ALU.mult))
                    st.did(dve.tensor_tensor(k4[:, 1, :], k2, sin, ALU.mult))
                    st.did(dve.tensor_tensor(k4[:, 2, :], k1, sin, ALU.mult))
                    st.did(dve.tensor_tensor(k4[:, 3, :], k2, cos, ALU.mult))
                    st.wait()
                    st.did(dve.tensor_tensor(kpad[:, s, NOPE:NOPE + HALF], k4[:, 0, :], k4[:, 1, :], ALU.subtract))
                    st.did(dve.tensor_tensor(kpad[:, s, NOPE + HALF:], k4[:, 2, :], k4[:, 3, :], ALU.add))
                    st.wait()
                    dve.sem_inc(lat_ready, 1)
                    st.end()

                def turn(t, s, r, first, last_tile):
                    st = Steps(dve, r_steps, t, ROTATE_STEPS)
                    dve.wait_ge(tp_done, t + 1)
                    dve.tensor_copy(cT[:, s, :, :], tp[:, 0:3, :]).then_inc(cT_ready, 1)
                    st.did(dve.tensor_copy(kT[NOPE:QK, s, :, :], tp[NOPE:QK, 3:4, :].broadcast_to([ROPE, H, P])))
                    st.wait()
                    dve.sem_inc(kT_ready, 1)
                    if not last_tile:
                        normalise(t + 1, 1 - s, r + s)
                    for n in range(2):
                        dve.wait_ge(kv_done, 2 * t + 1)
                        dve.tensor_copy(kT[0:NOPE, s, 4 * n:4 * n + 4, :], ktp[n][:, :, :]).then_inc(kT_ready, 1)
                    dve.wait_ge(q_copied, 2 * t + 2)
                    q1, q2 = q[:, :, NOPE:NOPE + HALF], q[:, :, NOPE + HALF:]
                    cosb = trig[:, ds(t, 1), 0:HALF].broadcast_to([P, H, HALF])
                    sinb = trig[:, ds(t, 1), HALF:].broadcast_to([P, H, HALF])
                    st.did(dve.tensor_tensor(t4[:, 0], q1, cosb, ALU.mult))
                    st.did(dve.tensor_tensor(t4[:, 1], q2, sinb, ALU.mult))
                    st.did(dve.tensor_tensor(t4[:, 2], q1, sinb, ALU.mult))
                    st.did(dve.tensor_tensor(t4[:, 3], q2, cosb, ALU.mult))
                    st.wait()
                    st.did(dve.tensor_tensor(q1, t4[:, 0], t4[:, 1], ALU.subtract))
                    st.did(dve.tensor_tensor(q2, t4[:, 2], t4[:, 3], ALU.add))
                    st.wait()
                    dve.sem_inc(q_rot, 1)
                    st.end()

                dve.sem_inc(ms_ready, 1)
                dve.sem_inc(kT_ready, 1)
                for s in range(2):
                    dve.sem_inc(c_stored[s], 16)
                dve.memset(kpad[:, :, :], 0.0).then_inc(w_split, 1)
                dve.wait_ge(g_loaded, 48)
                normalise(0, 0, 0)
                skewed_turns(dve, turn)

            @block.tensor
            def _(pe):
                def queries(t):
                    pe.wait_ge(q_rot, t + 1)
                    for n in range(2):
                        for h in range(4):
                            last = pe.transpose(qtp[n][:, h, :], q[:, 4 * n + h, :], ident[:, :])
                        last.then_inc(qt_done, 1)

                def turn(t, s, r, first, last_tile):
                    pe.wait_ge(lat_ready, t + 1)
                    for c in range(2):
                        pe.transpose(tp[:, c, :], cqn[:, c * P:(c + 1) * P], ident[:, :])
                    pe.transpose(tp[:, 2, :], ckvn[:, s, :], ident[:, :])
                    pe.transpose(tp[0:QK, 3, :], kpad[:, s, :], ident[:, :]).then_inc(tp_done, 1)
                    if not first:
                        queries(t - 1)
                    pe.wait_ge(cT_ready, t + 1)
                    for n in range(2):
                        for c in range(2):
                            last = pe.matmul(qp[n][:, :, :].rearrange("p h n -> p (h n)"), cT[:, s, c, :], wuq[:, c, 4 * QK * n:4 * QK * (n + 1)],
                                             start=(c == 0), stop=(c == 1))
                        last.then_inc(q_done, 1)
                    pe.wait_ge(kT_ready, 3 * t + 1)
                    for h in range(H):
                        last = pe.matmul(ktp[h // 4][:, h % 4, :], wuk[:, h, :], cT[:, s, 2, :], start=True, stop=True)
                    last.then_inc(kv_done, 1)
                    pe.wait_ge(v_ready, t + 1)
                    pe.matmul(vp[:, :], cT[:, s, 2, :], wuv[:, :, :].rearrange("p h n -> p (h n)"), start=True, stop=True).then_inc(kv_done, 1)

                pe.wait_ge(w_loaded, 32)
                pe.wait_ge(w_split, 3)
                skewed_turns(pe, turn)
                queries(NT - 1)



def attention(nc, d, layer, ident, cache):
    units = [(s, qb) for s in range(2) for qb in range(TP)]
    n_units = len(units)
    groups = [[range(g, min(g + 4, qb + 1)) for g in range(0, qb + 1, 4)] for _, qb in units]
    first_group = [sum(len(g) for g in groups[:u]) for u in range(n_units)]
    n_groups = sum(len(g) for g in groups)
    n_even, n_odd = (n_groups + 1) // 2, n_groups // 2
    with Phase(nc) as ph:
        qT = ph.sb("at_qT", [QK, 2, SEQ])
        kT = ph.sb("at_kT", [QK, 2, SEQ])
        v = ph.sb("at_v", [P, 2, TP, VD])
        mask = ph.sb("at_mask", [P, P])
        probs = ph.sb("at_p", [P, 2, SEQ])
        pT = ph.sb("at_pT", [P, 2, TP, P])
        mx = ph.sb("at_mx", [P, 2])
        nmx = ph.sb("at_nmx", [P, 2])
        total = ph.sb("at_total", [P, 2])
        inv = ph.sb("at_inv", [P, 2])
        y = ph.sb("at_y", [P, 2, TP, VD])
        sc = [ph.ps(f"at_s{i}", [P, SEQ]) for i in range(2)]
        tp = [ph.ps(f"at_tp{i}", [P, 4, P]) for i in range(2)]
        op = [ph.ps(f"at_o{i}", [P, VD]) for i in range(2)]
        mask_loaded, loaded, y_stored = ph.sem("mask_loaded"), ph.sem2("loaded"), ph.sem2("y_stored")
        head_free, s_done, steps, mx_ready = ph.sem("head_free"), ph.sem("s_done"), ph.sem("steps"), ph.sem("mx_ready")
        p_ready, tp_done, pT_dve, pT_act = ph.sem("p_ready"), ph.sem("tp_done"), ph.sem("pT_dve"), ph.sem("pT_act")
        o_done, y_ready = ph.sem("o_done"), ph.sem("y_ready")

        cwr = ph.sb("cv_wr", [P, 3, CONVW])
        cch = ph.sb("cv_cch", [P, 3, 2 * CONVW])
        cb = ph.sb("cv_b", [P, CONVW])
        u = ph.sb("cv_u", [P, 3, CONVW])
        yc = ph.sb("cv_y", [P, CONVW])
        cv_w, cv_in, cv_out, cv_state = (d["sw"][n] for n in ("cv_w", "cv_in", "cv_out", "cv_state"))
        cv, paced = ph.sem("cv"), ph.sem("paced")
        with nc.Block() as block:
            @block.sync
            def _(sp):
                sp.dma_start(mask[:, :], d["c_causal"]).then_inc(mask_loaded, 16)
                with sp.Fori(0, H // 2) as j:
                    for s in range(2):
                        head = 2 * j + s
                        sp.wait_ge(head_free, head + 1)
                        sp.dma_start(qT[:, s, :], d["QT"][ds(head, 1), :, 0:SEQ].rearrange("h p n -> (h p) n")).then_inc(loaded[s], 16)
                        sp.dma_start(kT[:, s, :], d["KT"][ds(head, 1), :, 0:SEQ].rearrange("h p n -> (h p) n")).then_inc(loaded[s], 16)
                        sp.dma_start(v[:, s, :, :], d["V"][0:SEQ, ds(head * VD, VD)].rearrange("(b p) n -> p b n", p=P)).then_inc(loaded[s], 16)
                        cache.load(sp, d, layer, cache.COUNTS[0] + 9 * head, 9, 1)

            def pair_turns(eng, turn):
                with eng.Fori(0, H // 2 - 1) as j:
                    turn(j, False)
                turn(H // 2 - 1, True)

            @block.tensor
            def _(pe):
                def scores(j, n):
                    s, qb = units[n % n_units]
                    if qb == 0:
                        pe.wait_ge(loaded[s], 48 * (j + n // n_units + 1))
                    keys = (qb + 1) * P
                    for c in range(0, keys, 512):
                        last = pe.matmul(sc[n % 2][:, c:min(c + 512, keys)], qT[:, s, qb * P:(qb + 1) * P],
                                         kT[:, s, c:min(c + 512, keys)], start=True, stop=True)
                    last.then_inc(s_done, 1)

                def turn(j, last_turn):
                    for n, (s, qb) in enumerate(units):
                        pe.wait_ge(p_ready, j * n_units + n + 1)
                        for g, blocks in enumerate(groups[n]):
                            m = first_group[n] + g
                            if m % 2 == 0:
                                pe.wait_ge(pT_dve, j * n_even + m // 2 + 1)
                            else:
                                pe.wait_ge(pT_act, j * n_odd + m // 2 + 1)
                            for kb in blocks:
                                last = pe.transpose(tp[m % 2][:, kb % 4, :], probs[:, n % 2, kb * P:(kb + 1) * P], ident[:, :])
                            last.then_inc(tp_done, 1)
                        if not (last_turn and n + 2 >= n_units):
                            scores(j, n + 2)
                        pe.wait_ge(y_ready, j * n_units + n + 1)
                        for g, blocks in enumerate(groups[n]):
                            m = first_group[n] + g
                            if m % 2 == 0:
                                pe.wait_ge(pT_dve, j * n_even + m // 2 + 2)
                            else:
                                pe.wait_ge(pT_act, j * n_odd + m // 2 + 2)
                            for kb in blocks:
                                last = pe.matmul(op[n % 2][:, :], pT[:, n % 2, kb, :], v[:, s, kb, :], start=(kb == 0), stop=(kb == qb))
                        last.then_inc(o_done, 1)

                scores(0, 0)
                scores(0, 1)
                pair_turns(pe, turn)

            @block.vector
            def _(dve):
                dve.sem_inc(head_free, 2)
                dve.sem_inc(pT_dve, 1)
                dve.sem_inc(y_ready, 2)
                dve.wait_ge(mask_loaded, 16)

                def maximum(st, j, n):
                    s, qb = units[n % n_units]
                    dve.wait_ge(s_done, j * n_units + n + 1)
                    diag = sc[n % 2][:, qb * P:(qb + 1) * P]
                    st.did(dve.tensor_tensor(diag, diag, mask[:, :], ALU.add))
                    st.wait()
                    st.did(dve.tensor_reduce(mx[:, n % 2:n % 2 + 1], sc[n % 2][:, 0:(qb + 1) * P], AX.X, ALU.max))
                    st.wait()
                    dve.tensor_scalar(nmx[:, n % 2:n % 2 + 1], mx[:, n % 2:n % 2 + 1], -SCALE, None, ALU.mult).then_inc(mx_ready, 1)

                def turn(j, last_turn):
                    st = Steps(dve, steps, j, 3 * n_units)
                    st.base = st.base + 4
                    for n, (s, qb) in enumerate(units):
                        for g, blocks in enumerate(groups[n]):
                            m = first_group[n] + g
                            if m % 2 == 0:
                                dve.wait_ge(tp_done, j * n_groups + m + 1)
                                dve.tensor_copy(pT[:, n % 2, blocks[0]:blocks[-1] + 1, :], tp[0][:, 0:len(blocks), :]).then_inc(pT_dve, 1)
                        dve.wait_ge(p_ready, j * n_units + n + 1)
                        st.did(dve.reciprocal(inv[:, n % 2:n % 2 + 1], total[:, n % 2:n % 2 + 1]))
                        st.wait()
                        if not (last_turn and n + 2 >= n_units):
                            maximum(st, j, n + 2)
                        if qb == 0:
                            dve.wait_ge(y_stored[s], 16 * (j + 1))
                        dve.wait_ge(o_done, j * n_units + n + 1)
                        dve.tensor_scalar(y[:, s, qb, :], op[n % 2][:, :], inv[:, n % 2:n % 2 + 1], None, ALU.mult).then_inc(y_ready, 1)
                        if qb == TP - 1:
                            dve.sem_inc(head_free, 1)
                first = Steps(dve, steps, 0, 4)
                for n in range(2):
                    maximum(first, 0, n)
                first.end()
                pair_turns(dve, turn)

            @block.scalar
            def _(act):
                act.sem_inc(pT_act, 1)
                for s in range(2):
                    act.sem_inc(y_stored[s], 16)

                def exponentials(j, n):
                    s, qb = units[n % n_units]
                    act.wait_ge(mx_ready, j * n_units + n + 1)
                    act.activation(probs[:, n % 2, 0:(qb + 1) * P], sc[n % 2][:, 0:(qb + 1) * P], ACT.Exp,
                                   bias=nmx[:, n % 2:n % 2 + 1], scale=SCALE, accum_out=total[:, n % 2:n % 2 + 1]).then_inc(p_ready, 1)

                def turn(j, last_turn):
                    for n, (s, qb) in enumerate(units):
                        for g, blocks in enumerate(groups[n]):
                            m = first_group[n] + g
                            if m % 2 == 1:
                                act.wait_ge(tp_done, j * n_groups + m + 1)
                                act.activation(pT[:, n % 2, blocks[0]:blocks[-1] + 1, :], tp[1][:, 0:len(blocks), :], ACT.Copy).then_inc(pT_act, 1)
                        if not (last_turn and n + 2 >= n_units):
                            exponentials(j, n + 2)
                        if qb == TP - 1:
                            act.wait_ge(y_ready, j * n_units + n + 3)
                            act.dma_start(d["Y"][0:SEQ, ds(CONVW + (2 * j + s) * VD, VD)].rearrange("(b p) n -> p b n", p=P),
                                          y[:, s, :, :]).then_inc(y_stored[s], 16)
                exponentials(0, 0)
                exponentials(0, 1)
                pair_turns(act, turn)
                for s in range(2):
                    act.wait_ge(y_stored[s], 16 * (H // 2 + 1))

            @block.gpsimd
            def _(pool):
                IN_ALL = 64 * TP + 48
                pool.dma_start(cwr[:, :, :].rearrange("p k n -> p (k n)"),
                               d["conv_w"].rearrange("l k n -> l (k n)")[ds(layer, 1), :].broadcast_to([P, 3 * CONVW])).then_inc(cv_w, 16)
                pool.wait_ge(cv_w, 16 * (layer + 1))
                pool.sem_inc(paced, 1)

                def gated(st, n):
                    for k in range(3):
                        st.did(pool.tensor_tensor(yc[0:n, :] if k == 0 else cch[0:n, k, 0:CONVW], u[0:n, k, :], cwr[0:n, k, :], ALU.mult))
                    for k in range(1, 3):
                        st.wait()
                        st.did(pool.tensor_tensor(yc[0:n, :], yc[0:n, :], cch[0:n, k, 0:CONVW], ALU.add))
                    st.wait()
                    st.did(pool.tensor_tensor(yc[0:n, :], yc[0:n, :], cb[0:n, :], ALU.mult))
                    st.wait()

                with pool.Fori(0, TP) as t:
                    st = Steps(pool, cv, t, 9)
                    for k in range(3):
                        pool.dma_start(cch[:, k, :], d["Z"][ds(t * P + k, P), C_CC:C_CC + 2 * CONVW]).then_inc(cv_in, 16)
                    pool.dma_start(cb[:, :], d["Z"][ds(PAD + t * P, P), C_CB:C_CB + CONVW]).then_inc(cv_in, 16)
                    pool.wait_ge(cv_in, IN_ALL * layer + 64 * (t + 1))
                    for k in range(3):
                        st.did(pool.tensor_tensor(u[:, k, :], cch[:, k, 0:CONVW], cch[:, k, CONVW:], ALU.mult))
                    st.wait()
                    gated(st, P)
                    st.end()
                    pool.dma_start(d["Y"][rows(t), 0:CONVW], yc[:, :]).then_inc(cv_out, 16)
                    pool.wait_ge(cv_out, 16 * (TP + 1) * layer + 16 * (t + 1))
                    pool.sem_inc(paced, 1)
                pool.dma_start(of_layer(d["conv_p"], layer), u[P - 2:P, 2, :]).then_inc(cv_state, 16)
                pool.wait_ge(cv_state, 32 * layer + 16)
                pool.sem_inc(paced, 1)
                s0 = PAD + SEQ
                pool.dma_start(cch[0:DECB, 2, :], d["Z"][s0:s0 + DECB, C_CC:C_CC + 2 * CONVW]).then_inc(cv_in, 16)
                pool.dma_start(cb[0:DECB, :], d["Z"][s0:s0 + DECB, C_CB:C_CB + CONVW]).then_inc(cv_in, 16)
                pool.dma_start(u[0:DECB, 0:2, :], of_layer(d["state_conv"], layer)).then_inc(cv_in, 16)
                pool.wait_ge(cv_in, IN_ALL * (layer + 1))
                st = Steps(pool, cv, TP, 7)
                st.base = 9 * TP
                st.did(pool.tensor_tensor(u[0:DECB, 2, :], cch[0:DECB, 2, 0:CONVW], cch[0:DECB, 2, CONVW:], ALU.mult))
                st.wait()
                gated(st, DECB)
                pool.dma_start(d["Y"][SEQ:SEQ + DECB, 0:CONVW], yc[0:DECB, :]).then_inc(cv_out, 16)
                pool.dma_start(of_layer(d["conv_s"], layer), u[0:DECB, 1:3, :]).then_inc(cv_state, 16)
                pool.wait_ge(cv_out, 16 * (TP + 1) * (layer + 1))
                pool.sem_inc(paced, 1)
                pool.wait_ge(cv_state, 32 * (layer + 1))
                pool.sem_inc(paced, 1)



VX = DH + 1


def mlstm_prompt(nc, d, layer, ident, cache):
    with Phase(nc) as ph:
        gz = ph.sb("ml_gz", [P, TP, 2 * NH])
        gbias = ph.sb("ml_gbias", [P, 2 * NH])
        headrow = ph.sb("ml_headrow", [NH, NH, P])
        maskT = ph.sb("ml_maskT", [P, P])
        fw = ph.sb("ml_fw", [P, 5, TP, NH])
        gi = ph.sb("ml_gi", [NH, SEQ])
        lf = ph.sb("ml_lf", [NH, SEQ])
        w1 = ph.sb("ml_w1", [NH, SEQ])
        w2 = ph.sb("ml_w2", [NH, SEQ])
        keep = ph.sb("ml_keep", [NH, SEQ])
        m = ph.sb("ml_m", [NH, SEQ])
        b = ph.sb("ml_b", [NH, SEQ])
        mprev = ph.sb("ml_mprev", [NH, TP])
        rows4 = ph.sb("ml_rows", [NH, 4, SEQ])
        a = ph.sb("ml_a", [NH, SEQ])
        cols = ph.sb("ml_cols", [P, 4, TP, NH])
        wold = ph.sb("ml_wold", [DH, NH, TP])
        x = ph.sb("ml_x", [P, 2, 3 * MW])
        ks = ph.sb("ml_ks", [P, 2, NH, DH])
        qs = ph.sb("ml_qs", [P, 2, NH, DH])
        vx = ph.sb("ml_vx", [P, 2, NH, VX])
        vw = ph.sb("ml_vw", [P, 2, NH, VX])
        qT = ph.sb("ml_qT", [DH, 2, NH, P])
        qsT = ph.sb("ml_qsT", [DH, 2, NH, P])
        kT = ph.sb("ml_kT", [DH, 2, NH, P])
        e = ph.sb("ml_e", [P, 2, NH, P])
        dd = ph.sb("ml_d", [P, 2, NH, P])
        sm = ph.sb("ml_s", [P, 2, NH, P])
        state = ph.sb("ml_state", [DH, 2, NH, VX])
        carry = ph.sb("ml_carry", [DH, NH, VX])
        den = ph.sb("ml_den", [P, NH])
        den2 = ph.sb("ml_den2", [P, NH])
        rden = ph.sb("ml_rden", [P, NH])
        so = ph.sb("ml_so", [P, TP, NH, DH])
        hh = ph.sb("ml_h", [P, NH, DH])
        y = ph.sb("ml_y", [P, 2, MW])
        cT = ph.sb("ml_cT", [VX, NH, DH])
        pg = [ph.ps(f"ml_pg{i}", [P, 512]) for i in range(3)]
        pa = ph.ps("ml_pa", [P, NH, P])
        pqk = ph.ps("ml_pqk", [P, NH, P])
        pn = ph.ps("ml_pn", [P, NH, VX])
        pu = ph.ps("ml_pu", [DH, NH, VX])
        px = ph.ps("ml_px", [P, 512])
        loaded0, x_loaded, y_stored = ph.sem("loaded0"), ph.sem2("x_loaded"), ph.sem2("y_stored")
        g_tp, g_steps, g_act, g_cols = ph.sem("g_tp"), ph.sem("g_steps"), ph.sem("g_act"), ph.sem("g_cols")
        v_steps, x_free, scaled, tp_done = ph.sem("v_steps"), ph.sem("x_free"), ph.sem("scaled"), ph.sem("tp_done")
        qT_ready, kT_ready, a_done, e_ready = ph.sem("qT_ready"), ph.sem("kT_ready"), ph.sem("a_done"), ph.sem("e_ready")
        d_ready, s_ready, n_done, u_done = ph.sem("d_ready"), ph.sem("s_ready"), ph.sem("n_done"), ph.sem("u_done")
        st_ready, den_ready, y_ready, so_ready = ph.sem("st_ready"), ph.sem("den_ready"), ph.sem("y_ready"), ph.sem("so_ready")
        carry_ready, so_loaded, b_done = ph.sem("carry_ready"), ph.sem("so_loaded"), ph.sem("b_done")
        final, out_done = ph.sem("final"), ph.sem("out_done")

        def chunks(eng, turn):
            with eng.Fori(0, TP // 2 - 1) as r:
                for s in range(2):
                    turn(2 * r + s, s, r, False)
            for s in range(2):
                turn(TP - 2 + s, s, TP // 2 - 1, s == 1)

        with nc.Block() as block:
            @block.sync
            def _(sp):
                sp.dma_start(gz[:, :, :], d["Z"][PAD:PAD + SEQ, C_MI:C_MI + 2 * NH].rearrange("(c p) n -> p c n", p=P)).then_inc(loaded0, 16)
                sp.dma_start(gbias[:, :], row_of_layer(d["mlstm_gate_b"], layer)).then_inc(loaded0, 16)
                sp.dma_start(headrow[:, :, :], d["c_headrow"]).then_inc(loaded0, 16)
                sp.dma_start(maskT[:, :], d["c_causalT"]).then_inc(loaded0, 16)
                sp.dma_start(so[:, :, :, :].rearrange("p c h n -> p c (h n)"),
                             d["Z"][PAD:PAD + SEQ, C_MO:C_MO + MW].rearrange("(c p) n -> p c n", p=P)).then_inc(so_loaded, 16)
                with sp.Fori(0, TP // 2) as r:
                    for s in range(2):
                        t = 2 * r + s
                        sp.wait_ge(x_free, t + 1)
                        sp.dma_start(x[:, s, :], d["Z"][ds(PAD + t * P, P), C_MQ:C_MQ + 3 * MW]).then_inc(x_loaded[s], 16)
                        cache.load(sp, d, layer, cache.COUNTS[0] + cache.COUNTS[1] + 3 * t, 3, 2)
                sp.wait_ge(final, 1)
                sp.dma_start(of_layer(d["C_p"], layer).rearrange("h v e -> v h e"), cT[0:DH, :, :]).then_inc(out_done, 16)
                sp.dma_start(of_layer(d["n_p"], layer).rearrange("(o h) e -> o h e", o=1), cT[DH:VX, :, :]).then_inc(out_done, 16)
                sp.dma_start(of_layer(d["m_p"], layer).rearrange("(h o) -> h o", o=1), m[:, SEQ - 1:SEQ]).then_inc(out_done, 16)
                sp.wait_ge(out_done, 48)

            @block.tensor
            def _(pe):
                pe.wait_ge(g_steps, 12)
                for c in range(TP):
                    pe.transpose(pg[c // 4][0:NH, (c % 4) * P:(c % 4 + 1) * P], gz[:, c, 0:NH], ident[:, :])
                for c in range(TP):
                    dst = (px, pg[2])[c // 4]
                    last = pe.transpose(dst[0:NH, (c % 4) * P:(c % 4 + 1) * P], gz[:, c, NH:], ident[:, :])
                last.then_inc(g_tp, 1)
                pe.wait_ge(g_cols, 1)
                for k in range(4):
                    for c in range(TP):
                        pe.transpose(pg[0][:, (k * TP + c) * NH:(k * TP + c + 1) * NH], rows4[:, k, c * P:(c + 1) * P], ident[0:NH, 0:NH])
                for h in range(NH):
                    last = pe.matmul(px[0:DH, h * TP:(h + 1) * TP], headrow[:, h, 0:DH],
                                     rows4[:, 1, :].rearrange("h (c t) -> h c t", c=TP)[:, :, P - 1], start=True, stop=True)
                last.then_inc(g_tp, 1)
                pe.wait_ge(g_cols, 2)
                def transposes(t, s, r):
                    pe.wait_ge(x_loaded[s], 16 * (r + 1))
                    pe.wait_ge(scaled, t + 1)
                    for h in range(NH):
                        last = pe.matmul(pa[:, h, :], headrow[:, h, :], a[:, ds(t * P, P)], start=True, stop=True)
                    last.then_inc(a_done, 1)
                    for h in range(NH):
                        pe.transpose(pg[0][0:DH, h * P:(h + 1) * P], x[:, s, h * DH:(h + 1) * DH], ident[:, :])
                    for h in range(NH):
                        pe.transpose(pg[1][0:DH, h * P:(h + 1) * P], qs[:, s, h, :], ident[:, :])
                    for h in range(NH):
                        last = pe.transpose(pg[2][0:DH, h * P:(h + 1) * P], ks[:, s, h, :], ident[:, :])
                    last.then_inc(tp_done, 1)

                def turn(t, s, r, last_chunk):
                    pe.wait_ge(qT_ready, 2 * (t + 1))
                    pe.wait_ge(kT_ready, t + 1)
                    for h in range(NH):
                        last = pe.matmul(pqk[:, h, :], kT[:, s, h, :], qT[:, s, h, :], start=True, stop=True)
                    last.then_inc(b_done, 1)
                    pe.wait_ge(st_ready, t + 1)
                    for h in range(NH):
                        last = pe.matmul(pu[:, h, :], ks[:, s, h, :], vw[:, s, h, :], start=True, stop=True)
                    last.then_inc(u_done, 1)
                    if not last_chunk:
                        transposes(t + 1, 1 - s, r + s)
                    pe.wait_ge(s_ready, t + 1)
                    for h in range(NH):
                        pe.matmul(pn[:, h, :], sm[:, s, h, :], vx[:, s, h, :], start=True, stop=False)
                        last = pe.matmul(pn[:, h, :], qsT[:, s, h, :], state[:, s, h, :], start=False, stop=True)
                    last.then_inc(n_done, 1)
                transposes(0, 0, 0)
                chunks(pe, turn)
                pe.wait_ge(carry_ready, 1)
                for h in range(NH):
                    last = pe.transpose(px[0:VX, h * DH:(h + 1) * DH], carry[:, h, :], ident[0:DH, 0:DH])
                last.then_inc(g_tp, 1)

            @block.vector
            def _(dve):
                g = Steps(dve, g_steps, 0, 29)
                dve.wait_ge(loaded0, 64)
                g.did(dve.tensor_tensor(gz[:, :, :], gz[:, :, :], gbias[:, :].unsqueeze(1).broadcast_to([P, TP, 2 * NH]), ALU.add))
                g.did(dve.memset(keep[:, :], 1.0))
                g.wait()
                g.did(dve.memset(keep[:, :].rearrange("h (c t) -> h c t", c=TP)[:, :, 0:1], 0.0))
                f, (neg, u, w, rw, c1) = gz[:, :, NH:], (fw[:, i] for i in range(5))
                g.did(dve.tensor_scalar(neg, f, -1.0, None, ALU.mult))
                g.wait()
                g.did(dve.tensor_tensor(neg, neg, f, ALU.min))
                dve.wait_ge(g_act, 1)
                g.did(dve.tensor_scalar(w, u, 1.0, None, ALU.add))
                g.wait()
                g.did(dve.tensor_scalar(c1, w, -1.0, None, ALU.add))
                g.wait()
                g.did(dve.tensor_tensor(c1, u, c1, ALU.subtract))
                g.did(dve.reciprocal(rw, w))
                g.wait()
                g.did(dve.tensor_tensor(c1, c1, rw, ALU.mult))
                dve.wait_ge(g_act, 2)
                g.wait()
                g.did(dve.tensor_tensor(c1, c1, neg, ALU.add))
                g.wait()
                g.did(dve.scalar_tensor_tensor(f, f, 0.0, c1, ALU.min, ALU.subtract))
                assert g.n == 12
                dve.wait_ge(g_tp, 1)
                for c in range(2):
                    half = slice(c * 512, (c + 1) * 512)
                    g.did(dve.tensor_copy(gi[:, half], pg[c][0:NH, :]))
                    g.did(dve.tensor_copy(lf[:, half], (px, pg[2])[c][0:NH, :]))
                g.wait()
                g.did(dve.tensor_tensor_scan(m[:, :], lf[:, :], gi[:, :], 0.0, ALU.add, ALU.max))
                g.did(dve.tensor_tensor_scan(b[:, :], keep[:, :], lf[:, :], 0.0, ALU.mult, ALU.add))
                g.did(dve.memset(mprev[:, 0:1], 0.0))
                g.wait()
                g.did(dve.tensor_copy(mprev[:, 1:TP], m[:, :].rearrange("h (c t) -> h c t", c=TP)[:, 0:TP - 1, P - 1]))
                g.did(dve.tensor_tensor(a[:, :], b[:, :], m[:, :], ALU.subtract))
                g.did(dve.tensor_tensor(rows4[:, 0, :], gi[:, :], b[:, :], ALU.subtract))
                g.wait()
                chunked = lambda ap: ap.rearrange("h (c t) -> h c t", c=TP)
                g.did(dve.tensor_tensor(chunked(w1[:, :]), chunked(a[:, :]), mprev[:, :].unsqueeze(2).broadcast_to([NH, TP, P]), ALU.add))
                g.did(dve.tensor_tensor(chunked(w2[:, :]), chunked(rows4[:, 0, :]), chunked(a[:, :])[:, :, P - 1:P].broadcast_to([NH, TP, P]), ALU.add))
                g.did(dve.memset(carry[:, :, :], 0.0))
                g.did(dve.memset(state[:, :, :, :], 0.0))
                g.did(dve.memset(vx[:, :, :, :], 1.0))
                g.wait()
                dve.wait_ge(g_tp, 2)
                g.did(dve.tensor_copy(cols[:, :, :, :].rearrange("p k c h -> p (k c h)"), pg[0][:, 0:4 * TP * NH]))
                g.did(dve.tensor_copy(wold[:, :, :].rearrange("p h c -> p (h c)"), px[0:DH, 0:NH * TP]))
                g.wait()
                g.end()
                dve.sem_inc(g_cols, 1)
                dve.sem_inc(st_ready, 1)
                AHEAD, TURN = 4, 9

                def scale(v, t, s, r):
                    wi, ws = (cols[:, k, ds(t, 1), :].rearrange("p c h -> p (c h)") for k in (1, 2))
                    xq, xk, xv = (x[:, s, i * MW:(i + 1) * MW].rearrange("p (h n) -> p h n", h=NH) for i in range(3))
                    dve.wait_ge(x_loaded[s], 16 * (r + 1))
                    dve.wait_ge(n_done, t + 1)
                    v.did(dve.tensor_scalar(ks[:, s], xk, DH ** -0.5, None, ALU.mult))
                    v.did(dve.tensor_tensor(qs[:, s], xq, wi.unsqueeze(2).broadcast_to([P, NH, DH]), ALU.mult))
                    v.did(dve.tensor_copy(vx[:, s, :, 0:DH], xv))
                    v.wait()
                    v.did(dve.tensor_tensor(vw[:, s], vx[:, s], ws.unsqueeze(2).broadcast_to([P, NH, VX]), ALU.mult))
                    v.wait()
                    dve.sem_inc(scaled, 1)

                def decay_and_keys(t, s):
                    dve.wait_ge(a_done, t + 1)
                    dve.tensor_tensor(e[:, s], pa[:, :, :], maskT[:, :].unsqueeze(1).broadcast_to([P, NH, P]), ALU.add).then_inc(e_ready, 1)
                    dve.wait_ge(tp_done, t + 1)
                    dve.tensor_copy(kT[:, s], pg[2][0:DH, :].rearrange("p (h n) -> p h n", h=NH)).then_inc(kT_ready, 1)

                def turn(t, s, r, last_chunk):
                    v = Steps(dve, v_steps, t, TURN)
                    v.base = v.base + AHEAD
                    if not last_chunk:
                        scale(v, t + 1, 1 - s, r + s)
                    dve.wait_ge(d_ready, t + 1)
                    dve.wait_ge(b_done, t + 1)
                    dve.tensor_tensor(sm[:, s], pqk[:, :, :], dd[:, s], ALU.mult).then_inc(s_ready, 1)
                    dve.wait_ge(u_done, t + 1)
                    dve.wait_ge(n_done, t + 2)
                    for h in range(NH):
                        last = dve.scalar_tensor_tensor(state[:, 1 - s, h, :], state[:, s, h, :], wold[:, h, ds(t, 1)], pu[:, h, :], ALU.mult, ALU.add)
                    v.did(last)
                    v.wait()
                    dve.sem_inc(st_ready, 1)
                    if not last_chunk:
                        decay_and_keys(t + 1, 1 - s)
                    em = cols[:, 3, ds(t, 1), :].rearrange("p c h -> p (c h)")
                    dve.wait_ge(den_ready, t + 1)
                    v.did(dve.tensor_tensor(den2[:, :], den[:, :], em, ALU.max))
                    v.wait()
                    v.did(dve.reciprocal(rden[:, :], den2[:, :]))
                    v.wait()
                    v.did(dve.tensor_tensor(hh[:, :, :], pn[:, :, 0:DH], rden[:, :].unsqueeze(2).broadcast_to([P, NH, DH]), ALU.mult))
                    v.wait()
                    dve.wait_ge(so_ready, 1)
                    dve.wait_ge(y_stored[s], 16 * (r + 1))
                    v.did(dve.tensor_tensor(y[:, s, :].rearrange("p (h n) -> p h n", h=NH), hh[:, :, :], so[:, ds(t, 1)].rearrange("p c h n -> p (c h) n"), ALU.mult))
                    v.wait()
                    dve.sem_inc(y_ready, 1)
                    assert v.n == TURN - (AHEAD if last_chunk else 0)
                scale(Steps(dve, v_steps, 0, AHEAD), 0, 0, 0)
                decay_and_keys(0, 0)
                chunks(dve, turn)
                v = Steps(dve, v_steps, TP, 2)
                v.base = 9 * TP
                v.did(dve.tensor_copy(carry[:, :, :], state[:, 0]))
                v.wait()
                dve.sem_inc(carry_ready, 1)
                dve.wait_ge(g_tp, 3)
                v.did(dve.tensor_copy(cT[:, :, :], px[0:VX, 0:NH * DH].rearrange("p (h n) -> p h n", h=NH)))
                v.wait()
                dve.sem_inc(final, 1)

            @block.scalar
            def _(act):
                for s in range(2):
                    act.sem_inc(y_stored[s], 16)
                act.sem_inc(n_done, 2)
                act.sem_inc(x_free, 2)
                act.wait_ge(so_loaded, 16)
                act.activation(so[:, :, :, :].rearrange("p c h n -> p (c h n)"), so[:, :, :, :].rearrange("p c h n -> p (c h n)"), ACT.Sigmoid).then_inc(so_ready, 1)
                act.wait_ge(g_steps, 5)
                act.activation(fw[:, 1], fw[:, 0], ACT.Exp).then_inc(g_act, 1)
                act.wait_ge(g_steps, 6)
                act.activation(fw[:, 0], fw[:, 2], ACT.Ln).then_inc(g_act, 1)
                act.wait_ge(g_steps, 24)
                act.activation(rows4[:, 1, :], w1[:, :], ACT.Exp)
                act.activation(rows4[:, 2, :], w2[:, :], ACT.Exp)
                act.activation(rows4[:, 3, :], m[:, :], ACT.Exp, scale=-1.0).then_inc(g_act, 1)
                act.wait_ge(g_act, 3)
                act.sem_inc(g_cols, 1)
                act.wait_ge(g_cols, 2)
                def ahead(t, s):
                    act.wait_ge(tp_done, t + 1)
                    act.activation(qT[:, s], pg[0][0:DH, :].rearrange("p (h n) -> p h n", h=NH), ACT.Copy).then_inc(qT_ready, 1)
                    act.activation(qsT[:, s], pg[1][0:DH, :].rearrange("p (h n) -> p h n", h=NH), ACT.Copy).then_inc(qT_ready, 1)
                    act.sem_inc(x_free, 1)
                    act.wait_ge(e_ready, t + 1)
                    for h in range(NH):
                        last = act.activation(dd[:, s, h, :], e[:, s, h, :], ACT.Exp, bias=cols[:, 0, ds(t, 1), h])
                    last.then_inc(d_ready, 1)

                def turn(t, s, r, last_chunk):
                    if not last_chunk:
                        ahead(t + 1, 1 - s)
                    act.wait_ge(n_done, t + 3)
                    act.activation(den[:, :], pn[:, :, DH], ACT.Abs).then_inc(den_ready, 1)
                    act.wait_ge(y_ready, t + 1)
                    act.dma_start(d["Y"][rows(t), CONVW + H * VD:], y[:, s, :]).then_inc(y_stored[s], 16)
                ahead(0, 0)
                chunks(act, turn)
                for s in range(2):
                    act.wait_ge(y_stored[s], 16 * (TP // 2 + 1))



BHN, VG, VR = DECB * NH, 4, DH // 4
G_Q, G_K, G_N, G_I, G_F, G_M, G_BI, G_BF, G_ALL = 0, 64, 128, 192, 193, 194, 195, 196, 197


class StepInputs:

    def __init__(self, ph):
        self.g = ph.sb("ms_g", [BHN, G_ALL])
        self.rep = ph.sb("ms_rep", [BHN, P])
        self.v = ph.sb("ms_v", [P, VR])
        self.o = ph.sb("ms_o", [P, VR])
        self.C = ph.sb("ms_C", [P, VR, DH])
        self.loaded = ph.sem("step_loaded")

    def load(self, eng, d, layer):
        z = d["Z"][PAD + SEQ:PAD + SEQ + DECB]
        for c0, w, src in ((G_Q, DH, z[:, C_MQ:C_MQ + MW].rearrange("b (h n) -> b h n", h=NH)),
                           (G_K, DH, z[:, C_MK:C_MK + MW].rearrange("b (h n) -> b h n", h=NH)),
                           (G_I, 1, z[:, C_MI:C_MI + NH].rearrange("b (h o) -> b h o", o=1)),
                           (G_F, 1, z[:, C_MI + NH:C_MI + 2 * NH].rearrange("b (h o) -> b h o", o=1)),
                           (G_N, DH, of_layer(d["state_mlstm_n"], layer)),
                           (G_M, 1, of_layer(d["state_mlstm_m"], layer).rearrange("b (h o) -> b h o", o=1)),
                           (G_BI, 1, d["mlstm_gate_b"][ds(layer, 1), 0:NH].unsqueeze(2).broadcast_to([DECB, NH, 1])),
                           (G_BF, 1, d["mlstm_gate_b"][ds(layer, 1), NH:].unsqueeze(2).broadcast_to([DECB, NH, 1]))):
            eng.dma_start(self.g[:, c0:c0 + w], src).then_inc(self.loaded, 16)
        eng.dma_start(self.v[:, :], z[:, C_MV:C_MV + MW].rearrange("b (q n) -> b q n", n=VR)).then_inc(self.loaded, 16)
        eng.dma_start(self.o[:, :], z[:, C_MO:C_MO + MW].rearrange("b (q n) -> b q n", n=VR)).then_inc(self.loaded, 16)
        eng.dma_start(self.rep[:, :], d["c_rep"]).then_inc(self.loaded, 16)
        eng.dma_start(self.C[:, :, :].rearrange("p v n -> p (v n)"),
                     of_layer(d["state_mlstm_C"], layer).rearrange("b h (g v) n -> (b h g) (v n)", g=VG)).then_inc(self.loaded, 16)


class OutputInputs:

    def __init__(self, ph):
        self.wout = ph.sb("op_wout", [P, KC, D])
        self.wpg = ph.sb("op_wpg", [P, KC, D])
        self.y = ph.sb("op_y", [P, 2, D])
        self.mixg = ph.sb("op_mixg", [P, D])
        self.mixg_loaded = ph.sem("mixg_loaded")
        self.wout_loaded, self.wpg_loaded, self.y_loaded = ph.sem("wout_loaded"), ph.sem("wpg_loaded"), ph.sem2("y_loaded")

    def load_weights(self, eng, d, layer, buf, src, loaded):
        eng.dma_start(buf[:, :, :].rearrange("p k n -> p (k n)"), of_layer(d[src], layer).rearrange("(p k) n -> p (k n)", k=KC)).then_inc(loaded, 16)

    def load_y(self, eng, d, t):
        eng.dma_start(self.y[:, t % 2, :], d["Y"][rows(t)]).then_inc(self.y_loaded[t % 2], 16)



def sample_attention(nc, d, layer, ident, cache, step):
    BH = DECB * H
    ckv, kr = cache.ckv, cache.kr
    with Phase(nc) as ph:
        cn = ph.sb("sa_cn", [DECB, LX])
        krn = ph.sb("sa_krn", [DECB, ROPE])
        own = ph.sb("sa_own", [DECB, DECB, H])
        ones = ph.sb("sa_ones", [BH, P])
        wukv = ph.sb("sa_wukv", [P, H, NOPE + VD])
        wukT = ph.sb("sa_wukT", [NOPE, H, P])
        wuv = ph.sb("sa_wuv", [P, H, VD])
        qTs = ph.sb("sa_qT", [QK, H, DECB])
        qlat = ph.sb("sa_qlat", [P, DECB, H])
        qr = ph.sb("sa_qr", [ROPE, DECB, H])
        qrd = ph.sb("sa_qrd", [P, DECB, 4, H])
        cnT = ph.sb("sa_cnT", [P, DECB])
        krnT = ph.sb("sa_krnT", [ROPE, DECB])
        cT = ph.sb("sa_cT", [P, 2, PAGES, P])
        krT = ph.sb("sa_krT", [P, 2, PAGES // 4, P])
        S = ph.sb("sa_S", [P, DECB, PAGES, H])
        SX = ph.sb("sa_SX", [DECB, BH])
        mxp = ph.sb("sa_mxp", [P, DECB, H])
        mcol = ph.sb("sa_mcol", [BH, 1])
        mdiag = ph.sb("sa_mdiag", [BH, BH])
        mb = ph.sb("sa_mb", [P, DECB, H])
        pst = ph.sb("sa_pst", [P, 2, PAGES, H])
        pxst = ph.sb("sa_pxst", [DECB, 2, H])
        on = ph.sb("sa_on", [H, DECB, KVR])
        ro = ph.sb("sa_ro", [H, 2])
        ol = ph.sb("sa_ol", [P, H, DECB])
        att = ph.sb("sa_att", [DECB, H * VD])
        tpb = [ph.ps(f"sa_tp{i}", [P, 4, P]) for i in range(4)]
        ktp = ph.ps("sa_ktp", [P, 4, P])
        scp = [ph.ps(f"sa_sc{i}", [P, PAGES, H]) for i in range(2)]
        misc = ph.ps("sa_misc", [P, 512])
        loaded0 = ph.sem("loaded0")
        prep, pe_prep, st_q = ph.sem("prep"), ph.sem("pe_prep"), ph.sem("st_q")
        tp_done, cT_dve, cT_act, sc_done = ph.sem("tp_done"), ph.sem("cT_dve"), ph.sem("cT_act"), ph.sem("sc_done")
        S_ready, mx_done, glob, p_ready = ph.sem("S_ready"), ph.sem("mx_done"), ph.sem("glob"), ph.sem("p_ready")
        pst_ready, o_done, on_ready, oT_done = ph.sem("pst_ready"), ph.sem("o_done"), ph.sem("on_ready"), ph.sem("oT_done")
        ol_ready, b_steps, att_done, att_ready, out_done = (ph.sem(n) for n in ("ol_ready", "b_steps", "att_done", "att_ready", "out_done"))
        with nc.Block() as block:
            @block.sync
            def _(sp):
                sp.dma_start(wukv[:, :, :].rearrange("p h n -> p (h n)"), of_layer(d["w_ukv"], layer)).then_inc(loaded0, 16)
                sp.dma_start(qTs[:, :, :], d["QT"][:, :, SEQ:SEQ + DECB].rearrange("h p n -> p h n")).then_inc(loaded0, 16)
                sp.dma_start(cn[:, 0:KVR], of_layer(d["ckv_all"], layer)[SEQ:SEQ + DECB]).then_inc(loaded0, 16)
                sp.dma_start(krn[:, :], of_layer(d["krope_all"], layer)[SEQ:SEQ + DECB]).then_inc(loaded0, 16)
                sp.dma_start(own[:, :, :].rearrange("p b h -> p (b h)"), d["c_own"]).then_inc(loaded0, 16)
                step.load(sp, d, layer)
                sp.wait_ge(att_ready, 1)
                sp.dma_start(d["Y"][SEQ:SEQ + DECB, CONVW:CONVW + H * VD], att[:, :]).then_inc(out_done, 16)
                sp.wait_ge(out_done, 16)

            @block.gpsimd
            def _(pool):
                pool.memset(ones[:, :], 1.0).then_inc(prep, 1)
                pool.memset(qrd[:, :, :, :], 0.0).then_inc(prep, 1)
                pool.memset(cn[:, KVR:], 1.0).then_inc(prep, 1)
                pool.memset(ckv[:, :, KVR:], 1.0).then_inc(prep, 1)

            @block.tensor
            def _(pe):
                pe.wait_ge(loaded0, 80)
                for h in range(H):
                    last = pe.transpose(tpb[h // 4][0:NOPE, h % 4, :], wukv[:, h, 0:NOPE], ident[:, :])
                pe.transpose(misc[:, 0:DECB], cn[:, 0:KVR], ident[0:DECB, 0:DECB])
                pe.transpose(misc[0:ROPE, DECB:2 * DECB], krn[:, :], ident[0:DECB, 0:DECB]).then_inc(pe_prep, 1)
                pe.wait_ge(st_q, 1)
                for h in range(H):
                    last = pe.matmul(misc[:, 64 + h * DECB:64 + (h + 1) * DECB], wukT[:, h, :], qTs[0:NOPE, h, :], start=True, stop=True)
                last.then_inc(pe_prep, 1)
                pe.wait_ge(st_q, 2)
                pe.matmul(misc[0:DECB, 256:256 + BH], cnT[:, :], qlat[:, :, :].rearrange("p b h -> p (b h)"), start=True, stop=False)
                pe.matmul(misc[0:DECB, 256:256 + BH], krnT[:, :], qr[0:ROPE, :, :].rearrange("p b h -> p (b h)"), start=False, stop=True).then_inc(pe_prep, 1)
                for n, loaded in zip(cache.COUNTS, cache.pages_loaded):
                    pe.wait_ge(loaded, 32 * n)
                for b in range(DECB + 1):
                    if b < DECB:
                        for g in range(4):
                            pe.wait_ge((cT_dve, cT_act)[g % 2], (3 if g % 2 == 0 else 2) * b + (g // 2) + 1)
                            for c in range(4):
                                last = pe.transpose(tpb[g][:, c, :], ckv[:, b * PAGES + 4 * g + c, 0:KVR], ident[:, :])
                            last.then_inc(tp_done, 1)
                        pe.wait_ge(cT_dve, 3 * b + 3)
                        for c in range(4):
                            last = pe.transpose(ktp[:, c, :], kr[:, b * PAGES + 4 * c:b * PAGES + 4 * c + 4, :].rearrange("k o n -> k (o n)"), ident[:, :])
                        last.then_inc(tp_done, 1)
                    if b == 0:
                        continue
                    a, s = b - 1, (b - 1) % 2
                    pe.wait_ge(cT_dve, 3 * a + 6)
                    pe.wait_ge(cT_act, 2 * a + 4)
                    pe.wait_ge(S_ready, a + 1)
                    for g in range(4):
                        pe.matmul(scp[s][:, 4 * g:4 * g + 4, :].rearrange("k c h -> k (c h)"), krT[:, s, g, :],
                                  qrd[:, a].rearrange("p c h -> p (c h)"), start=True, stop=True)
                        for c in range(4 * g, 4 * g + 4):
                            last = pe.matmul(scp[s][:, c, :], cT[:, s, c, :], qlat[:, a, :], start=False, stop=True, skip_group_check=True)
                    last.then_inc(sc_done, 1)
                pe.wait_ge(mx_done, DECB + 1)
                pe.transpose(tpb[0][0:BH, 0, :], mxp[:, :, :].rearrange("p b h -> p (b h)"), ident[:, :])
                pe.transpose(tpb[0][0:BH, 1, 0:DECB], SX[:, :], ident[0:DECB, 0:DECB]).then_inc(glob, 1)
                pe.wait_ge(mx_done, DECB + 2)
                pe.matmul(tpb[1][:, 0, 0:BH], ones[:, :], mdiag[:, :], start=True, stop=True).then_inc(glob, 1)
                with pe.Fori(0, DECB // 2) as r:
                    for s in range(2):
                        b = 2 * r + s
                        pe.wait_ge(on_ready, b + 1)
                        pe.wait_ge(pst_ready, b + 1)
                        o = tpb[2 + s][0:H, :, :].rearrange("p a b -> p (a b)")[:, 0:LX]
                        for c in range(PAGES):
                            pe.matmul(o, pst[:, s, c, :], ckv[:, ds(b * PAGES + c, 1), :].rearrange("k o n -> k (o n)"), start=(c == 0), stop=False)
                        pe.matmul(o, pxst[:, s, :], cn[:, :], start=False, stop=True).then_inc(o_done, 1)
                pe.wait_ge(on_ready, DECB + 2)
                for b in range(DECB):
                    last = pe.transpose(tpb[0][:, 0, b * H:(b + 1) * H], on[:, b, :], ident[0:H, 0:H])
                last.then_inc(oT_done, 1)
                pe.wait_ge(ol_ready, 1)
                for h in range(H):
                    last = pe.matmul(misc[0:DECB, h * VD:(h + 1) * VD], ol[:, h, :], wuv[:, h, :], start=True, stop=True)
                last.then_inc(att_done, 1)

            @block.vector
            def _(dve):
                dve.sem_inc(cT_dve, 3)
                dve.sem_inc(on_ready, 2)
                dve.sem_inc(S_ready, 1)
                dve.wait_ge(loaded0, 80)
                dve.wait_ge(prep, 4)
                st = Steps(dve, b_steps, 0, 0)
                st.did(dve.tensor_copy(wuv[:, :, :], wukv[:, :, NOPE:]))
                dve.wait_ge(pe_prep, 1)
                for g in range(2):
                    st.did(dve.tensor_copy(wukT[:, 4 * g:4 * g + 4, :], tpb[g][0:NOPE, :, :]))
                st.did(dve.tensor_copy(cnT[:, :], misc[:, 0:DECB]))
                st.did(dve.tensor_copy(krnT[:, :], misc[0:ROPE, DECB:2 * DECB]))
                st.did(dve.tensor_copy(qr[:, :, :], qTs[NOPE:QK, :, :].rearrange("p h b -> p b h")))
                for g in range(4):
                    st.did(dve.tensor_copy(qrd[32 * g:32 * g + 32, :, g, :], qTs[NOPE:QK, :, :].rearrange("p h b -> p b h")))
                st.wait()
                dve.sem_inc(st_q, 1)
                dve.wait_ge(pe_prep, 2)
                st.did(dve.tensor_copy(qlat[:, :, :], misc[:, 64:64 + BH].rearrange("p (h b) -> p b h", h=H)))
                st.wait()
                dve.sem_inc(st_q, 1)
                dve.wait_ge(pe_prep, 3)
                st.did(dve.tensor_tensor(SX[:, :], misc[0:DECB, 256:256 + BH], own[:, :, :].rearrange("p b h -> p (b h)"), ALU.add))
                st.wait()
                dve.sem_inc(mx_done, 1)
                n0 = st.n
                with dve.Fori(0, DECB // 2) as r:
                    for s in range(2):
                        b = 2 * r + s
                        for g in (0, 2):
                            dve.wait_ge(tp_done, 5 * b + g + 1)
                            dve.tensor_copy(cT[:, s, 4 * g:4 * g + 4, :], tpb[g][:, :, :]).then_inc(cT_dve, 1)
                        dve.wait_ge(tp_done, 5 * b + 5)
                        dve.tensor_copy(krT[:, s, :, :], ktp[:, :, :]).then_inc(cT_dve, 1)
                        dve.wait_ge(S_ready, b + 2)
                        dve.tensor_reduce(mxp[:, ds(b, 1), :].rearrange("p o h -> p (o h)"), S[:, ds(b, 1)].rearrange("p o c h -> p h (o c)"), AX.X, ALU.max).then_inc(mx_done, 1)
                st.n = n0
                dve.wait_ge(glob, 1)
                st.did(dve.tensor_reduce(mcol[:, :], tpb[0][0:BH, 0:2, :].rearrange("p a b -> p (a b)")[:, 0:P + DECB], AX.X, ALU.max))
                st.wait()
                st.did(dve.tensor_scalar(mdiag[:, :], ident[0:BH, 0:BH], mcol[:, 0:1], None, ALU.mult))
                st.wait()
                dve.sem_inc(mx_done, 1)
                dve.wait_ge(glob, 2)
                st.did(dve.tensor_copy(mb[:, :, :].rearrange("p b h -> p (b h)"), tpb[1][:, 0, 0:BH]))
                st.wait()
                dve.wait_ge(S_ready, DECB + 1)
                for b in range(DECB):
                    st.did(dve.tensor_tensor(S[:, b], S[:, b], mb[:, b:b + 1, :].broadcast_to([P, PAGES, H]), ALU.subtract))
                st.did(dve.tensor_tensor(SX[:, :], SX[:, :], mb[0:DECB, :, :].rearrange("p b h -> p (b h)"), ALU.subtract))
                st.wait()
                dve.sem_inc(glob, 1)
                dve.wait_ge(p_ready, 2)
                n1 = st.n

                def weights_of(b, s):
                    dve.tensor_copy(pst[:, s], S[:, ds(b, 1)].rearrange("p o c h -> p (o c) h"))
                    dve.tensor_copy(pxst[:, s, :], SX[:, ds(b * H, H)]).then_inc(pst_ready, 1)

                def outputs_of(b, s):
                    dve.wait_ge(o_done, b + 1)
                    o = tpb[2 + s][0:H, :, :].rearrange("p a b -> p (a b)")[:, 0:LX]
                    dve.reciprocal(ro[:, s:s + 1], o[:, KVR:]).then_inc(b_steps, 1)
                    dve.wait_ge(b_steps, b + n1 + 1)
                    dve.tensor_scalar(on[:, ds(b, 1), :].rearrange("p o n -> p (o n)"), o[:, 0:KVR], ro[:, s:s + 1], None, ALU.mult).then_inc(on_ready, 1)

                weights_of(0, 0)
                with dve.Fori(0, DECB // 2 - 1) as r:
                    for s in range(2):
                        weights_of(2 * r + s + 1, 1 - s)
                        outputs_of(2 * r + s, s)
                weights_of(DECB - 1, 1)
                for s in range(2):
                    outputs_of(DECB - 2 + s, s)
                dve.wait_ge(oT_done, 1)
                dve.tensor_copy(ol[:, :, :], tpb[0][:, 0, 0:BH].rearrange("p (b h) -> p h b", b=DECB)).then_inc(ol_ready, 1)
                dve.wait_ge(att_done, 1)
                dve.tensor_copy(att[:, :], misc[0:DECB, 0:H * VD]).then_inc(att_ready, 1)

            @block.scalar
            def _(act):
                act.sem_inc(cT_act, 2)
                with act.Fori(0, DECB // 2) as r:
                    for s in range(2):
                        b = 2 * r + s
                        for g in (1, 3):
                            act.wait_ge(tp_done, 5 * b + g + 1)
                            act.activation(cT[:, s, 4 * g:4 * g + 4, :], tpb[g][:, :, :], ACT.Copy).then_inc(cT_act, 1)
                        act.wait_ge(sc_done, b + 1)
                        act.activation(S[:, ds(b, 1)].rearrange("p o c h -> p (o c) h"), scp[s][:, :, :], ACT.Copy).then_inc(S_ready, 1)
                act.wait_ge(glob, 3)
                act.activation(S[:, :, :, :].rearrange("p b c h -> p (b c h)"), S[:, :, :, :].rearrange("p b c h -> p (b c h)"), ACT.Exp, scale=SCALE).then_inc(p_ready, 1)
                act.activation(SX[:, :], SX[:, :], ACT.Exp, scale=SCALE).then_inc(p_ready, 1)



def mlstm_sample(nc, d, layer, ident, step, out):
    g, rep, v, o, C, loaded = step.g, step.rep, step.v, step.o, step.C, step.loaded
    with Phase(nc) as ph:
        G = ph.sb("ms_G", [P, G_ALL])
        CQ = ph.sb("ms_CQ", [P, VR, DH])
        VK = ph.sb("ms_VK", [P, VR, DH])
        c = ph.sb("ms_c", [P, 32])
        big = ph.sb("ms_big", [P, 2, DH])
        n1 = ph.sb("ms_n1", [P, DH])
        num = ph.sb("ms_num", [P, VR])
        dv = ph.sb("ms_dv", [P, VR])
        y = ph.sb("ms_y", [P, VR])
        gp = ph.ps("ms_gp", [P, G_ALL])
        repd, steps, acts, out_done = ph.sem("repd"), ph.sem("steps"), ph.sem("acts"), ph.sem("out_done")
        ready = ph.sem("ready")
        col = lambda i: c[:, i:i + 1]
        with nc.Block() as block:
            @block.sync
            def _(sp):
                sp.dma_start(out.mixg[:, :], row_of_layer(d["mix_norm_g"], layer)).then_inc(out.mixg_loaded, 16)
                for t in range(2):
                    out.load_y(sp, d, t)
                out.load_weights(sp, d, layer, out.wout, "w_out", out.wout_loaded)
                sp.wait_ge(ready, 1)
                sp.dma_start(d["Y"][SEQ:SEQ + DECB, CONVW + H * VD:].rearrange("b (q n) -> b q n", n=VR), y[:, :]).then_inc(out_done, 16)
                sp.dma_start(of_layer(d["C_s"], layer).rearrange("r (g m) -> (r g) m", g=VG), C[:, :, :].rearrange("p v n -> p (v n)")).then_inc(out_done, 16)
                sp.dma_start(of_layer(d["n_s"], layer), n1[0:P:VG, :]).then_inc(out_done, 16)
                sp.dma_start(of_layer(d["m_s"], layer).rearrange("(r o) -> r o", o=1), c[0:P:VG, 10:11]).then_inc(out_done, 16)
                sp.wait_ge(out_done, 64)

            @block.tensor
            def _(pe):
                pe.wait_ge(loaded, 192)
                pe.matmul(gp[:, :], rep[:, :], g[:, :], start=True, stop=True).then_inc(repd, 1)

            @block.scalar
            def _(act):
                act.wait_ge(loaded, 192)
                act.activation(o[:, :], o[:, :], ACT.Sigmoid).then_inc(acts, 1)
                act.wait_ge(steps, 5)
                act.activation(col(3), col(2), ACT.Exp).then_inc(acts, 1)
                act.wait_ge(steps, 6)
                act.activation(col(8), col(4), ACT.Ln).then_inc(acts, 1)
                act.wait_ge(steps, 16)
                act.activation(c[:, 13:15], c[:, 11:13], ACT.Exp).then_inc(acts, 1)
                act.activation(col(15), col(10), ACT.Exp, scale=-1.0).then_inc(acts, 1)
                act.wait_ge(steps, 26)
                act.activation(col(20), col(19), ACT.Abs).then_inc(acts, 1)

            @block.vector
            def _(dve):
                st = Steps(dve, steps, 0, 34)

                def do(ins):
                    st.did(ins)
                    st.wait()
                TT, TS = dve.tensor_tensor, dve.tensor_scalar
                dve.wait_ge(repd, 1)
                do(dve.tensor_copy(G[:, :], gp[:, :]))
                q, k, n, i, f, m0 = G[:, G_Q:G_K], G[:, G_K:G_N], G[:, G_N:G_I], G[:, G_I:G_F], G[:, G_F:G_M], G[:, G_M:G_BI]
                do(TT(col(0), i, G[:, G_BI:G_BF], ALU.add))
                do(TT(col(1), f, G[:, G_BF:G_ALL], ALU.add))
                do(TS(col(16), col(1), -1.0, None, ALU.mult))
                do(TT(col(2), col(1), col(16), ALU.min))
                dve.wait_ge(acts, 2)
                do(TS(col(4), col(3), 1.0, None, ALU.add))
                do(TS(col(5), col(4), -1.0, None, ALU.add))
                do(TT(col(5), col(3), col(5), ALU.subtract))
                do(dve.reciprocal(col(6), col(4)))
                do(TT(col(5), col(5), col(6), ALU.mult))
                dve.wait_ge(acts, 3)
                do(TT(col(5), col(5), col(8), ALU.add))
                do(dve.scalar_tensor_tensor(col(7), col(1), 0.0, col(5), ALU.min, ALU.subtract))
                do(TT(col(9), col(7), m0, ALU.add))
                do(TT(col(10), col(9), col(0), ALU.max))
                do(TT(col(11), col(0), col(10), ALU.subtract))
                do(TT(col(12), col(9), col(10), ALU.subtract))
                do(TS(k, k, DH ** -0.5, None, ALU.mult))
                st.did(TT(big[:, 0, :], q, k, ALU.mult))
                do(TT(big[:, 1, :], q, n, ALU.mult))
                do(dve.tensor_reduce(c[:, 17:19], big[:, :, :], AX.X, ALU.add))
                st.did(TT(CQ[:, :, :], C[:, :, :], q.unsqueeze(1).broadcast_to([P, VR, DH]), ALU.mult))
                dve.wait_ge(acts, 5)
                dd, w, em = col(13), col(14), col(15)
                do(TT(col(21), col(17), dd, ALU.mult))
                do(dve.tensor_reduce(num[:, :], CQ[:, :, :], AX.X, ALU.add))
                do(dve.scalar_tensor_tensor(col(19), col(18), w, col(21), ALU.mult, ALU.add))
                do(TS(num[:, :], num[:, :], w, None, ALU.mult))
                do(dve.scalar_tensor_tensor(num[:, :], v[:, :], col(21), num[:, :], ALU.mult, ALU.add))
                dve.wait_ge(acts, 6)
                do(TT(col(22), col(20), em, ALU.max))
                do(dve.reciprocal(col(23), col(22)))
                do(dve.scalar_tensor_tensor(y[:, :], num[:, :], col(23), o[:, :], ALU.mult, ALU.mult))
                do(TS(dv[:, :], v[:, :], dd, None, ALU.mult))
                do(TT(VK[:, :, :], dv[:, :].unsqueeze(2).broadcast_to([P, VR, DH]), k.unsqueeze(1).broadcast_to([P, VR, DH]), ALU.mult))
                do(dve.scalar_tensor_tensor(C[:, :, :], C[:, :, :], w, VK[:, :, :], ALU.mult, ALU.add))
                do(TS(n1[:, :], k, dd, None, ALU.mult))
                do(dve.scalar_tensor_tensor(n1[:, :], n, w, n1[:, :], ALU.mult, ALU.add))
                dve.sem_inc(ready, 1)
                st.end()



NR = NG + NE

STAGES = [("A", 0)] + [st for t in range(1, NT) for st in (("A", t), ("B", t - 1))] + [("B", NT - 1)]


def output_and_route(nc, d, layer, ident, out, h1):
    w_tok, dx = d["sb_weight"], d["sb_row"]
    wout, wpg, mixg, y, y_loaded = out.wout, out.wpg, out.mixg, out.y, out.y_loaded
    with Phase(nc) as ph:
        wpe = ph.sb("op_wpe", [P, 2, D])
        wr = ph.sb("op_wr", [P, KC, NR])
        g1 = ph.sb("op_g1", [P, D])
        b1 = ph.sb("op_b1", [P, D])
        x = ph.sb("op_x", [P, 2, D])
        pp = ph.sb("op_p", [P, 2, DPLE])
        T = ph.sb("op_T", [P, 2, KC, P])
        pT = ph.sb("op_pT", [P, 2, 2, P])
        sq = ph.sb("op_sq", [P, D])
        sig = ph.sb("op_sig", [P, D])
        base = ph.sb("op_base", [P, D])
        ss = ph.sb("op_ss", [P, 16])
        sd = ph.sb("op_sd", [P, 16])
        vx = ph.sb("op_vx", [P, 1])
        dx1 = ph.sb("op_dx1", [P, 1])
        rx = ph.sb("op_rx", [P, 1])
        stats = ph.sb("op_stats", [P, 2, 6])
        mv = ph.sb("op_mv", [P, 2])
        hold = ph.sb("op_hold", [1, 1])
        L = ph.sb("op_L", [P, NT, NR])
        tp = [ph.ps(f"op_tp{i}", [P, 4, P]) for i in range(2)]
        op = [ph.ps(f"op_o{i}", [P, 512]) for i in range(2)]
        gp = [ph.ps(f"op_gp{i}", [P, 512]) for i in range(2)]
        lp = ph.ps("op_lp", [P, 512])
        ptp = ph.ps("op_pt", [P, 2, P])
        c_loaded, r_loaded = ph.sem("c_loaded"), ph.sem("r_loaded")
        x_loaded, base_stored = ph.sem2("x_loaded"), ph.sem("base_stored")
        steps, sq_done, ms_ready, sd_done = (ph.sem(n) for n in ("steps", "sq_done", "ms_ready", "sd_done"))
        y_ready, tp_done, T_dve, T_act, o_done = (ph.sem(n) for n in ("y_ready", "tp_done", "T_dve", "T_act", "o_done"))
        x_ready, var_ready, xd_done = (ph.sem(n) for n in ("x_ready", "var_ready", "xd_done"))
        h1_ready, pt_done, pT_ready, g_done, e_done = (ph.sem(n) for n in ("h1_ready", "pt_done", "pT_ready", "g_done", "e_done"))
        sig_done, mul_done, base_ready = (ph.sem(n) for n in ("sig_done", "mul_done", "base_ready"))
        rb = ph.sb("ro_b", [P, NR])
        idx = ph.sb("ro_idx", [P, NE])
        idxm = ph.sb("ro_idxm", [P, EPG])
        valid = ph.sb("ro_valid", [P, NT])
        before = ph.sb("ro_before", [P, P])
        ones = ph.sb("ro_ones", [P, P])
        part = ph.sb("ro_part", [P, 1])
        m1 = ph.sb("ro_m1", [P, NT])
        m2 = ph.sb("ro_m2", [P, NT])
        f1 = ph.sb("ro_f1", [P, NT])
        gd = ph.sb("ro_gd", [P, NT, NG])
        ge = ph.sb("ro_ge", [P, NT, NG])
        gw = ph.sb("ro_gw", [P, NT])
        ohg = ph.sb("ro_ohg", [P, NT, NG])
        ein = ph.sb("ro_ein", [P, NT, EPG])
        oh = ph.sb("ro_oh", [P, 2, NT, EPG])
        big = ph.sb("ro_big", [P, NT, NE])
        OH = ph.sb("ro_OH", [P, 2, NT, NE])
        OS = ph.sb("ro_OS", [P, NT, NE])
        pre = ph.sb("ro_pre", [P, NT, NE])
        rank = ph.sb("ro_rank", [P, NT, NE])
        cnt = ph.sb("ro_cnt", [P, NE])
        cnti = ph.sb("ro_cnti", [P, NE], I32)
        nb = ph.sb("ro_nb", [P, NE])
        one = ph.sb("ro_one", [P, NE])
        incl = ph.sb("ro_incl", [P, NE])
        start = ph.sb("ro_start", [P, NE])
        bincl = ph.sb("ro_bincl", [P, NE])
        bstart = ph.sb("ro_bstart", [P, NE])
        tx = ph.sb("ro_tx", [P, NE])
        ty = ph.sb("ro_ty", [P, NE])
        sx = ph.sb("ro_sx", [P, NT, NE])
        dxf = ph.sb("ro_dxf", [P, 2, NT])
        tabf = ph.sb("ro_tabf", [P, 4])
        tab = ph.sb("ro_tab", [P, 4], I32)
        r_steps, r_act, r_pe, tab_stored = (ph.sem(n) for n in ("r_steps", "r_act", "r_pe", "tab_stored"))
        r_ready = ph.sem("r_ready")
        with nc.Block() as block:
            @block.sync
            def _(sp):
                def load_x(t):
                    sp.dma_start(x[:, t % 2, :], d["y_all"][rows(t)]).then_inc(x_loaded[t % 2], 16)
                    sp.dma_start(pp[:, t % 2, :], of_layer(d["p_all"], layer)[rows(t)]).then_inc(x_loaded[t % 2], 16)

                for buf, src in ((g1[:, :], row_of_layer(d["ln1_g"], layer)),
                                 (b1[:, :], row_of_layer(d["ln1_b"], layer))):
                    sp.dma_start(buf, src).then_inc(c_loaded, 16)
                load_x(0)
                out.load_weights(sp, d, layer, wpg, "w_pg", out.wpg_loaded)
                load_x(1)
                for buf, src in ((rb[:, :], row_of_layer(d["b_route"], layer)),
                                 (wr[:, :, :].rearrange("p k n -> p (k n)"), of_layer(d["w_route"], layer).rearrange("(p k) n -> p (k n)", k=KC)),
                                 (wpe[:, :, :].rearrange("p k n -> p (k n)"), of_layer(d["w_pe"], layer).rearrange("(p k) n -> p (k n)", k=2)),
                                 (idx[:, :], d["c_idx"]), (valid[:, :], d["c_valid"]), (before[:, :], d["c_before"]), (part[:, :], d["c_part"])):
                    sp.dma_start(buf, src).then_inc(r_loaded, 16)
                for k, (stage, t) in enumerate(STAGES):
                    if t + 2 < NT:
                        sp.wait_ge(tp_done, 2 * (k + 1))
                        if stage == "A":
                            out.load_y(sp, d, t + 2)
                        else:
                            sp.wait_ge(pt_done, t + 1)
                            load_x(t + 2)
                sp.wait_ge(r_ready, 2)
                sp.dma_start(d["BTAB"].rearrange("o (b n) -> (o b) n", n=4), tab[:, :]).then_inc(tab_stored, 16)
                sp.wait_ge(tab_stored, 16)

            @block.tensor
            def _(pe):
                def transposes(k):
                    stage, t = STAGES[k]
                    if stage == "A":
                        pe.wait_ge(y_ready, t + 1)
                    else:
                        pe.wait_ge(h1_ready, t + 1)
                    if k:
                        pe.wait_ge(T_dve, k)
                        pe.wait_ge(T_act, k)
                    for c in range(KC):
                        last = pe.transpose(tp[c // 4][:, c % 4, :], y[:, t % 2, c::KC] if stage == "A" else h1[:, t, c::KC], ident[:, :])
                        if c % 4 == 3:
                            last.then_inc(tp_done, 1)
                    if stage == "B":
                        if t >= 1:
                            pe.wait_ge(pT_ready, t)
                        pe.wait_ge(x_loaded[t % 2], 32 * (t // 2 + 1))
                        for c in range(2):
                            last = pe.transpose(ptp[:, c, :], pp[:, t % 2, c::2], ident[:, :])
                        last.then_inc(pt_done, 1)

                transposes(0)
                late = (0, 1, len(STAGES) - 2)
                for k, (stage, t) in enumerate(STAGES):
                    if k + 1 < len(STAGES) and k not in late:
                        transposes(k + 1)
                    pe.wait_ge(T_dve, k + 1)
                    pe.wait_ge(T_act, k + 1)
                    if stage == "A":
                        pe.wait_ge(out.wout_loaded, 16)
                        if t >= 1:
                            pe.wait_ge(x_ready, 2 * t)
                        if t >= 2:
                            pe.wait_ge(mul_done, t - 1)
                        for n in range(2):
                            for c in range(KC):
                                last = pe.matmul(op[n][:, :], T[:, k % 2, c, :], wout[:, c, n * 512:(n + 1) * 512], start=(c == 0), stop=(c == KC - 1))
                            last.then_inc(o_done, 1)
                    else:
                        pe.wait_ge(out.wpg_loaded, 16)
                        pe.wait_ge(r_loaded, 16 * 7)
                        if t >= 1:
                            pe.wait_ge(sig_done, 2 * t)
                            pe.wait_ge(mul_done, t)
                        for n in range(2):
                            for c in range(KC):
                                last = pe.matmul(gp[n][:, :], T[:, k % 2, c, :], wpg[:, c, n * 512:(n + 1) * 512], start=(c == 0), stop=(c == KC - 1))
                            last.then_inc(g_done, 1)
                        for c in range(KC):
                            last = pe.matmul(lp[:, 0:NR], T[:, k % 2, c, :], wr[:, c, :], start=(c == 0), stop=(c == KC - 1))
                        pe.wait_ge(pT_ready, t + 1)
                        pe.wait_ge(x_ready, 2 * min(t + 2, NT))
                        for n in range(2):
                            for c in range(2):
                                last = pe.matmul(op[n][:, :], pT[:, t % 2, c, :], wpe[:, c, n * 512:(n + 1) * 512], start=(c == 0), stop=(c == 1))
                        last.then_inc(e_done, 1)
                    if k in late:
                        transposes(k + 1)
                pe.wait_ge(r_ready, 1)
                pe.matmul(gp[0][:, 0:NT * NE], ones[:, :], OS[:, :, :].rearrange("p t e -> p (t e)"), start=True, stop=True)
                pe.matmul(gp[1][:, 0:NT * NE], before[:, :], OS[:, :, :].rearrange("p t e -> p (t e)"), start=True, stop=True).then_inc(r_pe, 1)

            @block.scalar
            def _(act):
                def head_squares(t):
                    act.wait_ge(y_loaded[t % 2], 16 * (t // 2 + 1))
                    if t >= 1:
                        act.wait_ge(y_ready, t)
                    act.activation(sq[:, :], y[:, t % 2, :], ACT.Square).then_inc(sq_done, 1)
                    act.wait_ge(ms_ready, t + 1)
                    act.activation(sd[:, :], ss[:, :], ACT.Sqrt).then_inc(sd_done, 1)

                def copy(k):
                    act.wait_ge(tp_done, 2 * k + 2)
                    act.activation(T[:, k % 2, 4:8, :], tp[1][:, :, :], ACT.Copy).then_inc(T_act, 1)
                for t in range(2):
                    head_squares(t)
                    copy(t)
                for t in range(NT + 1):
                    if t < NT:
                        act.wait_ge(var_ready, t + 1)
                        act.activation(dx1[:, :], vx[:, :], ACT.Sqrt).then_inc(xd_done, 1)
                    if t >= 1:
                        if t >= 2:
                            act.wait_ge(mul_done, t - 1)
                        for n in range(2):
                            act.wait_ge(g_done, 2 * (t - 1) + n + 1)
                            act.activation(sig[:, n * 512:(n + 1) * 512], gp[n][:, :], ACT.Sigmoid).then_inc(sig_done, 1)
                    if t < NT:
                        copy(STAGES.index(("B", t)))
                        act.wait_ge(pt_done, t + 1)
                        act.activation(pT[:, t % 2], ptp[:, :, :], ACT.Copy).then_inc(pT_ready, 1)
                    if t >= 1:
                        act.wait_ge(base_ready, t)
                        act.dma_start(d["BASE"][rows(t - 1)], base[:, :]).then_inc(base_stored, 16)
                    if t + 2 < NT:
                        head_squares(t + 2)
                        copy(STAGES.index(("A", t + 2)))
                act.wait_ge(base_stored, 16 * NT)
                act.wait_ge(r_steps, 2)
                act.activation(ge[:, :, :], gd[:, :, :], ACT.Exp).then_inc(r_act, 1)
                act.wait_ge(r_steps, 26)
                act.activation(f1[:, :], m1[:, :], ACT.Exp).then_inc(r_act, 1)

            @block.vector
            def _(dve):
                dve.wait_ge(out.mixg_loaded, 16)
                st = Steps(dve, steps, 0, 0)

                def head_norm(t):
                    s = t % 2
                    y16 = y[:, s, :].rearrange("p (h n) -> p h n", h=16)
                    dve.wait_ge(sq_done, t + 1)
                    st.did(dve.tensor_reduce(ss[:, :], sq[:, :].rearrange("p (h n) -> p h n", h=16), AX.X, ALU.add))
                    st.wait()
                    dve.tensor_scalar(ss[:, :], ss[:, :], 1.0 / 64, RMS_EPS, ALU.mult, ALU.add).then_inc(ms_ready, 1)
                    dve.wait_ge(sd_done, t + 1)
                    st.did(dve.reciprocal(ss[:, :], sd[:, :]))
                    st.wait()
                    st.did(dve.tensor_tensor(y16, y16, ss[:, :].unsqueeze(2).broadcast_to([P, 16, 64]), ALU.mult))
                    st.wait()
                    dve.tensor_tensor(y[:, s, :], y[:, s, :], mixg[:, :], ALU.mult).then_inc(y_ready, 1)

                def copy(k):
                    dve.wait_ge(tp_done, 2 * k + 1)
                    dve.tensor_copy(T[:, k % 2, 0:4, :], tp[0][:, :, :]).then_inc(T_dve, 1)

                def residual_norm(t):
                    s = t % 2
                    dve.wait_ge(x_loaded[s], 32 * (t // 2 + 1))
                    dve.wait_ge(c_loaded, 32)
                    for n in range(2):
                        dve.wait_ge(o_done, 2 * t + n + 1)
                        dve.scalar_tensor_tensor(x[:, s, n * 512:(n + 1) * 512], x[:, s, n * 512:(n + 1) * 512], ALPHA, op[n][:, :], ALU.mult, ALU.add).then_inc(x_ready, 1)
                    dve.wait_ge(x_ready, 2 * t + 2)
                    layer_norm_steps(dve, st, x[:, s, :], stats, mv[:, :], vx[:, :], hold[:, :])
                    st.wait()
                    dve.sem_inc(var_ready, 1)
                    dve.wait_ge(xd_done, t + 1)
                    st.did(dve.reciprocal(rx[:, :], dx1[:, :]))
                    st.wait()
                    st.did(dve.tensor_scalar(h1[:, t, :], x[:, s, :], mv[:, 0:1], rx[:, 0:1], ALU.subtract, ALU.mult))
                    st.wait()
                    st.did(dve.tensor_tensor(h1[:, t, :], h1[:, t, :], g1[:, :], ALU.mult))
                    st.wait()
                    dve.tensor_tensor(h1[:, t, :], h1[:, t, :], b1[:, :], ALU.add).then_inc(h1_ready, 1)

                def gate(t):
                    dve.wait_ge(r_loaded, 16 * 7)
                    dve.wait_ge(e_done, t + 1)
                    st.did(dve.tensor_tensor(L[:, t, :], lp[:, 0:NR], rb[:, :], ALU.add))
                    if t >= 1:
                        dve.wait_ge(base_stored, 16 * t)
                    for n in range(2):
                        half = slice(n * 512, (n + 1) * 512)
                        dve.wait_ge(sig_done, 2 * t + n + 1)
                        st.did(dve.tensor_tensor(base[:, half], op[n][:, :], sig[:, half], ALU.mult))
                    st.wait()
                    dve.sem_inc(mul_done, 1)

                for t in range(2):
                    head_norm(t)
                    copy(t)
                for t in range(NT + 1):
                    if t < NT:
                        residual_norm(t)
                    if t >= 1:
                        gate(t - 1)
                    if t < NT:
                        copy(STAGES.index(("B", t)))
                    if t >= 1:
                        dve.scalar_tensor_tensor(base[:, :], h1[:, t - 1, :], ALPHA, base[:, :], ALU.mult, ALU.add).then_inc(base_ready, 1)
                    if t + 2 < NT:
                        head_norm(t + 2)
                        copy(STAGES.index(("A", t + 2)))
                q = Steps(dve, r_steps, 0, 0)

                def do(ins):
                    q.did(ins)
                    q.wait()
                TT = dve.tensor_tensor
                bt = lambda ap, n: ap.unsqueeze(2).broadcast_to([P, NT, n])
                lg, le = L[:, :, 0:NG], L[:, :, NG:].rearrange("p t (g e) -> p t g e", g=NG)
                st.wait()
                do(dve.tensor_reduce(m1[:, :], lg, AX.X, ALU.max))
                do(TT(gd[:, :, :], lg, bt(m1[:, :], NG), ALU.subtract))
                do(TT(ohg[:, :, :], lg, bt(m1[:, :], NG), ALU.is_equal))
                do(dve.tensor_scalar(idxm[:, :], idx[:, 0:EPG], -64.0, None, ALU.add))
                mid = lambda n: idxm[:, 0:n].unsqueeze(1).broadcast_to([P, NT, n])

                def first_of(onehot, n):
                    do(TT(onehot, onehot, mid(n), ALU.mult))
                    do(dve.tensor_reduce(m2[:, :], onehot, AX.X, ALU.min))
                    do(TT(onehot, mid(n), bt(m2[:, :], n), ALU.is_equal))
                first_of(ohg[:, :, :], NG)
                dve.wait_ge(r_act, 1)
                do(dve.tensor_reduce(gw[:, :], ge[:, :, :], AX.X, ALU.add))
                do(dve.reciprocal(gw[:, :], gw[:, :]))
                for g in range(NG):
                    do(TT(big[:, :, g * EPG:(g + 1) * EPG], le[:, :, g, :], ohg[:, :, g:g + 1].broadcast_to([P, NT, EPG]), ALU.mult))
                do(dve.tensor_reduce(ein[:, :, :], big[:, :, :].rearrange("p t (g e) -> p t e g", g=NG), AX.X, ALU.add))
                do(dve.tensor_reduce(m1[:, :], ein[:, :, :], AX.X, ALU.max))
                do(TT(oh[:, 0], ein[:, :, :], bt(m1[:, :], EPG), ALU.is_equal))
                first_of(oh[:, 0], EPG)
                do(dve.scalar_tensor_tensor(ein[:, :, :], oh[:, 0], NEG, ein[:, :, :], ALU.mult, ALU.add))
                do(dve.tensor_reduce(f1[:, :], ein[:, :, :], AX.X, ALU.max))
                do(TT(oh[:, 1], ein[:, :, :], bt(f1[:, :], EPG), ALU.is_equal))
                first_of(oh[:, 1], EPG)
                do(TT(m1[:, :], f1[:, :], m1[:, :], ALU.subtract))
                assert q.n == 26
                for k in range(2):
                    for g in range(NG):
                        q.did(TT(OH[:, k, :, g * EPG:(g + 1) * EPG], oh[:, k], ohg[:, :, g:g + 1].broadcast_to([P, NT, EPG]), ALU.mult))
                q.wait()
                for k in range(2):
                    q.did(TT(OH[:, k], OH[:, k], bt(valid[:, :], NE), ALU.mult))
                q.did(dve.memset(ones[:, :], 1.0))
                q.did(dve.memset(one[:, :], 1.0))
                q.wait()
                do(TT(OS[:, :, :], OH[:, 0], OH[:, 1], ALU.add))
                dve.sem_inc(r_ready, 1)
                dve.wait_ge(r_act, 2)
                do(dve.tensor_scalar(m1[:, :], f1[:, :], 1.0, None, ALU.add))
                do(dve.reciprocal(m1[:, :], m1[:, :]))
                do(TT(w_tok[:, 0, :], m1[:, :], gw[:, :], ALU.mult))
                do(TT(w_tok[:, 1, :], w_tok[:, 0, :], f1[:, :], ALU.mult))
                dve.wait_ge(r_pe, 1)
                q.did(dve.memset(pre[:, 0, :], 0.0))
                for t in range(1, NT):
                    q.wait()
                    q.did(TT(pre[:, t, :], gp[0][:, (t - 1) * NE:t * NE], pre[:, t - 1, :], ALU.add))
                q.wait()
                do(TT(cnt[:, :], gp[0][:, (NT - 1) * NE:NT * NE], pre[:, NT - 1, :], ALU.add))
                do(TT(rank[:, :, :].rearrange("p t e -> p (t e)"), gp[1][:, 0:NT * NE], pre[:, :, :].rearrange("p t e -> p (t e)"), ALU.add))
                do(dve.tensor_scalar(cnti[:, :], cnt[:, :], float(P - 1), None, ALU.add))
                do(dve.tensor_scalar(cnti[:, :], cnti[:, :], 7, None, ALU.arith_shift_right))
                do(dve.tensor_copy(nb[:, :], cnti[:, :]))
                do(dve.tensor_tensor_scan(incl[:, :], one[:, :], cnt[:, :], 0.0, ALU.mult, ALU.add))
                do(dve.tensor_tensor_scan(bincl[:, :], one[:, :], nb[:, :], 0.0, ALU.mult, ALU.add))
                do(TT(start[:, :], incl[:, :], cnt[:, :], ALU.subtract))
                do(TT(bstart[:, :], bincl[:, :], nb[:, :], ALU.subtract))
                do(dve.tensor_scalar(bstart[:, :], bstart[:, :], float(P), None, ALU.mult))
                do(TT(sx[:, :, :], rank[:, :, :], start[:, :].unsqueeze(1).broadcast_to([P, NT, NE]), ALU.add))
                for k in range(2):
                    do(TT(big[:, :, :], sx[:, :, :], OH[:, k], ALU.mult))
                    do(dve.tensor_reduce(dxf[:, k, :], big[:, :, :], AX.X, ALU.add))
                do(dve.tensor_copy(dx[:, :, :], dxf[:, :, :]))
                do(dve.tensor_scalar(tx[:, :], bincl[:, :], part[:, 0:1], None, ALU.is_le))
                do(dve.tensor_reduce(tabf[:, 0:1], tx[:, :], AX.X, ALU.add))
                do(dve.tensor_scalar(tx[:, :], idx[:, :], tabf[:, 0:1], None, ALU.is_equal))
                do(TT(ty[:, :], start[:, :], bstart[:, :], ALU.subtract))
                do(TT(ty[:, :], ty[:, :], tx[:, :], ALU.mult))
                do(dve.tensor_reduce(tabf[:, 1:2], ty[:, :], AX.X, ALU.add))
                do(dve.scalar_tensor_tensor(tabf[:, 1:2], part[:, :], float(P), tabf[:, 1:2], ALU.mult, ALU.add))
                do(dve.tensor_copy(tabf[:, 2:3], bincl[:, NE - 1:NE]))
                do(dve.memset(tabf[:, 3:4], 0.0))
                do(dve.tensor_copy(tab[:, :], tabf[:, :]))
                dve.sem_inc(r_ready, 1)



SLOTS = 4


def block_turns(eng, blocks):
    with eng.Fori(0, -(-blocks // SLOTS)) as r:
        for slot in range(SLOTS):
            yield SLOTS * r + slot, slot, r


def overlapped_turns(eng, used, step):
    assert 2 * (SEQ + DECB) > 2 * P
    step((0, 0, 0), None, (1, 1, 0))
    with eng.Fori(0, -(-BLOCKS // SLOTS)) as r:
        with eng.If(SLOTS * r < used):
            for i in range(SLOTS):
                b = SLOTS * r + i + 1
                before, now, after = ((b + k, (i + 1 + k) % SLOTS, r + (i + 1 + k) // SLOTS) for k in (-1, 0, 1))
                with eng.If(b + 1 < used):
                    step(now, before, after)
                with eng.If(b + 1 == used):
                    step(now, before, None)
                with eng.If(b == used):
                    step(None, before, None)


def experts(nc, d, layer, ident, h1):
    with Phase(nc) as ph:
        tab = ph.sb("ex_tab", [1, 4 * P], I32)
        wgu = ph.sb("ex_wgu", [P, SLOTS, 2, KC, DE])
        wd = ph.sb("ex_wd", [P, SLOTS, 2, D])
        x = ph.sb("ex_x", [P, SLOTS, D])
        xT = ph.sb("ex_xT", [P, 2, KC, P])
        sil = ph.sb("ex_sil", [P, 2, DE])
        h = ph.sb("ex_h", [P, 2, DE])
        hT = ph.sb("ex_hT", [P, 2, 2, P])
        y = ph.sb("ex_y", [P, 2, D])
        tp = [ph.ps(f"ex_tp{i}", [P, 4, P]) for i in range(2)]
        gu = [ph.ps(f"ex_gu{i}", [P, 2, DE]) for i in range(2)]
        htp = [ph.ps(f"ex_ht{i}", [P, 2, P]) for i in range(2)]
        yp = [ph.ps(f"ex_yp{i}", [P, 512]) for i in range(2)]
        tab_loaded = ph.sem("tab_loaded")
        loaded = [ph.sem(f"loaded{i}") for i in range(SLOTS)]
        stored = ph.sem2("stored")
        slot_free, tp_done, xT_dve, gu_done = (ph.sem(n) for n in ("slot_free", "tp_done", "xT_dve", "gu_done"))
        sil_done, h_ready, ht_done, hT_ready, y_done = (ph.sem(n) for n in ("sil_done", "h_ready", "ht_done", "hT_ready", "y_done"))
        y_dve, last_stored = ph.sem("y_dve"), ph.sem("last_stored")
        dx, scattered = d["sb_row"], d["sw"]["scattered"]
        SCATTERS = 16 * 2 * NT
        TOTAL = 2
        assert SLOTS % 2 == 0
        with nc.Block() as block:
            @block.sync
            def _(sp):
                sp.dma_start(tab[:, :], d["BTAB"]).then_inc(tab_loaded, 16)
                sp.wait_ge(tab_loaded, 16)
                used = sp.value_load(tab[0:1, TOTAL:TOTAL + 1], min_val=0, max_val=BLOCKS)

                def expert_of(b):
                    return sp.value_load(tab[0:1, ds(4 * b, 1)], min_val=0, max_val=NE - 1)

                def row_of(b):
                    return sp.value_load(tab[0:1, ds(4 * b + 1, 1)], min_val=0, max_val=XROWS - P)

                def load_rows(row, s):
                    sp.dma_start(x[:, s, :], d["XR"][ds(row, P)]).then_inc(loaded[s], 16)

                def load_weights(e, s):
                    for n, w in enumerate(("e_gate", "e_up")):
                        sp.dma_start(wgu[:, s, n].rearrange("p k n -> p (k n)"),
                                     d[w][ds(layer, 1), ds(e, 1)].rearrange("l e (p k) n -> (l e p) (k n)", k=KC)).then_inc(loaded[s], 16)
                    sp.dma_start(wd[:, s].rearrange("p k n -> p (k n)"),
                                 d["e_down"][ds(layer, 1), ds(e, 1)].rearrange("l e (p k) n -> (l e p) (k n)", k=2)).then_inc(loaded[s], 16)

                assert 2 * (SEQ + DECB) > SLOTS * P
                load_weights(expert_of(0), 0)
                row = row_of(0)
                sp.wait_ge(scattered, SCATTERS * (layer + 1))
                load_rows(row, 0)
                for b in range(1, SLOTS):
                    load_rows(row_of(b), b)
                    load_weights(expert_of(b), b)
                with sp.Fori(1, -(-BLOCKS // SLOTS)) as r:
                    for s in range(SLOTS):
                        b = SLOTS * r + s
                        with sp.If(b < used):
                            e, row = expert_of(b), row_of(b)
                            sp.wait_ge(slot_free, b + 1)
                            load_rows(row, s)
                            load_weights(e, s)

            @block.gpsimd
            def _(pool):
                for t in range(NT):
                    m = P if t < TP else DECB
                    for k in range(2):
                        pool.indirect_dma_start(d["XR"], bass.IndirectOffsetOnAxis(ap=dx[0:m, k, t:t + 1], axis=0),
                                                h1[0:m, t, :], None, bounds_check=XROWS - P - 1, oob_is_err=True).then_inc(scattered, 16)

            @block.tensor
            def _(pe):
                pe.sem_inc(slot_free, SLOTS)
                pe.wait_ge(tab_loaded, 16)
                used = pe.value_load(tab[0:1, TOTAL:TOTAL + 1], min_val=0, max_val=BLOCKS)

                def transposes(b, s, r):
                    pe.wait_ge(loaded[s], 64 * (r + 1))
                    pe.wait_ge(xT_dve, 2 * b + 2)
                    for c in range(KC):
                        last = pe.transpose(tp[c // 4][:, c % 4, :], x[:, s, c::KC], ident[:, :])
                        if c % 4 == 3:
                            last.then_inc(tp_done, 1)

                def step(now, before, after):
                    if now:
                        b, s, r = now
                        pe.wait_ge(xT_dve, 2 * b + 4)
                        for c in range(KC):
                            last = pe.matmul(gu[s % 2][:, :, :], xT[:, s % 2, c, :], wgu[:, s, :, c, :], start=(c == 0), stop=(c == KC - 1))
                        last.then_inc(gu_done, 1)
                    if after:
                        transposes(*after)
                    if before:
                        b0, s0, r0 = before
                        pe.wait_ge(y_dve, 2 * b0 + 2)
                        pe.wait_ge(hT_ready, b0 + 1)
                        for n in range(2):
                            for c in range(2):
                                last = pe.matmul(yp[n][:, :], hT[:, s0 % 2, c, :], wd[:, s0, c, n * 512:(n + 1) * 512], start=(c == 0), stop=(c == 1))
                            if n == 0:
                                last.then_inc(y_done, 1)
                        last.then_inc(slot_free, 1)
                    if now:
                        pe.wait_ge(h_ready, b + 1)
                        for c in range(2):
                            last = pe.transpose(htp[s % 2][:, c, :], h[:, s % 2, c::2], ident[:, :])
                        last.then_inc(ht_done, 1)
                transposes(0, 0, 0)
                overlapped_turns(pe, used, step)

            @block.vector
            def _(dve):
                dve.sem_inc(xT_dve, 2)
                dve.sem_inc(y_dve, 2)
                dve.wait_ge(tab_loaded, 16)
                used = dve.value_load(tab[0:1, TOTAL:TOTAL + 1], min_val=0, max_val=BLOCKS)

                def rows_turned(b, s, r):
                    for n in range(2):
                        dve.wait_ge(tp_done, 2 * b + n + 1)
                        dve.tensor_copy(xT[:, s % 2, 4 * n:4 * n + 4, :], tp[n][:, :, :]).then_inc(xT_dve, 1)

                def step(now, before, after):
                    if now:
                        b, s, r = now
                        dve.wait_ge(sil_done, b + 1)
                        dve.tensor_tensor(h[:, s % 2, :], sil[:, s % 2, :], gu[s % 2][:, 1, :], ALU.mult).then_inc(h_ready, 1)
                    if after:
                        rows_turned(*after)
                    if before:
                        b0, s0, r0 = before
                        dve.wait_ge(stored[s0 % 2], 16 * (SLOTS // 2 * r0 + s0 // 2 + 1))
                        dve.wait_ge(y_done, b0 + 1)
                        dve.tensor_copy(y[:, s0 % 2, 0:512], yp[0][:, :]).then_inc(y_dve, 1)
                        dve.wait_ge(slot_free, b0 + SLOTS + 1)
                        dve.tensor_copy(y[:, s0 % 2, 512:], yp[1][:, :]).then_inc(y_dve, 1)
                    if now:
                        dve.wait_ge(ht_done, b + 1)
                        dve.tensor_copy(hT[:, s % 2, :, :], htp[s % 2][:, :, :]).then_inc(hT_ready, 1)
                rows_turned(0, 0, 0)
                overlapped_turns(dve, used, step)

            @block.scalar
            def _(act):
                for s in range(2):
                    act.sem_inc(stored[s], 16)
                act.wait_ge(tab_loaded, 16)
                used = act.value_load(tab[0:1, TOTAL:TOTAL + 1], min_val=0, max_val=BLOCKS)

                def step(now, before, after):
                    if now:
                        b, s, r = now
                        act.wait_ge(gu_done, b + 1)
                        act.activation(sil[:, s % 2, :], gu[s % 2][:, 0, :], ACT.Silu).then_inc(sil_done, 1)
                    if before:
                        b0, s0, r0 = before
                        turn = SLOTS // 2 * r0 + s0 // 2
                        row = act.value_load(tab[0:1, ds(4 * b0 + 1, 1)], min_val=0, max_val=XROWS - P)
                        act.wait_ge(y_dve, 2 * b0 + 4)
                        act.wait_ge(stored[1 - s0 % 2], 16 * (turn + s0 % 2 + 1))
                        act.dma_start(d["YR"][ds(row, P)], y[:, s0 % 2, :]).then_inc(stored[s0 % 2], 16)
                overlapped_turns(act, used, step)
                act.wait_ge(stored[0], 16 * ((used + 1) // 2) + 16)
                act.wait_ge(stored[1], 16 * (used // 2) + 16)
                act.sem_inc(last_stored, 1)





def decoder_trunk(nc, d):
    for name, shape in (("Z", (PAD + ROWS, N_IN)), ("XR", (XROWS, D)), ("YR", (XROWS, D)),
                        ("Y", (ROWS, D)), ("QT", (H, QK, ROWS)), ("KT", (H, QK, ROWS)), ("V", (ROWS, H * VD)),
                        ("BASE", (ROWS, D)), ("BTAB", (1, 4 * P))):
        d[name] = nc.dram_tensor(f"scratch_{name}", shape, I32 if name == "BTAB" else F32, kind="Internal").ap()
    with ExitStack() as ctx:
        ident = ctx.enter_context(nc.sbuf_tensor("ident", [P, P], F32))
        d["sb_weight"] = ctx.enter_context(nc.sbuf_tensor("route_weight", [P, 2, NT], F32))
        d["sb_row"] = ctx.enter_context(nc.sbuf_tensor("route_row", [P, 2, NT], mybir.dt.uint32))
        d["sw"] = {n: ctx.enter_context(nc.semaphore(f"sw_{n}")) for n in
                   ("zero_stored", "cv_w", "cv_in", "cv_out", "cv_state", "scattered", "gathered0", "gathered1", "gathered2")}
        with Phase(nc) as ph:
            got = ph.sem("ident_loaded")
            with nc.Block() as block:
                @block.sync
                def _(sp):
                    sp.dma_start(ident[:, :], d["c_ident"]).then_inc(got, 16)
                    sp.wait_ge(got, 16)
        stream_and_project(nc, d, None, ident)
        with nc.Fori(0, LAYERS) as layer:
            with Phase(nc) as samples:
                step = StepInputs(samples)
                with Phase(nc) as prompt:
                    cache = PagedCache(prompt)
                    mla_prepare(nc, d, layer, ident, cache)
                    attention(nc, d, layer, ident, cache)
                    mlstm_prompt(nc, d, layer, ident, cache)
                    sample_attention(nc, d, layer, ident, cache, step)
                with Phase(nc) as rest:
                    h1 = rest.sb("h1", [P, NT, D])
                    with Phase(nc) as inputs:
                        out = OutputInputs(inputs)
                        mlstm_sample(nc, d, layer, ident, step, out)
                        output_and_route(nc, d, layer, ident, out, h1)
                    experts(nc, d, layer, ident, h1)
            stream_and_project(nc, d, layer, ident)



LAYERS = DEPTH


def constants():
    import numpy as np
    inv = (np.float32(10000.0) ** (-np.arange(HALF, dtype=np.float32) / np.float32(HALF))).astype(np.float32)
    pos = np.concatenate([np.arange(SEQ), np.full(P, PAST)]).astype(np.float32)
    ang = (pos[:, None] * inv).astype(np.float32)
    q, k = np.arange(P)[:, None], np.arange(P)[None, :]
    return {
        "c_ident": np.eye(P, dtype=np.float32),
        "c_trig": np.concatenate([np.cos(ang), np.sin(ang)], 1).astype(np.float32),
        "c_causal": np.where(k <= q, 0.0, NEG).astype(np.float32),
        "c_causalT": np.where(q <= k, 0.0, NEG).astype(np.float32),
        "c_own": np.repeat(np.where(np.eye(DECB) > 0, 0.0, NEG).astype(np.float32), H, 1),
        "c_rep": np.repeat(np.eye(DECB * NH, dtype=np.float32), 4, 1),
        "c_idx": np.tile(np.arange(NE, dtype=np.float32), (P, 1)),
        "c_valid": (np.arange(NT)[None, :] * P + q < SEQ + DECB).astype(np.float32),
        "c_part": np.arange(P, dtype=np.float32)[:, None],
        "c_before": (q < k).astype(np.float32),
        "c_headrow": np.repeat(np.eye(NH, dtype=np.float32)[:, :, None], P, 2),
    }


OUTS = [("y_all", (ROWS, D)), ("ckv_all", (DEPTH, ROWS, KVR)), ("krope_all", (DEPTH, ROWS, ROPE)),
        ("conv_p", (DEPTH, 2, CONVW)), ("C_p", (DEPTH, NH, DH, DH)), ("n_p", (DEPTH, NH, DH)), ("m_p", (DEPTH, NH)),
        ("conv_s", (DEPTH, DECB, 2, CONVW)), ("C_s", (DEPTH, DECB * NH, DH * DH)), ("n_s", (DEPTH, DECB * NH, DH)),
        ("m_s", (DEPTH, DECB * NH))]
PLAIN = ["cache_ckv", "cache_krope", "state_conv", "state_mlstm_C", "state_mlstm_n", "state_mlstm_m", "page_table",
         "ln0_g", "ln0_b", "w_in", "conv_w", "q_norm_g", "w_uq", "kv_norm_g", "w_ukv", "mlstm_gate_b", "mix_norm_g",
         "w_out", "ln1_g", "ln1_b", "e_gate", "e_up", "e_down", "w_pe", "w_pg", "ln2_g", "ln2_b"]


def laid_out(inputs):
    import numpy as np
    a = {n: np.ascontiguousarray(inputs[n]) for n in PLAIN}
    rest = ROWS - SEQ - DECB
    xp, xs = np.asarray(inputs["x_prompt"])[0], np.asarray(inputs["x_sample"])[:, 0]
    a["x_all"] = np.concatenate([xp, xs, np.zeros((rest, D), np.float32)], 0)
    pp, ps = np.asarray(inputs["p_prompt"])[:, 0], np.asarray(inputs["p_sample"])[:, :, 0]
    a["p_all"] = np.concatenate([pp, ps, np.zeros((DEPTH, rest, DPLE), np.float32)], 1)
    a["w_route"] = np.concatenate([np.asarray(inputs["w_group"]), np.asarray(inputs["w_expert"])], 2)
    a["b_route"] = np.concatenate([np.asarray(inputs["b_group"]), np.asarray(inputs["b_expert"])], 1)
    a["page_table"] = np.asarray(inputs["page_table"]).reshape(1, DECB * PAGES)
    a.update(constants())
    return a


def kernel(**inputs):
    import concourse.bacc as _bacc
    from concourse.bass_utils import run_bass_kernel_spmd as _run

    arrays = laid_out(inputs)
    nc = _bacc.Bacc("TRN2", target_bir_lowering=False, num_devices=1)
    d = {n: nc.dram_tensor(f"in_{n}", a.shape, mybir.dt.from_np(a.dtype), kind="ExternalInput").ap()
         for n, a in arrays.items()}
    for n, shape in OUTS:
        d[n] = nc.dram_tensor(f"out_{n}", shape, F32, kind="ExternalOutput").ap()
    decoder_trunk(nc, d)
    r = _run(nc, [{f"in_{n}": a for n, a in arrays.items()}], core_ids=[0])
    o = {n: r.results[0][f"out_{n}"] for n, _ in OUTS}
    y, ckv, kr, dec = o["y_all"], o["ckv_all"], o["krope_all"], SEQ + DECB
    return (y[None, :SEQ], y[SEQ:dec, None], ckv[:, None, :SEQ], kr[:, None, :SEQ], o["conv_p"][:, None],
            o["C_p"][:, None], o["n_p"][:, None], o["m_p"][:, None],
            ckv[:, SEQ:dec, None], kr[:, SEQ:dec, None], o["conv_s"],
            o["C_s"].reshape(DEPTH, DECB, NH, DH, DH), o["n_s"].reshape(DEPTH, DECB, NH, DH),
            o["m_s"].reshape(DEPTH, DECB, NH))
```
